# Optimizing a Trainium2 kernel written in Bass

```python
import jax, jax.numpy as jnp
from jax import lax
import numpy as np
import math

D_MODEL = 1024
BATCH = 1
SEQ = 512
DEPTH = 2

GRID_W = 64
CTX_LEN = 256
MLA_HEADS = 8
MLA_NOPE = 64
MLA_ROPE = 32
MLA_V = 64
MLA_QK = MLA_NOPE + MLA_ROPE
MLA_WIDTH = MLA_HEADS * MLA_V
Q_RANK = 256
KV_RANK = 128
SC_WIDTH = 256
SC_K = 3
CF_WIDTH = 256
CF_K = 31
D_MIX = MLA_WIDTH + SC_WIDTH + CF_WIDTH
IN_SPLITS = (Q_RANK, KV_RANK, MLA_ROPE, MLA_WIDTH, SC_WIDTH, SC_WIDTH, SC_WIDTH, SC_WIDTH, 2 * CF_WIDTH, CF_WIDTH)
D_IN = Q_RANK + KV_RANK + MLA_ROPE + MLA_WIDTH + 4 * SC_WIDTH + 3 * CF_WIDTH
ROPE_THETA = 10000.0
Q_BLOCK = 128
EPS = 1e-6
LN_EPS = 1e-5


def rms_norm(x, w):
    xf = x.astype(jnp.float32)
    y = xf * lax.rsqrt(jnp.mean(xf * xf, axis=-1, keepdims=True) + EPS)
    return (y * w.astype(jnp.float32)).astype(x.dtype)

def layer_norm(x, w, b):
    xf = x.astype(jnp.float32)
    mu = jnp.mean(xf, axis=-1, keepdims=True)
    var = jnp.mean(jnp.square(xf - mu), axis=-1, keepdims=True)
    y = (xf - mu) * lax.rsqrt(var + LN_EPS)
    return (y * w.astype(jnp.float32) + b.astype(jnp.float32)).astype(x.dtype)

def axial_rope_tables(T):
    rows = T // GRID_W
    pos_r = jnp.repeat(jnp.arange(rows, dtype=jnp.float32), GRID_W)
    pos_c = jnp.tile(jnp.arange(GRID_W, dtype=jnp.float32), rows)
    n_freq = MLA_ROPE // 4
    inv = ROPE_THETA ** (-jnp.arange(n_freq, dtype=jnp.float32) / n_freq)
    ang = jnp.concatenate([pos_r[:, None] * inv, pos_c[:, None] * inv], axis=-1)
    return jnp.cos(ang), jnp.sin(ang)

def apply_rope(x, cos, sin):
    half = x.shape[-1] // 2
    x1, x2 = x[..., :half], x[..., half:]
    cs = cos[None, :, None, :].astype(x.dtype)
    sn = sin[None, :, None, :].astype(x.dtype)
    return jnp.concatenate([x1 * cs - x2 * sn, x2 * cs + x1 * sn], axis=-1)

def dwconv(x, w):
    return lax.conv_general_dilated(x, w[:, None, :], window_strides=(1,), padding='SAME',
                                    dimension_numbers=('NWC', 'WIO', 'NWC'),
                                    feature_group_count=x.shape[-1])

def split_in(u):
    offsets = np.cumsum(IN_SPLITS)[:-1].tolist()
    return jnp.split(u, offsets, axis=-1)

def mla_q(cq, q_norm_w, w_uq, q_head_norm_w, cos, sin):
    B, T, _ = cq.shape
    q = (rms_norm(cq, q_norm_w) @ w_uq).reshape(B, T, MLA_HEADS, MLA_QK)
    q = rms_norm(q, q_head_norm_w)
    if cos is not None:
        q = jnp.concatenate([q[..., :MLA_NOPE], apply_rope(q[..., MLA_NOPE:], cos, sin)], axis=-1)
    return q

def mla_kv(ckv, kr, kv_norm_w, w_ukv, k_head_norm_w, cos, sin):
    B, T, _ = ckv.shape
    kv = (rms_norm(ckv, kv_norm_w) @ w_ukv).reshape(B, T, MLA_HEADS, MLA_NOPE + MLA_V)
    k_nope, v = kv[..., :MLA_NOPE], kv[..., MLA_NOPE:]
    k_rope = jnp.broadcast_to(kr[:, :, None, :], (B, T, MLA_HEADS, MLA_ROPE))
    k = rms_norm(jnp.concatenate([k_nope, k_rope], axis=-1), k_head_norm_w)
    if cos is not None:
        k = jnp.concatenate([k[..., :MLA_NOPE], apply_rope(k[..., MLA_NOPE:], cos, sin)], axis=-1)
    return k, v

def attend(q, k, v):
    B, T, H, Dq = q.shape
    nb = T // Q_BLOCK
    qb = q.reshape(B, nb, Q_BLOCK, H, Dq).transpose(1, 0, 2, 3, 4)
    sm_scale = MLA_QK ** -0.5

    def one_block(qi):
        s = jnp.einsum('bqhd,bkhd->bhqk', qi, k).astype(jnp.float32) * sm_scale
        p = jax.nn.softmax(s, axis=-1).astype(v.dtype)
        return jnp.einsum('bhqk,bkhd->bqhd', p, v)

    o = lax.map(one_block, qb)
    return o.transpose(1, 0, 2, 3, 4).reshape(B, T, H * MLA_V)

def mixer_branches(parts, attn, sc_conv_w, cf_conv_w, cf_conv_b, cf_ln_w, cf_ln_b, cf_pw_w, cf_pw_b):
    _, _, _, g_a, sc_in, sc_b, sc_c, g_b, cf_glu, g_c = parts
    y_a = attn * jax.nn.silu(g_a)
    y_b = sc_b * dwconv(sc_c * sc_in, sc_conv_w) * jax.nn.silu(g_b)
    a, g = jnp.split(cf_glu, 2, axis=-1)
    z = dwconv(a * jax.nn.sigmoid(g), cf_conv_w) + cf_conv_b
    z = jax.nn.silu(layer_norm(z, cf_ln_w, cf_ln_b))
    y_c = (z @ cf_pw_w + cf_pw_b) * jax.nn.silu(g_c)
    return jnp.concatenate([y_a, y_b, y_c], axis=-1)

def first_inputs(seed: int = 0) -> dict:
    key = jax.random.key(seed)
    ks = jax.random.split(key, 24)
    f32 = jnp.float32
    nrm = lambda k, shape, s: jax.random.normal(k, shape, f32) * s
    return {
        'x': nrm(ks[0], (BATCH, SEQ, D_MODEL), 1.0),
        'c': nrm(ks[1], (BATCH, D_MODEL), 1.0),
        'ctx': nrm(ks[2], (BATCH, CTX_LEN, D_MODEL), 1.0),
        'c_ctx': nrm(ks[3], (D_MODEL,), 1.0),
        'norm_w': 1.0 + nrm(ks[4], (DEPTH, D_MODEL), 0.02),
        'w_mod': nrm(ks[5], (DEPTH, D_MODEL, 3 * D_MODEL), D_MODEL ** -0.5),
        'b_mod': nrm(ks[6], (DEPTH, 3 * D_MODEL), 0.02),
        'w_in': nrm(ks[7], (DEPTH, D_MODEL, D_IN), D_MODEL ** -0.5),
        'q_norm_w': 1.0 + nrm(ks[8], (DEPTH, Q_RANK), 0.02),
        'w_uq': nrm(ks[9], (DEPTH, Q_RANK, MLA_HEADS * MLA_QK), Q_RANK ** -0.5),
        'kv_norm_w': 1.0 + nrm(ks[10], (DEPTH, KV_RANK), 0.02),
        'w_ukv': nrm(ks[11], (DEPTH, KV_RANK, MLA_HEADS * (MLA_NOPE + MLA_V)), KV_RANK ** -0.5),
        'q_head_norm_w': 1.0 + nrm(ks[12], (DEPTH, MLA_QK), 0.02),
        'k_head_norm_w': 1.0 + nrm(ks[13], (DEPTH, MLA_QK), 0.02),
        'sc_conv_w': nrm(ks[14], (DEPTH, SC_K, SC_WIDTH), SC_K ** -0.5),
        'cf_conv_w': nrm(ks[15], (DEPTH, CF_K, CF_WIDTH), CF_K ** -0.5),
        'cf_conv_b': nrm(ks[16], (DEPTH, CF_WIDTH), 0.02),
        'cf_ln_w': 1.0 + nrm(ks[17], (DEPTH, CF_WIDTH), 0.02),
        'cf_ln_b': nrm(ks[18], (DEPTH, CF_WIDTH), 0.02),
        'cf_pw_w': nrm(ks[19], (DEPTH, CF_WIDTH, CF_WIDTH), CF_WIDTH ** -0.5),
        'cf_pw_b': nrm(ks[20], (DEPTH, CF_WIDTH), 0.02),
        'w_out': nrm(ks[21], (DEPTH, D_MIX, D_MODEL), D_MIX ** -0.5),
    }

def first_block(x, c, ctx, c_ctx, norm_w, w_mod, b_mod, w_in, q_norm_w, w_uq, kv_norm_w, w_ukv,
              q_head_norm_w, k_head_norm_w, sc_conv_w, cf_conv_w, cf_conv_b, cf_ln_w, cf_ln_b,
              cf_pw_w, cf_pw_b, w_out):
    T = x.shape[1]
    cos, sin = axial_rope_tables(T)
    xc = ctx
    for l in range(DEPTH):
        last = l == DEPTH - 1
        shift, scale, gate = jnp.split(jax.nn.silu(c) @ w_mod[l] + b_mod[l], 3, axis=-1)
        shift_c, scale_c, gate_c = jnp.split(jax.nn.silu(c_ctx) @ w_mod[l] + b_mod[l], 3, axis=-1)
        h = rms_norm(x, norm_w[l]) * (1.0 + scale[:, None, :]) + shift[:, None, :]
        hc = rms_norm(xc, norm_w[l]) * (1.0 + scale_c) + shift_c

        parts = split_in(h @ w_in[l])
        q = mla_q(parts[0], q_norm_w[l], w_uq[l], q_head_norm_w[l], cos, sin)
        k, v = mla_kv(parts[1], parts[2], kv_norm_w[l], w_ukv[l], k_head_norm_w[l], cos, sin)

        if last:
            ckv_c, kr_c = jnp.split(hc @ w_in[l][:, Q_RANK:Q_RANK + KV_RANK + MLA_ROPE], [KV_RANK], axis=-1)
            parts_c = None
        else:
            parts_c = split_in(hc @ w_in[l])
            ckv_c, kr_c = parts_c[1], parts_c[2]
        kc, vc = mla_kv(ckv_c, kr_c, kv_norm_w[l], w_ukv[l], k_head_norm_w[l], None, None)

        attn = attend(q, jnp.concatenate([kc, k], axis=1), jnp.concatenate([vc, v], axis=1))
        y = mixer_branches(parts, attn, sc_conv_w[l], cf_conv_w[l], cf_conv_b[l], cf_ln_w[l],
                           cf_ln_b[l], cf_pw_w[l], cf_pw_b[l])
        x_new = x + gate[:, None, :] * (y @ w_out[l])

        if not last:
            qc = mla_q(parts_c[0], q_norm_w[l], w_uq[l], q_head_norm_w[l], None, None)
            attn_c = attend(qc, kc, vc)
            yc = mixer_branches(parts_c, attn_c, sc_conv_w[l], cf_conv_w[l], cf_conv_b[l], cf_ln_w[l],
                                cf_ln_b[l], cf_pw_w[l], cf_pw_b[l])
            xc = xc + gate_c * (yc @ w_out[l])
        x = x_new
    return x


DEPTH_2 = 1

HEAD_DIM = 64
N_HEADS_DIL = 8
N_HEADS_FOX = 8
D_DIL = N_HEADS_DIL * HEAD_DIM
D_FOX = N_HEADS_FOX * HEAD_DIM
D_MIX_2 = D_DIL + D_FOX
D_IN_2 = 3 * D_DIL + 3 * D_FOX + N_HEADS_FOX
DILATED_BRANCHES = ((128, 1), (512, 4), (2048, 16))
SEG = 128
BLOCK_Q = 128
N_BUCKETS = 32
MAX_DISTANCE = 2048
N_GROUPS = 4
EXPERTS_PER_GROUP = 8
N_EXPERTS = N_GROUPS * EXPERTS_PER_GROUP
TOP_K_IN_GROUP = 2
D_EXPERT = 256
SCALE = HEAD_DIM ** -0.5
NEG_INF = -1e30


def _rmsnorm(x, g):
    x32 = x.astype(jnp.float32)
    y = x32 * lax.rsqrt(jnp.mean(x32 * x32, axis=-1, keepdims=True) + EPS)
    return (y * g.astype(jnp.float32)).astype(x.dtype)

def _t5_bucket(dist):
    max_exact = N_BUCKETS // 2
    d32 = jnp.maximum(dist, 1).astype(jnp.float32)
    large = max_exact + (jnp.log(d32 / max_exact) / math.log(MAX_DISTANCE / max_exact)
                         * (N_BUCKETS - max_exact)).astype(jnp.int32)
    large = jnp.minimum(large, N_BUCKETS - 1)
    return jnp.where(dist < max_exact, dist, large)

def _dilated_branch(q, k, v, rel_bias, dilation):
    B, T, H, Dh = q.shape
    L = T // dilation
    nb = -(-L // SEG)
    L_pad = nb * SEG

    def to_sub(a):
        a = a.reshape(B, L, dilation, H, Dh).transpose(0, 2, 1, 3, 4)
        a = jnp.pad(a, ((0, 0), (0, 0), (0, L_pad - L), (0, 0), (0, 0)))
        return a.reshape(B, dilation, nb, SEG, H, Dh)

    qs, ks, vs = to_sub(q), to_sub(k), to_sub(v)

    def with_prev(a):
        prev = jnp.pad(a, ((0, 0), (0, 0), (1, 0), (0, 0), (0, 0), (0, 0)))[:, :, :-1]
        return jnp.concatenate([prev, a], axis=3)

    kk, vv = with_prev(ks), with_prev(vs)

    i = jnp.arange(SEG)[:, None]
    j = jnp.arange(2 * SEG)[None, :]
    m = i - j + SEG
    band = (m >= 0) & (m <= SEG)
    bias = rel_bias[_t5_bucket(jnp.clip(m, 0, SEG) * dilation)]
    bias = bias.transpose(2, 0, 1).astype(jnp.float32)
    blk = jnp.arange(nb)[:, None, None]
    valid = band[None] & (blk * SEG - SEG + j[None] >= 0)

    s = jnp.einsum('brnqhd,brnkhd->brnhqk', qs, kk,
                   preferred_element_type=jnp.float32) * SCALE + bias
    s = jnp.where(valid[:, None], s, NEG_INF)
    mx = jnp.max(s, axis=-1, keepdims=True)
    p = jnp.exp(s - mx)
    den = jnp.sum(p, axis=-1, keepdims=True)
    o = jnp.einsum('brnhqk,brnkhd->brnqhd', (p / den).astype(v.dtype), vv)
    lse = (mx + jnp.log(den))[..., 0].transpose(0, 1, 2, 4, 3)

    def from_sub(a):
        a = a.reshape(B, dilation, L_pad, *a.shape[4:])[:, :, :L]
        a = jnp.moveaxis(a, 1, 2)
        return a.reshape(B, T, *a.shape[3:])

    return from_sub(o), from_sub(lse)

def _dilated_attention(q, k, v, rel_bias):
    outs, lses = [], []
    for _, dilation in DILATED_BRANCHES:
        o, l = _dilated_branch(q, k, v, rel_bias, dilation)
        outs.append(o)
        lses.append(l)
    w = jax.nn.softmax(jnp.stack(lses), axis=0)
    return jnp.einsum('gbth,gbthd->bthd', w.astype(q.dtype), jnp.stack(outs))

def _forgetting_attention(q, k, v, log_f):
    B, T, H, Dh = q.shape
    nq = T // BLOCK_Q
    c = jnp.cumsum(log_f, axis=1)
    c_k = c.transpose(0, 2, 1)
    k_pos = jnp.arange(T)
    qb = q.reshape(B, nq, BLOCK_Q, H, Dh).transpose(1, 0, 2, 3, 4)
    cb = c.reshape(B, nq, BLOCK_Q, H).transpose(1, 0, 3, 2)
    starts = jnp.arange(nq) * BLOCK_Q

    def block(args):
        qi, ci, t0 = args
        s = jnp.einsum('bqhd,bkhd->bhqk', qi, k, preferred_element_type=jnp.float32) * SCALE
        s = s + ci[..., None] - c_k[:, :, None, :]
        q_pos = t0 + jnp.arange(BLOCK_Q)
        s = jnp.where(k_pos[None, :] <= q_pos[:, None], s, NEG_INF)
        p = jax.nn.softmax(s, axis=-1)
        return jnp.einsum('bhqk,bkhd->bqhd', p.astype(v.dtype), v)

    o = lax.map(block, (qb, cb, starts))
    return o.transpose(1, 0, 2, 3, 4).reshape(B, T, H, Dh)

def _hierarchical_moe(xt, w_rg, b_rg, w_re, b_re, w_gate, w_up, w_down):
    N = xt.shape[0]
    group_logits = (xt @ w_rg + b_rg).astype(jnp.float32)
    group_probs = jax.nn.softmax(group_logits, axis=-1)
    g1, g_idx = lax.top_k(group_probs, 1)
    expert_logits = (xt @ w_re + b_re).astype(jnp.float32).reshape(N, N_GROUPS, EXPERTS_PER_GROUP)
    sel = jnp.take_along_axis(expert_logits, g_idx[:, :, None], axis=1)[:, 0]
    top_v, top_i = lax.top_k(sel, TOP_K_IN_GROUP)
    g2 = jax.nn.softmax(top_v, axis=-1)
    expert_id = g_idx * EXPERTS_PER_GROUP + top_i
    combine = jnp.sum(jax.nn.one_hot(expert_id, N_EXPERTS, dtype=jnp.float32)
                      * (g1 * g2)[..., None], axis=1).astype(xt.dtype)
    y = jnp.zeros_like(xt)
    for e in range(N_EXPERTS):
        he = jax.nn.silu(xt @ w_gate[e]) * (xt @ w_up[e])
        y = y + combine[:, e:e + 1] * (he @ w_down[e])
    return y

def second_inputs(seed: int = 0) -> dict:
    key = jax.random.key(seed)
    ks = jax.random.split(key, 20)
    f32 = jnp.float32
    nrm = lambda k, shape, s: jax.random.normal(k, shape, f32) * s
    return {
        "x": nrm(ks[0], (BATCH, SEQ, D_MODEL), 1.0),
        "w_in": nrm(ks[1], (DEPTH_2, D_MODEL, D_IN_2), D_MODEL ** -0.5),
        "b_forget": 2.0 + nrm(ks[2], (DEPTH_2, N_HEADS_FOX), 0.5),
        "attn_norm": 1.0 + nrm(ks[3], (DEPTH_2, D_MODEL), 0.02),
        "out_norm_dil": 1.0 + nrm(ks[4], (DEPTH_2, D_DIL), 0.02),
        "out_norm_fox": 1.0 + nrm(ks[5], (DEPTH_2, D_FOX), 0.02),
        "w_out": nrm(ks[6], (DEPTH_2, D_MIX_2, D_MODEL), D_MIX_2 ** -0.5),
        "ffn_norm": 1.0 + nrm(ks[7], (DEPTH_2, D_MODEL), 0.02),
        "w_router_group": nrm(ks[8], (DEPTH_2, D_MODEL, N_GROUPS), D_MODEL ** -0.5),
        "b_router_group": nrm(ks[9], (DEPTH_2, N_GROUPS), 0.01),
        "w_router_expert": nrm(ks[10], (DEPTH_2, D_MODEL, N_EXPERTS), D_MODEL ** -0.5),
        "b_router_expert": nrm(ks[11], (DEPTH_2, N_EXPERTS), 0.01),
        "w_expert_gate": nrm(ks[12], (DEPTH_2, N_EXPERTS, D_MODEL, D_EXPERT), D_MODEL ** -0.5),
        "w_expert_up": nrm(ks[13], (DEPTH_2, N_EXPERTS, D_MODEL, D_EXPERT), D_MODEL ** -0.5),
        "w_expert_down": nrm(ks[14], (DEPTH_2, N_EXPERTS, D_EXPERT, D_MODEL), D_EXPERT ** -0.5),
        "rel_bias": nrm(ks[15], (N_BUCKETS, N_HEADS_DIL), 0.5),
        "final_norm": 1.0 + nrm(ks[16], (D_MODEL,), 0.02),
    }

def second_block(x, w_in, b_forget, attn_norm, out_norm_dil, out_norm_fox, w_out, ffn_norm,
              w_router_group, b_router_group, w_router_expert, b_router_expert,
              w_expert_gate, w_expert_up, w_expert_down, rel_bias, final_norm):
    B, T, D = x.shape
    splits = [D_DIL, 2 * D_DIL, 3 * D_DIL, 3 * D_DIL + D_FOX, 3 * D_DIL + 2 * D_FOX,
              3 * D_DIL + 3 * D_FOX]
    for layer in range(DEPTH_2):
        h = _rmsnorm(x, attn_norm[layer])
        proj = h @ w_in[layer]
        qa, ka, va, qf, kf, vf, f_pre = jnp.split(proj, splits, axis=-1)
        heads = lambda a, n: a.reshape(B, T, n, HEAD_DIM)
        o_dil = _dilated_attention(heads(qa, N_HEADS_DIL), heads(ka, N_HEADS_DIL),
                                   heads(va, N_HEADS_DIL), rel_bias)
        log_f = jax.nn.log_sigmoid((f_pre + b_forget[layer]).astype(jnp.float32))
        o_fox = _forgetting_attention(heads(qf, N_HEADS_FOX), heads(kf, N_HEADS_FOX),
                                      heads(vf, N_HEADS_FOX), log_f)
        o_dil = _rmsnorm(o_dil.reshape(B, T, D_DIL), out_norm_dil[layer])
        o_fox = _rmsnorm(o_fox.reshape(B, T, D_FOX), out_norm_fox[layer])
        x = x + jnp.concatenate([o_dil, o_fox], axis=-1) @ w_out[layer]
        h2 = _rmsnorm(x, ffn_norm[layer]).reshape(B * T, D)
        y = _hierarchical_moe(h2, w_router_group[layer], b_router_group[layer],
                              w_router_expert[layer], b_router_expert[layer],
                              w_expert_gate[layer], w_expert_up[layer], w_expert_down[layer])
        x = x + y.reshape(B, T, D)
    return _rmsnorm(x, final_norm)


def setup_inputs(seed=0):
    out = dict(first_inputs(seed))
    for name, value in second_inputs(seed + 1).items():
        if name != "x":
            out[name + "_2"] = value
    return out


def reference(
    x, c, ctx, c_ctx, norm_w, w_mod, b_mod, w_in, q_norm_w, w_uq, kv_norm_w, w_ukv,
    q_head_norm_w, k_head_norm_w, sc_conv_w, cf_conv_w, cf_conv_b, cf_ln_w, cf_ln_b, cf_pw_w,
    cf_pw_b, w_out, w_in_2, b_forget_2, attn_norm_2, out_norm_dil_2, out_norm_fox_2, w_out_2,
    ffn_norm_2, w_router_group_2, b_router_group_2, w_router_expert_2, b_router_expert_2,
    w_expert_gate_2, w_expert_up_2, w_expert_down_2, rel_bias_2, final_norm_2,
):
    x = first_block(
        x, c, ctx, c_ctx, norm_w, w_mod, b_mod, w_in, q_norm_w, w_uq, kv_norm_w, w_ukv,
        q_head_norm_w, k_head_norm_w, sc_conv_w, cf_conv_w, cf_conv_b, cf_ln_w, cf_ln_b,
        cf_pw_w, cf_pw_b, w_out,
    )
    return second_block(
        x, w_in_2, b_forget_2, attn_norm_2, out_norm_dil_2, out_norm_fox_2, w_out_2, ffn_norm_2,
        w_router_group_2, b_router_group_2, w_router_expert_2, b_router_expert_2,
        w_expert_gate_2, w_expert_up_2, w_expert_down_2, rel_bias_2, final_norm_2,
    )


_drawn_inputs = setup_inputs


def setup_inputs(seed=0):
    import zlib

    import numpy as np

    out = dict(_drawn_inputs(seed))
    spreads = {}
    factors = {'q_norm_w': 8.0,
     'kv_norm_w': 5.466,
     'q_head_norm_w': 8.0,
     'k_head_norm_w': 8.0,
     'cf_conv_b': 3.1,
     'cf_ln_w': 4.962,
     'cf_ln_b': 4.354,
     'cf_pw_b': 3.43,
     'out_norm_dil_2': 4.054,
     'out_norm_fox_2': 3.52,
     'ffn_norm_2': 3.076,
     'b_router_group_2': 8.0,
     'b_router_expert_2': 8.0,
     'final_norm_2': 2.739}
    for name, (base, spread) in spreads.items():
        noise = np.random.default_rng([zlib.crc32(name.encode()), seed]).standard_normal(out[name].shape)
        drawn = base * np.exp(spread * noise) if base else spread * noise
        out[name] = __import__('jax').numpy.asarray(drawn.astype(out[name].dtype))
    for name, factor in factors.items():
        out[name] = (out[name] * factor).astype(out[name].dtype)
    return out
```

```python
from contextlib import ExitStack

import numpy as np

import concourse.bass as bass
from concourse import mybir

F32 = mybir.dt.float32
F32R = mybir.dt.float32r
I32 = mybir.dt.int32
U32 = mybir.dt.uint32
ACT = mybir.ActivationFunctionType
ALU = mybir.AluOpType
AX = mybir.AxisListType

NX = 512
NC = 256
NT = NX + NC
D = 1024
KT = 8
HEADS = 8
QK = 96
EPS = 1e-6
LN_EPS = 1e-5

COLS = dict(cq=0, ckv=256, kr=384, ga=416, sc_in=928, sc_b=1184, sc_c=1440, gb=1696, glu=1952, gc=2464)


def _tile_starts():
    t = [("cq", 0), ("cq", 1), ("ckv", 0)]
    t += [("glu", 2), ("glu", 3), ("glu", 0), ("glu", 1)]
    for i in range(2):
        t += [("sc_in", i), ("sc_c", i), ("sc_b", i), ("gb", i)]
    t += [("ga", i) for i in range(4)] + [("gc", i) for i in range(2)]
    return t


TILES = _tile_starts()

SMALL = {}


def _small_columns():
    at = 0
    for name, n in (("norm_w", 16), ("b_mod", 48), ("qn_w", 4), ("kvn_w", 2), ("sc_w", 12), ("cf_w", 124),
                    ("cf_b", 4), ("ln_w", 4), ("ln_b", 4), ("pw_b", 4), ("qh_w", 2), ("kh_w", 2), ("c", 16)):
        SMALL[name] = at
        at += n
    SMALL["n"] = at


_small_columns()

SMALL2 = dict(norm=0, on=8, bf=16, n=17)


class Queue:

    def __init__(self, sem):
        self.sem, self.count, self.ops = sem, 0, []

    def __call__(self, make, *after, signal=True):
        self.ops.append((_tokens(after), make, (self.sem, 1) if signal else None))
        if not signal:
            return None
        self.count += 1
        return (self.sem, self.count)

    def dma(self, out, src, slot, *after):
        slot.count += 16
        self.ops.append((_tokens(after), lambda e: e.dma_start(out, src), (slot.sem, 16)))
        return (slot.sem, slot.count)

    def last(self):
        return (self.sem, self.count)

    def play(self, e):
        self.regs = {}
        self.run(e, self.ops, {})

    def run(self, e, ops, seen):
        for op in ops:
            if op[0] == "register":
                _, name, ap, after, top = op
                e.wait_ge(*after)
                self.regs[name] = e.value_load(ap, min_val=0, max_val=top)
                continue
            if op[0] == "guard":
                _, test, body, raised = op
                with e.If(test(self.regs)):
                    self.run(e, body, dict(seen))
                with e.Else():
                    for sem, before, by in raised:
                        e.wait_ge(sem, before)
                        e.sem_inc(sem, by)
                continue
            after, make, signal = op
            for sem, value in after:
                if seen.get(sem.num, 0) < value:
                    e.wait_ge(sem, value)
                    seen[sem.num] = value
            ins = make(e)
            if signal:
                ins.then_inc(*signal)


class Slot:

    def __init__(self, sem):
        self.sem, self.count = sem, 0

    def token(self):
        self.count += 16
        return (self.sem, self.count)


class Buf:

    def __init__(self, ap, slot=None):
        self.ap, self.free, self.slot, self.was = ap, [], slot, None


class Ring:
    def __init__(self, bufs):
        self.bufs = list(bufs)

    def take(self):
        b = self.bufs.pop(0)
        assert b.free is not None, "taken before its last readers are known"
        b.was, b.free = b.free, None
        self.bufs.append(b)
        return b

    def hold(self):
        b = self.take()
        self.bufs.remove(b)
        return b

    def release(self, b):
        self.bufs.append(b)


def _tokens(after):
    out = []
    for a in after:
        if a is None:
            continue
        if isinstance(a, tuple) and len(a) == 2 and isinstance(a[1], int):
            out.append(a)
        else:
            out += _tokens(a)
    return out


def plan(items, base, end):
    rng = np.random.default_rng(0)
    order = sorted(items, key=lambda x: (-(x[3] - x[2]), -x[1]))
    weight = {x[0]: float(i) for i, x in enumerate(order)}
    for _ in range(20000):
        placed = []
        for name, size, a, b in sorted(items, key=lambda x: weight[x[0]]):
            size = (size + 31) // 32 * 32
            spans = sorted((o, o + s) for _, o, s, p, q in placed if not (q < a or b < p))
            at = base
            for lo, hi in spans:
                if at + size <= lo:
                    break
                at = max(at, hi)
            if at + size > end:
                weight[name] -= 8 + 8 * rng.random()
                break
            placed.append((name, at, size, a, b))
        else:
            return {name: at for name, at, _, _, _ in placed}
    assert False, "no room"


class Ctx:
    pass


def setup(nc, ctx, dram):
    K = Ctx()
    K.nc, K.d = nc, dram
    sem = lambda name: ctx.enter_context(nc.semaphore(name))
    K.pe, K.act, K.dve, K.pool, K.sp = (Queue(sem(n)) for n in ("s_pe", "s_act", "s_dve", "s_pool", "s_sp"))
    K.slot = lambda name: Slot(sem(name))

    kb = 1024
    row = NT * 4
    items = [
        ("ident", 512, 0, 199), ("ones", 512, 0, 199), ("ctab", 512, 0, 99), ("stab", 512, 0, 99),
        ("small", 4 * SMALL["n"], 0, 99), ("c2T", 1024, 0, 75), ("nhalf", 64, 0, 199),
        ("mod", 4 * 8 * 2 * 4, 0, 99), ("rope_w", 4 * 128, 0, 99), ("rope_t", 4 * 512, 0, 99),
        ("whead", 32, 0, 99), ("stat", 4 * 256, 0, 199),
        ("raw", 2 * 4 * kb, 0, 130), ("whi", 2 * 4 * kb, 0, 113), ("wlo", 2 * 4 * kb, 0, 113),
        ("xc", 8 * row, 0, 0), ("wmod0", 64 * kb, 0, 0), ("wmod1", 64 * kb, 40, 49),
        ("wgate0", 16 * kb, 10, 10), ("wgate1", 16 * kb, 60, 60), ("modrow", 2 * kb, 0, 75),
        ("tmpa", 5 * 3264, 0, 25), ("tmpc", 5 * 3264, 40, 75),
        ("tmpe", 5 * 3264, 90, 100),
        ("x1", 8 * 512 * 4, 40, 100), ("xc1", 8 * 256 * 4, 40, 50), ("xr", 3 * row, 40, 40),
    ]
    for l, a in ((0, 0), (1, 50)):
        nt = 6 if l == 0 else 4
        r = row if l == 0 else 512 * 4
        items += [
            (f"hh{l}", 8 * row, a, a + 20), (f"hl{l}", 8 * row, a, a + 20),
            (f"cqw{l}", 3 * row, a + 10, a + 25), (f"krT{l}", row, a + 10, a + 10), (f"krN{l}", 6 * 32 * 4, a + 10, a + 25),
            (f"wkr{l}", 1024, a + 10, a + 10), (f"wkrh{l}", 1024, a + 10, a + 10), (f"wkrl{l}", 1024, a + 10, a + 10),
            (f"wuq{l}", 6 * kb, a + 10, a + 25), (f"wukv{l}", 4 * kb, a + 10, a + 25), (f"pw{l}", 2 * kb, a + 10, a + 25),
            (f"glu{l}", 2 * 828 * 4, a + 10, a + 25), (f"z{l}", 2 * 798 * 4, a + 10, a + 25),
            (f"scp{l}", 2 * 772 * 4, a + 10, a + 20), (f"scz{l}", 772 * 4, a + 10, a + 20),
            (f"qN{l}", nt * 768 * 4, a + 25, a + 30), (f"kN{l}", 6 * 768 * 4, a + 25, a + 30),
            (f"vN{l}", 6 * 512 * 4, a + 25, a + 30),
            (f"ybh{l}", 4 * r, a + 10, a + 40), (f"ybl{l}", 4 * r, a + 10, a + 40),
            (f"yah{l}", 4 * r, a + 30, a + 40), (f"yal{l}", 4 * r, a + 30, a + 40),
            (f"ga{l}", 4 * r, a + 20, a + 30), (f"gc{l}", 2 * r, a + 20, a + 25),
            (f"qT{l}", 4 * r, a + 30, a + 30), (f"kT{l}", 4 * row, a + 30, a + 30),
            (f"P{l}", 3 * row, a + 30, a + 30), (f"PT{l}", 12 * 2 * kb, a + 30, a + 30),
            (f"PTc{l}", 4 * kb if l == 0 else 32, a + 30, a + 30),
        ]
    items += [
        ("small2", 4 * SMALL2["n"], 0, 199), ("xN", 16 * kb, 100, 199), ("hh2", 16 * kb, 100, 113), ("hl2", 16 * kb, 100, 113),
        ("wf", 256, 100, 110), ("wfh", 256, 100, 110), ("wfl", 256, 100, 110),
        ("tmpf", 4 * 2 * kb, 110, 130), ("fC", 2 * kb, 110, 120), ("self", 4 * kb, 110, 110), ("sel", 4 * kb, 110, 120),
        ("vdil", 8 * kb, 110, 113), ("vfox", 8 * kb, 110, 120), ("q2", 16 * kb, 110, 120), ("k2", 8 * kb, 110, 120),
        ("tab", 3 * 2 * kb, 110, 113), ("lnn", 2 * kb, 110, 113), ("tri", 2 * kb, 110, 120),
        ("P2", 4 * 2 * kb, 110, 120), ("PT2", 16 * kb, 110, 120),
        ("y2h", 16 * kb, 110, 130), ("y2l", 16 * kb, 110, 130),
        ("wo2d", 32 * kb, 114, 130), ("wo2f", 32 * kb, 114, 130),
        ("row1", 4 * kb, 130, 139), ("row2", 4 * kb, 150, 199), ("kept", 4 * (3 * (GROUPS + MORE) + 24), 131, 199), ("ctl", 64, 131, 199), ("h2N", 16 * kb, 131, 139), ("h2T", 16 * kb, 131, 139),
        ("wr", 8 * 36 * 4, 131, 139), ("rt", 12 * kb, 131, 139), ("rc", 4 * kb, 131, 139),
        ("xg", 4 * 4 * kb, 140, 149), ("xg2_", 2 * 4 * kb, 140, 149), ("XT", 2 * 4 * kb, 140, 149), ("XT2_", 4 * kb, 140, 149),
        ("he", 4 * kb, 140, 149), ("Y", 3 * 4 * kb, 140, 149), ("Y2_", 2 * 4 * kb, 140, 149),
        ("yin", 4 * 8 * kb, 150, 199),
    ] + [(f"we{i}", 24 * kb, 130 if i < 2 else 131, 149) for i in range(5)]
    base = 16512
    K.at = plan(items, base, 229344)

    def sb(name, shape, dt=F32, where=None, skip=0):
        return nc.alloc_sbuf_tensor_at(name, shape, dt, offset=K.at[where or name] + skip)
    K.sb = sb
    return K


class Weights:

    def __init__(self, K, srcs):
        self.K, self.srcs, self.done = K, srcs, []
        self.raw = [Buf(K.sb(f"raw{i}", [128, 1024], F32, "raw", 4096 * i), K.slot(f"s_raw{i}")) for i in range(2)]
        self.hi = [Buf(K.sb(f"whi{i}", [128, 1024], F32R, "whi", 4096 * i)) for i in range(2)]
        self.lo = [Buf(K.sb(f"wlo{i}", [128, 1024], F32R, "wlo", 4096 * i)) for i in range(2)]
        self.loaded, self.limit, self.place = [], len(srcs), {}
        self.load()
        self.load()

    def load(self):
        i = len(self.loaded)
        if i < len(self.srcs):
            b = self.raw[i % 2]
            self.loaded.append(self.K.sp.dma(b.ap[:, :], self.srcs[i], b.slot, b.free))

    def split(self):
        K, i = self.K, len(self.done)
        if i >= len(self.srcs):
            return
        raw, hi, lo = self.raw[i % 2], *self.place.get(i, (self.hi[i % 2], self.lo[i % 2]))
        t_hi = K.act(lambda e: e.activation(hi.ap[:, :], raw.ap[:, :], ACT.Copy), self.loaded[i], hi.free)
        t_lo = K.pool(lambda e: e.tensor_tensor(lo.ap[:, :], raw.ap[:, :], hi.ap[:, :].bitcast(F32), ALU.subtract),
                      self.loaded[i], t_hi, lo.free)
        raw.free = [t_hi, t_lo]
        self.done.append((hi, lo, t_hi, t_lo))
        self.load()

    def get(self, i):
        while len(self.done) < min(i + 2, self.limit):
            self.split()
        return self.done[i]


class Pair:

    def __init__(self, hi, lo, t_hi, t_lo):
        self.hi, self.lo, self.t_hi, self.t_lo = hi, lo, t_hi, t_lo


def mm3(K, dst, ws, xs, m=128):
    tok = None
    n = len(ws)
    for k in range(n):
        w, x = ws[k], xs[k]
        for a, b, need, p in ((w.hi, x.hi, (w.t_hi, x.t_hi), 0), (w.hi, x.lo, (x.t_lo,), 1), (w.lo, x.hi, (w.t_lo,), 2)):
            for j, (o, c, cols) in enumerate(dst):
                start, stop = k == 0 and p == 0, k == n - 1 and p == 2
                tok = K.pe(lambda e, o=o, a=a, b=b, c=c, cols=cols, start=start, stop=stop:
                           e.matmul(o, a, b[:, c:c + cols], start=start, stop=stop),
                           *need, signal=stop and j == len(dst) - 1)
    return tok


def tile_pairs(w, m=128):
    hi, lo, t_hi, t_lo = w
    return [Pair(hi.ap[:, 128 * k:128 * k + m], lo.ap[:, 128 * k:128 * k + m], t_hi, t_lo) for k in range(KT)]


def begin(K):
    nc, d = K.nc, K.d
    pe, act, dve, pool, sp = K.pe, K.act, K.dve, K.pool, K.sp
    sb = K.sb
    K.ident = sb("ident", [128, 128])
    K.ones = sb("ones", [128, 128])
    K.ctab = sb("ctab", [128, 4, 32])
    K.stab = sb("stab", [128, 4, 32])
    K.small = sb("small", [128, SMALL["n"]])
    K.c2T = sb("c2T", [128, KT, 32])
    K.nhalf = sb("nhalf", [128, 16])
    K.mod = sb("mod", [128, 4, KT, 2])
    K.rope_w = sb("rope_w", [128, 4, 32])
    K.rope_t = sb("rope_t", [128, 4, 4, 32])
    K.stat = sb("stat", [128, 256])
    K.modrow = sb("modrow", [128, 512])
    K.t_small = sp.dma(K.small[:, :], d["small"], K.slot("s_small"))
    K.t_ident = sp.dma(K.ident[:, :], d["ident"], K.slot("s_ident"))
    K.t_tab = [sp.dma(K.ctab[:, :, :], d["ctab"], K.slot("s_ctab")), sp.dma(K.stab[:, :, :], d["stab"], K.slot("s_stab"))]
    K.t_ones = dve(lambda e: e.memset(K.ones[:, :], 1.0))
    K.t_nhalf = dve(lambda e: e.memset(K.nhalf[:, :], -0.5))
    t = dve(lambda e: e.memset(K.c2T[:, :, :], 0.0))
    K.t_c2 = act(lambda e: e.activation(K.c2T[:, :, 0:2],
                                        K.small[:, SMALL["c"]:SMALL["c"] + 16].rearrange("p (k v) -> p k v", v=2),
                                        ACT.Silu), K.t_small, t)
    K.ps = Ring([Buf(K.ctx.enter_context(nc.psum_tensor(f"ps{i}", [128, 1024], F32))) for i in range(4)])
    K.s_rope = K.slot("s_rope")
    K.t_mod_read = []


def small(K, name, l, n, i=0, cols=1):
    at = SMALL[name] + n * l + i
    return K.small[:, at:at + cols]


def mod_shift_scale(K, l, wm, t_wm):
    pe, act, dve = K.pe, K.act, K.dve
    s = K.ps.take()
    for k in range(KT):
        for j in range(4):
            tok = pe(lambda e, k=k, j=j: e.matmul(s.ap[32 * j:32 * j + 32, 0:512], K.c2T[:, k, :], wm[:, k, 512 * j:512 * j + 512],
                                                  start=k == 0, stop=k == KT - 1, skip_group_check=True),
                     K.t_c2, t_wm[k], s.was if k == 0 else None, signal=k == KT - 1 and j == 3)
    K.t_wm_read = tok
    t = act(lambda e: e.activation(K.modrow[:, :], s.ap[:, 0:512], ACT.Copy), tok, K.t_mod_read)
    s.free = [t]
    s2 = K.ps.take()
    for q in range(4):
        tok = pe(lambda e, q=q: e.transpose(s2.ap[:, 128 * q:128 * q + 128], K.modrow[:, 128 * q:128 * q + 128], K.ident[:, :]),
                 t, K.t_ident, s2.was if q == 0 else None, signal=q == 3)
    K.t_mod_read = [tok]
    view = s2.ap[:, 0:512].rearrange("p (t j r) -> p t j r", t=4, j=4)
    out = []
    for j in range(4):
        b = small(K, "b_mod", l, 24, 8 * (j // 2) + 4 * (j % 2), 4).unsqueeze(2).to_broadcast([128, 4, 2])
        dst = K.mod[:, 0 if j < 2 else 3, 4 * (j % 2):4 * (j % 2) + 4, :]
        out.append(dve(lambda e, dst=dst, j=j, b=b: e.tensor_tensor(dst, view[:, :, j, 0:2], b, ALU.add), tok, K.t_small))
    s2.free = [out[-1]]
    nw = small(K, "norm_w", l, 8, 0, 8).unsqueeze(2).to_broadcast([128, KT, 2])
    t = dve(lambda e: e.tensor_scalar(K.mod[:, 3, :, :], K.mod[:, 3, :, :], 1.0, None, ALU.add), out[-1])
    K.t_mod = [dve(lambda e: e.tensor_tensor(K.mod[:, 1, :, :], K.mod[:, 3, :, :], nw, ALU.mult), t)]


def mod_gate(K, l):
    pe, act, dve = K.pe, K.act, K.dve
    wg = [Buf(K.sb(f"wgate{l}_{i}", [128, 2, 1024], F32, f"wgate{l}", 8192 * i), K.s_gate[i]) for i in range(2)]
    s = K.ps.take()
    toks = []
    for q in range(4):
        g = wg[q % 2]
        t = K.sp.dma(g.ap[:, :, :], K.d["w_mod"][l, 2 * q:2 * q + 2, :, 2048:3072].rearrange("k p c -> p k c"), g.slot, g.free, K.gate_after)
        for k in range(2):
            for c in range(2):
                j = 2 * (q % 2) + c
                tok = pe(lambda e, g=g, k=k, c=c, j=j, q=q: e.matmul(
                    s.ap[32 * j:32 * j + 32, 0:512], K.c2T[:, 2 * q + k, :], g.ap[:, k, 512 * c:512 * c + 512],
                    start=q < 2 and k == 0, stop=q >= 2 and k == 1, skip_group_check=True),
                    t, s.was if q == 0 else None, signal=k == 1 and c == 1)
        g.free = [tok]
    t = act(lambda e: e.activation(K.modrow[:, :], s.ap[:, 0:512], ACT.Copy), tok, K.t_mod_read)
    s.free = [t]
    s2 = K.ps.take()
    for q in range(4):
        tok = pe(lambda e, q=q: e.transpose(s2.ap[:, 128 * q:128 * q + 128], K.modrow[:, 128 * q:128 * q + 128], K.ident[:, :]),
                 t, s2.was if q == 0 else None, signal=q == 3)
    K.t_mod_read = [tok]
    view = s2.ap[:, 0:512].rearrange("p (t j r) -> p t j r", t=4, j=4)
    for c in range(2):
        b = small(K, "b_mod", l, 24, 16 + 4 * c, 4).unsqueeze(2).to_broadcast([128, 4, 2])
        dst = K.mod[:, 2, 4 * c:4 * c + 4, :]
        t = dve(lambda e, dst=dst, c=c, b=b: e.tensor_tensor(dst, view[:, :, c, 0:2], b, ALU.add), tok, K.t_gate_read)
        t = dve(lambda e, dst=dst, c=c: e.tensor_tensor(dst, view[:, :, 2 + c, 0:2], dst, ALU.add), t)
    s2.free = [t]
    K.t_gate = t


class Norm:

    def __init__(self, K, nt, d=D, eps=EPS, nk=KT, ring=None):
        self.K, self.nt, self.d, self.eps, self.nk, self.k = K, nt, d, eps, nk, 0
        self.ring = ring or K.ps
        self.s = self.ring.hold()

    def add(self, sq, tok):
        K, k = self.K, self.k
        for i in range(self.nt):
            self.tok = K.pe(lambda e, i=i: e.matmul(self.s.ap[:, i:i + 1], sq[:, 128 * i:128 * i + 128], K.ones[:, 0:1],
                                                    start=k == 0 and i == 0, stop=k == self.nk - 1, skip_group_check=True),
                            tok, K.t_ones, self.s.was if k == 0 and i == 0 else None, signal=i == self.nt - 1)
        self.k += 1
        return self.tok

    def finish(self, ms, rstd, *after):
        K, n = self.K, self.nt
        t = K.dve(lambda e: e.tensor_scalar(ms, self.s.ap[:, 0:n], 1.0 / self.d, self.eps, ALU.mult, ALU.add), self.tok, *after)
        self.s.free = [t]
        self.ring.release(self.s)
        return K.pool(lambda e: e.tensor_tensor(rstd, ms, K.nhalf[:, 0:n], ALU.pow), t, K.t_nhalf)


def across(K, rstd, t_rstd, nt, diag, t_diag_free):
    s = K.ps.take()
    for i in range(nt):
        g = diag[i % len(diag)]
        t = K.dve(lambda e, g=g, i=i: e.tensor_scalar(g.ap, K.ident[:, :], rstd[:, i:i + 1], None, ALU.mult), t_rstd, K.t_ident, g.free, t_diag_free)
        tok = K.pe(lambda e, g=g, i=i: e.matmul(s.ap[:, 128 * i:128 * i + 128], K.ones[:, :], g.ap, start=True, stop=True),
                   t, s.was if i == 0 else None)
        g.free = [tok]
    return s, tok


def modulate(K, l, xs, t_xs, segs, rb, t_rb, hh, hl, tmps, after):
    out = []
    n = segs[-1][0] + segs[-1][1]
    for k in range(KT):
        b = tmps.take()
        for c, m, v in segs:
            t = K.dve(lambda e, b=b, k=k, c=c, m=m, v=v: e.scalar_tensor_tensor(
                b.ap[:, c:c + m], xs(k, c, m), K.mod[:, 1, k, v:v + 1], rb.ap[:, c:c + m], ALU.mult, ALU.mult),
                t_rb, K.t_mod, t_xs[k], b.was)
        for c, m, v in segs:
            t_hi = K.act(lambda e, b=b, k=k, c=c, m=m, v=v: e.activation(
                hh[:, k, c:c + m], b.ap[:, c:c + m], ACT.Identity, bias=K.mod[:, 0, k, v:v + 1]), t, after)
        for c, m, v in segs:
            t_lo = K.dve(lambda e, b=b, k=k, c=c, m=m, v=v: e.scalar_tensor_tensor(
                hl[:, k, c:c + m], b.ap[:, c:c + m], K.mod[:, 0, k, v:v + 1], hh[:, k, c:c + m].bitcast(F32), ALU.add, ALU.subtract),
                t_hi, after)
        b.free = [t_hi, t_lo]
        if k == KT - 1:
            rb.free = [t]
        out.append(Pair(hh[:, k, :], hl[:, k, :], t_hi, t_lo))
    return out


def tmp_ring(K, name, n, width=816):
    return Ring([Buf(K.sb(f"{name}_{i}", [128, width], F32, name, 4 * width * i)) for i in range(n)])


def first_layer_block(K, l, hT, wt, w0, tmps, bg):
    pe, act, dve, pool, sp, d = K.pe, K.act, K.dve, K.pool, K.sp, K.d
    both = l == 0
    n_own = NT if both else NX
    segs = [(0, NX), (NX, NC)] if both else [(0, NX)]
    all_segs = [(0, NX), (NX, NC)]
    nt_q = 6 if both else 4
    sb = lambda name, shape, dt=F32: K.sb(name + str(l), shape, dt)

    wuq, wukv, pw = sb("wuq", [128, 2, 768]), sb("wukv", [128, 1024]), sb("pw", [128, 2, 256])
    wkr = sb("wkr", [128, KT, 32])
    wkrh, wkrl = sb("wkrh", [128, KT, 32], F32R), sb("wkrl", [128, KT, 32], F32R)
    after = K.free_a
    t_wkr = sp.dma(wkr[:, :, :], d["w_kr"][l], K.s_wkr, after)
    t_wuq = sp.dma(wuq[:, :, :], d["w_uq"][l], K.s_wuq, after)
    t_wukv = sp.dma(wukv[:, :], d["w_ukv"][l], K.s_wukv, after)
    t_pw = sp.dma(pw[:, :, :], d["pw"][l], K.s_pw, after)
    t_rw = sp.dma(K.rope_w[:, :, :], d["rope_w"][l], K.s_rope, K.free_rope)
    t_h = act(lambda e: e.activation(wkrh[:, :, :], wkr[:, :, :], ACT.Copy), t_wkr, after)
    t_l = pool(lambda e: e.tensor_tensor(wkrl[:, :, :], wkr[:, :, :], wkrh[:, :, :].bitcast(F32), ALU.subtract), t_h, t_wkr, after)
    kr_pairs = [Pair(wkrh[:, k, :], wkrl[:, k, :], t_h, t_l) for k in range(KT)]
    for i, tab in ((0, K.ctab), (1, K.stab), (2, K.ctab), (3, K.stab)):
        t_rope = pool(lambda e, i=i, tab=tab: e.tensor_tensor(
            K.rope_t[:, i, :, :], tab[:, :, :], K.rope_w[:, i, :].unsqueeze(1).to_broadcast([128, 4, 32]), ALU.mult), t_rw, K.t_tab, K.free_rope)

    cqw = sb("cqw", [128, 3, NT])
    krT, krN = sb("krT", [32, NT]), sb("krN", [128, 6, 32])
    glu, z = sb("glu", [128, 2, 828]), sb("z", [128, 2, 798])
    scp, scz = sb("scp", [128, 2, 772]), sb("scz", [128, 772])
    ga, gc = sb("ga", [128, 4, n_own]), sb("gc", [128, 2, n_own])
    ybh, ybl = sb("ybh", [128, 4, n_own], F32R), sb("ybl", [128, 4, n_own], F32R)
    t_pad = pool(lambda e: e.memset(glu[:, :, :], 0.0), after)
    t_padp = pool(lambda e: e.memset(scp[:, :, :], 0.0), after)
    yp = [None] * KT
    st = Ctx()
    st.norm = [None, None]
    sumq = Ctx()

    def product(i, m=128, cols=None, pairs=None):
        s = K.ps.take()
        dst = [(s.ap[0:m, c:c + n], c, n) for c, n in (cols or segs)]
        ws = pairs or tile_pairs(wt.get(i), m)
        ws2 = [Pair(p.hi, p.lo, [p.t_hi, s.was], p.t_lo) for p in ws[:1]] + ws[1:]
        tok = mm3(K, dst, ws2, hT)
        if pairs is None:
            hi, lo, _, _ = wt.done[i]
            hi.free, lo.free = [tok], [tok]
        return s, tok

    norms = {}

    def ev_c(s, tok, name, i):
        f = i if name == "cq" else 2
        nn = NT if (both or name == "ckv") else NX
        w = small(K, "qn_w", l, 2, i) if name == "cq" else small(K, "kvn_w", l, 1)
        t = act(lambda e: e.activation(cqw[:, f, 0:nn], s.ap[:, 0:nn], ACT.Copy, scale=w), tok, K.t_small, after)
        b = tmps.take()
        t2 = act(lambda e: e.activation(b.ap[:, 0:nn], s.ap[:, 0:nn], ACT.Square), tok, b.was)
        s.free = [t2]
        st.cqw[f] = t
        if i == 0:
            norms[name] = Norm(K, nn // 128, 256 if name == "cq" else 128, EPS, 2 if name == "cq" else 1)
        b.free = [norms[name].add(b.ap, t2)]

    st.cqw = [None] * 3
    stat = K.stat
    rq, rkv = stat[:, 0:6], stat[:, 8:14]

    def ev_glu(s, tok, i):
        if i >= 2:
            b = st.sig[i - 2] = tmps.take()
            st.t_sig[i - 2] = act(lambda e: e.activation(b.ap[:, 0:n_own], s.ap[:, 0:n_own], ACT.Sigmoid), tok, b.was)
            s.free = [st.t_sig[i - 2]]
            return
        b = st.sig[i]
        for c, n in segs:
            o = 15 + (c if c == 0 else c + 30)
            t = dve(lambda e, c=c, n=n, o=o: e.tensor_tensor(glu[:, i, o:o + n], s.ap[:, c:c + n], b.ap[:, c:c + n], ALU.mult),
                    tok, st.t_sig[i], t_pad)
        s.free = b.free = [t]
        st.t_glu[i] = t

    st.sig, st.t_sig, st.t_glu = [None, None], [None, None], [None, None]
    width = 798 if both else 512
    wide = 770 if both else 512

    def conv():
        t = [None, None]
        for j in range(31):
            for i in range(2):
                w = small(K, "cf_w", l, 62, 31 * i + j)
                x = glu[:, i, j:j + width]
                o = z[:, i, 0:width]
                if j == 0:
                    t[i] = dve(lambda e, o=o, x=x, w=w, i=i: e.tensor_scalar(o, x, w, small(K, "cf_b", l, 2, i), ALU.mult, ALU.add),
                               st.t_glu[i], K.t_small, after)
                else:
                    t[i] = dve(lambda e, o=o, x=x, w=w: e.scalar_tensor_tensor(o, x, w, o, ALU.mult, ALU.add), t[i])
                yield
        st.t_z = t

    def split_y(k, src, t_src, buf, hi, lo):
        t_hi = act(lambda e: e.activation(hi, src, ACT.Copy), t_src, K.free_y)
        t_lo = pool(lambda e: e.tensor_tensor(lo, src, hi.bitcast(F32), ALU.subtract), t_src, t_hi, K.free_y)
        buf.free = [t_hi, t_lo]
        yp[k] = Pair(hi, lo, t_hi, t_lo)

    def ev_sc(s, tok, name, i):
        if name == "sc_in":
            b = st.sin = tmps.take()
            st.t_sin = act(lambda e: e.activation(b.ap[:, 0:n_own], s.ap[:, 0:n_own], ACT.Copy), tok, b.was)
            s.free = [st.t_sin]
        elif name == "sc_c":
            b = st.sin
            for c, n in segs:
                o = 1 + (c if c == 0 else c + 2)
                t = dve(lambda e, c=c, n=n, o=o: e.tensor_tensor(scp[:, i, o:o + n], s.ap[:, c:c + n], b.ap[:, c:c + n], ALU.mult),
                        tok, st.t_sin, t_padp)
            s.free = b.free = [t]
            zz = scz[:, 0:wide]
            t = dve(lambda e: e.tensor_scalar(zz, scp[:, i, 0:wide], small(K, "sc_w", l, 6, 3 * i), None, ALU.mult), t, st.t_u, after)
            for j in (1, 2):
                t = dve(lambda e, j=j: e.scalar_tensor_tensor(zz, scp[:, i, j:j + wide], small(K, "sc_w", l, 6, 3 * i + j), zz, ALU.mult, ALU.add), t)
            st.t_scz = t
        elif name == "sc_b":
            b = st.u = tmps.take()
            for c, n in segs:
                o = c if c == 0 else c + 2
                t = dve(lambda e, c=c, n=n, o=o: e.tensor_tensor(b.ap[:, c:c + n], s.ap[:, c:c + n], scz[:, o:o + n], ALU.mult), tok, st.t_scz, b.was)
            s.free = [t]
            st.t_u = t
        else:
            b, u = tmps.take(), st.u
            t = act(lambda e: e.activation(b.ap[:, 0:n_own], s.ap[:, 0:n_own], ACT.Silu), tok, b.was)
            s.free = [t]
            t = pool(lambda e: e.tensor_tensor(u.ap[:, 0:n_own], u.ap[:, 0:n_own], b.ap[:, 0:n_own], ALU.mult), t, st.t_u)
            b.free = [t]
            split_y(4 + i, u.ap[:, 0:n_own], t, u, ybh[:, i, :], ybl[:, i, :])

    st.t_u = None
    t_g = [None] * 6

    def ev_g(s, tok, name, i):
        dst = ga[:, i, :] if name == "ga" else gc[:, i, :]
        j = i if name == "ga" else 4 + i
        t_g[j] = act(lambda e: e.activation(dst, s.ap[:, 0:n_own], ACT.Silu), tok, K.free_g)
        s.free = [t_g[j]]

    conv_bg = conv()
    more = lambda n: [next(conv_bg, None) for _ in range(n)]
    for at, (name, i) in enumerate(TILES):
        cols = all_segs if name == "ckv" else segs
        s, tok = product(w0 + at, cols=cols)
        if name in ("cq", "ckv"):
            ev_c(s, tok, name, i)
        elif name == "glu":
            ev_glu(s, tok, i)
        elif name in ("ga", "gc"):
            ev_g(s, tok, name, i)
        else:
            ev_sc(s, tok, name, i)
        if name == "ckv":
            s, tok = product(None, m=32, cols=all_segs, pairs=kr_pairs)
            t = act(lambda e, s=s: e.activation(krT[:, :], s.ap[0:32, 0:NT], ACT.Copy), tok, after)
            s.free = [t]
            st.t_rq = norms["cq"].finish(stat[:, 16:16 + nt_q], rq[:, 0:nt_q], K.free_stat)
            st.t_rkv = norms["ckv"].finish(stat[:, 24:30], rkv, K.free_stat)
            st.t_krT = t
        if name == "glu" and i == 3:
            s = K.ps.take()
            for j in range(6):
                tok = pe(lambda e, s=s, j=j: e.transpose(s.ap[:, 32 * j:32 * j + 32], krT[:, 128 * j:128 * j + 128], K.ident[0:32, 0:32]),
                         st.t_krT, K.t_ident, s.was if j == 0 else None, signal=j == 5)
            t = act(lambda e, s=s: e.activation(krN[:, :, :], s.ap[:, 0:192].rearrange("p (t c) -> p t c", c=32), ACT.Copy), tok, after)
            s.free = [t]
            st.t_krN = t
        if name not in ("cq", "ckv", "glu"):
            more(6 if both else 5)
        if at == 8 and bg:
            bg()
    K.t_h_read = pe.last()
    more(62)

    qN, kN, vN = sb("qN", [128, nt_q, HEADS, QK]), sb("kN", [128, 6, HEADS, QK]), sb("vN", [128, 6, 512])
    after = K.free_q = [K.t_h_read, act.last(), dve.last()]
    krS = stat[:, 32:38]
    t_kr2 = []
    for i in range(6):
        b = tmps.take()
        t_kr2.append(act(lambda e, i=i, b=b: e.activation(b.ap[:, 0:32], krN[:, i, :], ACT.Square, accum_out=krS[:, i:i + 1]), st.t_krN, b.was))
        b.free = [t_kr2[-1]]
    t_q, t_k, t_v = [None] * 6, [None] * 6, [None] * 6

    def rope(x, i, q):
        h = x.shape[1]
        r = 0 if q else 2
        if i >= 4:
            w = K.rope_w[:, r, :].unsqueeze(1).to_broadcast([128, h, 32])
            return lambda t: pool(lambda e: e.tensor_tensor(x, x, w, ALU.mult), t, t_rw)
        cs = K.rope_t[:, r, i, :].unsqueeze(1).to_broadcast([128, h, 32])
        sn = K.rope_t[:, r + 1, i, :]

        def go(t):
            b = tmps.take()
            o = b.ap[:, 0:32 * h].rearrange("p (h c) -> p h c", c=32)
            for a in range(2):
                t1 = pool(lambda e, a=a: e.tensor_tensor(o[:, :, 16 * a:16 * a + 16], x[:, :, 16 - 16 * a:32 - 16 * a],
                                                         sn[:, 16 * a:16 * a + 16].unsqueeze(1).to_broadcast([128, h, 16]), ALU.mult), t, t_rope, b.was)
            t2 = pool(lambda e: e.tensor_tensor(x, x, cs, ALU.mult), t1)
            t3 = pool(lambda e: e.tensor_tensor(x, x, o, ALU.add), t2)
            b.free = [t3]
            return t3
        return go

    for i in range(6):
        b16 = 64 + 64 * (i % 2)
        ss, rs, ff = stat[:, b16:b16 + 16], stat[:, b16 + 16:b16 + 32], stat[:, b16 + 32:b16 + 48]
        has_q = i < nt_q
        cols = slice(128 * i, 128 * i + 128)
        if has_q:
            sq_ = K.ps.take()
            for c in range(2):
                for k in range(2):
                    tok_q = pe(lambda e, sq_=sq_, cols=cols, c=c, k=k: e.matmul(sq_.ap[:, 512 * c:512 * c + 384], cqw[:, k, cols], wuq[:, k, 384 * c:384 * c + 384],
                                                            start=k == 0, stop=k == 1),
                               st.cqw[0], st.cqw[1], t_wuq, sq_.was, signal=c == 1 and k == 1)
            q4 = sq_.ap[:, :].rearrange("p (c n) -> p c n", c=2)[:, :, 0:384]
        sk_ = K.ps.take()
        for c in range(2):
            tok_k = pe(lambda e, sk_=sk_, cols=cols, c=c: e.matmul(sk_.ap[:, 512 * c:512 * c + 512], cqw[:, 2, cols], wukv[:, 512 * c:512 * c + 512], start=True, stop=True),
                       st.cqw[2], t_wukv, sk_.was, signal=c == 1)
        b2 = tmps.take()
        t_k2 = act(lambda e, b2=b2, i=i, sk_=sk_: e.activation(b2.ap[:, 0:512], sk_.ap[:, 0:512], ACT.Square, scale=rkv[:, i:i + 1]), tok_k, st.t_rkv, b2.was)
        t_v[i] = act(lambda e, i=i, sk_=sk_: e.activation(vN[:, i, :], sk_.ap[:, 512:1024], ACT.Copy, scale=rkv[:, i:i + 1]), tok_k, after)
        t = dve(lambda e, b2=b2, ss=ss: e.tensor_reduce(ss[:, 8:16], b2.ap[:, 0:512].rearrange("p (h c) -> p h c", c=64), AX.X, ALU.add), t_k2, K.st_free[i % 2])
        b2.free = [t]
        t = dve(lambda e, ss=ss, i=i: e.tensor_scalar(ss[:, 8:16], ss[:, 8:16], krS[:, i:i + 1], None, ALU.add), t, t_kr2[i])
        lo = 8
        if has_q:
            b1 = tmps.take()
            t_q2 = act(lambda e, b1=b1, q4=q4, i=i: e.activation(b1.ap[:, 0:768].rearrange("p (c n) -> p c n", c=2), q4, ACT.Square, scale=rq[:, i:i + 1]),
                       tok_q, st.t_rq, b1.was)
            t = dve(lambda e, b1=b1, ss=ss: e.tensor_reduce(ss[:, 0:8], b1.ap[:, 0:768].rearrange("p (h c) -> p h c", c=QK), AX.X, ALU.add), t_q2)
            b1.free = [t]
            lo = 0
        t = dve(lambda e, ss=ss, lo=lo: e.tensor_scalar(ss[:, lo:16], ss[:, lo:16], 1.0 / QK, EPS, ALU.mult, ALU.add), t)
        t_r = pool(lambda e, ss=ss, rs=rs, lo=lo: e.tensor_tensor(rs[:, lo:16], ss[:, lo:16], K.nhalf[:, lo:16], ALU.pow), t, K.t_nhalf)
        t = dve(lambda e, ff=ff, rs=rs, i=i: e.tensor_scalar(ff[:, 8:16], rs[:, 8:16], rkv[:, i:i + 1], None, ALU.mult), t_r, st.t_rkv)
        if has_q:
            t1 = dve(lambda e, ff=ff, rs=rs, i=i: e.tensor_scalar(ff[:, 0:8], rs[:, 0:8], rq[:, i:i + 1], None, ALU.mult), t_r, st.t_rq)
        t2 = dve(lambda e, i=i, ff=ff, sk_=sk_: e.tensor_tensor(kN[:, i, :, 0:64], sk_.ap[:, 0:512].rearrange("p (h c) -> p h c", c=64),
                                                                ff[:, 8:16].unsqueeze(2).to_broadcast([128, 8, 64]), ALU.mult), t, tok_k, t_v[i], after)
        sk_.free = [t2, t_v[i]]
        t3 = rope(krN[:, i:i + 1, :], i, False)(t_kr2[i])
        t4 = pool(lambda e, i=i, rs=rs: e.tensor_tensor(kN[:, i, :, 64:96], krN[:, i:i + 1, :].to_broadcast([128, 8, 32]),
                                                        rs[:, 8:16].unsqueeze(2).to_broadcast([128, 8, 32]), ALU.mult), t3, t_r, after)
        t_k[i] = [t2, t4]
        K.st_free[i % 2] = [t2, t4]
        if has_q:
            for c in range(2):
                t = dve(lambda e, i=i, c=c, ff=ff, sq_=sq_: e.tensor_tensor(
                    qN[:, i, 4 * c:4 * c + 4, :], sq_.ap[:, 512 * c:512 * c + 384].rearrange("p (h c) -> p h c", c=QK),
                    ff[:, 4 * c:4 * c + 4].unsqueeze(2).to_broadcast([128, 4, QK]), ALU.mult), t1, t_q2, after)
            sq_.free = [t]
            t_q[i] = rope(qN[:, i, :, 64:96], i, True)(t)
            K.st_free[i % 2] = [t2, t4, t]
    K.free_rope = [pool.last()]

    nn = n_own
    zc = [(c, n, c if c == 0 else c + 30) for c, n in segs]
    s = K.ps.take()
    for c, n, o in zc:
        for k in range(2):
            tok = pe(lambda e, s=s, c=c, n=n, o=o, k=k: e.matmul(s.ap[:, c:c + n], K.ones[:, :], z[:, k, o:o + n], start=k == 0, stop=k == 1),
                     st.t_z, s.was, signal=k == 1)
    nz = Norm(K, nn // 128, 256, LN_EPS, 2)
    for k in range(2):
        b = tmps.take()
        for c, n, o in zc:
            t = dve(lambda e, s=s, k=k, c=c, n=n, o=o: e.scalar_tensor_tensor(
                z[:, k, o:o + n], s.ap[:, c:c + n], -1.0 / 256, z[:, k, o:o + n], ALU.mult, ALU.add), tok)
            t2 = act(lambda e, b=b, k=k, c=c, n=n, o=o: e.activation(b.ap[:, c:c + n], z[:, k, o:o + n], ACT.Square), t, b.was)
        b.free = [nz.add(b.ap, t2)]
    s.free = [t]
    t_r = nz.finish(stat[:, 40:40 + nn // 128], stat[:, 48:48 + nn // 128], K.free_stat)
    db = tmps.take()
    diag = [Buf(db.ap[:, 128 * q:128 * q + 128]) for q in range(6)]
    rb, t_rb = across(K, stat[:, 48:54], t_r, nn // 128, diag, db.was)
    db.free = [t_rb]
    t_zs = [None, None]
    for k in range(2):
        for c, n, o in zc:
            t = dve(lambda e, k=k, c=c, n=n, o=o: e.tensor_tensor(z[:, k, o:o + n], z[:, k, o:o + n], rb.ap[:, c:c + n], ALU.mult), t_rb)
            t_zs[k] = act(lambda e, k=k, n=n, o=o: e.activation(z[:, k, o:o + n], z[:, k, o:o + n], ACT.Silu,
                                                               scale=small(K, "ln_w", l, 2, k), bias=small(K, "ln_b", l, 2, k)), t)
    rb.free = [t]
    for f in range(2):
        s = K.ps.take()
        for c, n, o in zc:
            for k in range(2):
                tok = pe(lambda e, s=s, c=c, n=n, o=o, k=k, f=f: e.matmul(s.ap[:, c:c + n], pw[:, k, 128 * f:128 * f + 128], z[:, k, o:o + n],
                                                                         start=k == 0, stop=k == 1), t_zs, t_pw, s.was, signal=k == 1)
        b = tmps.take()
        t = dve(lambda e, b=b, f=f, s=s: e.scalar_tensor_tensor(b.ap[:, 0:nn], s.ap[:, 0:nn], small(K, "pw_b", l, 2, f), gc[:, f, :], ALU.add, ALU.mult),
                tok, t_g[4 + f], b.was)
        s.free = [t]
        split_y(6 + f, b.ap[:, 0:nn], t, b, ybh[:, 2 + f, :], ybl[:, 2 + f, :])
    K.free_stat = [pool.last(), dve.last(), act.last()]

    attention(K, l, qN, kN, vN, t_q, t_k, t_v, ga, t_g, yp)
    return yp


def attention(K, l, qN, kN, vN, t_q, t_k, t_v, ga, t_g, yp):
    pe, act, dve, pool = K.pe, K.act, K.dve, K.pool
    both = l == 0
    n_own = NT if both else NX
    nt_q = n_own // 128
    sm = float(np.float32(QK) ** np.float32(-0.5))
    after = [pe.last(), act.last(), dve.last(), pool.last()]
    qT = K.sb(f"qT{l}", [128, 2, 2, n_own], F32R)
    kT = K.sb(f"kT{l}", [128, 2, 2, NT], F32R)
    P = Ring([Buf(K.sb(f"P{l}_{i}", [128, NT], F32, f"P{l}", 4 * NT * i)) for i in range(3)])
    for b in P.bufs:
        b.free = list(after)
    PT = K.sb(f"PT{l}", [128, 2, 6, 512])
    PTc = K.sb(f"PTc{l}", [128, 2, 2, 256]) if both else None
    yah, yal = K.sb(f"yah{l}", [128, 4, n_own], F32R), K.sb(f"yal{l}", [128, 4, n_own], F32R)
    stat = K.stat
    t_pv = [after, after]
    heads, units = {}, []
    for h in range(HEADS):
        units += [(h, i) for i in range(4)] + ([(h, 4)] if both else [])
    S, Pn = {}, {}

    def turn(h):
        b = h % 2
        need = heads[h - 2][2] if h >= 2 else after
        out = []
        for src, toks, dst, name, nt in ((qN, t_q, qT, "qh_w", nt_q), (kN, t_k, kT, "kh_w", 6)):
            s = K.ps.take()
            for i in range(nt):
                tok = pe(lambda e, i=i, s=s, src=src: e.transpose(s.ap[0:QK, 128 * i:128 * i + 128], src[:, i, h, :], K.ident[:, :]),
                         toks[i], s.was if i == 0 else None, signal=i == nt - 1)
            w = small(K, name, l, 1)[0:QK, :]
            n = 128 * nt
            hi, lo = dst[0:QK, b, 0, 0:n], dst[0:QK, b, 1, 0:n]
            t_hi = act(lambda e, s=s, hi=hi, w=w, n=n: e.activation(hi, s.ap[0:QK, 0:n], ACT.Copy, scale=w), tok, need)
            t_lo = dve(lambda e, s=s, hi=hi, lo=lo, w=w, n=n: e.scalar_tensor_tensor(lo, s.ap[0:QK, 0:n], w, hi.bitcast(F32), ALU.mult, ALU.subtract), t_hi, need)
            s.free = [t_lo]
            out.append(Pair(hi, lo, t_hi, t_lo))
        heads[h] = [out[0], out[1], None]

    def scores(u):
        h, i = units[u]
        q, k, _ = heads[h]
        s = S[u] = K.ps.take()
        if i < 4:
            jobs = [(i, [(0, 0, NX), (512, NX, NC)])]
        else:
            jobs = [(4, [(0, NX, NC)]), (5, [(512, NX, NC)])]
        for n, (t, outs) in enumerate(jobs):
            qh, ql = q.hi[:, 128 * t:128 * t + 128], q.lo[:, 128 * t:128 * t + 128]
            for p, (a, b, need) in enumerate(((qh, k.hi, (q.t_hi, k.t_hi, s.was)), (qh, k.lo, (k.t_lo,)), (ql, k.hi, (q.t_lo,)))):
                for o, c, w in outs:
                    tok = pe(lambda e, o=o, c=c, w=w, a=a, b=b, p=p: e.matmul(s.ap[:, o:o + w], a, b[:, c:c + w], start=p == 0, stop=p == 2),
                             need, signal=p == 2 and n == len(jobs) - 1 and o == outs[-1][0])
        heads[h][2] = [tok]
        c0 = 192 + 8 * (u % 4)
        P_ = P.take()
        v = K.stat_free[u % 4]
        if i < 4:
            spans = [(slice(0, NT), slice(0, NT))]
        else:
            spans = [(slice(0, 256), slice(0, 256)), (slice(512, 768), slice(256, 512))]
        for j, (a, b) in enumerate(spans):
            t = dve(lambda e, a=a, j=j: e.tensor_reduce(stat[:, c0 + j:c0 + j + 1], s.ap[:, a], AX.X, ALU.max), tok, v)
        n = len(spans)
        t = dve(lambda e: e.tensor_scalar(stat[:, c0 + 2:c0 + 2 + n], stat[:, c0:c0 + n], -sm, None, ALU.mult), t)
        for j, (a, b) in enumerate(spans):
            t1 = act(lambda e, a=a, b=b, j=j: e.activation(P_.ap[:, b], s.ap[:, a], ACT.Exp, scale=sm, bias=stat[:, c0 + 2 + j:c0 + 3 + j],
                                                           accum_out=stat[:, c0 + 4 + j:c0 + 5 + j]), t, P_.was)
        s.free = [t1]
        Pn[u] = [P_, t1, c0, spans, None]

    def normalise(u):
        P_, t, c0, spans, _ = Pn[u]
        n = len(spans)
        t = dve(lambda e: e.reciprocal(stat[:, c0 + 6:c0 + 6 + n], stat[:, c0 + 4:c0 + 4 + n]), t)
        for j, (a, b) in enumerate(spans):
            t1 = pool(lambda e, b=b, j=j: e.tensor_scalar(P_.ap[:, b], P_.ap[:, b], stat[:, c0 + 6 + j:c0 + 7 + j], 0.0, ALU.mult, ALU.add), t)
        Pn[u][4] = t1
        K.stat_free[u % 4] = [t1]

    def turn_p(u):
        h, i = units[u]
        P_, _, _, _, t = Pn[u]
        e_ = h % 2
        s = K.ps.take()
        if i < 4:
            for kt in range(6):
                tok = pe(lambda e, kt=kt: e.transpose(s.ap[:, 128 * kt:128 * kt + 128], P_.ap[:, 128 * kt:128 * kt + 128], K.ident[:, :]),
                         t, s.was, signal=kt == 5)
            dst = PT[:, e_, :, 128 * i:128 * i + 128]
            src = s.ap[:, 0:768].rearrange("p (t q) -> p t q", q=128)
        else:
            for kt in range(2):
                for j in range(2):
                    o = 128 * (2 * kt + j)
                    tok = pe(lambda e, o=o, kt=kt, j=j: e.transpose(s.ap[:, o:o + 128], P_.ap[:, 256 * j + 128 * kt:256 * j + 128 * kt + 128], K.ident[:, :]),
                             t, s.was, signal=kt == 1 and j == 1)
            dst = PTc[:, e_, :, :].rearrange("p t q -> p (t q)")
            src = s.ap[:, 0:512]
        P_.free = [tok]
        if u % 2:
            t1 = act(lambda e: e.activation(dst, src, ACT.Copy), tok, t_pv[0])
        else:
            t1 = dve(lambda e: e.tensor_copy(dst, src), tok, t_pv[0])
        s.free = [t1]
        t_pt.append(t1)

    def values(p):
        s = K.ps.take()
        for kt in range(6):
            for e_ in range(2):
                h = 2 * p + e_
                tok = pe(lambda e, kt=kt, e_=e_, h=h: e.matmul(s.ap[64 * e_:64 * e_ + 64, 0:512], vN[:, kt, 64 * h:64 * h + 64], PT[:, e_, kt, :],
                                                               start=kt == 0, stop=kt == 5, skip_group_check=True),
                         t_pt, t_v, s.was, signal=kt == 5 and e_ == 1)
        if both:
            for kt in (4, 5):
                for e_ in range(2):
                    h = 2 * p + e_
                    tok = pe(lambda e, kt=kt, e_=e_, h=h: e.matmul(s.ap[64 * e_:64 * e_ + 64, 512:768], vN[:, kt, 64 * h:64 * h + 64], PTc[:, e_, kt - 4, :],
                                                                   start=kt == 4, stop=kt == 5, skip_group_check=True),
                             signal=kt == 5 and e_ == 1)
        t_pv[0] = [tok]
        t_pt.clear()
        o = s.ap[:, 0:n_own]
        t = dve(lambda e: e.tensor_tensor(o, o, ga[:, p, :], ALU.mult), tok, t_g[p])
        t_hi = act(lambda e: e.activation(yah[:, p, :], o, ACT.Copy), t, after)
        t_lo = dve(lambda e: e.tensor_tensor(yal[:, p, :], o, yah[:, p, :].bitcast(F32), ALU.subtract), t, t_hi, after)
        s.free = [t_lo]
        yp[p] = Pair(yah[:, p, :], yal[:, p, :], t_hi, t_lo)

    t_pt = []
    turn(0)
    scores(0)
    scores(1)
    normalise(0)
    n = len(units)
    per = n // HEADS
    for u in range(n):
        if u + 1 < n:
            normalise(u + 1)
        if u + 2 < n:
            if units[u + 2][1] == 0:
                pass
            scores(u + 2)
        if u >= 1 and u % (2 * per) == 0:
            values(u // (2 * per) - 1)
        turn_p(u)
        if u % per == 1 and u // per + 1 < HEADS:
            turn(u // per + 1)
    values(HEADS // 2 - 1)


def residual(K, l, wt, w0, yp, xs, t_xs, segs, out, each):
    pe, act, dve = K.pe, K.act, K.dve
    pend = None
    for f in range(KT):
        s = K.ps.take()
        ws = tile_pairs(wt.get(w0 + f))
        ws[0] = Pair(ws[0].hi, ws[0].lo, [ws[0].t_hi, s.was], ws[0].t_lo)
        tok = mm3(K, [(s.ap[:, c:c + n], c, n) for c, n, _ in segs], ws, yp)
        hi, lo, _, _ = wt.done[w0 + f]
        hi.free, lo.free = [tok], [tok]
        if pend:
            pend()
        t = []
        src, t_src = xs(f)
        for c, n, v in segs:
            t.append(dve(lambda e, c=c, n=n, v=v, src=src, s=s, f=f: e.scalar_tensor_tensor(
                out(f, c, n), s.ap[:, c:c + n], K.mod[:, 2, f, v:v + 1], src(c, n), ALU.mult, ALU.add), tok, t_src, K.t_gate, K.free_x))
        s.free = [t[-1]]
        pend = each(f, t)
    pend()
    K.t_gate_read = dve.last()


def first_block(K):
    pe, act, dve, pool, sp, d, sb = K.pe, K.act, K.dve, K.pool, K.sp, K.d, K.sb
    begin(K)
    K.s_wkr, K.s_wuq, K.s_wukv, K.s_pw = (K.slot("s_" + n) for n in ("wkr", "wuq", "wukv", "pw"))
    K.s_gate = [K.slot(f"s_gate{i}") for i in range(2)]
    s_mod = [K.slot(f"s_mod{i}") for i in range(KT)]
    xc = sb("xc", [128, KT, NT])
    t_xc = []
    for i in range(4):
        t_xc += 2 * [sp.dma(xc[:, 2 * i:2 * i + 2, :], d["xc"][:, 2 * i:2 * i + 2, :], K.slot(f"s_xc{i}"))]
    wm = sb("wmod0", [128, KT, 2048])
    t_wm = [sp.dma(wm[:, k, :], d["w_mod"][0, k, :, 0:2048], s_mod[k]) for k in range(KT)]
    w_in, w_out = [], []
    srcs = []
    for l in range(2):
        w_in.append(len(srcs))
        srcs += [d["w_in"][l, i] for i in range(len(TILES))]
        w_out.append(len(srcs))
        srcs += [d["w_out"][l, i] for i in range(KT)]
    M = K.moe = Ctx()
    M.h2d = K.nc.dram_tensor("h2d", [NX, D], F32).ap()
    M.meta = K.nc.dram_tensor("meta", [ROWS, 4], F32).ap()
    M.ybuf = K.nc.dram_tensor("ybuf", [2 * NX, D], F32).ap()
    M.t_meta0 = act.dma(M.meta.rearrange("(g p) w -> g (p w)", p=128), d["empty"], K.slot("s_meta0"))
    K.w2 = len(srcs)
    srcs += [d["w_in2"][i] for i in range(24)]
    limit = len(srcs)
    srcs += [d["w_out2"][k] for k in range(KT)]
    wt = K.wt = Weights(K, srcs)
    wt.limit = limit
    K.free_rope, K.free_stat, K.st_free, K.stat_free = [], [], [[], []], [[], [], [], []]
    K.t_gate_read, K.free_x = None, []
    stat = K.stat
    tmps = tmp_ring(K, "tmpa", 5)
    both = [(0, NX, 0), (NX, NC, 1)]

    N = Norm(K, 6)
    for k in range(KT):
        b = tmps.take()
        t = act(lambda e, k=k, b=b: e.activation(b.ap[:, 0:NT], xc[:, k, :], ACT.Square), t_xc[k], b.was)
        b.free = [N.add(b.ap, t)]
    t_r = N.finish(stat[:, 0:6], stat[:, 8:14])
    K.t_mod_free = []
    for l in range(2):
        n_own = NT if l == 0 else NX
        mod_shift_scale(K, l, wm, t_wm)
        db = tmps.take()
        diag = [Buf(db.ap[:, 128 * q:128 * q + 128]) for q in range(6)]
        rb, t_rb = across(K, stat[:, 8:14], t_r, 6, diag, db.was)
        db.free = [t_rb]
        hh, hl = sb(f"hh{l}", [128, KT, NT], F32R), sb(f"hl{l}", [128, KT, NT], F32R)
        if l == 0:
            xs, t_xs = lambda k, c, m: xc[:, k, c:c + m], t_xc
        else:
            xs, t_xs = lambda k, c, m: x1[:, k, :] if c == 0 else xc1[:, k, :], t_x1
        hT = modulate(K, l, xs, t_xs, both, rb, t_rb, hh, hl, tmps, [K.t_wm_read, K.free_x])
        K.t_mod_free = [act.last(), dve.last()]
        K.free_a = K.free_y = K.free_g = [pe.last(), act.last(), dve.last(), pool.last()]
        K.gate_after = K.free_a
        yp = first_layer_block(K, l, hT, wt, w_in[l], tmps, lambda: mod_gate(K, l))
        fence = [pe.last(), act.last(), dve.last(), pool.last()]
        N = Norm(K, 6 if l == 0 else 4)
        if l == 0:
            wm = sb("wmod1", [128, KT, 2048])
            t_wm = [sp.dma(wm[:, k, :], d["w_mod"][1, k, :, 0:2048], s_mod[k], fence) for k in range(KT)]
            x1, xc1 = sb("x1", [128, KT, NX]), sb("xc1", [128, KT, NC])
            xr = Ring([Buf(sb(f"xr_{i}", [128, NT], F32, "xr", 4 * NT * i), K.slot(f"s_xr{i}")) for i in range(3)])
            for b in xr.bufs:
                b.free = fence

            def source(f):
                b = xr.take()
                t = act.dma(b.ap[:, :], d["xc"][:, f, :], b.slot, b.was)
                st_x.append(b)
                return (lambda c, n: b.ap[:, c:c + n]), t
            st_x = []
            out = lambda f, c, n: x1[:, f, :] if c == 0 else xc1[:, f, :]
            segs = both
        else:
            source = lambda f: ((lambda c, n: x1[:, f, :]), t_x1[f])
            out = lambda f, c, n: x1[:, f, :]
            segs = both[:1]
        tmps = tmp_ring(K, "tmpc" if l == 0 else "tmpe", 5)
        for b in tmps.bufs:
            b.free = fence
        K.free_x = fence
        t_next = []

        def each(f, t):
            if l == 0:
                st_x[f].free = [t[-1]]
            b = tmps.take()
            for (c, n, v), tt in zip(segs, t):
                t2 = act(lambda e, c=c, n=n, f=f, out=out: e.activation(b.ap[:, c:c + n], out(f, c, n), ACT.Square), tt, b.was)
            t_next.append(t)

            def add():
                b.free = [N.add(b.ap, t2)]
            return add
        residual(K, l, wt, w_out[l], yp, source, None, segs, out, each)
        t_x1 = t_next
        K.free_x = [pe.last(), act.last(), dve.last(), pool.last()]
        t_r = N.finish(stat[:, 0:N.nt], stat[:, 8:8 + N.nt], K.free_stat)
    K.tmps = tmps
    return x1, t_x1, t_r


NE, DE = 32, 256
PAIRS, GROUPS = 16, 32
MORE = 7
ROWS = 128 * (GROUPS + MORE)
BIG = 1.0e30
T2 = 4
RC = dict(desc4=0, desc32=4, thr=36, base=40, over=72, ids=104, pow2=136, nth=152, tri=160, n=288)


def second_block(K, x1, t_x1, t_r, out):
    pe, act, dve, pool, sp, d, sb, nc = K.pe, K.act, K.dve, K.pool, K.sp, K.d, K.sb, K.nc
    stat, wt = K.stat, K.wt
    fence = lambda: [pe.last(), act.last(), dve.last(), pool.last()]
    start = fence()
    small2 = sb("small2", [128, SMALL2["n"]])
    t_small2 = sp.dma(small2[:, :], d["small2"], K.slot("s_small2"), start)
    wf, wfh, wfl = sb("wf", [128, KT, 8]), sb("wfh", [128, KT, 8], F32R), sb("wfl", [128, KT, 8], F32R)
    t_wf = sp.dma(wf[:, :, :], d["w_f"], K.slot("s_wf"), start)
    t_wfh = act(lambda e: e.activation(wfh[:, :, :], wf[:, :, :], ACT.Copy), t_wf, start)
    t_wfl = pool(lambda e: e.tensor_tensor(wfl[:, :, :], wf[:, :, :], wfh[:, :, :].bitcast(F32), ALU.subtract), t_wfh, start)

    tmps = K.tmps
    db = tmps.take()
    diag = [Buf(db.ap[:, 128 * q:128 * q + 128]) for q in range(6)]
    rb, t_rb = across(K, stat[:, 8:12], t_r, 4, diag, db.was)
    db.free = [t_rb]
    hh, hl = sb("hh2", [128, KT, NX], F32R), sb("hl2", [128, KT, NX], F32R)
    xN = sb("xN", [128, T2, D])
    hT = []
    for k in range(KT):
        b = tmps.take()
        t = dve(lambda e, k=k, b=b: e.scalar_tensor_tensor(b.ap[:, 0:NX], x1[:, k, :], small2[:, k:k + 1], rb.ap[:, 0:NX], ALU.mult, ALU.mult),
                t_rb, t_x1[k], t_small2, b.was)
        t_hi = act(lambda e, k=k, b=b: e.activation(hh[:, k, :], b.ap[:, 0:NX], ACT.Copy), t, start)
        t_lo = pool(lambda e, k=k, b=b: e.tensor_tensor(hl[:, k, :], b.ap[:, 0:NX], hh[:, k, :].bitcast(F32), ALU.subtract), t, t_hi, start)
        b.free = [t_hi, t_lo]
        hT.append(Pair(hh[:, k, :], hl[:, k, :], t_hi, t_lo))
    rb.free = [t]
    t_xN = []
    for t_ in range(T2):
        s = K.ps.take()
        for k in range(KT):
            tok = pe(lambda e, s=s, t_=t_, k=k: e.transpose(s.ap[:, 128 * k:128 * k + 128], x1[:, k, 128 * t_:128 * t_ + 128], K.ident[:, :]),
                     t_x1, s.was, signal=k == KT - 1)
        t_xN.append(act(lambda e, s=s, t_=t_: e.activation(xN[:, t_, :], s.ap[:, :], ACT.Copy), tok, start))
        s.free = [t_xN[-1]]
    K.bk = Ring([Buf(b.ap[:, 512 * i:512 * i + 512]) for b in K.ps.bufs for i in range(2)])
    for i, b in enumerate(K.bk.bufs):
        b.free = K.ps.bufs[i // 2].free
    bk = K.bk
    after = fence()

    tmps = tmp_ring(K, "tmpf", 4, 512)
    for b in tmps.bufs:
        b.free = after
    s = bk.take()
    tok = mm3(K, [(s.ap[0:8, 0:NX], 0, NX)], [Pair(wfh[:, k, :], wfl[:, k, :], [t_wfh, s.was], t_wfl) for k in range(KT)], hT)
    fa, fb, fc = tmps.take(), tmps.take(), tmps.take()
    A, B_, C_ = fa.ap[0:8, :], fb.ap[0:8, :], fc.ap[0:8, :]
    t = dve(lambda e, s=s: e.tensor_scalar(A, s.ap[0:8, 0:NX], small2[0:8, 16:17], None, ALU.add), tok, t_small2, fa.was)
    s.free = [t]
    t = dve(lambda e: e.scalar_tensor_tensor(B_, A, -1.0, A, ALU.mult, ALU.max), t, fb.was)
    t = act(lambda e: e.activation(B_, B_, ACT.Exp, scale=-1.0), t)
    t = act(lambda e: e.activation(B_, B_, ACT.Ln, bias=1.0), t)
    t2 = dve(lambda e: e.tensor_scalar(C_, A, -1.0, 0.0, ALU.mult, ALU.max), t, fc.was)
    t = dve(lambda e: e.tensor_tensor(B_, B_, C_, ALU.add), t2)
    t_o8 = dve(lambda e: e.memset(A, 1.0), t)
    t = dve(lambda e: e.tensor_tensor_scan(C_, A, B_, 0.0, ALU.mult, ALU.add), t, t_o8)
    fC = sb("fC", [128, NX], F32R)
    t0 = dve(lambda e: e.memset(fC[:, :].bitcast(F32), 0.0), after)
    t_c = act(lambda e: e.activation(fC[0:8, :], C_, ACT.Copy), t, t0)
    t1 = dve(lambda e: e.tensor_tensor(B_, C_, fC[0:8, :].bitcast(F32), ALU.subtract), t_c)
    t_fC = [t_c, act(lambda e: e.activation(fC[32:40, :], B_, ACT.Copy), t1, t0)]
    fa.free = fb.free = fc.free = [t_fC[1], t]
    self_, sel = sb("self", [128, 1024]), sb("sel", [128, HEADS, 128], F32R)
    t = sp.dma(self_[:, :], d["sel"], K.slot("s_sel"), after)
    t_sel = act(lambda e: e.activation(sel[:, :, :].rearrange("p h c -> p (h c)"), self_[:, :], ACT.Copy), t, after)
    tri = sb("tri", [128, 512])
    lnn = sb("lnn", [128, 512])
    t_tri = sp.dma(tri[:, :], d["causal"], K.slot("s_tri"), after)
    t_lnn = sp.dma(lnn[:, :], d["lnn"], K.slot("s_lnn"), after)
    tabs = Ring([Buf(sb(f"tab{i}", [128, 512], F32, "tab", 2048 * i), K.slot(f"s_tab{i}")) for i in range(3)])
    for b in tabs.bufs:
        b.free = after
    vT = [sb("vdil", [128, T2, 512]), sb("vfox", [128, T2, 512])]
    t_vT = [[None] * T2, [None] * T2]
    q2 = [[[sb(f"q2_{i}{e}{p}", [128, NX], F32R, "q2", 2048 * (4 * i + 2 * e + p)) for p in range(2)] for e in range(2)] for i in range(2)]
    k2 = [[sb(f"k2_{i}{p}", [128, NX], F32R, "k2", 2048 * (2 * i + p)) for p in range(2)] for i in range(2)]
    t_z = []
    for i in range(2):
        for e_ in range(2):
            for p in range(2):
                half = slice(64, 128) if e_ == 0 else slice(0, 64)
                t_z.append(dve(lambda e, i=i, e_=e_, p=p, half=half: e.memset(q2[i][e_][p][half, :].bitcast(F32), 0.0), after))
    P = Ring([Buf(sb(f"P2_{i}", [128, 512], F32, "P2", 2048 * i)) for i in range(4)])
    for b in P.bufs:
        b.free = after
    PT = sb("PT2", [128, 2, T2, 512])
    yh, yl = sb("y2h", [128, KT, NX], F32R), sb("y2l", [128, KT, NX], F32R)
    yp = [None] * KT
    w0 = K.w2
    heads, S, Pn, t_pt = {}, {}, {}, []
    pv = Ctx()
    pv.t, pv.norm, pv.rstd = after, [None, None], [None, None]
    qk_read = {}

    def values_chunk(which, at):
        banks = [bk.take() for _ in range(T2)]
        for kk in range(4):
            hi, lo, t_hi, t_lo = wt.get(at + kk)
            for t_ in range(T2):
                for j in range(2):
                    x = hT[2 * kk + j]
                    c = slice(128 * t_, 128 * t_ + 128)
                    for p, (a, b, need) in enumerate(((x.hi, hi, (x.t_hi, t_hi, banks[t_].was)), (x.lo, hi, (x.t_lo,)), (x.hi, lo, (t_lo,)))):
                        last = kk == 3 and j == 1 and p == 2
                        tok = pe(lambda e, t_=t_, a=a, b=b, c=c, j=j, kk=kk, p=p, last=last: e.matmul(
                            banks[t_].ap[:, :], a[:, c], b.ap[:, 512 * j:512 * j + 512], start=kk == 0 and j == 0 and p == 0, stop=last),
                            need, signal=last or (t_ == T2 - 1 and j == 1 and p == 2))
                if kk == 3:
                    t_vT[which][t_] = act(lambda e, t_=t_: e.activation(vT[which][:, t_, :], banks[t_].ap[:, :], ACT.Copy), tok, after)
                    banks[t_].free = [t_vT[which][t_]]
            hi.free, lo.free = [tok], [tok]
            yield

    def tile_product(p, which, at):
        s = bk.take()
        w = tile_pairs(wt.get(at))
        w[0] = Pair(w[0].hi, w[0].lo, [w[0].t_hi, s.was], w[0].t_lo)
        for c in range(4):
            for k in (2 * c, 2 * c + 1):
                for a, b, need, q in ((w[k].hi, hT[k].hi, (w[k].t_hi, hT[k].t_hi), 0), (w[k].hi, hT[k].lo, (hT[k].t_lo,), 1), (w[k].lo, hT[k].hi, (w[k].t_lo,), 2)):
                    tok = pe(lambda e, a=a, b=b, k=k, q=q: e.matmul(s.ap[:, :], a, b, start=k == 0 and q == 0, stop=k == KT - 1 and q == 2),
                             need, signal=k == KT - 1 and q == 2)
            if c < 3:
                yield
        hi, lo, _, _ = wt.done[at]
        hi.free, lo.free = [tok], [tok]
        i = p % 2
        need = qk_read.get(p - 2, after)
        if which == 0:
            pr = []
            for e_ in range(2):
                r = slice(64 * e_, 64 * e_ + 64)
                h_, l_ = q2[i][e_]
                th = act(lambda e, r=r, h_=h_: e.activation(h_[r, :], s.ap[r, :], ACT.Copy, scale=0.125), tok, need)
                tl = dve(lambda e, r=r, h_=h_, l_=l_: e.scalar_tensor_tensor(l_[r, :], s.ap[r, :], 0.125, h_[r, :].bitcast(F32), ALU.mult, ALU.subtract), th, need)
                pr.append(Pair(h_[:, :], l_[:, :], th, tl))
            s.free = [tl]
            heads[p] = [pr, None]
        else:
            h_, l_ = k2[i]
            th = act(lambda e: e.activation(h_[:, :], s.ap[:, :], ACT.Copy), tok, need)
            tl = dve(lambda e: e.tensor_tensor(l_[:, :], s.ap[:, :], h_[:, :].bitcast(F32), ALU.subtract), th, need)
            s.free = [tl]
            heads[p][1] = Pair(h_[:, :], l_[:, :], th, tl)
        yield

    def table(h):
        b = tabs.take()
        t = sp.dma(b.ap[:, :], d["bias"][h], b.slot, b.was)
        b.tok = pool(lambda e: e.tensor_tensor(b.ap[:, :], b.ap[:, :], lnn[:, :], ALU.add), t, t_lnn)
        tab_of[h] = b

    tab_of = {}
    units = [(p, e_, i) for p in range(HEADS) for e_ in range(2) for i in range(T2)]

    def scores(u):
        p, e_, i = units[u]
        q, k = heads[p][0][e_], heads[p][1]
        fox = p >= 4
        s = bk.take()
        n, w = 128 * (i + 1), max(256, 128 * (i + 1))
        c = slice(128 * i, 128 * i + 128)
        jobs = [(q.hi[:, c], k.hi, (q.t_hi, k.t_hi, t_z, s.was)), (q.hi[:, c], k.lo, (k.t_lo,)), (q.lo[:, c], k.hi, (q.t_lo,))]
        if fox:
            jobs.append((sel[:, 2 * (p - 4) + e_, :], fC, (t_sel, t_fC)))
        for j, (a, b, need) in enumerate(jobs):
            tok = pe(lambda e, j=j, a=a, b=b: e.matmul(s.ap[:, 0:w], a, b[:, 0:w], start=j == 0, stop=j == len(jobs) - 1), need, signal=j == len(jobs) - 1)
        qk_read[p] = [tok]
        c0 = 192 + 8 * (u % 4)
        P_ = P.take()
        if fox:
            tab, t_tab = tri[:, 512 - n:512], t_tri
        else:
            b = tab_of[2 * p + e_]
            tab, t_tab = b.ap[:, 512 - n:512], b.tok
        t = dve(lambda e: e.tensor_tensor_reduce(P_.ap[:, 0:n], s.ap[:, 0:n], tab, 1.0, -3.0e38, ALU.add, ALU.max, stat[:, c0:c0 + 1]),
                tok, t_tab, P_.was, K.stat_free[u % 4])
        s.free = [t]
        if not fox and i == 3:
            b.free = [t]
        t = dve(lambda e: e.tensor_scalar(stat[:, c0 + 1:c0 + 2], stat[:, c0:c0 + 1], -1.0, None, ALU.mult), t)
        t = act(lambda e: e.activation(P_.ap[:, 0:n], P_.ap[:, 0:n], ACT.Exp, bias=stat[:, c0 + 1:c0 + 2], accum_out=stat[:, c0 + 2:c0 + 3]), t)
        Pn[u] = [P_, t, c0, n, None]

    def normalise(u):
        P_, t, c0, n, _ = Pn[u]
        t = dve(lambda e: e.reciprocal(stat[:, c0 + 3:c0 + 4], stat[:, c0 + 2:c0 + 3]), t)
        t = pool(lambda e: e.tensor_scalar(P_.ap[:, 0:n], P_.ap[:, 0:n], stat[:, c0 + 3:c0 + 4], 0.0, ALU.mult, ALU.add), t)
        Pn[u][4] = t
        K.stat_free[u % 4] = [t]

    def turn_p(u):
        p, e_, i = units[u]
        P_, _, _, n, t = Pn[u]
        s = bk.take()
        for kt in range(i + 1):
            tok = pe(lambda e, kt=kt: e.transpose(s.ap[:, 128 * kt:128 * kt + 128], P_.ap[:, 128 * kt:128 * kt + 128], K.ident[:, :]), t, s.was, signal=kt == i)
        P_.free = [tok]
        dst = PT[:, e_, 0:i + 1, 128 * i:128 * i + 128]
        src = s.ap[:, 0:n].rearrange("p (t q) -> p t q", q=128)
        if u % 2:
            t1 = act(lambda e: e.activation(dst, src, ACT.Copy), tok, pv.t)
        else:
            t1 = dve(lambda e: e.tensor_copy(dst, src), tok, pv.t)
        s.free = [t1]
        t_pt.append(t1)

    def weigh(p):
        s = bk.take()
        fox = p // 4
        for kt in range(T2):
            for e_ in range(2):
                h = 2 * (p % 4) + e_
                tok = pe(lambda e, kt=kt, e_=e_, h=h: e.matmul(s.ap[64 * e_:64 * e_ + 64, 128 * kt:512], vT[fox][:, kt, 64 * h:64 * h + 64], PT[:, e_, kt, 128 * kt:512],
                                                               start=kt == 0, stop=kt == 3, skip_group_check=True),
                         t_pt, t_vT[fox], s.was, signal=kt == 3 and e_ == 1)
        pv.t = [tok]
        t_pt.clear()
        b = tmps.take()
        w = small2[:, 8 + p:9 + p]
        t_hi = act(lambda e: e.activation(yh[:, p, :], s.ap[:, :], ACT.Copy, scale=w), tok, after)
        t_sq = act(lambda e: e.activation(b.ap[:, :], s.ap[:, :], ACT.Square), tok, b.was)
        t_lo = dve(lambda e: e.scalar_tensor_tensor(yl[:, p, :], s.ap[:, :], w, yh[:, p, :].bitcast(F32), ALU.mult, ALU.subtract), t_hi, t_sq, after)
        s.free = [t_lo]
        yp[p] = Pair(yh[:, p, :], yl[:, p, :], t_hi, t_lo)

        def add():
            if p % 4 == 0:
                pv.norm[fox] = Norm(K, T2, 512, EPS, 4, bk)
            b.free = [pv.norm[fox].add(b.ap, t_sq)]
            if p % 4 == 3:
                pv.rstd[fox] = pv.norm[fox].finish(stat[:, 16 + 8 * fox:20 + 8 * fox], stat[:, 32 + 8 * fox:36 + 8 * fox], K.free_stat)
        return add

    t_x = list(t_xN)

    def begin_out():
        done = fence()
        wo = []
        for half, name in enumerate(("wo2d", "wo2f")):
            for k in range(4):
                hb, lb = (Buf(K.sb(f"{name}{p}{k}", [128, 1024], F32R, name, 4096 * (2 * k + j))) for j, p in enumerate("hl"))
                hb.free = lb.free = done
                wt.place[K.w2 + 24 + 4 * half + k] = (hb, lb)

        def split(n):
            for _ in range(n):
                wt.split()
                hb, lb, t_hi, t_lo = wt.done[-1]
                wo.append([Pair(hb.ap[:, 512 * c:512 * c + 512], lb.ap[:, 512 * c:512 * c + 512], t_hi, t_lo) for c in range(2)])

        def product(half, t_, c):
            s = bk.take()
            cols = slice(128 * t_, 128 * t_ + 128)
            for k in range(4 * half, 4 * half + 4):
                y, w = yp[k], wo[k][c]
                for q, (a, b, need) in enumerate(((y.hi[:, cols], w.hi, (y.t_hi, w.t_hi, s.was)), (y.lo[:, cols], w.hi, (y.t_lo,)), (y.hi[:, cols], w.lo, (w.t_lo,)))):
                    last = k == 4 * half + 3 and q == 2
                    tok = pe(lambda e, s=s, a=a, b=b, k=k, q=q, last=last: e.matmul(s.ap[:, :], a, b, start=k == 4 * half and q == 0, stop=last), need, signal=last)
            x = xN[:, t_, 512 * c:512 * c + 512]
            r = stat[:, 32 + 8 * half + t_:33 + 8 * half + t_]
            t = dve(lambda e: e.scalar_tensor_tensor(x, s.ap[:, :], r, x, ALU.mult, ALU.add), tok, pv.rstd[half], t_x[t_])
            s.free = [t]
            t_x[t_] = t
        for _ in range(4):
            split(1)
            yield
        for t_ in range(T2):
            for c in range(2):
                if t_ < 2:
                    split(1) if 2 * t_ + c < 4 else None
                product(0, t_, c)
                yield
        while len(wo) < 8:
            split(1)
        yield from last_part(lambda t_, c: product(1, t_, c))

    def last_part(product):
        M = K.moe
        M.after = fence()
        row1 = sb("row1", [128, D])
        t_rows = sp.dma(row1[:, :], d["rows"][:, 0, :], K.slot("s_row1"), M.after)
        M.experts = Experts(K, M.after)
        M.experts.load(2)
        M.wr, M.rc = None, None
        for t_ in range(T2):
            for c in range(2):
                product(t_, c)
            if t_ == 0:
                M.after2 = fence()
                h2N, h2T = sb("h2N", [128, T2, D]), sb("h2T", [128, KT, NX])
                M.wr, M.rc = sb("wr", [128, KT, 36]), sb("rc", [128, RC["n"] + 36])
                M.h2N, M.h2T = h2N, h2T
            yield
        done = fence()
        M.t_wr = sp.dma(M.wr[:, :, :], d["w_r"], K.slot("s_wr"), done)
        M.t_rc = sp.dma(M.rc[:, :], d["rc"], K.slot("s_rc"), done)
        M.experts.after = done
        M.experts.load(3)
        ms, rs = stat[:, 48:52], stat[:, 56:60]
        M.t_h2T, M.t_h2d = [], []
        M.slot_h = [K.slot(f"s_h2{i}") for i in range(T2)]
        for t_ in range(T2):
            sq = h2N[:, t_, :]
            t = act(lambda e, t_=t_, sq=sq: e.activation(sq, xN[:, t_, :], ACT.Square, accum_out=ms[:, t_:t_ + 1]), t_x[t_], done)
            t = dve(lambda e, t_=t_: e.tensor_scalar(ms[:, t_:t_ + 1], ms[:, t_:t_ + 1], 1.0 / D, EPS, ALU.mult, ALU.add), t)
            t = pool(lambda e, t_=t_: e.tensor_tensor(rs[:, t_:t_ + 1], ms[:, t_:t_ + 1], K.nhalf[:, 0:1], ALU.pow), t)
            t = dve(lambda e, t_=t_, sq=sq: e.scalar_tensor_tensor(sq, xN[:, t_, :], rs[:, t_:t_ + 1], row1[:, :], ALU.mult, ALU.mult), t, t_rows)
            M.t_h2d.append(act.dma(M.h2d[128 * t_:128 * t_ + 128, :], sq, M.slot_h[t_], t))
            for c in range(2):
                s = bk.take()
                for k in range(4):
                    tok = pe(lambda e, s=s, t_=t_, c=c, k=k: e.transpose(s.ap[:, 128 * k:128 * k + 128], h2N[:, t_, 512 * c + 128 * k:512 * c + 128 * k + 128], K.ident[:, :]),
                             t, s.was, signal=k == 3)
                M.t_h2T.append(act(lambda e, s=s, t_=t_, c=c: e.activation(h2T[:, 4 * c:4 * c + 4, 128 * t_:128 * t_ + 128],
                                                                          s.ap[:, :].rearrange("p (k q) -> p k q", q=128), ACT.Copy), tok, done))
                s.free = [M.t_h2T[-1]]
        M.s_log = s = bk.take()
        for t_ in range(T2):
            for k in range(KT):
                M.t_log = pe(lambda e, s=s, t_=t_, k=k: e.matmul(s.ap[:, 64 * t_:64 * t_ + 36], h2T[:, k, 128 * t_:128 * t_ + 128], M.wr[:, k, :],
                                                                start=k == 0, stop=k == KT - 1), M.t_h2T[2 * t_:2 * t_ + 2], M.t_wr, s.was, signal=k == KT - 1)

    for h in range(2):
        table(h)
    for _ in values_chunk(0, w0):
        pass
    work = []
    for which in range(2):
        for _ in tile_product(0, which, w0 + 4 + which):
            pass

    def products():
        at = w0 + 6
        for p in range(1, HEADS):
            for which in range(2):
                for _ in tile_product(p, which, at):
                    yield p
                at += 1
            if p == 2:
                for _ in values_chunk(1, at):
                    yield p
                at += 4
    bg = products()
    more = lambda n: [next(bg, None) for _ in range(n)]
    scores(0)
    scores(1)
    normalise(0)
    pend = None
    out_gen = None
    nu = len(units)
    for u in range(nu):
        p, e_, i = units[u]
        if u + 1 < nu:
            normalise(u + 1)
        r = u % 8
        more((2, 1, 1, 2, 1, 1, 0, 0)[r] if p != 1 else (2, 2, 2, 2, 2, 2, 0, 0)[r])
        if u % 4 == 1 and 2 * p + e_ + 1 < 8 and u // 4 + 1 >= 2:
            table(u // 4 + 1)
        if u + 2 < nu:
            scores(u + 2)
        if pend:
            pend()
            pend = None
        if r == 0 and p:
            pend = weigh(p - 1)
        turn_p(u)
        if u == 54:
            out_gen = begin_out()
        if u >= 54:
            next(out_gen)
            if u >= 62:
                next(out_gen)
    if pend:
        pend()
    weigh(HEADS - 1)()
    if not out_gen:
        out_gen = begin_out()
    for _ in out_gen:
        pass
    route(K)
    experts(K, xN, t_x, out)


class Experts:

    def __init__(self, K, after):
        self.K, self.after, self.n = K, after, 0
        self.bufs = []
        for i in range(5):
            b = Buf(None)
            b.gu = K.sb(f"we_gu{i}", [128, KT, 2 * DE], F32, f"we{i}")
            b.dn = K.sb(f"we_dn{i}", [128, 2, D], F32, f"we{i}", 16384)
            b.slots = [K.slot(f"s_gu{i}"), K.slot(f"s_dn{i}")]
            b.free = None
            self.bufs.append(b)
        self.ready = []

    def load(self, n=1):
        for _ in range(n):
            if self.n >= NE:
                return
            b = self.bufs[self.n % 5]
            free = self.after if self.n < 5 else b.free
            b.free = None
            self.ready.append((b, self.K.sp.dma(b.gu[:, :, :], self.K.d["w_gu"][self.n], b.slots[0], free),
                               self.K.sp.dma(b.dn[:, :, :], self.K.d["w_dn"][self.n], b.slots[1], free)))
            self.n += 1


def route(K):
    pe, act, dve, pool, sp, M = K.pe, K.act, K.dve, K.pool, K.sp, K.moe
    rt = K.sb("rt", [128, 3072])
    at = Ctx()
    at.n = 0

    def new(*shape, dt=None):
        n = 1
        for x in shape:
            n *= x
        v = rt[:, at.n:at.n + n]
        at.n += n
        if dt:
            v = v.bitcast(dt)
        if len(shape) == 2:
            v = v.rearrange("p (a b) -> p a b", b=shape[1])
        if len(shape) == 3:
            v = v.rearrange("p (a b c) -> p a b c", b=shape[1], c=shape[2])
        return v
    const = lambda name, n: M.rc[:, RC[name]:RC[name] + n]
    over = lambda v, n: v.unsqueeze(2).to_broadcast([128, v.shape[1], n])
    along = lambda v, n: v.unsqueeze(1).to_broadcast([128, n, v.shape[1]])
    fl = lambda v: v.rearrange("p a b -> p (a b)")

    st = Ctx()
    st.t = [M.t_log, M.t_rc]

    def tt(out, a, b, op, *more):
        st.t = dve(lambda e: e.tensor_tensor(out, a, b, op), st.t, *more)

    def ts(out, a, s1, s2, op0, op1=None):
        st.t = dve(lambda e: e.tensor_scalar(out, a, s1, s2, op0, op1) if op1 else e.tensor_scalar(out, a, s1, None, op0), st.t)

    def red(out, a, op):
        st.t = dve(lambda e: e.tensor_reduce(out, a, AX.X, op), st.t)

    def recip(out, a):
        st.t = dve(lambda e: e.reciprocal(out, a), st.t)

    def exp(out, a):
        st.t = act(lambda e: e.activation(out, a, ACT.Exp), st.t)

    lg = M.s_log.ap[:, 0:256].rearrange("p (t c) -> p t c", c=64)
    Lg, Le = new(T2, 4), new(T2, NE)
    bias = M.rc[:, RC["n"]:RC["n"] + 36]
    tt(Lg, lg[:, :, 0:4], along(bias[:, 0:4], T2), ALU.add)
    tt(Le, lg[:, :, 4:36], along(bias[:, 4:36], T2), ALU.add)
    M.s_log.free = [st.t]
    m4, s4, g1 = new(T2), new(T2), new(T2)
    E4, key4 = new(T2, 4), new(T2, 4)
    red(m4, Lg, ALU.max)
    tt(E4, Lg, over(m4, 4), ALU.subtract)
    exp(E4, E4)
    red(s4, E4, ALU.add)
    recip(s4, s4)
    tt(E4, E4, over(s4, 4), ALU.mult)
    red(g1, E4, ALU.max)

    def first(v, best, desc, out, n):
        k = new(T2)
        tt(out, v, over(best, n), ALU.is_ge)
        tt(out, out, along(desc, T2), ALU.mult)
        red(k, out, ALU.max)
        tt(out, out, over(k, n), ALU.is_equal)
    first(E4, g1, const("desc4", 4), key4, 4)
    ng = new(T2, 4)
    ts(ng, key4, -1.0, BIG, ALU.add, ALU.mult)
    L16 = Le.rearrange("p t (g j) -> p (t g) j", j=8)
    tt(L16, L16, over(fl(key4), 8), ALU.mult)
    tt(L16, L16, over(fl(ng), 8), ALU.add)
    v1, v2 = new(T2), new(T2)
    M1, M2 = new(T2, NE), new(T2, NE)
    red(v1, Le, ALU.max)
    first(Le, v1, const("desc32", NE), M1, NE)
    st.t = dve(lambda e: e.scalar_tensor_tensor(fl(Le), fl(M1), -10 * BIG, fl(Le), ALU.mult, ALU.add), st.t)
    red(v2, Le, ALU.max)
    first(Le, v2, const("desc32", NE), M2, NE)
    ed, w12 = new(T2), new(T2, 2)
    tt(ed, v2, v1, ALU.subtract)
    exp(ed, ed)
    r = new(T2)
    ts(r, ed, 1.0, None, ALU.add)
    recip(r, r)
    tt(w12[:, :, 0], g1, r, ALU.mult)
    tt(w12[:, :, 1], w12[:, :, 0], ed, ALU.mult)
    A, C, pos, cnt = new(T2, NE), new(T2 + 1, NE), new(T2, NE), None
    tt(A, M1, M2, ALU.add)
    s = K.bk.take()
    pe(lambda e: e.matmul(s.ap[:, 0:128], M.rc[:, RC["tri"]:RC["tri"] + 128], fl(A), start=True, stop=True), st.t, s.was, signal=False)
    tok = pe(lambda e: e.matmul(s.ap[:, 128:256], K.ones[:, :], fl(A), start=True, stop=True))
    st.t = dve(lambda e: e.memset(C[:, 0, :], 0.0), tok)
    for t_ in range(T2):
        tt(C[:, t_ + 1, :], C[:, t_, :], s.ap[:, 128 + NE * t_:128 + NE * t_ + NE], ALU.add)
    tt(fl(pos), fl(C[:, 0:T2, :]), s.ap[:, 0:128], ALU.add)
    s.free = [st.t]
    cnt = C[:, T2, :]
    cmp, nb, inc, far = new(NE, 4), new(NE), new(NE), new(NE)
    tt(cmp, over(cnt, 4), along(const("thr", 4), NE), ALU.is_gt)
    red(nb, cmp, ALU.add)
    st.t = dve(lambda e: e.tensor_tensor_scan(inc, K.ones[:, 0:NE], nb, 0.0, ALU.mult, ALU.add), st.t)
    tt(far, inc, nb, ALU.subtract)
    st.t = dve(lambda e: e.scalar_tensor_tensor(far, far, 128.0, const("over", NE), ALU.mult, ALU.add), st.t)
    G, H, slot, slotU = new(T2, NE), new(T2, NE), new(T2, 2), new(T2, 2, dt=U32)
    ts(fl(G), fl(pos), 63.5, 64.0, ALU.is_gt, ALU.mult)
    tt(G, G, along(const("base", NE), T2), ALU.add)
    ts(fl(H), fl(pos), 127.5, None, ALU.is_gt)
    tt(H, H, along(far, T2), ALU.mult)
    tt(fl(G), fl(G), fl(H), ALU.add)
    tt(fl(G), fl(G), fl(pos), ALU.add)
    for c, m in enumerate((M1, M2)):
        tt(fl(H), fl(m), fl(G), ALU.mult)
        red(slot[:, :, c], H, ALU.add)
    st.t = dve(lambda e: e.tensor_copy(fl(slotU), fl(slot)), st.t)
    t_slot = st.t
    row = new(T2 * 2, 4)
    ids = M.rc[:, RC["ids"]:RC["ids"] + 32].rearrange("p (c w) -> p c w", w=4)
    st.t = dve(lambda e: e.tensor_copy(row, ids), st.t)
    st.t = dve(lambda e: e.tensor_copy(row[:, :, 2], fl(w12)), st.t)
    su = fl(slotU)
    s_sc = K.slot("s_scatter")
    for j in range(2 * T2):
        s_sc.count += 16
        pool.ops.append((_tokens([st.t, M.t_meta0]), lambda e, j=j: e.indirect_dma_start(
            out=M.meta, out_offset=bass.IndirectOffsetOnAxis(ap=su[:, j:j + 1], axis=0), in_=row[:, j, :], in_offset=None,
            bounds_check=ROWS - 1, oob_is_err=False), (s_sc.sem, 16)))
    t_list = (s_sc.sem, s_sc.count)
    f32_, p16, nbt = new(NE), new(PAIRS), new(1)
    ctl = new(2 + MORE)
    eq = new(MORE, NE)
    M.ctl = K.sb("ctl", [128, 2 + MORE], I32)
    ts(f32_, cnt, 64.5, None, ALU.is_gt)
    red(p16, f32_.rearrange("p (a b) -> p a b", b=2), ALU.max)
    tt(p16, p16, const("pow2", PAIRS), ALU.mult)
    red(ctl[:, 0:1], p16, ALU.add)
    st.t = dve(lambda e: e.tensor_copy(ctl[:, 1:2], inc[:, NE - 1:NE]), st.t)
    tt(eq, along(inc, MORE), over(const("nth", MORE), NE), ALU.is_le)
    red(ctl[:, 2:2 + MORE], eq, ALU.add)
    ts(ctl[:, 2:2 + MORE], ctl[:, 2:2 + MORE], float(NE - 1), None, ALU.min)
    M.t_ctl = dve(lambda e: e.tensor_copy(M.ctl[:, :], ctl), st.t)
    g = GROUPS + MORE
    lst = K.sb("list", [g, 512], F32, "h2N")
    t = sp.dma(lst[:, :], M.meta.rearrange("(g p) w -> g (p w)", p=128), K.slot("s_list"), t_list, M.t_h2d, M.t_log, pe.last())
    s3 = K.bk.take()
    for w in range(3):
        tok = pe(lambda e, w=w: e.transpose(s3.ap[:, 64 * w:64 * w + g], lst[:, :].rearrange("g (p w) -> g w p", w=4)[:, w, :], K.ident[0:g, 0:g]), t, s3.was, signal=w == 2)
    kept = K.sb("kept", [128, 3 * g + 24])
    M.tok, M.row, M.w = kept[:, 0:g].bitcast(U32), kept[:, g:2 * g].bitcast(U32), kept[:, 2 * g:3 * g]
    M.tick = kept[:, 3 * g:3 * g + 24]
    for v, w in ((M.tok, 0), (M.row, 1), (M.w, 2)):
        M.t_list = dve(lambda e, v=v, w=w: e.tensor_copy(v, s3.ap[:, 64 * w:64 * w + g]), tok)
    s3.free = [M.t_list]
    assert at.n <= 3072, at.n


class Guarded:

    def __init__(self, queues):
        self.at = [(q, len(q.ops)) for q in queues]

    def close(self, test):
        for q, start in self.at:
            body = q.ops[start:]
            del q.ops[start:]
            if not body:
                continue
            n = raises(body, q.sem)
            q.ops.append(("guard", test, body, [(q.sem, q.count - n, n)] if n else []))


def raises(ops, sem):
    n = 0
    for op in ops:
        if op[0] == "guard":
            n += sum(by for _, _, by in op[3])
        elif op[0] != "register" and op[2] and op[2][0].num == sem.num:
            n += 1
    return n


def experts(K, xN, t_x, out):
    pe, act, dve, pool, sp, d, M, sb = K.pe, K.act, K.dve, K.pool, K.sp, K.d, K.moe, K.sb
    E, bk = M.experts, K.bk
    fence = lambda: [pe.last(), act.last(), dve.last(), pool.last()]
    start = fence() + [M.t_list]
    for q in (pe, act, dve, pool, sp):
        q.ops.append(("register", "pairs", M.ctl[0:1, 0:1], M.t_ctl, 2 ** PAIRS - 1))
        q.ops.append(("register", "more", M.ctl[0:1, 1:2], M.t_ctl, MORE))

    def bufs(name, n, shape=(D,), slots=True):
        out = []
        for i in range(n):
            b = Buf(sb(f"{name}{i}", [128, *shape], F32, name, 4096 * i), K.slot(f"s_{name}{i}") if slots else None)
            b.free = start
            out.append(b)
        return Ring(out)
    xg, xg2 = bufs("xg", 4), bufs("xg2_", 2, slots=False)
    XT, XT2 = bufs("XT", 2, (KT, 128), False), bufs("XT2_", 1, (KT, 128), False)
    Y, Y2 = bufs("Y", 3), bufs("Y2_", 2, slots=False)
    he = sb("he", [128, 512])
    heT = sb("heT", [128, 2, 128], F32, "he", 2048)
    t_he = [start, start]
    for b in xg.bufs + xg2.bufs:
        b.free = [dve(lambda e, b=b: e.memset(b.ap[:, :], 0.0), start)]

    def gather(b, g, slot):
        t = slot.token()
        pool.ops.append((_tokens([b.was, M.t_list, M.t_h2d]), lambda e: e.indirect_dma_start(
            out=b.ap[:, :], out_offset=None, in_=M.h2d, in_offset=bass.IndirectOffsetOnAxis(ap=M.tok[:, g:g + 1], axis=0),
            bounds_check=NX - 1, oob_is_err=False), (slot.sem, 16)))
        return b, t

    def turn_x(ring, b, t):
        x = ring.take()
        for c in range(2):
            s = bk.take()
            for k in range(4):
                tok = pe(lambda e, s=s, c=c, k=k: e.transpose(s.ap[:, 128 * k:128 * k + 128], b.ap[:, 512 * c + 128 * k:512 * c + 128 * k + 128], K.ident[:, :]),
                         t, s.was, signal=k == 3)
            src = s.ap[:, :].rearrange("p (k q) -> p k q", q=128)
            if c:
                t1 = act(lambda e, src=src: e.activation(x.ap[:, 4:8, :], src, ACT.Copy), tok, x.was)
            else:
                t0 = t1 = dve(lambda e, src=src: e.tensor_copy(x.ap[:, 0:4, :], src), tok, x.was)
            s.free = [t1]
        b.free = [tok]
        return x, [t0, t1]

    def mlp(x, t_x_, ws, y, g, beside=lambda: None):
        n = 128 // len(ws)
        s = bk.take()
        for k in range(KT):
            for j, (b, t_gu, t_dn) in enumerate(ws):
                o = slice(n * j, n * j + n)
                tok = pe(lambda e, k=k, o=o, b=b: e.matmul(s.ap[o, :], x.ap[:, k, o], b.gu[:, k, :], start=k == 0, stop=k == KT - 1, skip_group_check=True),
                         t_x_, t_gu, s.was, signal=k == KT - 1 and j == len(ws) - 1)
        x.free = [tok]
        t = act(lambda e: e.activation(he[:, 0:256], s.ap[:, 0:256], ACT.Silu), tok, t_he[0])
        t = dve(lambda e: e.tensor_tensor(he[:, 256:512], s.ap[:, 256:512], he[:, 0:256], ALU.mult), t)
        s.free = [t]
        got = beside()
        s2 = bk.take()
        for k in range(2):
            tok = pe(lambda e, k=k: e.transpose(s2.ap[:, 128 * k:128 * k + 128], he[:, 256 + 128 * k:384 + 128 * k], K.ident[:, :]), t, s2.was, signal=k == 1)
        t_he[0] = tok
        t = dve(lambda e: e.tensor_copy(heT[:, :, :], s2.ap[:, 0:256].rearrange("p (k q) -> p k q", q=128)), tok, t_he[1])
        s2.free = [t]
        ts = []
        for c in range(2):
            s = bk.take()
            for k in range(2):
                for j, (b, t_gu, t_dn) in enumerate(ws):
                    o = slice(n * j, n * j + n)
                    tok = pe(lambda e, s=s, k=k, o=o, b=b, c=c: e.matmul(s.ap[o, :], heT[:, k, o], b.dn[:, k, 512 * c:512 * c + 512], start=k == 0, stop=k == 1, skip_group_check=True),
                             t, t_dn, s.was, signal=k == 1 and j == len(ws) - 1)
            w = M.w[:, g:g + 1]
            if c:
                ts.append(dve(lambda e, s=s: e.tensor_scalar(y.ap[:, 512:1024], s.ap[:, :], w, None, ALU.mult), tok, y.was, M.t_list))
            else:
                ts.append(act(lambda e, s=s: e.activation(y.ap[:, 0:512], s.ap[:, :], ACT.Copy, scale=w), tok, y.was, M.t_list))
            s.free = [ts[-1]]
        t_he[1] = tok
        return ts, got

    def scatter(y, g, slot, *after):
        t = slot.token()
        pool.ops.append((_tokens(after), lambda e: e.indirect_dma_start(
            out=M.ybuf, out_offset=bass.IndirectOffsetOnAxis(ap=M.row[:, g:g + 1], axis=0), in_=y.ap[:, :], in_offset=None,
            bounds_check=2 * NX - 1, oob_is_err=False), (slot.sem, 16)))
        return t

    def guarded(queues, test, body):
        before = {id(b): b.free for b in bk.bufs}
        he_before = list(t_he)
        g = Guarded(queues)
        got = body()
        g.close(test)
        for b in bk.bufs:
            if b.free is not before[id(b)]:
                b.free = [before[id(b)], b.free]
        t_he[:] = [[x, y] for x, y in zip(he_before, t_he)]
        return got

    crowded = lambda i: lambda r: ((r["pairs"] >> i) & 1) > 0
    second = {}

    def gather2(i):
        st = second[i] = Ctx()
        st.slots = [K.slot(f"s_second{i}_{c}") for c in range(2)]
        b = xg2.take()
        g = Guarded((pool,))
        st.x = gather(b, 2 * i + 1, st.slots[0])
        g.close(crowded(i))

    def scatter2(i, y, ts):
        g = Guarded((pool,))
        second[i].stored = scatter(y, 2 * i + 1, second[i].slots[1], ts)
        g.close(crowded(i))

    def stored2(i):
        g = Guarded((pool,))
        second[i].y.free = [pool(lambda e: e.memset(M.tick[:, i:i + 1], 0.0), second[i].stored)]
        g.close(crowded(i))

    firsts = [gather(xg.take(), 2 * i, b.slot) for i, b in enumerate(list(xg.bufs))]
    gather2(0)
    gather2(1)
    nxt = turn_x(XT, *firsts[0])
    for i in range(PAIRS):
        ws = [E.ready[2 * i], E.ready[2 * i + 1]]
        y = Y.take()
        ts, nxt = mlp(*nxt, ws, y, 2 * i, lambda: turn_x(XT, *firsts[i + 1]) if i + 1 < PAIRS else None)
        y.free = [scatter(y, 2 * i, y.slot, ts)]
        y2 = second[i].y = Y2.take()
        ts = guarded((pe, act, dve), crowded(i), lambda: mlp(*turn_x(XT2, *second[i].x), ws, y2, 2 * i + 1)[0])
        for w, _, _ in ws:
            w.free = [pe.last()]
        E.load(2)
        scatter2(i, y2, ts)
        if i + 4 < PAIRS:
            b = xg.take()
            firsts.append(gather(b, 2 * i + 8, b.slot))
        if i + 2 < PAIRS:
            gather2(i + 2)
        if i >= 1:
            stored2(i - 1)
    stored2(PAIRS - 1)

    w = Buf(None)
    w.gu, w.dn = E.bufs[0].gu, E.bufs[0].dn

    def far(n):
        after = [b.free for b in E.bufs[:1]] + [pe.last()]

        def load(e, dst, src):
            v = e.value_load(M.ctl[0:1, 2 + n:3 + n], min_val=0, max_val=NE - 1)
            return e.dma_start(dst, src[bass.ds(v, 1)].rearrange("o p k c -> (o p) k c"))
        s_far = [K.slot(f"s_far_{n}{c}") for c in range(4)]
        t = [s_.token() for s_ in s_far[0:2]]
        sp.ops.append((_tokens(after), lambda e: load(e, w.gu[:, :, :], d["w_gu"]), (s_far[0].sem, 16)))
        sp.ops.append(([], lambda e: load(e, w.dn[:, :, :], d["w_dn"]), (s_far[1].sem, 16)))
        y, b = Y2.take(), xg2.take()
        ts, _ = mlp(*turn_x(XT2, *gather(b, GROUPS + n, s_far[2])), [(w, t[0], t[1])], y, GROUPS + n)
        y.free = [pool(lambda e: e.memset(M.tick[:, PAIRS + n:PAIRS + n + 1], 0.0), scatter(y, GROUPS + n, s_far[3], y.was, ts))]

    def all_far():
        far(0)
        for n in range(1, MORE):
            g = Guarded((pe, act, dve, pool, sp))
            far(n)
            g.close(lambda r, n=n: r["more"] > n)
    stored = [b.free for b in Y.bufs + Y2.bufs]
    g = Guarded((pe, act, dve, pool, sp))
    all_far()
    g.close(lambda r: r["more"] > 0)
    finish(K, xN, t_x, [stored, pool.last()], out)


def finish(K, xN, t_x, stored, out):
    act, dve, pool, sp, M, sb = K.act, K.dve, K.pool, K.sp, K.moe, K.sb
    after = [K.pe.last(), act.last(), dve.last(), pool.last()]
    row2 = sb("row2", [128, D])
    t_row2 = sp.dma(row2[:, :], K.d["rows"][:, 1, :], K.slot("s_row2"), after)
    yin = Ring([Buf(sb(f"yin{i}", [128, 2, D], F32, "yin", 8192 * i), K.slot(f"s_yin{i}")) for i in range(4)])
    for b in yin.bufs:
        b.free = after
    ms, rs = K.stat[:, 64:68], K.stat[:, 72:76]
    t_out = []
    s_out = [K.slot(f"s_out{i}") for i in range(T2)]
    for t_ in range(T2):
        b = yin.take()
        x = xN[:, t_, :]
        t = sp.dma(b.ap[:, :, :], M.ybuf[256 * t_:256 * t_ + 256, :].rearrange("(p c) n -> p c n", c=2), b.slot, b.was, stored)
        t = dve(lambda e, b=b, x=x: e.tensor_tensor(x, x, b.ap[:, 0, :], ALU.add), t, t_x[t_])
        t = dve(lambda e, b=b, x=x: e.tensor_tensor(x, x, b.ap[:, 1, :], ALU.add), t)
        t = act(lambda e, b=b, x=x, t_=t_: e.activation(b.ap[:, 0, :], x, ACT.Square, accum_out=ms[:, t_:t_ + 1]), t)
        t = dve(lambda e, t_=t_: e.tensor_scalar(ms[:, t_:t_ + 1], ms[:, t_:t_ + 1], 1.0 / D, EPS, ALU.mult, ALU.add), t)
        t = pool(lambda e, t_=t_: e.tensor_tensor(rs[:, t_:t_ + 1], ms[:, t_:t_ + 1], K.nhalf[:, 0:1], ALU.pow), t)
        t = dve(lambda e, b=b, x=x, t_=t_: e.scalar_tensor_tensor(b.ap[:, 1, :], x, rs[:, t_:t_ + 1], row2[:, :], ALU.mult, ALU.mult), t, t_row2)
        t = act.dma(out[128 * t_:128 * t_ + 128, :], b.ap[:, 1, :], s_out[t_], t)
        b.free = [t]
        t_out.append(t)
    sp.ops.append((_tokens(t_out), lambda e: None, None))


def buckets(dist):
    d32 = np.maximum(dist, 1).astype(np.float32)
    large = 16 + (np.log(d32 / np.float32(16)) / np.float32(np.log(128.0)) * np.float32(16)).astype(np.int32)
    return np.where(dist < 16, dist, np.minimum(large, 31))


def host(inputs):
    f = lambda n: np.asarray(inputs[n])
    out = {}
    x, ctx = f("x")[0], f("ctx")[0]
    cols = lambda a, n: a.reshape(n, 128).T
    out["xc"] = np.concatenate([x.T.reshape(KT, 128, NX), ctx.T.reshape(KT, 128, NC)], 2).transpose(1, 0, 2)
    sm = np.zeros((128, SMALL["n"]), np.float32)

    def put(name, a):
        a = a.reshape(128, -1)
        sm[:, SMALL[name]:SMALL[name] + a.shape[1]] = a
    put("norm_w", np.concatenate([cols(a, 8) for a in f("norm_w")], 1))
    put("b_mod", np.concatenate([cols(a, 24) for a in f("b_mod")], 1))
    put("qn_w", np.concatenate([cols(a, 2) for a in f("q_norm_w")], 1))
    put("kvn_w", f("kv_norm_w").T)
    put("sc_w", f("sc_conv_w").reshape(2, 3, 2, 128).transpose(3, 0, 2, 1))
    put("cf_w", f("cf_conv_w").reshape(2, 31, 2, 128).transpose(3, 0, 2, 1))
    for n, s in (("cf_b", "cf_conv_b"), ("ln_w", "cf_ln_w"), ("ln_b", "cf_ln_b"), ("pw_b", "cf_pw_b")):
        put(n, np.concatenate([cols(a, 2) for a in f(s)], 1))
    for n, s in (("qh_w", "q_head_norm_w"), ("kh_w", "k_head_norm_w")):
        a = np.ones((128, 2), np.float32)
        a[0:64] = f(s)[:, 0:64].T
        put(n, a)
    put("c", np.stack([cols(f("c")[0], 8), cols(f("c_ctx"), 8)], 2))
    out["small"] = sm
    out["ident"] = np.eye(128, dtype=np.float32)
    pos = np.arange(NX)
    inv = (10000.0 ** (-np.arange(8, dtype=np.float64) / 8)).astype(np.float32)
    ang = np.concatenate([(pos // 64)[:, None].astype(np.float32) * inv, (pos % 64)[:, None].astype(np.float32) * inv], 1)
    cos, sin = np.cos(ang), np.sin(ang)
    lay = lambda a: a.reshape(4, 128, 32).transpose(1, 0, 2).astype(np.float32)
    out["ctab"] = lay(np.concatenate([cos, cos], 1))
    out["stab"] = lay(np.concatenate([-sin, sin], 1))
    rw = []
    for l in range(2):
        q, k = f("q_head_norm_w")[l, 64:], f("k_head_norm_w")[l, 64:]
        rw.append(np.stack([q, np.concatenate([q[16:], q[:16]]), k, np.concatenate([k[16:], k[:16]])]))
    out["rope_w"] = np.broadcast_to(np.stack(rw)[:, None], (2, 128, 4, 32))
    out["w_mod"] = f("w_mod").reshape(2, KT, 128, 3072)
    w = f("w_in")
    tile = lambda l, c: w[l][:, c:c + 128].reshape(KT, 128, 128).transpose(1, 0, 2).reshape(128, 1024)
    out["w_in"] = np.stack([np.stack([tile(l, COLS[n] + 128 * i) for n, i in TILES]) for l in range(2)])
    out["w_kr"] = np.stack([w[l][:, 384:416].reshape(KT, 128, 32).transpose(1, 0, 2) for l in range(2)])
    out["w_uq"] = f("w_uq").reshape(2, 2, 128, 768).transpose(0, 2, 1, 3)
    kv = f("w_ukv").reshape(2, 128, HEADS, 128)
    out["w_ukv"] = np.concatenate([kv[..., :64].reshape(2, 128, 512), kv[..., 64:].reshape(2, 128, 512)], 2)
    out["pw"] = f("cf_pw_w").reshape(2, 2, 128, 256).transpose(0, 2, 1, 3)
    out["w_out"] = f("w_out").reshape(2, KT, 128, KT, 128).transpose(0, 3, 2, 1, 4).reshape(2, KT, 128, 1024)
    s2 = np.zeros((128, SMALL2["n"]), np.float32)
    s2[:, 0:8] = cols(f("attn_norm_2")[0], 8)
    s2[:, 8:12] = cols(f("out_norm_dil_2")[0], 4)
    s2[:, 12:16] = cols(f("out_norm_fox_2")[0], 4)
    s2[0:8, 16] = f("b_forget_2")[0]
    out["small2"] = s2
    w = f("w_in_2")[0]
    t2 = lambda c: w[:, c:c + 128].reshape(KT, 128, 128).transpose(1, 0, 2).reshape(128, 1024)
    v2 = lambda c: [w[256 * k:256 * k + 256, c:c + 512].reshape(2, 128, 512).transpose(1, 0, 2).reshape(128, 1024) for k in range(4)]
    tiles = v2(1024)
    for p in range(8):
        o = 128 * p if p < 4 else 1536 + 128 * (p - 4)
        tiles += [t2(o), t2(o + 512)]
        if p == 2:
            tiles += v2(2560)
    out["w_in2"] = np.stack(tiles)
    out["w_out2"] = f("w_out_2").reshape(KT, 128, 1024)
    out["rows"] = np.broadcast_to(np.stack([f("ffn_norm_2")[0], f("final_norm_2")]), (128, 2, 1024))
    w_r = np.concatenate([f("w_router_group_2")[0], f("w_router_expert_2")[0]], 1)
    out["w_r"] = w_r.reshape(KT, 128, 36).transpose(1, 0, 2)
    gu = np.concatenate([f("w_expert_gate_2")[0], f("w_expert_up_2")[0]], 2)
    out["w_gu"] = gu.reshape(NE, KT, 128, 2 * DE).transpose(0, 2, 1, 3)
    out["w_dn"] = f("w_expert_down_2")[0].reshape(NE, 2, 128, D).transpose(0, 2, 1, 3)
    out["empty"] = np.tile(np.array([1e6, 1e6, 0, 0], np.float32), (GROUPS + MORE, 128))
    rc = np.zeros((128, RC["n"] + 36), np.float32)
    e = np.arange(NE)
    rc[:, 0:4] = 4 - np.arange(4)
    rc[:, 4:36] = 32 - e
    rc[:, 36:40] = 128 * np.arange(1, 5) + 0.5
    base = 256 * (e // 2) + 64 * (e % 2)
    rc[:, RC["base"]:RC["base"] + NE] = base
    rc[:, RC["over"]:RC["over"] + NE] = 128 * GROUPS - 128 - 64 - base - 0
    tok = 128 * np.arange(T2)[None, :] + np.arange(128)[:, None]
    ids = np.zeros((128, T2, 2, 4), np.float32)
    ids[..., 0] = tok[..., None]
    ids[..., 1] = 2 * tok[..., None] + np.arange(2)
    rc[:, RC["ids"]:RC["ids"] + 32] = ids.reshape(128, 32)
    rc[:, RC["pow2"]:RC["pow2"] + PAIRS] = 2.0 ** np.arange(PAIRS)
    rc[:, RC["nth"]:RC["nth"] + MORE] = np.arange(MORE)
    rc[:, RC["tri"]:RC["tri"] + 128] = np.arange(128)[:, None] < np.arange(128)[None, :]
    rc[:, RC["n"]:] = np.concatenate([f("b_router_group_2")[0], f("b_router_expert_2")[0]])
    out["rc"] = rc
    out["w_f"] = w[:, 3072:3080].reshape(KT, 128, 8).transpose(1, 0, 2)
    sel = np.zeros((128, 8, 128), np.float32)
    for h in range(8):
        sel[h, h] = sel[32 + h, h] = 1
    out["sel"] = sel.reshape(128, 1024)
    dist = np.arange(128)[:, None] + 384 - np.arange(512)[None, :]
    n = (dist <= 128) * 1 + (dist % 4 == 0) + (dist % 16 == 0)
    ok = (dist >= 0) & (n > 0)
    out["lnn"] = np.where(ok, np.log(np.maximum(n, 1)), -BIG).astype(np.float32)
    out["causal"] = np.where(dist >= 0, 0, -BIG).astype(np.float32)
    out["bias"] = f("rel_bias_2")[buckets(np.maximum(dist, 0))].transpose(2, 0, 1)
    return {k: np.ascontiguousarray(v) for k, v in out.items()}


def play(K):
    with K.nc.Block() as block:
        block.sync(K.sp.play)
        block.tensor(K.pe.play)
        block.vector(K.dve.play)
        block.scalar(K.act.play)
        block.gpsimd(K.pool.play)


def program(nc, dram, out):
    with ExitStack() as ctx:
        K = setup(nc, ctx, dram)
        K.ctx = ctx
        x1, t_x1, t_r = first_block(K)
        second_block(K, x1, t_x1, t_r, out)
        play(K)


def kernel(**inputs):
    import concourse.bacc as _bacc
    from concourse.bass_utils import run_bass_kernel_spmd as _run

    nc = _bacc.Bacc("TRN2", target_bir_lowering=False, num_devices=1)
    arrays, dram = {}, {}
    for name, a in host(inputs).items():
        arrays[f"in_{name}_dram"] = a
        dram[name] = nc.dram_tensor(f"in_{name}_dram", a.shape, mybir.dt.from_np(a.dtype), kind="ExternalInput").ap()
    out = nc.dram_tensor("out_0_dram", (NX, D), F32, kind="ExternalOutput").ap()
    program(nc, dram, out)
    r = _run(nc, [arrays], core_ids=[0])
    return r.results[0]["out_0_dram"].reshape(1, NX, D)
```

```python
from contextlib import ExitStack

import numpy as np

import concourse.bass as bass
from concourse import mybir

F32 = mybir.dt.float32
F32R = mybir.dt.float32r
I32 = mybir.dt.int32
U32 = mybir.dt.uint32
ACT = mybir.ActivationFunctionType
ALU = mybir.AluOpType
AX = mybir.AxisListType

NX = 512
NC = 256
NT = NX + NC
D = 1024
KT = 8
HEADS = 8
QK = 96
EPS = 1e-6
LN_EPS = 1e-5

COLS = dict(cq=0, ckv=256, kr=384, ga=416, sc_in=928, sc_b=1184, sc_c=1440, gb=1696, glu=1952, gc=2464)


def _tile_starts():
    t = [("cq", 0), ("cq", 1), ("glu", 2), ("ckv", 0)]
    t += [("glu", 3), ("glu", 0), ("glu", 1)]
    for i in range(2):
        t += [("sc_in", i), ("sc_c", i), ("sc_b", i), ("gb", i)]
    t += [("gc", i) for i in range(2)] + [("ga", i) for i in range(4)]
    return t


TILES = _tile_starts()

SMALL = {}


def _small_columns():
    at = 0
    for name, n in (("norm_w", 16), ("b_mod", 48), ("qn_w", 4), ("kvn_w", 2), ("sc_w", 12), ("cf_w", 124),
                    ("cf_b", 4), ("ln_w", 4), ("ln_b", 4), ("pw_b", 4), ("qh_w", 2), ("kh_w", 2), ("c", 16)):
        SMALL[name] = at
        at += n
    SMALL["n"] = at


_small_columns()

SMALL2 = dict(norm=0, on=8, bf=16, n=17)


class Queue:

    def __init__(self, sem):
        self.sem, self.count, self.ops = sem, 0, []

    def __call__(self, make, *after, signal=True):
        self.ops.append((_tokens(after), make, (self.sem, 1) if signal else None))
        if not signal:
            return None
        self.count += 1
        return (self.sem, self.count)

    def dma(self, out, src, slot, *after):
        slot.count += 16
        self.ops.append((_tokens(after), lambda e: e.dma_start(out, src), (slot.sem, 16)))
        return (slot.sem, slot.count)

    def last(self):
        return (self.sem, self.count)

    def play(self, e):
        self.regs = {}
        self.run(e, self.ops, {})

    def run(self, e, ops, seen):
        for op in ops:
            if op[0] == "register":
                _, name, ap, after, top = op
                e.wait_ge(*after)
                self.regs[name] = e.value_load(ap, min_val=0, max_val=top)
                continue
            if op[0] == "guard":
                _, test, body, raised = op
                with e.If(test(self.regs)):
                    self.run(e, body, dict(seen))
                with e.Else():
                    for sem, before, by in raised:
                        e.wait_ge(sem, before)
                        e.sem_inc(sem, by)
                continue
            after, make, signal = op
            for sem, value in after:
                if seen.get(sem.num, 0) < value:
                    e.wait_ge(sem, value)
                    seen[sem.num] = value
            ins = make(e)
            if signal:
                ins.then_inc(*signal)


class Slot:

    def __init__(self, sem):
        self.sem, self.count = sem, 0

    def token(self):
        self.count += 16
        return (self.sem, self.count)


class Buf:

    def __init__(self, ap, slot=None):
        self.ap, self.free, self.slot, self.was = ap, [], slot, None


class Ring:
    def __init__(self, bufs):
        self.bufs = list(bufs)

    def take(self):
        b = self.bufs.pop(0)
        assert b.free is not None, "taken before its last readers are known"
        b.was, b.free = b.free, None
        self.bufs.append(b)
        return b

    def hold(self):
        b = self.take()
        self.bufs.remove(b)
        return b

    def release(self, b):
        self.bufs.append(b)


def _tokens(after):
    out = []
    for a in after:
        if a is None:
            continue
        if isinstance(a, tuple) and len(a) == 2 and isinstance(a[1], int):
            out.append(a)
        else:
            out += _tokens(a)
    return out


def plan(items, base, end):
    rng = np.random.default_rng(0)
    order = sorted(items, key=lambda x: (-(x[3] - x[2]), -x[1]))
    weight = {x[0]: float(i) for i, x in enumerate(order)}
    for _ in range(20000):
        placed = []
        for name, size, a, b in sorted(items, key=lambda x: weight[x[0]]):
            size = (size + 31) // 32 * 32
            spans = sorted((o, o + s) for _, o, s, p, q in placed if not (q < a or b < p))
            at = base
            for lo, hi in spans:
                if at + size <= lo:
                    break
                at = max(at, hi)
            if at + size > end:
                weight[name] -= 8 + 8 * rng.random()
                break
            placed.append((name, at, size, a, b))
        else:
            return {name: at for name, at, _, _, _ in placed}
    assert False, "no room"


class Ctx:
    pass


def setup(nc, ctx, dram):
    K = Ctx()
    K.nc, K.d = nc, dram
    sem = lambda name: ctx.enter_context(nc.semaphore(name))
    K.pe, K.act, K.dve, K.pool, K.sp = (Queue(sem(n)) for n in ("s_pe", "s_act", "s_dve", "s_pool", "s_sp"))
    K.slot = lambda name: Slot(sem(name))

    kb = 1024
    row = NT * 4
    items = [
        ("ident", 512, 0, 199), ("ones", 512, 0, 199), ("ctab", 512, 0, 75), ("stab", 512, 0, 75),
        ("small", 4 * SMALL["n"], 0, 99), ("c2T", 1024, 0, 20), ("nhalf", 64, 0, 199),
        ("mod", 2 * 4 * 8 * 2 * 4, 0, 99), ("rope_w", 4 * 128, 0, 75), ("rope_t", 4 * 512, 0, 75),
        ("stat", 4 * 256, 0, 199),
        ("raw", 2 * 4 * kb, 0, 130), ("whi", 2 * 4 * kb, 0, 113), ("wlo", 2 * 4 * kb, 0, 113),
        ("xc", 8 * row, 0, 0), ("wmod0", 64 * kb, 0, 0), ("wgate", 16 * kb, 10, 10), ("modrow", 2 * kb, 0, 10),
        ("tmpa", 5 * 3264, 0, 24), ("tmpc", 5 * 3264, 40, 74), ("tmpe", 5 * 3264, 90, 100),
        ("x1", 8 * 512 * 4, 40, 100), ("xc1", 8 * 256 * 4, 42, 44), ("xr", 3 * 2 * kb, 40, 42), ("acc", 2 * kb, 40, 44), ("accc", 1024, 42, 60), ("acc2", 2 * kb, 90, 100),
        ("wv", 16 * kb, 92, 100),
    ]
    for l, a in ((0, 0), (1, 50)):
        nt = 6 if l == 0 else 4
        r = row if l == 0 else 512 * 4
        kv = a + 20 if l == 0 else a + 10
        items += [
            (f"hxh{l}", 16 * kb, a if l == 0 else 42, a + 24), (f"hxl{l}", 16 * kb, a if l == 0 else 42, a + 24),
            (f"hch{l}", 8 * kb, a if l == 0 else 44, a + (24 if l == 0 else 10)), (f"hcl{l}", 8 * kb, a if l == 0 else 44, a + (24 if l == 0 else 10)),
            (f"cqw{l}", 3 * row, a + 10, a + 20), (f"krT{l}", row, a + 10, a + 10), (f"krN{l}", 6 * 32 * 4, a + 10, a + 20),
            (f"wkr{l}", 1024, a + 10, a + 10), (f"wkrh{l}", 1024, a + 10, a + 10), (f"wkrl{l}", 1024, a + 10, a + 10),
            (f"wuq{l}", 6 * kb, a + 10, a + 20), (f"wukv{l}", 4 * kb, a + 10, a + 20), (f"pw{l}", 2 * kb, a + 10, a + 24),
            (f"glu{l}", 2 * 828 * 4, a + 10, a + 24), (f"z{l}", 2 * 798 * 4, a + 10, a + 24),
            (f"scp{l}", 2 * 772 * 4, a + 20, a + 20), (f"scz{l}", 772 * 4, a + 20, a + 20),
            (f"qN{l}", nt * 768 * 4, kv, a + 30), (f"kN{l}", 6 * 768 * 4, kv, a + 30), (f"vN{l}", 6 * 512 * 4, kv, a + 30),
            (f"ga{l}", 4 * r, a + 24, a + 30), (f"gc{l}", 2 * r, a + 24, a + 24),
            (f"qT{l}", 4 * r, a + 30, a + 30), (f"kT{l}", 4 * row, a + 30, a + 30),
            (f"P{l}", 4 * row, a + 30, a + 30), (f"PTa{l}", 12 * kb, a + 30, a + 30), (f"PTb{l}", 6 * kb, a + 30, a + 30),
            (f"PTc{l}", 4 * kb if l == 0 else 32, a + 30, a + 30), (f"og{l}", 3 * kb, a + 30, a + 30),
            (f"wo{l}", 48 * kb, a + 40, a + 42),
            (f"yax{l}", 16 * kb, a + 30, a + 40 + 2 * l), (f"ysx{l}", 8 * kb, a + 20, a + 40 + 2 * l), (f"ypx{l}", 8 * kb, a + 24, a + 40 + 2 * l),
        ]
        if l == 0:
            items += [("yac0", 8 * kb, 30, 42), ("ysc0", 4 * kb, 20, 42), ("ypc0", 4 * kb, 24, 42)]
    items += [
        ("small2", 4 * SMALL2["n"], 0, 199), ("xN", 16 * kb, 100, 199), ("hh2", 16 * kb, 92, 113), ("hl2", 16 * kb, 92, 113),
        ("wf", 256, 92, 110), ("wfh", 256, 92, 110), ("wfl", 256, 92, 110),
        ("tmpf", 4 * 2 * kb, 110, 130), ("fC", 2 * kb, 110, 120), ("self", 4 * kb, 110, 110), ("sel", 4 * kb, 110, 120),
        ("vdil", 8 * kb, 100, 113), ("vfox", 8 * kb, 110, 120), ("q2", 16 * kb, 110, 120), ("k2", 8 * kb, 110, 120),
        ("tab", 3 * 2 * kb, 110, 113), ("lnn", 2 * kb, 110, 113), ("tri", 2 * kb, 110, 120),
        ("P2", 4 * 2 * kb, 110, 120), ("PT2", 16 * kb, 110, 120),
        ("y2h", 16 * kb, 110, 130), ("y2l", 16 * kb, 110, 130),
        ("wo2d", 32 * kb, 114, 130), ("wo2f", 32 * kb, 114, 130),
        ("row1", 4 * kb, 130, 139), ("row2", 4 * kb, 140, 199), ("kept", 4 * (3 * (GROUPS + MORE) + 24), 131, 199), ("ctl", 64, 131, 199), ("h2N", 16 * kb, 131, 139), ("h2T", 16 * kb, 131, 139),
        ("wr", 8 * 36 * 4, 131, 139), ("rt", 12 * kb, 131, 139), ("rc", 4 * kb, 131, 139),
        ("xg", 4 * 4 * kb, 140, 149), ("xg2_", 2 * 4 * kb, 140, 149), ("XT", 2 * 4 * kb, 140, 149), ("XT2_", 4 * kb, 140, 149),
        ("he", 4 * kb, 140, 149), ("Y", 3 * 4 * kb, 140, 149), ("Y2_", 2 * 4 * kb, 140, 149),
        ("yin", 4 * 8 * kb, 150, 199),
    ] + [(f"we{i}", 24 * kb, 130 if i < 2 else 131, 149) for i in range(5)]
    base = 16512
    K.at = plan(items, base, 229344)

    def sb(name, shape, dt=F32, where=None, skip=0):
        return nc.alloc_sbuf_tensor_at(name, shape, dt, offset=K.at[where or name] + skip)
    K.sb = sb
    return K


class Weights:

    def __init__(self, K, srcs):
        self.K, self.srcs, self.done = K, srcs, []
        self.raw = [Buf(K.sb(f"raw{i}", [128, 1024], F32, "raw", 4096 * i), K.slot(f"s_raw{i}")) for i in range(2)]
        self.hi = [Buf(K.sb(f"whi{i}", [128, 1024], F32R, "whi", 4096 * i)) for i in range(2)]
        self.lo = [Buf(K.sb(f"wlo{i}", [128, 1024], F32R, "wlo", 4096 * i)) for i in range(2)]
        self.loaded, self.limit, self.place = [], len(srcs), {}
        self.load()
        self.load()

    def load(self):
        i = len(self.loaded)
        if i < len(self.srcs):
            b = self.raw[i % 2]
            self.loaded.append(self.K.sp.dma(b.ap[:, :], self.srcs[i], b.slot, b.free))

    def split(self):
        K, i = self.K, len(self.done)
        if i >= len(self.srcs):
            return
        raw, hi, lo = self.raw[i % 2], *self.place.get(i, (self.hi[i % 2], self.lo[i % 2]))
        assert hi.free is not None and lo.free is not None
        t_hi = K.act(lambda e: e.activation(hi.ap[:, :], raw.ap[:, :], ACT.Copy), self.loaded[i], hi.free)
        t_lo = K.pool(lambda e: e.tensor_tensor(lo.ap[:, :], raw.ap[:, :], hi.ap[:, :].bitcast(F32), ALU.subtract),
                      self.loaded[i], t_hi, lo.free)
        raw.free = [t_hi, t_lo]
        hi.free = lo.free = None
        self.done.append((hi, lo, t_hi, t_lo))
        self.load()

    def get(self, i):
        while len(self.done) < min(i + 2, self.limit):
            self.split()
        return self.done[i]

    def release(self, i, tok):
        hi, lo, _, _ = self.done[i]
        hi.free = lo.free = [tok]


class Beside:

    def __init__(self):
        self.jobs = []

    def add(self, steps, rate, wait=0):
        self.jobs.append([steps, rate, -wait])

    def gap(self):
        for j in list(self.jobs):
            j[2] += j[1]
            while j[2] >= 1:
                j[2] -= 1
                if next(j[0], self) is self:
                    self.jobs.remove(j)
                    break

    def drain(self):
        while self.jobs:
            self.gap()


class Pair:

    def __init__(self, hi, lo, t_hi, t_lo):
        self.hi, self.lo, self.t_hi, self.t_lo = hi, lo, t_hi, t_lo


def mm3(K, dst, ws, xs, gap=None, order=None):
    tok = None
    order = order or list(range(len(ws)))
    for k in order:
        w = ws[k]
        for a, part, p in ((w.hi, 0, 0), (w.hi, 1, 1), (w.lo, 0, 2)):
            for j, (o, seg, c, cols) in enumerate(dst):
                x = xs[seg][k]
                b = (x.hi, x.lo)[part][:, c:c + cols]
                start, stop = k == order[0] and p == 0, k == order[-1] and p == 2
                tok = K.pe(lambda e, o=o, a=a, b=b, start=start, stop=stop: e.matmul(o, a, b, start=start, stop=stop),
                           (w.t_hi, x.t_hi, w.t_lo)[p], (x.t_hi, x.t_lo, x.t_hi)[p], signal=stop and j == len(dst) - 1)
        if gap and order.index(k) % 2:
            gap()
    return tok


def tile_pairs(w, m=128):
    hi, lo, t_hi, t_lo = w
    return [Pair(hi.ap[:, 128 * k:128 * k + m], lo.ap[:, 128 * k:128 * k + m], t_hi, t_lo) for k in range(KT)]


def begin(K):
    nc, d = K.nc, K.d
    pe, act, dve, pool, sp = K.pe, K.act, K.dve, K.pool, K.sp
    sb = K.sb
    K.ident = sb("ident", [128, 128])
    K.ones = sb("ones", [128, 128])
    K.ctab = sb("ctab", [128, 4, 32])
    K.stab = sb("stab", [128, 4, 32])
    K.small = sb("small", [128, SMALL["n"]])
    K.c2T = sb("c2T", [128, KT, 32])
    K.nhalf = sb("nhalf", [128, 16])
    K.mod = sb("mod", [128, 2, 4, KT, 2])
    K.rope_w = sb("rope_w", [128, 4, 32])
    K.rope_t = sb("rope_t", [128, 4, 4, 32])
    K.stat = sb("stat", [128, 256])
    K.modrow = sb("modrow", [128, 512])
    K.t_small = sp.dma(K.small[:, :], d["small"], K.slot("s_small"))
    K.t_ident = act.dma(K.ident[:, :], d["ident"], K.slot("s_ident"))
    K.t_ones = dve(lambda e: e.memset(K.ones[:, :], 1.0))
    K.t_nhalf = dve(lambda e: e.memset(K.nhalf[:, :], -0.5))
    t = dve(lambda e: e.memset(K.c2T[:, :, :], 0.0))
    K.t_c2 = act(lambda e: e.activation(K.c2T[:, :, 0:2],
                                        K.small[:, SMALL["c"]:SMALL["c"] + 16].rearrange("p (k v) -> p k v", v=2),
                                        ACT.Silu), K.t_small, t)
    K.psum = K.ctx.enter_context(nc.psum_tensor("ps", [128, 4096], F32))
    ps = [Buf(K.psum[:, 1024 * i:1024 * i + 1024]) for i in range(4)]
    K.ps, K.px = Ring(ps[:2]), Ring(ps[2:])
    K.s_rope = K.slot("s_rope")
    K.t_mod_read = []
    K.beside = Beside()


def fence(K):
    return [q.last() for q in (K.pe, K.act, K.dve, K.pool)]


def small(K, name, l, n, i=0, cols=1):
    at = SMALL[name] + n * l + i
    return K.small[:, at:at + cols]


def mod_columns(K, l, part, view, pairs, tok, *after):
    dve, mod = K.dve, K.mod
    for c, js in enumerate(pairs):
        b = small(K, "b_mod", l, 24, 8 * part + 4 * c, 4).unsqueeze(2).to_broadcast([128, 4, 2])
        dst = mod[:, l, part, 4 * c:4 * c + 4, :]
        for j in js:
            t = dve(lambda e, dst=dst, j=j, b=b: e.tensor_tensor(dst, view[:, :, j, 0:2], b, ALU.add), tok, K.t_small, *after)
            b, tok = dst, t
    t_read = t
    if part == 1:
        nw = small(K, "norm_w", l, 8, 0, 8).unsqueeze(2).to_broadcast([128, KT, 2])
        t = dve(lambda e: e.scalar_tensor_tensor(mod[:, l, 1, :, :], mod[:, l, 1, :, :], 1.0, nw, ALU.add, ALU.mult), t)
    return t_read, t


def mod_first(K, wm, t_wm):
    pe, act = K.pe, K.act
    s = K.px.take()
    for k in range(KT):
        for j in range(4):
            tok = pe(lambda e, k=k, j=j: e.matmul(s.ap[32 * j:32 * j + 32, 0:512], K.c2T[:, k, :], wm[:, k, 512 * j:512 * j + 512],
                                                  start=k == 0, stop=k == KT - 1, skip_group_check=True),
                     K.t_c2, t_wm[k], s.was if k == 0 else None, signal=k == KT - 1 and j == 3)
    t = act(lambda e: e.activation(K.modrow[:, :], s.ap[:, 0:512], ACT.Copy), tok)
    for q in range(4):
        tok = pe(lambda e, q=q: e.transpose(s.ap[:, 512 + 128 * q:640 + 128 * q], K.modrow[:, 128 * q:128 * q + 128], K.ident[:, :]),
                 t, K.t_ident, signal=q == 3)
    K.t_mod_read = [tok]
    view = s.ap[:, 512:1024].rearrange("p (t j r) -> p t j r", t=4, j=4)
    _, t_scale = mod_columns(K, 0, 1, view, ((2,), (3,)), tok)
    t_read, t = mod_columns(K, 0, 0, view, ((0,), (1,)), tok)
    s.free = [t_read]
    K.t_mod = [[t_scale, t], None]


def mod_rest(K, after):
    pe, act = K.pe, K.act
    parts = [(0, 2), (1, 0), (1, 1), (1, 2)]
    wg = [Buf(K.sb(f"wgate_{i}", [128, 2, 1024], F32, "wgate", 8192 * i), K.slot(f"s_gate{i}")) for i in range(2)]
    for g in wg:
        g.free = after
    jobs = [(l, part, q) for l, part in parts for q in range(4)]

    def load(j):
        if j < len(jobs):
            l, part, q = jobs[j]
            g = wg[j % 2]
            g.tok = K.sp.dma(g.ap[:, :, :], K.d["w_mod"][l, 2 * q:2 * q + 2, :, 1024 * part:1024 * part + 1024].rearrange("k p c -> p k c"), g.slot, g.free)
    load(0)
    load(1)
    yield
    t_done = {}
    for at, (l, part, q) in enumerate(jobs):
        if q == 0:
            s = K.px.hold()
        g = wg[at % 2]
        for k in range(2):
            for c in range(2):
                j = 2 * (q % 2) + c
                tok = pe(lambda e, g=g, k=k, c=c, j=j, q=q, s=s: e.matmul(
                    s.ap[32 * j:32 * j + 32, 0:512], K.c2T[:, 2 * q + k, :], g.ap[:, k, 512 * c:512 * c + 512],
                    start=q < 2 and k == 0, stop=q >= 2 and k == 1, skip_group_check=True),
                    g.tok, s.was if q == 0 else None, signal=k == 1 and c == 1)
        g.free = [tok]
        load(at + 2)
        if q < 3:
            yield
            continue
        t = act(lambda e, s=s: e.activation(K.modrow[:, :], s.ap[:, 0:512], ACT.Copy), tok, K.t_mod_read)
        yield
        for r in range(4):
            tok = pe(lambda e, r=r, s=s: e.transpose(s.ap[:, 512 + 128 * r:640 + 128 * r], K.modrow[:, 128 * r:128 * r + 128], K.ident[:, :]), t, signal=r == 3)
        K.t_mod_read = [tok]
        yield
        view = s.ap[:, 512:1024].rearrange("p (t j r) -> p t j r", t=4, j=4)
        t_read, t_done[l, part] = mod_columns(K, l, part, view, ((0, 2), (1, 3)), tok)
        s.free = [t_read]
        K.px.release(s)
        yield
    K.t_mod[1] = [t_done[1, 0], t_done[1, 1]]
    K.t_gate = [t_done[0, 2], t_done[1, 2]]


class Norm:

    def __init__(self, K, nt, d=D, eps=EPS, nk=KT, ring=None, c=0):
        self.K, self.nt, self.d, self.eps, self.nk, self.k, self.c = K, nt, d, eps, nk, 0, c
        self.ring = ring or K.px
        self.s = self.ring.hold()

    def add(self, sq, tok):
        K, k = self.K, self.k
        for i in range(self.nt):
            self.tok = K.pe(lambda e, i=i: e.matmul(self.s.ap[:, i:i + 1], sq[:, 128 * i:128 * i + 128], K.ones[:, 0:1],
                                                    start=k == 0 and i == 0, stop=k == self.nk - 1, skip_group_check=True),
                            tok, K.t_ones, self.s.was if k == 0 and i == 0 else None, signal=i == self.nt - 1)
        self.k += 1
        return self.tok

    def finish(self, ms, rstd, *after):
        K, n = self.K, self.nt
        t = K.dve(lambda e: e.tensor_scalar(ms, self.s.ap[:, 0:n], 1.0 / self.d, self.eps, ALU.mult, ALU.add), self.tok, *after)
        self.s.free = [t]
        self.ring.release(self.s)
        return K.pool(lambda e: e.tensor_tensor(rstd, ms, K.nhalf[:, 0:n], ALU.pow), t, K.t_nhalf)


def across(K, rstd, t_rstd, nt, diag, t_diag_free, c=0):
    s = K.px.take()
    for i in range(nt):
        g = diag[i % len(diag)]
        t = K.dve(lambda e, g=g, i=i: e.tensor_scalar(g.ap, K.ident[:, :], rstd[:, i:i + 1], None, ALU.mult), t_rstd, K.t_ident, g.free, t_diag_free)
        tok = K.pe(lambda e, g=g, i=i: e.matmul(s.ap[:, 128 * i:128 * i + 128], K.ones[:, :], g.ap, start=True, stop=True),
                   t, s.was if i == 0 else None)
        g.free = [tok]
    return s, tok


def spread(K, nt, rstd, t_r, tmps):
    db = tmps.take()
    rb, t = across(K, rstd, t_r, nt, [Buf(db.ap[:, 128 * q:128 * q + 128]) for q in range(6)], db.was)
    db.free = [t]
    return rb, t


def next_h(K, acc, t_acc, nt, c, n, x, t_x, v, out, l, tmps, at, after, res):
    N = Norm(K, nt, nk=1)
    N.add(acc, t_acc)
    ms, rs = K.stat[:, at:at + nt], K.stat[:, at + 8:at + 8 + nt]
    t_r = N.finish(ms, rs, after)
    yield
    rb, t_rb = spread(K, nt, rs, t_r, tmps)
    yield
    hh, hl = out
    pend = None
    for k in range(KT):
        b = tmps.hold()
        o = b.ap[:, 0:n]
        w = K.mod[:, l, 1, k, v:v + 1] if l < 2 else K.small2[:, k:k + 1]
        t = K.dve(lambda e, k=k, o=o, w=w: e.scalar_tensor_tensor(o, x(k), w, rb.ap[:, 0:n], ALU.mult, ALU.mult),
                  t_rb, K.t_mod[l] if l < 2 else K.t_small2, t_x[k], b.was)
        if k == KT - 1:
            rb.free = [t]
        hi, lo = hh[:, k, c:c + n], hl[:, k, c:c + n]
        if l < 2:
            shift = K.mod[:, l, 0, k, v:v + 1]
            t_hi = K.act(lambda e, hi=hi, o=o, shift=shift: e.activation(hi, o, ACT.Identity, bias=shift), t, after)
            make = lambda o=o, hi=hi, lo=lo, shift=shift, t_hi=t_hi: K.dve(
                lambda e: e.scalar_tensor_tensor(lo, o, shift, hi.bitcast(F32), ALU.add, ALU.subtract), t_hi, after)
        else:
            t_hi = K.act(lambda e, hi=hi, o=o: e.activation(hi, o, ACT.Copy), t, after)
            make = lambda o=o, hi=hi, lo=lo, t=t, t_hi=t_hi: K.pool(
                lambda e: e.tensor_tensor(lo, o, hi.bitcast(F32), ALU.subtract), t, t_hi, after)

        def finish(k=k, b=b, make=make, t_hi=t_hi):
            t_lo = make()
            b.free = [t_hi, t_lo]
            tmps.release(b)
            res.append(Pair(hh[:, k, :], hl[:, k, :], t_hi, t_lo))
        if pend:
            pend()
        pend = finish
        if k == KT - 1:
            pend()
        yield


def tmp_ring(K, name, n, width=816):
    return Ring([Buf(K.sb(f"{name}_{i}", [128, width], F32, name, 4 * width * i)) for i in range(n)])


def first_layer_block(K, l, hT, wt, w0, tmps):
    pe, act, dve, pool, sp, d, px = K.pe, K.act, K.dve, K.pool, K.sp, K.d, K.px
    both = l == 0
    n_own = NT if both else NX
    segs = [(0, NX), (NX, NC)] if both else [(0, NX)]
    all_segs = [(0, NX), (NX, NC)]
    nt_q = 6 if both else 4
    sb = lambda name, shape, dt=F32: K.sb(name + str(l), shape, dt)
    beside = K.beside

    wuq, wukv, pw = sb("wuq", [128, 2, 768]), sb("wukv", [128, 1024]), sb("pw", [128, 2, 256])
    wkr = sb("wkr", [128, KT, 32])
    wkrh, wkrl = sb("wkrh", [128, KT, 32], F32R), sb("wkrl", [128, KT, 32], F32R)
    after = fence(K)
    wt.get(w0)
    t_wkr = sp.dma(wkr[:, :, :], d["w_kr"][l], K.s_wkr, after)
    t_wuq = sp.dma(wuq[:, :, :], d["w_uq"][l], K.s_wuq, after)
    t_wukv = sp.dma(wukv[:, :], d["w_ukv"][l], K.s_wukv, after)
    t_pw = sp.dma(pw[:, :, :], d["pw"][l], K.s_pw, after)
    t_rw = sp.dma(K.rope_w[:, :, :], d["rope_w"][l], K.s_rope, K.free_rope)
    if both:
        K.t_tab = [sp.dma(K.ctab[:, :, :], d["ctab"], K.slot("s_ctab")), sp.dma(K.stab[:, :, :], d["stab"], K.slot("s_stab"))]
        beside.add(mod_rest(K, after), 1, 8)

    cqw = sb("cqw", [128, 3, NT])
    krT, krN = sb("krT", [32, NT]), sb("krN", [128, 6, 32])
    glu, z = sb("glu", [128, 2, 828]), sb("z", [128, 2, 798])
    t_pad = pool(lambda e: e.memset(glu[:, :, :], 0.0), after)
    yp = [[None] * KT, [None] * KT]
    st = Ctx()
    stat = K.stat
    rq, rkv = stat[:, 0:6], stat[:, 8:14]

    def product(i, m=128, cols=None, pairs=None):
        s = K.ps.take()
        dst = [(s.ap[0:m, c:c + n], c // NX, 0, n) for c, n in (cols or segs)]
        ws = pairs or tile_pairs(wt.get(i), m)
        ws2 = [Pair(p.hi, p.lo, [p.t_hi, s.was], p.t_lo) for p in ws[:1]] + ws[1:]
        tok = mm3(K, dst, ws2, hT, beside.gap)
        if pairs is None:
            wt.release(i, tok)
        return s, tok

    def ev_c(s, tok, name, i):
        f = i if name == "cq" else 2
        nn = NT if (both or name == "ckv") else NX
        w = small(K, "qn_w", l, 2, i) if name == "cq" else small(K, "kvn_w", l, 1)
        t = act(lambda e: e.activation(cqw[:, f, 0:nn], s.ap[:, 0:nn], ACT.Copy, scale=w), tok, K.t_small, after)
        b = tmps.hold()
        t2 = act(lambda e: e.activation(b.ap[:, 0:nn], s.ap[:, 0:nn], ACT.Square), tok, b.was)
        s.free = [t2]
        st.cqw[f] = t
        if name == "cq" and i == 0:
            st.sq0 = (b, t2)
            return
        if name == "cq":
            b0, t0 = st.sq0
            t2 = pool(lambda e: e.tensor_tensor(b.ap[:, 0:nn], b.ap[:, 0:nn], b0.ap[:, 0:nn], ALU.add), t0, t2)
            b0.free = [t2]
            tmps.release(b0)

        def go():
            N = Norm(K, nn // 128, 256 if name == "cq" else 128, EPS, 1)
            b.free = [N.add(b.ap, t2)]
            tmps.release(b)
            if name == "cq":
                st.t_rq = N.finish(stat[:, 16:16 + nt_q], rq[:, 0:nt_q], K.free_stat)
            else:
                st.t_rkv = N.finish(stat[:, 24:30], rkv, K.free_stat)
        st.later.append(go)

    st.cqw, st.later = [None] * 3, []

    def ev_glu(s, tok, i):
        if i >= 2:
            b = st.sig[i - 2] = tmps.hold()
            st.t_sig[i - 2] = act(lambda e: e.activation(b.ap[:, 0:n_own], s.ap[:, 0:n_own], ACT.Sigmoid), tok, b.was)
            s.free = [st.t_sig[i - 2]]
            return
        b = st.sig[i]
        for c, n in segs:
            o = 15 + (c if c == 0 else c + 30)
            t = dve(lambda e, c=c, n=n, o=o: e.tensor_tensor(glu[:, i, o:o + n], s.ap[:, c:c + n], b.ap[:, c:c + n], ALU.mult),
                    tok, st.t_sig[i], t_pad)
        s.free = b.free = [t]
        tmps.release(b)
        st.t_glu[i] = t

    st.sig, st.t_sig, st.t_glu = [None, None], [None, None], [None, None]
    width = 798 if both else 512
    wide = 770 if both else 512

    def conv():
        t = [None, None]
        for j in range(31):
            for i in range(2):
                w = small(K, "cf_w", l, 62, 31 * i + j)
                x = glu[:, i, j:j + width]
                o = z[:, i, 0:width]
                if j == 0:
                    t[i] = dve(lambda e, o=o, x=x, w=w, i=i: e.tensor_scalar(o, x, w, small(K, "cf_b", l, 2, i), ALU.mult, ALU.add),
                               st.t_glu[i], K.t_small, after)
                else:
                    t[i] = dve(lambda e, o=o, x=x, w=w: e.scalar_tensor_tensor(o, x, w, o, ALU.mult, ALU.add), t[i])
                yield
        st.t_z = t

    def split_y(k, name, src, t_src, buf, after):
        for g, (c, n) in enumerate(segs):
            hi, lo = (K.sb(f"{name}{g}{k}{l}{p}", [128, n], F32R, f"{name}{'xc'[g]}{l}", 4 * n * (2 * (k % 2) + p)) for p in range(2))
            t_hi = act(lambda e, hi=hi, c=c, n=n: e.activation(hi[:, :], src[:, c:c + n], ACT.Copy), t_src, after)
            t_lo = pool(lambda e, hi=hi, lo=lo, c=c, n=n: e.tensor_tensor(lo[:, :], src[:, c:c + n], hi[:, :].bitcast(F32), ALU.subtract), t_src, t_hi, after)
            yp[g][k] = Pair(hi, lo, t_hi, t_lo)
        buf.free = [t_hi, t_lo]

    def ev_sc(s, tok, name, i):
        if name == "sc_in":
            b = st.sin = tmps.hold()
            st.t_sin = act(lambda e: e.activation(b.ap[:, 0:n_own], s.ap[:, 0:n_own], ACT.Copy), tok, b.was)
            s.free = [st.t_sin]
        elif name == "sc_c":
            b = st.sin
            for c, n in segs:
                o = 1 + (c if c == 0 else c + 2)
                t = dve(lambda e, c=c, n=n, o=o: e.tensor_tensor(scp[:, i, o:o + n], s.ap[:, c:c + n], b.ap[:, c:c + n], ALU.mult),
                        tok, st.t_sin, st.t_padp)
            s.free = b.free = [t]
            tmps.release(b)
            zz = scz[:, 0:wide]
            t = dve(lambda e: e.tensor_scalar(zz, scp[:, i, 0:wide], small(K, "sc_w", l, 6, 3 * i), None, ALU.mult), t, st.t_u, after20)
            for j in (1, 2):
                t = dve(lambda e, j=j: e.scalar_tensor_tensor(zz, scp[:, i, j:j + wide], small(K, "sc_w", l, 6, 3 * i + j), zz, ALU.mult, ALU.add), t)
            st.t_scz = t
        elif name == "sc_b":
            b = st.u = tmps.hold()
            for c, n in segs:
                o = c if c == 0 else c + 2
                t = dve(lambda e, c=c, n=n, o=o: e.tensor_tensor(b.ap[:, c:c + n], s.ap[:, c:c + n], scz[:, o:o + n], ALU.mult), tok, st.t_scz, b.was)
            s.free = [t]
            st.t_u = t
        else:
            b, u = tmps.take(), st.u
            t = act(lambda e: e.activation(b.ap[:, 0:n_own], s.ap[:, 0:n_own], ACT.Silu), tok, b.was)
            s.free = [t]
            t = pool(lambda e: e.tensor_tensor(u.ap[:, 0:n_own], u.ap[:, 0:n_own], b.ap[:, 0:n_own], ALU.mult), t, st.t_u)
            b.free = [t]
            split_y(4 + i, "ys", u.ap, t, u, after20)
            tmps.release(u)

    st.t_u = None
    t_g = [None] * 6

    def ev_g(s, tok, name, i):
        dst = ga[:, i, :] if name == "ga" else gc[:, i, :]
        j = i if name == "ga" else 4 + i
        t_g[j] = act(lambda e: e.activation(dst, s.ap[:, 0:n_own], ACT.Silu), tok, after24)
        s.free = [t_g[j]]

    t_q, t_k, t_v = [None] * 6, [None] * 6, [None] * 6

    def rope(x, i, q):
        h = x.shape[1]
        r = 0 if q else 2
        if i >= 4:
            w = K.rope_w[:, r, :].unsqueeze(1).to_broadcast([128, h, 32])
            return lambda t: pool(lambda e: e.tensor_tensor(x, x, w, ALU.mult), t, t_rw)
        cs = K.rope_t[:, r, i, :].unsqueeze(1).to_broadcast([128, h, 32])
        sn = K.rope_t[:, r + 1, i, :]

        def go(t):
            b = tmps.take()
            o = b.ap[:, 0:32 * h].rearrange("p (h c) -> p h c", c=32)
            for a in range(2):
                t1 = pool(lambda e, a=a: e.tensor_tensor(o[:, :, 16 * a:16 * a + 16], x[:, :, 16 - 16 * a:32 - 16 * a],
                                                         sn[:, 16 * a:16 * a + 16].unsqueeze(1).to_broadcast([128, h, 16]), ALU.mult), t, st.t_rope, b.was)
            t2 = pool(lambda e: e.tensor_tensor(x, x, cs, ALU.mult), t1)
            t3 = pool(lambda e: e.tensor_tensor(x, x, o, ALU.add), t2)
            b.free = [t3]
            return t3
        return go

    def qkv():
        qN, kN, vN = st.qN, st.kN, st.vN
        krS = stat[:, 32:38]
        for i, tab in ((0, K.ctab), (1, K.stab), (2, K.ctab), (3, K.stab)):
            st.t_rope = pool(lambda e, i=i, tab=tab: e.tensor_tensor(
                K.rope_t[:, i, :, :], tab[:, :, :], K.rope_w[:, i, :].unsqueeze(1).to_broadcast([128, 4, 32]), ALU.mult), t_rw, K.t_tab, K.free_rope)
        t_kr2 = []
        for i in range(6):
            b = tmps.take()
            t_kr2.append(act(lambda e, i=i, b=b: e.activation(b.ap[:, 0:32], krN[:, i, :], ACT.Square, accum_out=krS[:, i:i + 1]), st.t_krN, b.was, K.free_stat))
            b.free = [t_kr2[-1]]
        yield
        for i in range(6):
            b16 = 64 + 64 * (i % 2)
            ss, rs, ff = stat[:, b16:b16 + 16], stat[:, b16 + 16:b16 + 32], stat[:, b16 + 32:b16 + 48]
            has_q = i < nt_q
            cols = slice(128 * i, 128 * i + 128)
            if has_q:
                sq_ = px.take()
                for c in range(2):
                    for k in range(2):
                        tok_q = pe(lambda e, sq_=sq_, cols=cols, c=c, k=k: e.matmul(sq_.ap[:, 512 * c:512 * c + 384], cqw[:, k, cols], wuq[:, k, 384 * c:384 * c + 384],
                                                                start=k == 0, stop=k == 1),
                                   st.cqw[0], st.cqw[1], t_wuq, sq_.was, signal=c == 1 and k == 1)
                q4 = sq_.ap[:, :].rearrange("p (c n) -> p c n", c=2)[:, :, 0:384]
            sk_ = px.take()
            for c in range(2):
                tok_k = pe(lambda e, sk_=sk_, cols=cols, c=c: e.matmul(sk_.ap[:, 512 * c:512 * c + 512], cqw[:, 2, cols], wukv[:, 512 * c:512 * c + 512], start=True, stop=True),
                           st.cqw[2], t_wukv, sk_.was, signal=c == 1)
            b1 = tmps.hold()
            if has_q:
                t_q2 = act(lambda e, b1=b1, q4=q4, i=i: e.activation(b1.ap[:, 0:768].rearrange("p (c n) -> p c n", c=2), q4, ACT.Square, scale=rq[:, i:i + 1]),
                           tok_q, st.t_rq, b1.was)
            b2 = tmps.hold()
            t_k2 = act(lambda e, b2=b2, i=i, sk_=sk_: e.activation(b2.ap[:, 0:512], sk_.ap[:, 0:512], ACT.Square, scale=rkv[:, i:i + 1]), tok_k, st.t_rkv, b2.was)
            t_v[i] = act(lambda e, i=i, sk_=sk_: e.activation(vN[:, i, :], sk_.ap[:, 512:1024], ACT.Copy, scale=rkv[:, i:i + 1]), tok_k, st.after_q)
            yield
            t = []
            if has_q:
                t.append(dve(lambda e, b1=b1, ss=ss: e.tensor_reduce(ss[:, 0:8], b1.ap[:, 0:768].rearrange("p (h c) -> p h c", c=QK), AX.X, ALU.add), t_q2, K.st_free[i % 2]))
            b1.free = t or b1.was
            tmps.release(b1)
            t.append(dve(lambda e, b2=b2, ss=ss: e.tensor_reduce(ss[:, 8:16], b2.ap[:, 0:512].rearrange("p (h c) -> p h c", c=64), AX.X, ALU.add), t_k2, K.st_free[i % 2]))
            b2.free = [t[-1]]
            tmps.release(b2)
            t.append(dve(lambda e, ss=ss, i=i: e.tensor_scalar(ss[:, 8:16], ss[:, 8:16], krS[:, i:i + 1], None, ALU.add), t[-1], t_kr2[i]))
            lo = 0 if has_q else 8
            t = dve(lambda e, ss=ss, lo=lo: e.tensor_scalar(ss[:, lo:16], ss[:, lo:16], 1.0 / QK, EPS, ALU.mult, ALU.add), t)
            t_r = pool(lambda e, ss=ss, rs=rs, lo=lo: e.tensor_tensor(rs[:, lo:16], ss[:, lo:16], K.nhalf[:, lo:16], ALU.pow), t, K.t_nhalf, K.st_free[i % 2])
            yield
            yield
            yield
            t = dve(lambda e, ff=ff, rs=rs, i=i: e.tensor_scalar(ff[:, 8:16], rs[:, 8:16], rkv[:, i:i + 1], None, ALU.mult), t_r, st.t_rkv)
            if has_q:
                t1 = dve(lambda e, ff=ff, rs=rs, i=i: e.tensor_scalar(ff[:, 0:8], rs[:, 0:8], rq[:, i:i + 1], None, ALU.mult), t_r, st.t_rq)
            t2 = dve(lambda e, i=i, ff=ff, sk_=sk_: e.tensor_tensor(kN[:, i, :, 0:64], sk_.ap[:, 0:512].rearrange("p (h c) -> p h c", c=64),
                                                                    ff[:, 8:16].unsqueeze(2).to_broadcast([128, 8, 64]), ALU.mult), t, tok_k, t_v[i], st.after_q)
            sk_.free = [t2, t_v[i]]
            if has_q:
                for c in range(2):
                    t = dve(lambda e, i=i, c=c, ff=ff, sq_=sq_: e.tensor_tensor(
                        qN[:, i, 4 * c:4 * c + 4, :], sq_.ap[:, 512 * c:512 * c + 384].rearrange("p (h c) -> p h c", c=QK),
                        ff[:, 4 * c:4 * c + 4].unsqueeze(2).to_broadcast([128, 4, QK]), ALU.mult), t1, t_q2, st.after_q)
                sq_.free = [t]
            t3 = rope(krN[:, i:i + 1, :], i, False)(t_kr2[i])
            t4 = pool(lambda e, i=i, rs=rs: e.tensor_tensor(kN[:, i, :, 64:96], krN[:, i:i + 1, :].to_broadcast([128, 8, 32]),
                                                            rs[:, 8:16].unsqueeze(2).to_broadcast([128, 8, 32]), ALU.mult), t3, t_r, st.after_q)
            t_k[i] = [t2, t4]
            K.st_free[i % 2] = [t2, t4]
            if has_q:
                t_q[i] = rope(qN[:, i, :, 64:96], i, True)(t)
                K.st_free[i % 2] = [t2, t4, t]
            yield
        K.free_rope = [pool.last()]

    def layer_norm():
        nn = n_own
        zc = [(c, n, c if c == 0 else c + 30) for c, n in segs]
        s = px.take()
        for c, n, o in zc:
            for k in range(2):
                tok = pe(lambda e, s=s, c=c, n=n, o=o, k=k: e.matmul(s.ap[:, c:c + n], K.ones[:, :], z[:, k, o:o + n], start=k == 0, stop=k == 1),
                         st.t_z, s.was, signal=k == 1)
        yield
        sq = []
        for k in range(2):
            b = tmps.hold()
            for c, n, o in zc:
                t = dve(lambda e, s=s, k=k, c=c, n=n, o=o: e.scalar_tensor_tensor(
                    z[:, k, o:o + n], s.ap[:, c:c + n], -1.0 / 256, z[:, k, o:o + n], ALU.mult, ALU.add), tok)
                t2 = act(lambda e, b=b, k=k, c=c, n=n, o=o: e.activation(b.ap[:, c:c + n], z[:, k, o:o + n], ACT.Square), t, b.was)
            sq.append((b, t2))
        s.free = [t]
        (b0, ta), (b1, tb) = sq
        t2 = pool(lambda e: e.tensor_tensor(b1.ap[:, 0:nn], b1.ap[:, 0:nn], b0.ap[:, 0:nn], ALU.add), ta, tb)
        b0.free = [t2]
        tmps.release(b0)
        yield
        yield
        nz = Norm(K, nn // 128, 256, LN_EPS, 1)
        b1.free = [nz.add(b1.ap, t2)]
        tmps.release(b1)
        t_r = nz.finish(stat[:, 40:40 + nn // 128], stat[:, 48:48 + nn // 128], K.free_stat)
        yield
        rb, t_rb = spread(K, nn // 128, stat[:, 48:54], t_r, tmps)
        yield
        t_zs = [None, None]
        for k in range(2):
            for c, n, o in zc:
                t = dve(lambda e, k=k, c=c, n=n, o=o: e.tensor_tensor(z[:, k, o:o + n], z[:, k, o:o + n], rb.ap[:, c:c + n], ALU.mult), t_rb)
                t_zs[k] = act(lambda e, k=k, n=n, o=o: e.activation(z[:, k, o:o + n], z[:, k, o:o + n], ACT.Silu,
                                                                   scale=small(K, "ln_w", l, 2, k), bias=small(K, "ln_b", l, 2, k)), t)
        rb.free = [t]
        yield
        for f in range(2):
            s = px.take()
            for c, n, o in zc:
                for k in range(2):
                    tok = pe(lambda e, s=s, c=c, n=n, o=o, k=k, f=f: e.matmul(s.ap[:, c:c + n], pw[:, k, 128 * f:128 * f + 128], z[:, k, o:o + n],
                                                                             start=k == 0, stop=k == 1), t_zs, t_pw, s.was, signal=k == 1)
            b = tmps.take()
            t = dve(lambda e, b=b, f=f, s=s: e.scalar_tensor_tensor(b.ap[:, 0:nn], s.ap[:, 0:nn], small(K, "pw_b", l, 2, f), gc[:, f, :], ALU.add, ALU.mult),
                    tok, t_g[4 + f], b.was)
            s.free = [t]
            split_y(6 + f, "yp", b.ap, t, b, after24)
            yield

    def begin_qkv():
        st.after_q = fence(K)
        st.qN, st.kN, st.vN = sb("qN", [128, nt_q, HEADS, QK]), sb("kN", [128, 6, HEADS, QK]), sb("vN", [128, 6, 512])
        beside.add(qkv(), 1)

    for at, (name, i) in enumerate(TILES):
        if at == TILES.index(("sc_in", 0)):
            beside.drain() if both else None
            after20 = fence(K)
            scp, scz = sb("scp", [128, 2, 772]), sb("scz", [128, 772])
            st.t_padp = pool(lambda e: e.memset(scp[:, :, :], 0.0), after20)
            if both:
                begin_qkv()
            beside.add(conv(), 1.5)
        if at == TILES.index(("gc", 0)):
            after24 = fence(K)
            ga, gc = sb("ga", [128, 4, n_own]), sb("gc", [128, 2, n_own])
        if (name, i) == ("ga", 1):
            beside.drain()
            beside.add(layer_norm(), 1)
        s, tok = product(w0 + at, cols=all_segs if name == "ckv" else segs)
        for go in st.later:
            go()
        st.later = []
        if name in ("cq", "ckv"):
            ev_c(s, tok, name, i)
        elif name == "glu":
            ev_glu(s, tok, i)
        elif name in ("ga", "gc"):
            ev_g(s, tok, name, i)
        else:
            ev_sc(s, tok, name, i)
        if name == "ckv":
            s, tok = product(None, m=32, cols=all_segs, pairs=[Pair(wkrh[:, k, :], wkrl[:, k, :], st.t_kh, st.t_kl) for k in range(KT)])
            t = act(lambda e, s=s: e.activation(krT[:, :], s.ap[0:32, 0:NT], ACT.Copy), tok, after)
            s.free = [t]
            st.t_krT = t
        if at == 0:
            st.t_kh = act(lambda e: e.activation(wkrh[:, :, :], wkr[:, :, :], ACT.Copy), t_wkr, after)
            st.t_kl = pool(lambda e: e.tensor_tensor(wkrl[:, :, :], wkr[:, :, :], wkrh[:, :, :].bitcast(F32), ALU.subtract), st.t_kh, t_wkr, after)
        if at and TILES[at - 1][0] == "ckv":
            s = px.take()
            for j in range(6):
                tok = pe(lambda e, s=s, j=j: e.transpose(s.ap[:, 32 * j:32 * j + 32], krT[:, 128 * j:128 * j + 128], K.ident[0:32, 0:32]),
                         st.t_krT, K.t_ident, s.was if j == 0 else None, signal=j == 5)
            t = act(lambda e, s=s: e.activation(krN[:, :, :], s.ap[:, 0:192].rearrange("p (t c) -> p t c", c=32), ACT.Copy), tok, after)
            s.free = [t]
            st.t_krN = t
            if not both:
                begin_qkv()
    beside.drain()
    K.free_stat = fence(K)
    attention(K, l, st.qN, st.kN, st.vN, t_q, t_k, t_v, ga, t_g, yp)
    return yp


def attention(K, l, qN, kN, vN, t_q, t_k, t_v, ga, t_g, yp):
    pe, act, dve, pool = K.pe, K.act, K.dve, K.pool
    both = l == 0
    n_own = NT if both else NX
    sm = float(np.float32(QK) ** np.float32(-0.5))
    after = [pe.last(), act.last(), dve.last(), pool.last()]
    ring = lambda name, n, shape: Ring([Buf(K.sb(f"{name}{l}_{i}", [128, *shape], F32, f"{name}{l}", 4 * int(np.prod(shape)) * i)) for i in range(n)])
    qT = K.sb(f"qT{l}", [128, 2, 2, n_own], F32R)
    kT = K.sb(f"kT{l}", [128, 2, 2, NT], F32R)
    P, PT0, PT1, gate = ring("P", 4, (NT,)), ring("PTa", 4, (6, 128)), ring("PTb", 2, (6, 128)), ring("og", 3, (256,))
    PTc = ring("PTc", 2, (2, 256)) if both else None
    for r in (P, PT0, PT1, gate) + ((PTc,) if both else ()):
        for b in r.bufs:
            b.free = after
    ps = K.psum
    S2 = [Buf(ps[:, o:o + NT]) for o in (0, 1024)]
    G = Ring([Buf(ps[:, 512 * i:512 * i + 512]) for i in range(4, 8)])
    for b in S2 + G.bufs:
        b.free = after
    ya = [[K.sb(f"ya{c}{l}{i}", [128, 4, n], F32R, f"ya{c}{l}", 16 * n * i) for i in range(2)] for c, n in ((("x", NX), ("c", NC)) if both else (("x", NX),))]
    stat = K.stat
    qs = stat[:, 60:61]
    t_qs = dve(lambda e: e.tensor_scalar(qs, small(K, "qh_w", l, 1), sm, None, ALU.mult), after, K.t_small)
    per = 5 if both else 4
    units = [(h, i) for h in range(HEADS) for i in range(per)]
    heads, Pn, PTs = {}, {}, {}

    def turn(h):
        b = h % 2
        need = heads[h - 2][2] if h >= 2 else after
        heads[h] = [[None, None], [None, None], None]
        pieces = [(1, 0), (1, 4), (0, 0)] + ([(0, 4)] if both else [])
        for which, t0 in pieces:
            src, toks, dst = ((qN, t_q, qT), (kN, t_k, kT))[which]
            w = (qs if which == 0 else small(K, "kh_w", l, 1))[0:QK, :]
            nt = 4 if t0 == 0 else 2
            s = G.take()
            for j in range(nt):
                tok = pe(lambda e, j=j, s=s, src=src, t0=t0: e.transpose(s.ap[0:QK, 128 * j:128 * j + 128], src[:, t0 + j, h, :], K.ident[:, :]),
                         toks[t0 + j], s.was if j == 0 else None, signal=j == nt - 1)
            c, n = 128 * t0, 128 * nt
            hi, lo = dst[0:QK, b, 0, c:c + n], dst[0:QK, b, 1, c:c + n]
            t_hi = act(lambda e, s=s, hi=hi, w=w, n=n: e.activation(hi, s.ap[0:QK, 0:n], ACT.Copy, scale=w), tok, need, t_qs)
            t_lo = dve(lambda e, s=s, hi=hi, lo=lo, w=w, n=n: e.scalar_tensor_tensor(lo, s.ap[0:QK, 0:n], w, hi.bitcast(F32), ALU.mult, ALU.subtract), t_hi, need)
            s.free = [t_lo]
            heads[h][which][t0 // 4] = (t_hi, t_lo)
            yield

    def scores(u):
        h, i = units[u]
        b = h % 2
        tq, tk = heads[h][0][i // 4], heads[h][1]
        s = S2[u % 2]
        if i < 4:
            jobs = [(i, [(0, 0, NX), (512, NX, NC)])]
        else:
            jobs = [(4, [(0, NX, NC)]), (5, [(256, NX, NC)])]
        for n, (t, outs) in enumerate(jobs):
            qh, ql = qT[0:QK, b, 0, 128 * t:128 * t + 128], qT[0:QK, b, 1, 128 * t:128 * t + 128]
            tkh = [x[0] for x in (tk if i < 4 else tk[1:])]
            tkl = [x[1] for x in (tk if i < 4 else tk[1:])]
            for p, (a, x, need) in enumerate(((qh, 0, (tq[0], tkh, s.free)), (qh, 1, (tkl,)), (ql, 0, (tq[1],)))):
                for o, c, w in outs:
                    tok = pe(lambda e, o=o, c=c, w=w, a=a, x=x, p=p: e.matmul(s.ap[:, o:o + w], a, kT[0:QK, b, x, c:c + w], start=p == 0, stop=p == 2),
                             need, signal=p == 2 and n == len(jobs) - 1 and o == outs[-1][0])
        heads[h][2] = [tok]
        c0 = 192 + 8 * (u % 4)
        P_ = P.take()
        n, w = (1, NT) if i < 4 else (2, NC)
        t = dve(lambda e: e.tensor_reduce(stat[:, c0:c0 + n], s.ap[:, 0:n * w].rearrange("p (n w) -> p n w", w=w), AX.X, ALU.max, negate=True),
                tok, K.stat_free[u % 4])
        for j in range(n):
            t1 = act(lambda e, j=j: e.activation(P_.ap[:, w * j:w * j + w], s.ap[:, w * j:w * j + w], ACT.Exp, bias=stat[:, c0 + j:c0 + j + 1],
                                                 accum_out=stat[:, c0 + 2 + j:c0 + 3 + j]), t, P_.was)
        s.free = [t1]
        Pn[u] = [P_, t1, c0, n, w]

    def normalise(u):
        P_, t, c0, n, w = Pn[u]
        t = dve(lambda e: e.reciprocal(stat[:, c0 + 4:c0 + 4 + n], stat[:, c0 + 2:c0 + 2 + n]), t)
        for j in range(n):
            t1 = pool(lambda e, j=j: e.tensor_scalar(P_.ap[:, w * j:w * j + w], P_.ap[:, w * j:w * j + w], stat[:, c0 + 4 + j:c0 + 5 + j], 0.0, ALU.mult, ALU.add), t)
        Pn[u][1] = t1
        K.stat_free[u % 4] = [t1]

    def turn_p(u):
        h, i = units[u]
        P_, t, _, _, _ = Pn.pop(u)
        if i < 4:
            d = (PT0, PT1)[h % 2].take()
            jobs = [([128 * j for j in range(4)], d.ap[:, 0:4, :]), ([512, 640], d.ap[:, 4:6, :])]
        else:
            d = PTc.take()
            jobs = [([256 * j + 128 * kt for kt in range(2) for j in range(2)], d.ap[:, :, :])]
        done = []
        for n, (cols, dst) in enumerate(jobs):
            s = G.take()
            for j, c in enumerate(cols):
                tok = pe(lambda e, s=s, j=j, c=c: e.transpose(s.ap[:, 128 * j:128 * j + 128], P_.ap[:, c:c + 128], K.ident[:, :]),
                         t, s.was if j == 0 else None, signal=j == len(cols) - 1)
            src = s.ap[:, 0:128 * len(cols)].rearrange("p (t q) -> p t q", q=dst.shape[2])
            if (u + n) % 2:
                t1 = act(lambda e, dst=dst, src=src: e.activation(dst, src, ACT.Copy), tok, d.was)
            else:
                t1 = dve(lambda e, dst=dst, src=src: e.tensor_copy(dst, src), tok, d.was)
            s.free = [t1]
            done.append(t1)
        P_.free = [tok]
        PTs[u] = (d, done)

    def values(u):
        h, i = units[u]
        p = h // 2
        pt = [PTs.pop(u - per), PTs.pop(u)]
        s = G.take()
        c, n = 128 * i, 128 if i < 4 else NC
        kts = range(6) if i < 4 else (4, 5)
        for kt in kts:
            for e_ in range(2):
                d, t = pt[e_]
                o = 64 * (h - 1 + e_)
                tok = pe(lambda e, kt=kt, e_=e_, d=d, o=o: e.matmul(
                    s.ap[64 * e_:64 * e_ + 64, 0:n], vN[:, kt, o:o + 64], d.ap[:, kt - kts[0], :],
                    start=kt == kts[0], stop=kt == 5, skip_group_check=True), t, t_v, s.was, signal=kt == 5 and e_ == 1)
        pt[0][0].free = pt[1][0].free = [tok]
        b = gate.take()
        t = dve(lambda e: e.tensor_tensor(b.ap[:, 0:n], s.ap[:, 0:n], ga[:, p, c:c + n], ALU.mult), tok, t_g[p], b.was)
        s.free = [t]
        yh, yl = ya[i // 4]
        hi, lo = (y[:, p, c % NX:c % NX + n] for y in (yh, yl))
        t_hi = act(lambda e: e.activation(hi, b.ap[:, 0:n], ACT.Copy), t, after)
        t_lo = pool(lambda e: e.tensor_tensor(lo, b.ap[:, 0:n], hi.bitcast(F32), ALU.subtract), t, t_hi, after)
        b.free = [t_hi, t_lo]
        yp[i // 4][p] = Pair(yh[:, p, :], yl[:, p, :], t_hi, t_lo)

    for _ in turn(0):
        pass
    n = len(units)
    nxt = turn(1)
    for u in range(3):
        scores(u)
        normalise(u) if u < 2 else None
    for u in range(n):
        h, i = units[u]
        turn_p(u)
        if i < 2:
            next(nxt, None)
            if i or h == 0:
                for _ in nxt:
                    pass
        elif i >= per - 2 and h + 2 < HEADS:
            if i == per - 2:
                nxt = turn(h + 2)
            next(nxt)
        if u + 2 < n:
            normalise(u + 2)
        if u + 3 < n:
            scores(u + 3)
        if u and units[u - 1][0] % 2:
            values(u - 1)
    values(n - 1)
    for b in K.ps.bufs + K.px.bufs:
        b.free = fence(K)


def out_pass(K, l, seg, c, n, wt, w0, yp, src, dst, acc, tmps, after, last, side=None):
    pe, act, dve, pool = K.pe, K.act, K.dve, K.pool
    out = []
    for f in range(KT):
        s = K.ps.take()
        ws = tile_pairs(wt.get(w0 + f))
        ws[4] = Pair(ws[4].hi, ws[4].lo, [ws[4].t_hi, s.was], ws[4].t_lo)
        tok = mm3(K, [(s.ap[:, 0:n], seg, c, n)], ws, yp, None, [4, 5, 6, 7, 0, 1, 2, 3])
        if last:
            wt.release(w0 + f, tok)
        if side:
            side(f)
        x, t_x, done = src(f)
        o = dst(f)
        t = dve(lambda e, s=s, x=x, o=o, f=f: e.scalar_tensor_tensor(o, s.ap[:, 0:n], K.mod[:, l, 2, f, seg:seg + 1], x, ALU.mult, ALU.add),
                tok, t_x, K.t_gate[l], after)
        s.free = [t]
        done([t])
        out.append(t)
        if f == 0:
            t_acc = act(lambda e, o=o: e.activation(acc, o, ACT.Square), t, after)
        else:
            b = tmps.take()
            t = act(lambda e, o=o, b=b: e.activation(b.ap[:, 0:n], o, ACT.Square), t, b.was)
            t_acc = pool(lambda e, b=b: e.tensor_tensor(acc, acc, b.ap[:, 0:n], ALU.add), t, t_acc)
            b.free = [t_acc]
    return out, t_acc


def place_out(K, l, w0, after):
    for f in range(2, KT):
        K.wt.place[w0 + f] = tuple(Buf(K.sb(f"wo{l}{f}{p}", [128, 1024], F32R, f"wo{l}", 4096 * (2 * (f - 2) + p))) for p in range(2))
        for b in K.wt.place[w0 + f]:
            b.free = after
    K.wt.limit = w0 + KT


def first_block(K):
    pe, act, dve, pool, sp, d, sb = K.pe, K.act, K.dve, K.pool, K.sp, K.d, K.sb
    begin(K)
    K.s_wkr, K.s_wuq, K.s_wukv, K.s_pw = (K.slot("s_" + n) for n in ("wkr", "wuq", "wukv", "pw"))
    xc = sb("xc", [128, KT, NT])
    t_xc = []
    for i in range(4):
        t_xc += 2 * [sp.dma(xc[:, 2 * i:2 * i + 2, :], d["xc"][:, 2 * i:2 * i + 2, :], K.slot(f"s_xc{i}"))]
    wm = sb("wmod0", [128, KT, 2048])
    t_wm = [sp.dma(wm[:, k, :], d["w_mod"][0, k, :, 0:2048], K.slot(f"s_mod{k}")) for k in range(KT)]
    w_in, w_out = [], []
    srcs = []
    for l in range(2):
        w_in.append(len(srcs))
        srcs += [d["w_in"][l, i] for i in range(len(TILES))]
        w_out.append(len(srcs))
        srcs += [d["w_out"][l, i] for i in range(KT)]
    K.w_out = w_out
    M = K.moe = Ctx()
    M.h2d = K.nc.dram_tensor("h2d", [NX, D], F32).ap()
    M.meta = K.nc.dram_tensor("meta", [ROWS, 4], F32).ap()
    M.ybuf = K.nc.dram_tensor("ybuf", [2 * NX, D], F32).ap()
    K.w2 = len(srcs)
    srcs += [d["w_in2"][i] for i in range(24)]
    srcs += [d["w_out2"][k] for k in range(KT)]
    wt = K.wt = Weights(K, srcs)
    for b in wt.hi + wt.lo:
        b.free = []
    wt.limit = w_out[0] + 2
    K.free_rope, K.free_stat, K.st_free, K.stat_free = [], [], [[], []], [[], [], [], []]
    stat = K.stat
    tmps = tmp_ring(K, "tmpa", 5)

    sums = tmps.hold()
    for k in range(KT):
        if k == 0:
            t_s = act(lambda e: e.activation(sums.ap[:, 0:NT], xc[:, 0, :], ACT.Square), t_xc[0])
            continue
        b = tmps.take()
        t = act(lambda e, k=k, b=b: e.activation(b.ap[:, 0:NT], xc[:, k, :], ACT.Square), t_xc[k], b.was)
        t_s = dve(lambda e, b=b: e.tensor_tensor(sums.ap[:, 0:NT], sums.ap[:, 0:NT], b.ap[:, 0:NT], ALU.add), t, t_s)
        b.free = [t_s]
    N = Norm(K, 6, nk=1)
    sums.free = [N.add(sums.ap, t_s)]
    tmps.release(sums)
    t_r = N.finish(stat[:, 0:6], stat[:, 8:14])
    rb, t_rb = spread(K, 6, stat[:, 8:14], t_r, tmps)
    t_xn = [dve(lambda e, k=k: e.tensor_tensor(xc[:, k, :], xc[:, k, :], rb.ap[:, 0:NT], ALU.mult), t_rb, t_xc[k]) for k in range(KT)]
    rb.free = [t_xn[-1]]
    mod_first(K, wm, t_wm)
    wt.get(0)
    both = [(0, NX, 0), (NX, NC, 1)]
    hT = [[], []]
    hx = [[sb(f"h{c}{p}0", [128, KT, n], F32R) for p in "hl"] for c, n in (("x", NX), ("c", NC))]
    pend = []
    for k in range(KT):
        b = tmps.hold()
        new = []
        for c, n, v in both:
            scale, shift = K.mod[:, 0, 1, k, v:v + 1], K.mod[:, 0, 0, k, v:v + 1]
            x, o = xc[:, k, c:c + n], b.ap[:, c:c + n]
            hi, lo = (h[:, k, :] for h in hx[v])
            t_hi = act(lambda e, hi=hi, x=x, scale=scale, shift=shift: e.activation(hi, x, ACT.Identity, bias=shift, scale=scale), t_xn[k], K.t_mod[0])
            t = dve(lambda e, o=o, x=x, scale=scale, shift=shift: e.tensor_scalar(o, x, scale, shift, ALU.mult, ALU.add), t_xn[k], K.t_mod[0], b.was)
            new.append((v, b, o, hi, lo, t_hi, t, pool if k % 2 else dve))
        for v, b_, o, hi, lo, t_hi, t, q in pend + (new if k == KT - 1 else []):
            t_lo = q(lambda e, o=o, hi=hi, lo=lo: e.tensor_tensor(lo, o, hi.bitcast(F32), ALU.subtract), t, t_hi)
            hT[v].append(Pair(hi, lo, t_hi, t_lo))
            b_.free = (b_.free or []) + [t_lo]
            if v:
                tmps.release(b_)
        pend = new
    M.t_meta0 = act.dma(M.meta.rearrange("(g p) w -> g (p w)", p=128), d["empty"], K.slot("s_meta0"))
    yp = first_layer_block(K, 0, hT, wt, w_in[0], tmps)

    after = fence(K)
    place_out(K, 0, w_out[0], after)
    x1, xc1 = sb("x1", [128, KT, NX]), sb("xc1", [128, KT, NC])
    xr = Ring([Buf(sb(f"xr_{i}", [128, NX], F32, "xr", 4 * NX * i), K.slot(f"s_xr{i}")) for i in range(3)])
    tmps = K.tmps = tmp_ring(K, "tmpc", 5)
    for b in xr.bufs + tmps.bufs:
        b.free = after

    def source(c, n):
        ahead = []

        def load(f):
            if f < KT:
                b = xr.take()
                ahead.append((b, act.dma(b.ap[:, 0:n], d["xc"][:, f, c:c + n], b.slot, b.was)))

        def src(f):
            if f == 0:
                load(0)
                load(1)
            load(f + 2)
            b, t = ahead[f]

            def done(t):
                b.free = t
            return b.ap[:, 0:n], t, done
        return src
    acc = sb("acc", [128, NX])
    t_x1, t_acc = out_pass(K, 0, 0, 0, NX, wt, w_out[0], yp, source(0, NX), lambda f: x1[:, f, :], acc[:, :], tmps, after, False)
    after = fence(K)
    hT = [[], []]
    hx = [[sb(f"h{c}{p}1", [128, KT, n], F32R) for p in "hl"] for c, n in (("x", NX), ("c", NC))]
    steps = next_h(K, acc, t_acc, 4, 0, NX, lambda k: x1[:, k, :], t_x1, 0, hx[0], 1, tmps, 0, after, hT[0])
    acc_c = sb("accc", [128, NC])
    t_xc1, t_acc = out_pass(K, 0, 1, 0, NC, wt, w_out[0], yp, source(NX, NC), lambda f: xc1[:, f, :], acc_c[:, :], tmps, after, True,
                            lambda f: [next(steps, None) for _ in range((0, 1, 1, 1, 2, 2, 2, 2)[f])])
    for _ in steps:
        pass
    wt.limit = w_out[1] + 2
    K.beside.add(next_h(K, acc_c, t_acc, 2, 0, NC, lambda k: xc1[:, k, :], t_xc1, 1, hx[1], 1, tmps, 32, fence(K), hT[1]), 1)
    yp = first_layer_block(K, 1, hT, wt, w_in[1], tmps)
    return x1, t_x1, yp


NE, DE = 32, 256
PAIRS, GROUPS = 16, 32
MORE = 7
ROWS = 128 * (GROUPS + MORE)
BIG = 1.0e30
T2 = 4
RC = dict(desc4=0, desc32=4, thr=36, base=40, over=72, ids=104, pow2=136, nth=152, tri=160, n=288)


def second_block(K, x1, t_x1, yp, out):
    pe, act, dve, pool, sp, d, sb, nc = K.pe, K.act, K.dve, K.pool, K.sp, K.d, K.sb, K.nc
    stat, wt, w0 = K.stat, K.wt, K.w2
    after = fence(K)
    place_out(K, 1, K.w_out[1], after)
    tmps = tmp_ring(K, "tmpe", 5)
    for b in tmps.bufs:
        b.free = after
    small2 = K.small2 = sb("small2", [128, SMALL2["n"]])
    t_small2 = K.t_small2 = sp.dma(small2[:, :], d["small2"], K.slot("s_small2"))
    acc = [sb(f"acc_{i}", [128, 256], F32, "acc2", 1024 * i) for i in range(2)]
    hh, hl = sb("hh2", [128, KT, NX], F32R), sb("hl2", [128, KT, NX], F32R)
    halves, t_x, steps = [[], []], [None, None], [None, None]
    for i in range(2):
        c = 256 * i
        x = lambda k, c=c: x1[:, k, c:c + 256]
        side = None if i == 0 else lambda f: [next(steps[0], None) for _ in range((0, 1, 1, 1, 2, 2, 2, 2)[f])]
        t_x[i], t_acc = out_pass(K, 1, 0, c, 256, wt, K.w_out[1], [yp[0]], lambda f, x=x: (x(f), t_x1[f], lambda t: None), x, acc[i][:, :], tmps, after, i == 1, side)
        if i == 0:
            after2 = fence(K)
            wf, wfh, wfl = sb("wf", [128, KT, 8]), sb("wfh", [128, KT, 8], F32R), sb("wfl", [128, KT, 8], F32R)
            t_wf = sp.dma(wf[:, :, :], d["w_f"], K.slot("s_wf"), after2)
            t_wfh = act(lambda e: e.activation(wfh[:, :, :], wf[:, :, :], ACT.Copy), t_wf)
            t_wfl = pool(lambda e: e.tensor_tensor(wfl[:, :, :], wf[:, :, :], wfh[:, :, :].bitcast(F32), ALU.subtract), t_wfh, t_wf)
        steps[i] = next_h(K, acc[i], t_acc, 2, c, 256, x, t_x[i], 0, (hh, hl), 2, tmps, 40 * i, after2, halves[i])
    for _ in steps[0]:
        pass
    start = fence(K)
    xN = sb("xN", [128, T2, D])
    vT = [sb("vdil", [128, T2, 512]), None]
    t_vT = [[None] * T2, [None] * T2]
    for kk in (2, 3):
        wt.place[w0 + kk] = tuple(Buf(sb(f"wv{kk}{p}", [128, 1024], F32R, "wv", 4096 * (2 * (kk - 2) + p))) for p in range(2))
        for b in wt.place[w0 + kk]:
            b.free = after2
    wt.limit = w0 + 4
    t_xN = [None] * T2
    for i in range(2):
        banks = [K.ps.take() for _ in range(2)]
        hT = halves[i]
        for kk in range(4):
            hi, lo, t_hi, t_lo = wt.get(w0 + kk)
            for t_ in range(2):
                c = slice(256 * i + 128 * t_, 256 * i + 128 * t_ + 128)
                for j in range(2):
                    x = hT[2 * kk + j]
                    for p, (a, b, need) in enumerate(((x.hi, hi, (x.t_hi, t_hi, banks[t_].was)), (x.lo, hi, (x.t_lo,)), (x.hi, lo, (t_lo,)))):
                        last = kk == 3 and j == 1 and p == 2
                        tok = pe(lambda e, t_=t_, a=a, b=b, c=c, j=j, kk=kk, p=p, last=last, banks=banks: e.matmul(
                            banks[t_].ap[:, 0:512], a[:, c], b.ap[:, 512 * j:512 * j + 512], start=kk == 0 and j == 0 and p == 0, stop=last),
                            need, signal=last or (t_ == 1 and j == 1 and p == 2))
                if kk == 3:
                    t_vT[0][2 * i + t_] = act(lambda e, t_=t_, i=i, banks=banks: e.activation(vT[0][:, 2 * i + t_, :], banks[t_].ap[:, 0:512], ACT.Copy), tok, start)
                    banks[t_].free = [t_vT[0][2 * i + t_]]
            if i == 1:
                wt.release(w0 + kk, tok)
            else:
                for _ in range((1, 1, 4, 4)[kk]):
                    next(steps[1], None)
        for t_ in range(2):
            s = K.px.take()
            for k in range(KT):
                tok = pe(lambda e, s=s, t_=t_, k=k, i=i: e.transpose(s.ap[:, 128 * k:128 * k + 128], x1[:, k, 256 * i + 128 * t_:256 * i + 128 * t_ + 128], K.ident[:, :]),
                         t_x[i], s.was, signal=k == KT - 1)
            t_xN[2 * i + t_] = act(lambda e, s=s, t_=t_, i=i: e.activation(xN[:, 2 * i + t_, :], s.ap[:, :], ACT.Copy), tok, start)
            s.free = [t_xN[2 * i + t_]]
        if i == 0:
            for _ in steps[1]:
                pass
    hT = [Pair(hh[:, k, :], hl[:, k, :], [h[k].t_hi for h in halves], [h[k].t_lo for h in halves]) for k in range(KT)]
    K.bk = Ring([Buf(b.ap[:, 512 * i:512 * i + 512]) for r in (K.px, K.ps) for b in r.bufs for i in range(2)])
    for i, b in enumerate(K.bk.bufs):
        b.free = (K.px.bufs + K.ps.bufs)[i // 2].free
    bk = K.bk
    wt.limit = w0 + 24
    after = fence(K)

    tmps = tmp_ring(K, "tmpf", 4, 512)
    for b in tmps.bufs:
        b.free = after
    s = bk.take()
    tok = mm3(K, [(s.ap[0:8, 0:NX], 0, 0, NX)], [Pair(wfh[:, k, :], wfl[:, k, :], [t_wfh, s.was], t_wfl) for k in range(KT)], [hT])
    fa, fb, fc = tmps.take(), tmps.take(), tmps.take()
    A, B_, C_ = fa.ap[0:8, :], fb.ap[0:8, :], fc.ap[0:8, :]
    t = dve(lambda e, s=s: e.tensor_scalar(A, s.ap[0:8, 0:NX], small2[0:8, 16:17], None, ALU.add), tok, t_small2, fa.was)
    s.free = [t]
    t = dve(lambda e: e.scalar_tensor_tensor(B_, A, -1.0, A, ALU.mult, ALU.max), t, fb.was)
    t = act(lambda e: e.activation(B_, B_, ACT.Exp, scale=-1.0), t)
    t = act(lambda e: e.activation(B_, B_, ACT.Ln, bias=1.0), t)
    t2 = dve(lambda e: e.tensor_scalar(C_, A, -1.0, 0.0, ALU.mult, ALU.max), t, fc.was)
    t = dve(lambda e: e.tensor_tensor(B_, B_, C_, ALU.add), t2)
    t_o8 = dve(lambda e: e.memset(A, 1.0), t)
    t = dve(lambda e: e.tensor_tensor_scan(C_, A, B_, 0.0, ALU.mult, ALU.add), t, t_o8)
    fC = sb("fC", [128, NX], F32R)
    t0 = dve(lambda e: e.memset(fC[:, :].bitcast(F32), 0.0), after)
    t_c = act(lambda e: e.activation(fC[0:8, :], C_, ACT.Copy), t, t0)
    t1 = dve(lambda e: e.tensor_tensor(B_, C_, fC[0:8, :].bitcast(F32), ALU.subtract), t_c)
    t_fC = [t_c, act(lambda e: e.activation(fC[32:40, :], B_, ACT.Copy), t1, t0)]
    fa.free = fb.free = fc.free = [t_fC[1], t]
    self_, sel = sb("self", [128, 1024]), sb("sel", [128, HEADS, 128], F32R)
    t = sp.dma(self_[:, :], d["sel"], K.slot("s_sel"), after)
    t_sel = act(lambda e: e.activation(sel[:, :, :].rearrange("p h c -> p (h c)"), self_[:, :], ACT.Copy), t, after)
    tri = sb("tri", [128, 512])
    lnn = sb("lnn", [128, 512])
    t_tri = sp.dma(tri[:, :], d["causal"], K.slot("s_tri"), after)
    t_lnn = sp.dma(lnn[:, :], d["lnn"], K.slot("s_lnn"), after)
    tabs = Ring([Buf(sb(f"tab{i}", [128, 512], F32, "tab", 2048 * i), K.slot(f"s_tab{i}")) for i in range(3)])
    for b in tabs.bufs:
        b.free = after
    vT[1] = sb("vfox", [128, T2, 512])
    q2 = [[[sb(f"q2_{i}{e}{p}", [128, NX], F32R, "q2", 2048 * (4 * i + 2 * e + p)) for p in range(2)] for e in range(2)] for i in range(2)]
    k2 = [[sb(f"k2_{i}{p}", [128, NX], F32R, "k2", 2048 * (2 * i + p)) for p in range(2)] for i in range(2)]
    t_z = []
    for i in range(2):
        for e_ in range(2):
            for p in range(2):
                half = slice(64, 128) if e_ == 0 else slice(0, 64)
                t_z.append(dve(lambda e, i=i, e_=e_, p=p, half=half: e.memset(q2[i][e_][p][half, :].bitcast(F32), 0.0), after))
    P = Ring([Buf(sb(f"P2_{i}", [128, 512], F32, "P2", 2048 * i)) for i in range(4)])
    for b in P.bufs:
        b.free = after
    PT = sb("PT2", [128, 2, T2, 512])
    yh, yl = sb("y2h", [128, KT, NX], F32R), sb("y2l", [128, KT, NX], F32R)
    yp = [None] * KT
    heads, S, Pn, t_pt = {}, {}, {}, []
    pv = Ctx()
    pv.t, pv.norm, pv.rstd = after, [None, None], [None, None]
    qk_read = {}

    def values_chunk(which, at):
        banks = [bk.take() for _ in range(T2)]
        for kk in range(4):
            hi, lo, t_hi, t_lo = wt.get(at + kk)
            for t_ in range(T2):
                for j in range(2):
                    x = hT[2 * kk + j]
                    c = slice(128 * t_, 128 * t_ + 128)
                    for p, (a, b, need) in enumerate(((x.hi, hi, (x.t_hi, t_hi, banks[t_].was)), (x.lo, hi, (x.t_lo,)), (x.hi, lo, (t_lo,)))):
                        last = kk == 3 and j == 1 and p == 2
                        tok = pe(lambda e, t_=t_, a=a, b=b, c=c, j=j, kk=kk, p=p, last=last: e.matmul(
                            banks[t_].ap[:, :], a[:, c], b.ap[:, 512 * j:512 * j + 512], start=kk == 0 and j == 0 and p == 0, stop=last),
                            need, signal=last or (t_ == T2 - 1 and j == 1 and p == 2))
                if kk == 3:
                    t_vT[which][t_] = act(lambda e, t_=t_: e.activation(vT[which][:, t_, :], banks[t_].ap[:, :], ACT.Copy), tok, after)
                    banks[t_].free = [t_vT[which][t_]]
            wt.release(at + kk, tok)
            yield

    def tile_product(p, which, at):
        s = bk.take()
        w = tile_pairs(wt.get(at))
        w[0] = Pair(w[0].hi, w[0].lo, [w[0].t_hi, s.was], w[0].t_lo)
        for c in range(4):
            for k in (2 * c, 2 * c + 1):
                for a, b, need, q in ((w[k].hi, hT[k].hi, (w[k].t_hi, hT[k].t_hi), 0), (w[k].hi, hT[k].lo, (hT[k].t_lo,), 1), (w[k].lo, hT[k].hi, (w[k].t_lo,), 2)):
                    tok = pe(lambda e, a=a, b=b, k=k, q=q: e.matmul(s.ap[:, :], a, b, start=k == 0 and q == 0, stop=k == KT - 1 and q == 2),
                             need, signal=k == KT - 1 and q == 2)
            if c < 3:
                yield
        wt.release(at, tok)
        i = p % 2
        need = qk_read.get(p - 2, after)
        if which == 0:
            pr = []
            for e_ in range(2):
                r = slice(64 * e_, 64 * e_ + 64)
                h_, l_ = q2[i][e_]
                th = act(lambda e, r=r, h_=h_: e.activation(h_[r, :], s.ap[r, :], ACT.Copy, scale=0.125), tok, need)
                tl = dve(lambda e, r=r, h_=h_, l_=l_: e.scalar_tensor_tensor(l_[r, :], s.ap[r, :], 0.125, h_[r, :].bitcast(F32), ALU.mult, ALU.subtract), th, need)
                pr.append(Pair(h_[:, :], l_[:, :], th, tl))
            s.free = [tl]
            heads[p] = [pr, None]
        else:
            h_, l_ = k2[i]
            th = act(lambda e: e.activation(h_[:, :], s.ap[:, :], ACT.Copy), tok, need)
            tl = dve(lambda e: e.tensor_tensor(l_[:, :], s.ap[:, :], h_[:, :].bitcast(F32), ALU.subtract), th, need)
            s.free = [tl]
            heads[p][1] = Pair(h_[:, :], l_[:, :], th, tl)
        yield

    def table(h):
        b = tabs.take()
        t = sp.dma(b.ap[:, :], d["bias"][h], b.slot, b.was)
        b.tok = pool(lambda e: e.tensor_tensor(b.ap[:, :], b.ap[:, :], lnn[:, :], ALU.add), t, t_lnn)
        tab_of[h] = b

    tab_of = {}
    units = [(p, e_, i) for p in range(HEADS) for e_ in range(2) for i in range(T2)]

    def scores(u):
        p, e_, i = units[u]
        q, k = heads[p][0][e_], heads[p][1]
        fox = p >= 4
        s = bk.take()
        n, w = 128 * (i + 1), max(256, 128 * (i + 1))
        c = slice(128 * i, 128 * i + 128)
        jobs = [(q.hi[:, c], k.hi, (q.t_hi, k.t_hi, t_z, s.was)), (q.hi[:, c], k.lo, (k.t_lo,)), (q.lo[:, c], k.hi, (q.t_lo,))]
        if fox:
            jobs.append((sel[:, 2 * (p - 4) + e_, :], fC, (t_sel, t_fC)))
        for j, (a, b, need) in enumerate(jobs):
            tok = pe(lambda e, j=j, a=a, b=b: e.matmul(s.ap[:, 0:w], a, b[:, 0:w], start=j == 0, stop=j == len(jobs) - 1), need, signal=j == len(jobs) - 1)
        qk_read[p] = [tok]
        c0 = 192 + 8 * (u % 4)
        P_ = P.take()
        if fox:
            tab, t_tab = tri[:, 512 - n:512], t_tri
        else:
            b = tab_of[2 * p + e_]
            tab, t_tab = b.ap[:, 512 - n:512], b.tok
        t = dve(lambda e: e.tensor_tensor_reduce(P_.ap[:, 0:n], s.ap[:, 0:n], tab, 1.0, -3.0e38, ALU.add, ALU.max, stat[:, c0:c0 + 1]),
                tok, t_tab, P_.was, K.stat_free[u % 4])
        s.free = [t]
        if not fox and i == 3:
            b.free = [t]
        t = dve(lambda e: e.tensor_scalar(stat[:, c0 + 1:c0 + 2], stat[:, c0:c0 + 1], -1.0, None, ALU.mult), t)
        t = act(lambda e: e.activation(P_.ap[:, 0:n], P_.ap[:, 0:n], ACT.Exp, bias=stat[:, c0 + 1:c0 + 2], accum_out=stat[:, c0 + 2:c0 + 3]), t)
        Pn[u] = [P_, t, c0, n, None]

    def normalise(u):
        P_, t, c0, n, _ = Pn[u]
        t = dve(lambda e: e.reciprocal(stat[:, c0 + 3:c0 + 4], stat[:, c0 + 2:c0 + 3]), t)
        t = pool(lambda e: e.tensor_scalar(P_.ap[:, 0:n], P_.ap[:, 0:n], stat[:, c0 + 3:c0 + 4], 0.0, ALU.mult, ALU.add), t)
        Pn[u][4] = t
        K.stat_free[u % 4] = [t]

    def turn_p(u):
        p, e_, i = units[u]
        P_, _, _, n, t = Pn[u]
        s = bk.take()
        for kt in range(i + 1):
            tok = pe(lambda e, kt=kt: e.transpose(s.ap[:, 128 * kt:128 * kt + 128], P_.ap[:, 128 * kt:128 * kt + 128], K.ident[:, :]), t, s.was, signal=kt == i)
        P_.free = [tok]
        dst = PT[:, e_, 0:i + 1, 128 * i:128 * i + 128]
        src = s.ap[:, 0:n].rearrange("p (t q) -> p t q", q=128)
        if u % 2:
            t1 = act(lambda e: e.activation(dst, src, ACT.Copy), tok, pv.t)
        else:
            t1 = dve(lambda e: e.tensor_copy(dst, src), tok, pv.t)
        s.free = [t1]
        t_pt.append(t1)

    def weigh(p):
        s = bk.take()
        fox = p // 4
        for kt in range(T2):
            for e_ in range(2):
                h = 2 * (p % 4) + e_
                tok = pe(lambda e, kt=kt, e_=e_, h=h: e.matmul(s.ap[64 * e_:64 * e_ + 64, 128 * kt:512], vT[fox][:, kt, 64 * h:64 * h + 64], PT[:, e_, kt, 128 * kt:512],
                                                               start=kt == 0, stop=kt == 3, skip_group_check=True),
                         t_pt, t_vT[fox], s.was, signal=kt == 3 and e_ == 1)
        pv.t = [tok]
        t_pt.clear()
        b = tmps.take()
        w = small2[:, 8 + p:9 + p]
        t_hi = act(lambda e: e.activation(yh[:, p, :], s.ap[:, :], ACT.Copy, scale=w), tok, after)
        t_sq = act(lambda e: e.activation(b.ap[:, :], s.ap[:, :], ACT.Square), tok, b.was)
        t_lo = dve(lambda e: e.scalar_tensor_tensor(yl[:, p, :], s.ap[:, :], w, yh[:, p, :].bitcast(F32), ALU.mult, ALU.subtract), t_hi, t_sq, after)
        s.free = [t_lo]
        yp[p] = Pair(yh[:, p, :], yl[:, p, :], t_hi, t_lo)

        def add():
            if p % 4 == 0:
                pv.norm[fox] = Norm(K, T2, 512, EPS, 4, bk)
            b.free = [pv.norm[fox].add(b.ap, t_sq)]
            if p % 4 == 3:
                pv.rstd[fox] = pv.norm[fox].finish(stat[:, 16 + 8 * fox:20 + 8 * fox], stat[:, 32 + 8 * fox:36 + 8 * fox], K.free_stat)
        return add

    t_x = list(t_xN)

    def begin_out():
        done = fence(K)
        wo = []
        for half, name in enumerate(("wo2d", "wo2f")):
            for k in range(4):
                hb, lb = (Buf(K.sb(f"{name}{p}{k}", [128, 1024], F32R, name, 4096 * (2 * k + j))) for j, p in enumerate("hl"))
                hb.free = lb.free = done
                wt.place[K.w2 + 24 + 4 * half + k] = (hb, lb)

        def split(n):
            for _ in range(n):
                wt.split()
                hb, lb, t_hi, t_lo = wt.done[-1]
                wo.append([Pair(hb.ap[:, 512 * c:512 * c + 512], lb.ap[:, 512 * c:512 * c + 512], t_hi, t_lo) for c in range(2)])

        def product(half, t_, c):
            s = bk.take()
            cols = slice(128 * t_, 128 * t_ + 128)
            for k in range(4 * half, 4 * half + 4):
                y, w = yp[k], wo[k][c]
                for q, (a, b, need) in enumerate(((y.hi[:, cols], w.hi, (y.t_hi, w.t_hi, s.was)), (y.lo[:, cols], w.hi, (y.t_lo,)), (y.hi[:, cols], w.lo, (w.t_lo,)))):
                    last = k == 4 * half + 3 and q == 2
                    tok = pe(lambda e, s=s, a=a, b=b, k=k, q=q, last=last: e.matmul(s.ap[:, :], a, b, start=k == 4 * half and q == 0, stop=last), need, signal=last)
            x = xN[:, t_, 512 * c:512 * c + 512]
            r = stat[:, 32 + 8 * half + t_:33 + 8 * half + t_]
            t = dve(lambda e: e.scalar_tensor_tensor(x, s.ap[:, :], r, x, ALU.mult, ALU.add), tok, pv.rstd[half], t_x[t_])
            s.free = [t]
            t_x[t_] = t
        for _ in range(4):
            split(1)
            yield
        for t_ in range(T2):
            for c in range(2):
                if t_ < 2:
                    split(1) if 2 * t_ + c < 4 else None
                product(0, t_, c)
                yield
        while len(wo) < 8:
            split(1)
        yield from last_part(lambda t_, c: product(1, t_, c))

    def last_part(product):
        M = K.moe
        M.after = fence(K)
        row1 = sb("row1", [128, D])
        t_rows = sp.dma(row1[:, :], d["rows"][:, 0, :], K.slot("s_row1"), M.after)
        M.experts = Experts(K, M.after)
        M.experts.load(2)
        M.wr, M.rc = None, None
        for t_ in range(T2):
            for c in range(2):
                product(t_, c)
            if t_ == 0:
                M.after2 = fence(K)
                h2N, h2T = sb("h2N", [128, T2, D]), sb("h2T", [128, KT, NX])
                M.wr, M.rc = sb("wr", [128, KT, 36]), sb("rc", [128, RC["n"] + 36])
                M.h2N, M.h2T = h2N, h2T
            yield
        done = fence(K)
        M.t_wr = sp.dma(M.wr[:, :, :], d["w_r"], K.slot("s_wr"), done)
        M.t_rc = sp.dma(M.rc[:, :], d["rc"], K.slot("s_rc"), done)
        M.experts.after = done
        M.experts.load(3)
        ms, rs = stat[:, 48:52], stat[:, 56:60]
        M.t_h2T, M.t_h2d = [], []
        M.slot_h = [K.slot(f"s_h2{i}") for i in range(T2)]
        for t_ in range(T2):
            sq = h2N[:, t_, :]
            t = act(lambda e, t_=t_, sq=sq: e.activation(sq, xN[:, t_, :], ACT.Square, accum_out=ms[:, t_:t_ + 1]), t_x[t_], done)
            t = dve(lambda e, t_=t_: e.tensor_scalar(ms[:, t_:t_ + 1], ms[:, t_:t_ + 1], 1.0 / D, EPS, ALU.mult, ALU.add), t)
            t = pool(lambda e, t_=t_: e.tensor_tensor(rs[:, t_:t_ + 1], ms[:, t_:t_ + 1], K.nhalf[:, 0:1], ALU.pow), t)
            t = dve(lambda e, t_=t_, sq=sq: e.scalar_tensor_tensor(sq, xN[:, t_, :], rs[:, t_:t_ + 1], row1[:, :], ALU.mult, ALU.mult), t, t_rows)
            M.t_h2d.append(act.dma(M.h2d[128 * t_:128 * t_ + 128, :], sq, M.slot_h[t_], t))
            for c in range(2):
                s = bk.take()
                for k in range(4):
                    tok = pe(lambda e, s=s, t_=t_, c=c, k=k: e.transpose(s.ap[:, 128 * k:128 * k + 128], h2N[:, t_, 512 * c + 128 * k:512 * c + 128 * k + 128], K.ident[:, :]),
                             t, s.was, signal=k == 3)
                M.t_h2T.append(act(lambda e, s=s, t_=t_, c=c: e.activation(h2T[:, 4 * c:4 * c + 4, 128 * t_:128 * t_ + 128],
                                                                          s.ap[:, :].rearrange("p (k q) -> p k q", q=128), ACT.Copy), tok, done))
                s.free = [M.t_h2T[-1]]
        M.s_log = s = bk.take()
        for t_ in range(T2):
            for k in range(KT):
                M.t_log = pe(lambda e, s=s, t_=t_, k=k: e.matmul(s.ap[:, 64 * t_:64 * t_ + 36], h2T[:, k, 128 * t_:128 * t_ + 128], M.wr[:, k, :],
                                                                start=k == 0, stop=k == KT - 1), M.t_h2T[2 * t_:2 * t_ + 2], M.t_wr, s.was, signal=k == KT - 1)

    for h in range(2):
        table(h)
    for which in range(2):
        for _ in tile_product(0, which, w0 + 4 + which):
            pass

    def products():
        at = w0 + 6
        for p in range(1, HEADS):
            for which in range(2):
                for _ in tile_product(p, which, at):
                    yield p
                at += 1
            if p == 2:
                for _ in values_chunk(1, at):
                    yield p
                at += 4
    bg = products()
    more = lambda n: [next(bg, None) for _ in range(n)]
    scores(0)
    scores(1)
    normalise(0)
    pend = None
    out_gen = None
    nu = len(units)
    for u in range(nu):
        p, e_, i = units[u]
        if u + 1 < nu:
            normalise(u + 1)
        r = u % 8
        more((2, 1, 1, 2, 1, 1, 0, 0)[r] if p != 1 else (2, 2, 2, 2, 2, 2, 0, 0)[r])
        if u % 4 == 1 and 2 * p + e_ + 1 < 8 and u // 4 + 1 >= 2:
            table(u // 4 + 1)
        if u + 2 < nu:
            scores(u + 2)
        if pend:
            pend()
            pend = None
        if r == 0 and p:
            pend = weigh(p - 1)
        turn_p(u)
        if u == 54:
            out_gen = begin_out()
        if u >= 54:
            next(out_gen)
            if u >= 62:
                next(out_gen)
    if pend:
        pend()
    weigh(HEADS - 1)()
    if not out_gen:
        out_gen = begin_out()
    for _ in out_gen:
        pass
    route(K)
    experts(K, xN, t_x, out)


class Experts:

    def __init__(self, K, after):
        self.K, self.after, self.n = K, after, 0
        self.bufs = []
        for i in range(5):
            b = Buf(None)
            b.gu = K.sb(f"we_gu{i}", [128, KT, 2 * DE], F32, f"we{i}")
            b.dn = K.sb(f"we_dn{i}", [128, 2, D], F32, f"we{i}", 16384)
            b.slots = [K.slot(f"s_gu{i}"), K.slot(f"s_dn{i}")]
            b.free = None
            self.bufs.append(b)
        self.ready = []

    def load(self, n=1):
        for _ in range(n):
            if self.n >= NE:
                return
            b = self.bufs[self.n % 5]
            free = self.after if self.n < 5 else b.free
            b.free = None
            self.ready.append((b, self.K.sp.dma(b.gu[:, :, :], self.K.d["w_gu"][self.n], b.slots[0], free),
                               self.K.sp.dma(b.dn[:, :, :], self.K.d["w_dn"][self.n], b.slots[1], free)))
            self.n += 1


def route(K):
    pe, act, dve, pool, sp, M = K.pe, K.act, K.dve, K.pool, K.sp, K.moe
    rt = K.sb("rt", [128, 3072])
    at = Ctx()
    at.n = 0

    def new(*shape, dt=None):
        n = 1
        for x in shape:
            n *= x
        v = rt[:, at.n:at.n + n]
        at.n += n
        if dt:
            v = v.bitcast(dt)
        if len(shape) == 2:
            v = v.rearrange("p (a b) -> p a b", b=shape[1])
        if len(shape) == 3:
            v = v.rearrange("p (a b c) -> p a b c", b=shape[1], c=shape[2])
        return v
    const = lambda name, n: M.rc[:, RC[name]:RC[name] + n]
    over = lambda v, n: v.unsqueeze(2).to_broadcast([128, v.shape[1], n])
    along = lambda v, n: v.unsqueeze(1).to_broadcast([128, n, v.shape[1]])
    fl = lambda v: v.rearrange("p a b -> p (a b)")

    st = Ctx()
    st.t = [M.t_log, M.t_rc]

    def tt(out, a, b, op, *more):
        st.t = dve(lambda e: e.tensor_tensor(out, a, b, op), st.t, *more)

    def ts(out, a, s1, s2, op0, op1=None):
        st.t = dve(lambda e: e.tensor_scalar(out, a, s1, s2, op0, op1) if op1 else e.tensor_scalar(out, a, s1, None, op0), st.t)

    def red(out, a, op):
        st.t = dve(lambda e: e.tensor_reduce(out, a, AX.X, op), st.t)

    def recip(out, a):
        st.t = dve(lambda e: e.reciprocal(out, a), st.t)

    def exp(out, a):
        st.t = act(lambda e: e.activation(out, a, ACT.Exp), st.t)

    lg = M.s_log.ap[:, 0:256].rearrange("p (t c) -> p t c", c=64)
    Lg, Le = new(T2, 4), new(T2, NE)
    bias = M.rc[:, RC["n"]:RC["n"] + 36]
    tt(Lg, lg[:, :, 0:4], along(bias[:, 0:4], T2), ALU.add)
    tt(Le, lg[:, :, 4:36], along(bias[:, 4:36], T2), ALU.add)
    M.s_log.free = [st.t]
    m4, s4, g1 = new(T2), new(T2), new(T2)
    E4, key4 = new(T2, 4), new(T2, 4)
    red(m4, Lg, ALU.max)
    tt(E4, Lg, over(m4, 4), ALU.subtract)
    exp(E4, E4)
    red(s4, E4, ALU.add)
    recip(s4, s4)
    tt(E4, E4, over(s4, 4), ALU.mult)
    red(g1, E4, ALU.max)

    def first(v, best, desc, out, n):
        k = new(T2)
        tt(out, v, over(best, n), ALU.is_ge)
        tt(out, out, along(desc, T2), ALU.mult)
        red(k, out, ALU.max)
        tt(out, out, over(k, n), ALU.is_equal)
    first(E4, g1, const("desc4", 4), key4, 4)
    ng = new(T2, 4)
    ts(ng, key4, -1.0, BIG, ALU.add, ALU.mult)
    L16 = Le.rearrange("p t (g j) -> p (t g) j", j=8)
    tt(L16, L16, over(fl(key4), 8), ALU.mult)
    tt(L16, L16, over(fl(ng), 8), ALU.add)
    v1, v2 = new(T2), new(T2)
    M1, M2 = new(T2, NE), new(T2, NE)
    red(v1, Le, ALU.max)
    first(Le, v1, const("desc32", NE), M1, NE)
    st.t = dve(lambda e: e.scalar_tensor_tensor(fl(Le), fl(M1), -10 * BIG, fl(Le), ALU.mult, ALU.add), st.t)
    red(v2, Le, ALU.max)
    first(Le, v2, const("desc32", NE), M2, NE)
    ed, w12 = new(T2), new(T2, 2)
    tt(ed, v2, v1, ALU.subtract)
    exp(ed, ed)
    r = new(T2)
    ts(r, ed, 1.0, None, ALU.add)
    recip(r, r)
    tt(w12[:, :, 0], g1, r, ALU.mult)
    tt(w12[:, :, 1], w12[:, :, 0], ed, ALU.mult)
    A, C, pos, cnt = new(T2, NE), new(T2 + 1, NE), new(T2, NE), None
    tt(A, M1, M2, ALU.add)
    s = K.bk.take()
    pe(lambda e: e.matmul(s.ap[:, 0:128], M.rc[:, RC["tri"]:RC["tri"] + 128], fl(A), start=True, stop=True), st.t, s.was, signal=False)
    tok = pe(lambda e: e.matmul(s.ap[:, 128:256], K.ones[:, :], fl(A), start=True, stop=True))
    st.t = dve(lambda e: e.memset(C[:, 0, :], 0.0), tok)
    for t_ in range(T2):
        tt(C[:, t_ + 1, :], C[:, t_, :], s.ap[:, 128 + NE * t_:128 + NE * t_ + NE], ALU.add)
    tt(fl(pos), fl(C[:, 0:T2, :]), s.ap[:, 0:128], ALU.add)
    s.free = [st.t]
    cnt = C[:, T2, :]
    cmp, nb, inc, far = new(NE, 4), new(NE), new(NE), new(NE)
    tt(cmp, over(cnt, 4), along(const("thr", 4), NE), ALU.is_gt)
    red(nb, cmp, ALU.add)
    st.t = dve(lambda e: e.tensor_tensor_scan(inc, K.ones[:, 0:NE], nb, 0.0, ALU.mult, ALU.add), st.t)
    tt(far, inc, nb, ALU.subtract)
    st.t = dve(lambda e: e.scalar_tensor_tensor(far, far, 128.0, const("over", NE), ALU.mult, ALU.add), st.t)
    G, H, slot, slotU = new(T2, NE), new(T2, NE), new(T2, 2), new(T2, 2, dt=U32)
    ts(fl(G), fl(pos), 63.5, 64.0, ALU.is_gt, ALU.mult)
    tt(G, G, along(const("base", NE), T2), ALU.add)
    ts(fl(H), fl(pos), 127.5, None, ALU.is_gt)
    tt(H, H, along(far, T2), ALU.mult)
    tt(fl(G), fl(G), fl(H), ALU.add)
    tt(fl(G), fl(G), fl(pos), ALU.add)
    for c, m in enumerate((M1, M2)):
        tt(fl(H), fl(m), fl(G), ALU.mult)
        red(slot[:, :, c], H, ALU.add)
    st.t = dve(lambda e: e.tensor_copy(fl(slotU), fl(slot)), st.t)
    t_slot = st.t
    row = new(T2 * 2, 4)
    ids = M.rc[:, RC["ids"]:RC["ids"] + 32].rearrange("p (c w) -> p c w", w=4)
    st.t = dve(lambda e: e.tensor_copy(row, ids), st.t)
    st.t = dve(lambda e: e.tensor_copy(row[:, :, 2], fl(w12)), st.t)
    su = fl(slotU)
    s_sc = K.slot("s_scatter")
    for j in range(2 * T2):
        s_sc.count += 16
        pool.ops.append((_tokens([st.t, M.t_meta0]), lambda e, j=j: e.indirect_dma_start(
            out=M.meta, out_offset=bass.IndirectOffsetOnAxis(ap=su[:, j:j + 1], axis=0), in_=row[:, j, :], in_offset=None,
            bounds_check=ROWS - 1, oob_is_err=False), (s_sc.sem, 16)))
    t_list = (s_sc.sem, s_sc.count)
    f32_, p16, nbt = new(NE), new(PAIRS), new(1)
    ctl = new(2 + MORE)
    eq = new(MORE, NE)
    M.ctl = K.sb("ctl", [128, 2 + MORE], I32)
    ts(f32_, cnt, 64.5, None, ALU.is_gt)
    red(p16, f32_.rearrange("p (a b) -> p a b", b=2), ALU.max)
    tt(p16, p16, const("pow2", PAIRS), ALU.mult)
    red(ctl[:, 0:1], p16, ALU.add)
    st.t = dve(lambda e: e.tensor_copy(ctl[:, 1:2], inc[:, NE - 1:NE]), st.t)
    tt(eq, along(inc, MORE), over(const("nth", MORE), NE), ALU.is_le)
    red(ctl[:, 2:2 + MORE], eq, ALU.add)
    ts(ctl[:, 2:2 + MORE], ctl[:, 2:2 + MORE], float(NE - 1), None, ALU.min)
    M.t_ctl = dve(lambda e: e.tensor_copy(M.ctl[:, :], ctl), st.t)
    g = GROUPS + MORE
    lst = K.sb("list", [g, 512], F32, "h2N")
    t = sp.dma(lst[:, :], M.meta.rearrange("(g p) w -> g (p w)", p=128), K.slot("s_list"), t_list, M.t_h2d, M.t_log, pe.last())
    s3 = K.bk.take()
    for w in range(3):
        tok = pe(lambda e, w=w: e.transpose(s3.ap[:, 64 * w:64 * w + g], lst[:, :].rearrange("g (p w) -> g w p", w=4)[:, w, :], K.ident[0:g, 0:g]), t, s3.was, signal=w == 2)
    kept = K.sb("kept", [128, 3 * g + 24])
    M.tok, M.row, M.w = kept[:, 0:g].bitcast(U32), kept[:, g:2 * g].bitcast(U32), kept[:, 2 * g:3 * g]
    M.tick = kept[:, 3 * g:3 * g + 24]
    for v, w in ((M.tok, 0), (M.row, 1), (M.w, 2)):
        M.t_list = dve(lambda e, v=v, w=w: e.tensor_copy(v, s3.ap[:, 64 * w:64 * w + g]), tok)
    s3.free = [M.t_list]
    assert at.n <= 3072, at.n


class Guarded:

    def __init__(self, queues):
        self.at = [(q, len(q.ops)) for q in queues]

    def close(self, test):
        for q, start in self.at:
            body = q.ops[start:]
            del q.ops[start:]
            if not body:
                continue
            n = raises(body, q.sem)
            q.ops.append(("guard", test, body, [(q.sem, q.count - n, n)] if n else []))


def raises(ops, sem):
    n = 0
    for op in ops:
        if op[0] == "guard":
            n += sum(by for _, _, by in op[3])
        elif op[0] != "register" and op[2] and op[2][0].num == sem.num:
            n += 1
    return n


def experts(K, xN, t_x, out):
    pe, act, dve, pool, sp, d, M, sb = K.pe, K.act, K.dve, K.pool, K.sp, K.d, K.moe, K.sb
    E, bk = M.experts, K.bk
    start = fence(K) + [M.t_list]
    for q in (pe, act, dve, pool, sp):
        q.ops.append(("register", "pairs", M.ctl[0:1, 0:1], M.t_ctl, 2 ** PAIRS - 1))
        q.ops.append(("register", "more", M.ctl[0:1, 1:2], M.t_ctl, MORE))

    def bufs(name, n, shape=(D,), slots=True):
        out = []
        for i in range(n):
            b = Buf(sb(f"{name}{i}", [128, *shape], F32, name, 4096 * i), K.slot(f"s_{name}{i}") if slots else None)
            b.free = start
            out.append(b)
        return Ring(out)
    M.row2 = sb("row2", [128, D])
    M.t_row2 = act.dma(M.row2[:, :], d["rows"][:, 1, :], K.slot("s_row2"), start)
    xg, xg2 = bufs("xg", 4), bufs("xg2_", 2, slots=False)
    XT, XT2 = bufs("XT", 2, (KT, 128), False), bufs("XT2_", 1, (KT, 128), False)
    Y, Y2 = bufs("Y", 3), bufs("Y2_", 2, slots=False)
    he = sb("he", [128, 512])
    heT = sb("heT", [128, 2, 128], F32, "he", 2048)
    t_he = [start, start]
    for b in xg.bufs + xg2.bufs:
        b.free = [dve(lambda e, b=b: e.memset(b.ap[:, :], 0.0), start)]

    def gather(b, g, slot):
        t = slot.token()
        pool.ops.append((_tokens([b.was, M.t_list, M.t_h2d]), lambda e: e.indirect_dma_start(
            out=b.ap[:, :], out_offset=None, in_=M.h2d, in_offset=bass.IndirectOffsetOnAxis(ap=M.tok[:, g:g + 1], axis=0),
            bounds_check=NX - 1, oob_is_err=False), (slot.sem, 16)))
        return b, t

    def turn_x(ring, b, t):
        x = ring.take()
        for c in range(2):
            s = bk.take()
            for k in range(4):
                tok = pe(lambda e, s=s, c=c, k=k: e.transpose(s.ap[:, 128 * k:128 * k + 128], b.ap[:, 512 * c + 128 * k:512 * c + 128 * k + 128], K.ident[:, :]),
                         t, s.was, signal=k == 3)
            src = s.ap[:, :].rearrange("p (k q) -> p k q", q=128)
            if c:
                t1 = act(lambda e, src=src: e.activation(x.ap[:, 4:8, :], src, ACT.Copy), tok, x.was)
            else:
                t0 = t1 = dve(lambda e, src=src: e.tensor_copy(x.ap[:, 0:4, :], src), tok, x.was)
            s.free = [t1]
        b.free = [tok]
        return x, [t0, t1]

    def mlp(x, t_x_, ws, y, g, beside=lambda: None):
        n = 128 // len(ws)
        s = bk.take()
        for k in range(KT):
            for j, (b, t_gu, t_dn) in enumerate(ws):
                o = slice(n * j, n * j + n)
                tok = pe(lambda e, k=k, o=o, b=b: e.matmul(s.ap[o, :], x.ap[:, k, o], b.gu[:, k, :], start=k == 0, stop=k == KT - 1, skip_group_check=True),
                         t_x_, t_gu, s.was, signal=k == KT - 1 and j == len(ws) - 1)
        x.free = [tok]
        t = act(lambda e: e.activation(he[:, 0:256], s.ap[:, 0:256], ACT.Silu), tok, t_he[0])
        t = dve(lambda e: e.tensor_tensor(he[:, 256:512], s.ap[:, 256:512], he[:, 0:256], ALU.mult), t)
        s.free = [t]
        got = beside()
        s2 = bk.take()
        for k in range(2):
            tok = pe(lambda e, k=k: e.transpose(s2.ap[:, 128 * k:128 * k + 128], he[:, 256 + 128 * k:384 + 128 * k], K.ident[:, :]), t, s2.was, signal=k == 1)
        t_he[0] = tok
        t = dve(lambda e: e.tensor_copy(heT[:, :, :], s2.ap[:, 0:256].rearrange("p (k q) -> p k q", q=128)), tok, t_he[1])
        s2.free = [t]
        ts = []
        for c in range(2):
            s = bk.take()
            for k in range(2):
                for j, (b, t_gu, t_dn) in enumerate(ws):
                    o = slice(n * j, n * j + n)
                    tok = pe(lambda e, s=s, k=k, o=o, b=b, c=c: e.matmul(s.ap[o, :], heT[:, k, o], b.dn[:, k, 512 * c:512 * c + 512], start=k == 0, stop=k == 1, skip_group_check=True),
                             t, t_dn, s.was, signal=k == 1 and j == len(ws) - 1)
            w = M.w[:, g:g + 1]
            if c:
                ts.append(dve(lambda e, s=s: e.tensor_scalar(y.ap[:, 512:1024], s.ap[:, :], w, None, ALU.mult), tok, y.was, M.t_list))
            else:
                ts.append(act(lambda e, s=s: e.activation(y.ap[:, 0:512], s.ap[:, :], ACT.Copy, scale=w), tok, y.was, M.t_list))
            s.free = [ts[-1]]
        t_he[1] = tok
        return ts, got

    def scatter(y, g, slot, *after):
        t = slot.token()
        pool.ops.append((_tokens(after), lambda e: e.indirect_dma_start(
            out=M.ybuf, out_offset=bass.IndirectOffsetOnAxis(ap=M.row[:, g:g + 1], axis=0), in_=y.ap[:, :], in_offset=None,
            bounds_check=2 * NX - 1, oob_is_err=False), (slot.sem, 16)))
        return t

    def guarded(queues, test, body):
        before = {id(b): b.free for b in bk.bufs}
        he_before = list(t_he)
        g = Guarded(queues)
        got = body()
        g.close(test)
        for b in bk.bufs:
            if b.free is not before[id(b)]:
                b.free = [before[id(b)], b.free]
        t_he[:] = [[x, y] for x, y in zip(he_before, t_he)]
        return got

    crowded = lambda i: lambda r: ((r["pairs"] >> i) & 1) > 0
    second = {}

    def gather2(i):
        st = second[i] = Ctx()
        st.slots = [K.slot(f"s_second{i}_{c}") for c in range(2)]
        b = xg2.take()
        g = Guarded((pool,))
        st.x = gather(b, 2 * i + 1, st.slots[0])
        g.close(crowded(i))

    def scatter2(i, y, ts):
        g = Guarded((pool,))
        second[i].stored = scatter(y, 2 * i + 1, second[i].slots[1], ts)
        g.close(crowded(i))

    def stored2(i):
        g = Guarded((pool,))
        second[i].y.free = [pool(lambda e: e.memset(M.tick[:, i:i + 1], 0.0), second[i].stored)]
        g.close(crowded(i))

    firsts = [gather(xg.take(), 2 * i, b.slot) for i, b in enumerate(list(xg.bufs))]
    gather2(0)
    gather2(1)
    nxt = turn_x(XT, *firsts[0])
    for i in range(PAIRS):
        ws = [E.ready[2 * i], E.ready[2 * i + 1]]
        y = Y.take()
        ts, nxt = mlp(*nxt, ws, y, 2 * i, lambda: turn_x(XT, *firsts[i + 1]) if i + 1 < PAIRS else None)
        y.free = [scatter(y, 2 * i, y.slot, ts)]
        y2 = second[i].y = Y2.take()
        ts = guarded((pe, act, dve), crowded(i), lambda: mlp(*turn_x(XT2, *second[i].x), ws, y2, 2 * i + 1)[0])
        for w, _, _ in ws:
            w.free = [pe.last()]
        E.load(2)
        scatter2(i, y2, ts)
        if i + 4 < PAIRS:
            b = xg.take()
            firsts.append(gather(b, 2 * i + 8, b.slot))
        if i + 2 < PAIRS:
            gather2(i + 2)
        if i >= 1:
            stored2(i - 1)
    stored2(PAIRS - 1)

    w = Buf(None)
    w.gu, w.dn = E.bufs[0].gu, E.bufs[0].dn

    def far(n):
        after = [b.free for b in E.bufs[:1]] + [pe.last()]

        def load(e, dst, src):
            v = e.value_load(M.ctl[0:1, 2 + n:3 + n], min_val=0, max_val=NE - 1)
            return e.dma_start(dst, src[bass.ds(v, 1)].rearrange("o p k c -> (o p) k c"))
        s_far = [K.slot(f"s_far_{n}{c}") for c in range(4)]
        t = [s_.token() for s_ in s_far[0:2]]
        sp.ops.append((_tokens(after), lambda e: load(e, w.gu[:, :, :], d["w_gu"]), (s_far[0].sem, 16)))
        sp.ops.append(([], lambda e: load(e, w.dn[:, :, :], d["w_dn"]), (s_far[1].sem, 16)))
        y, b = Y2.take(), xg2.take()
        ts, _ = mlp(*turn_x(XT2, *gather(b, GROUPS + n, s_far[2])), [(w, t[0], t[1])], y, GROUPS + n)
        y.free = [pool(lambda e: e.memset(M.tick[:, PAIRS + n:PAIRS + n + 1], 0.0), scatter(y, GROUPS + n, s_far[3], y.was, ts))]

    def all_far():
        far(0)
        for n in range(1, MORE):
            g = Guarded((pe, act, dve, pool, sp))
            far(n)
            g.close(lambda r, n=n: r["more"] > n)
    stored = [b.free for b in Y.bufs + Y2.bufs]
    g = Guarded((pe, act, dve, pool, sp))
    all_far()
    g.close(lambda r: r["more"] > 0)
    finish(K, xN, t_x, [stored, pool.last()], out)


def finish(K, xN, t_x, stored, out):
    act, dve, pool, sp, M, sb = K.act, K.dve, K.pool, K.sp, K.moe, K.sb
    after = [K.pe.last(), act.last(), dve.last(), pool.last()]
    yin = Ring([Buf(sb(f"yin{i}", [128, 2, D], F32, "yin", 8192 * i), K.slot(f"s_yin{i}")) for i in range(4)])
    for b in yin.bufs:
        b.free = after
    ms, rs = K.stat[:, 64:68], K.stat[:, 72:76]
    t_out = []
    s_out = [K.slot(f"s_out{i}") for i in range(T2)]
    for t_ in range(T2):
        b = yin.take()
        x = xN[:, t_, :]
        t = sp.dma(b.ap[:, :, :], M.ybuf[256 * t_:256 * t_ + 256, :].rearrange("(p c) n -> p c n", c=2), b.slot, b.was, stored)
        t = dve(lambda e, b=b, x=x: e.tensor_tensor(x, x, b.ap[:, 0, :], ALU.add), t, t_x[t_])
        t = dve(lambda e, b=b, x=x: e.tensor_tensor(x, x, b.ap[:, 1, :], ALU.add), t)
        t = act(lambda e, b=b, x=x, t_=t_: e.activation(b.ap[:, 0, :], x, ACT.Square, accum_out=ms[:, t_:t_ + 1]), t)
        t = dve(lambda e, t_=t_: e.tensor_scalar(ms[:, t_:t_ + 1], ms[:, t_:t_ + 1], 1.0 / D, EPS, ALU.mult, ALU.add), t)
        t = pool(lambda e, t_=t_: e.tensor_tensor(rs[:, t_:t_ + 1], ms[:, t_:t_ + 1], K.nhalf[:, 0:1], ALU.pow), t)
        t = dve(lambda e, b=b, x=x, t_=t_: e.scalar_tensor_tensor(b.ap[:, 1, :], x, rs[:, t_:t_ + 1], M.row2[:, :], ALU.mult, ALU.mult), t, M.t_row2)
        t = act.dma(out[128 * t_:128 * t_ + 128, :], b.ap[:, 1, :], s_out[t_], t)
        b.free = [t]
        t_out.append(t)
    sp.ops.append((_tokens(t_out), lambda e: None, None))


def buckets(dist):
    d32 = np.maximum(dist, 1).astype(np.float32)
    large = 16 + (np.log(d32 / np.float32(16)) / np.float32(np.log(128.0)) * np.float32(16)).astype(np.int32)
    return np.where(dist < 16, dist, np.minimum(large, 31))


def host(inputs):
    f = lambda n: np.asarray(inputs[n])
    out = {}
    x, ctx = f("x")[0], f("ctx")[0]
    cols = lambda a, n: a.reshape(n, 128).T
    out["xc"] = np.concatenate([x.T.reshape(KT, 128, NX), ctx.T.reshape(KT, 128, NC)], 2).transpose(1, 0, 2)
    sm = np.zeros((128, SMALL["n"]), np.float32)

    def put(name, a):
        a = a.reshape(128, -1)
        sm[:, SMALL[name]:SMALL[name] + a.shape[1]] = a
    put("norm_w", np.concatenate([cols(a, 8) for a in f("norm_w")], 1))
    put("b_mod", np.concatenate([cols(a, 24) for a in f("b_mod")], 1))
    put("qn_w", np.concatenate([cols(a, 2) for a in f("q_norm_w")], 1))
    put("kvn_w", f("kv_norm_w").T)
    put("sc_w", f("sc_conv_w").reshape(2, 3, 2, 128).transpose(3, 0, 2, 1))
    put("cf_w", f("cf_conv_w").reshape(2, 31, 2, 128).transpose(3, 0, 2, 1))
    for n, s in (("cf_b", "cf_conv_b"), ("ln_w", "cf_ln_w"), ("ln_b", "cf_ln_b"), ("pw_b", "cf_pw_b")):
        put(n, np.concatenate([cols(a, 2) for a in f(s)], 1))
    for n, s in (("qh_w", "q_head_norm_w"), ("kh_w", "k_head_norm_w")):
        a = np.ones((128, 2), np.float32)
        a[0:64] = f(s)[:, 0:64].T
        put(n, a)
    put("c", np.stack([cols(f("c")[0], 8), cols(f("c_ctx"), 8)], 2))
    out["small"] = sm
    out["ident"] = np.eye(128, dtype=np.float32)
    pos = np.arange(NX)
    inv = (10000.0 ** (-np.arange(8, dtype=np.float64) / 8)).astype(np.float32)
    ang = np.concatenate([(pos // 64)[:, None].astype(np.float32) * inv, (pos % 64)[:, None].astype(np.float32) * inv], 1)
    cos, sin = np.cos(ang), np.sin(ang)
    lay = lambda a: a.reshape(4, 128, 32).transpose(1, 0, 2).astype(np.float32)
    out["ctab"] = lay(np.concatenate([cos, cos], 1))
    out["stab"] = lay(np.concatenate([-sin, sin], 1))
    rw = []
    for l in range(2):
        q, k = f("q_head_norm_w")[l, 64:], f("k_head_norm_w")[l, 64:]
        rw.append(np.stack([q, np.concatenate([q[16:], q[:16]]), k, np.concatenate([k[16:], k[:16]])]))
    out["rope_w"] = np.broadcast_to(np.stack(rw)[:, None], (2, 128, 4, 32))
    out["w_mod"] = f("w_mod").reshape(2, KT, 128, 3072)
    w = f("w_in")
    tile = lambda l, c: w[l][:, c:c + 128].reshape(KT, 128, 128).transpose(1, 0, 2).reshape(128, 1024)
    out["w_in"] = np.stack([np.stack([tile(l, COLS[n] + 128 * i) for n, i in TILES]) for l in range(2)])
    out["w_kr"] = np.stack([w[l][:, 384:416].reshape(KT, 128, 32).transpose(1, 0, 2) for l in range(2)])
    out["w_uq"] = f("w_uq").reshape(2, 2, 128, 768).transpose(0, 2, 1, 3)
    kv = f("w_ukv").reshape(2, 128, HEADS, 128)
    out["w_ukv"] = np.concatenate([kv[..., :64].reshape(2, 128, 512), kv[..., 64:].reshape(2, 128, 512)], 2)
    out["pw"] = f("cf_pw_w").reshape(2, 2, 128, 256).transpose(0, 2, 1, 3)
    out["w_out"] = f("w_out").reshape(2, KT, 128, KT, 128).transpose(0, 3, 2, 1, 4).reshape(2, KT, 128, 1024)
    s2 = np.zeros((128, SMALL2["n"]), np.float32)
    s2[:, 0:8] = cols(f("attn_norm_2")[0], 8)
    s2[:, 8:12] = cols(f("out_norm_dil_2")[0], 4)
    s2[:, 12:16] = cols(f("out_norm_fox_2")[0], 4)
    s2[0:8, 16] = f("b_forget_2")[0]
    out["small2"] = s2
    w = f("w_in_2")[0]
    t2 = lambda c: w[:, c:c + 128].reshape(KT, 128, 128).transpose(1, 0, 2).reshape(128, 1024)
    v2 = lambda c: [w[256 * k:256 * k + 256, c:c + 512].reshape(2, 128, 512).transpose(1, 0, 2).reshape(128, 1024) for k in range(4)]
    tiles = v2(1024)
    for p in range(8):
        o = 128 * p if p < 4 else 1536 + 128 * (p - 4)
        tiles += [t2(o), t2(o + 512)]
        if p == 2:
            tiles += v2(2560)
    out["w_in2"] = np.stack(tiles)
    out["w_out2"] = f("w_out_2").reshape(KT, 128, 1024)
    out["rows"] = np.broadcast_to(np.stack([f("ffn_norm_2")[0], f("final_norm_2")]), (128, 2, 1024))
    w_r = np.concatenate([f("w_router_group_2")[0], f("w_router_expert_2")[0]], 1)
    out["w_r"] = w_r.reshape(KT, 128, 36).transpose(1, 0, 2)
    gu = np.concatenate([f("w_expert_gate_2")[0], f("w_expert_up_2")[0]], 2)
    out["w_gu"] = gu.reshape(NE, KT, 128, 2 * DE).transpose(0, 2, 1, 3)
    out["w_dn"] = f("w_expert_down_2")[0].reshape(NE, 2, 128, D).transpose(0, 2, 1, 3)
    out["empty"] = np.tile(np.array([1e6, 1e6, 0, 0], np.float32), (GROUPS + MORE, 128))
    rc = np.zeros((128, RC["n"] + 36), np.float32)
    e = np.arange(NE)
    rc[:, 0:4] = 4 - np.arange(4)
    rc[:, 4:36] = 32 - e
    rc[:, 36:40] = 128 * np.arange(1, 5) + 0.5
    base = 256 * (e // 2) + 64 * (e % 2)
    rc[:, RC["base"]:RC["base"] + NE] = base
    rc[:, RC["over"]:RC["over"] + NE] = 128 * GROUPS - 128 - 64 - base - 0
    tok = 128 * np.arange(T2)[None, :] + np.arange(128)[:, None]
    ids = np.zeros((128, T2, 2, 4), np.float32)
    ids[..., 0] = tok[..., None]
    ids[..., 1] = 2 * tok[..., None] + np.arange(2)
    rc[:, RC["ids"]:RC["ids"] + 32] = ids.reshape(128, 32)
    rc[:, RC["pow2"]:RC["pow2"] + PAIRS] = 2.0 ** np.arange(PAIRS)
    rc[:, RC["nth"]:RC["nth"] + MORE] = np.arange(MORE)
    rc[:, RC["tri"]:RC["tri"] + 128] = np.arange(128)[:, None] < np.arange(128)[None, :]
    rc[:, RC["n"]:] = np.concatenate([f("b_router_group_2")[0], f("b_router_expert_2")[0]])
    out["rc"] = rc
    out["w_f"] = w[:, 3072:3080].reshape(KT, 128, 8).transpose(1, 0, 2)
    sel = np.zeros((128, 8, 128), np.float32)
    for h in range(8):
        sel[h, h] = sel[32 + h, h] = 1
    out["sel"] = sel.reshape(128, 1024)
    dist = np.arange(128)[:, None] + 384 - np.arange(512)[None, :]
    n = (dist <= 128) * 1 + (dist % 4 == 0) + (dist % 16 == 0)
    ok = (dist >= 0) & (n > 0)
    out["lnn"] = np.where(ok, np.log(np.maximum(n, 1)), -BIG).astype(np.float32)
    out["causal"] = np.where(dist >= 0, 0, -BIG).astype(np.float32)
    out["bias"] = f("rel_bias_2")[buckets(np.maximum(dist, 0))].transpose(2, 0, 1)
    return {k: np.ascontiguousarray(v) for k, v in out.items()}


def play(K):
    with K.nc.Block() as block:
        block.sync(K.sp.play)
        block.tensor(K.pe.play)
        block.vector(K.dve.play)
        block.scalar(K.act.play)
        block.gpsimd(K.pool.play)


def program(nc, dram, out):
    with ExitStack() as ctx:
        K = setup(nc, ctx, dram)
        K.ctx = ctx
        second_block(K, *first_block(K), out)
        play(K)


def kernel(**inputs):
    import concourse.bacc as _bacc
    from concourse.bass_utils import run_bass_kernel_spmd as _run

    nc = _bacc.Bacc("TRN2", target_bir_lowering=False, num_devices=1)
    arrays, dram = {}, {}
    for name, a in host(inputs).items():
        arrays[f"in_{name}_dram"] = a
        dram[name] = nc.dram_tensor(f"in_{name}_dram", a.shape, mybir.dt.from_np(a.dtype), kind="ExternalInput").ap()
    out = nc.dram_tensor("out_0_dram", (NX, D), F32, kind="ExternalOutput").ap()
    program(nc, dram, out)
    r = _run(nc, [arrays], core_ids=[0])
    return r.results[0]["out_0_dram"].reshape(1, NX, D)
```

```python
from contextlib import ExitStack

import numpy as np

import concourse.bass as bass
from concourse import mybir

F32 = mybir.dt.float32
F32R = mybir.dt.float32r
I32 = mybir.dt.int32
U32 = mybir.dt.uint32
ACT = mybir.ActivationFunctionType
ALU = mybir.AluOpType
AX = mybir.AxisListType

NX = 512
NC = 256
NT = NX + NC
D = 1024
KT = 8
HEADS = 8
QK = 96
EPS = 1e-6
LN_EPS = 1e-5

COLS = dict(cq=0, ckv=256, kr=384, ga=416, sc_in=928, sc_b=1184, sc_c=1440, gb=1696, glu=1952, gc=2464)


def _tile_starts():
    t = [("glu", 2), ("glu", 0), ("glu", 3), ("glu", 1), ("ckv", 0), ("cq", 0), ("cq", 1)]
    for i in range(2):
        t += [("sc_in", i), ("sc_c", i), ("sc_b", i), ("gb", i)]
    t += [("gc", i) for i in range(2)] + [("ga", i) for i in range(4)]
    return t


TILES = _tile_starts()

SMALL = {}


def _small_columns():
    at = 0
    for name, n in (("norm_w", 16), ("b_mod", 48), ("qn_w", 4), ("kvn_w", 2), ("sc_w", 12), ("cf_w", 124),
                    ("cf_b", 4), ("ln_w", 4), ("ln_b", 4), ("pw_b", 4), ("qh_w", 2), ("kh_w", 2), ("c", 16)):
        SMALL[name] = at
        at += n
    SMALL["n"] = at


_small_columns()

SMALL2 = dict(norm=0, on=8, bf=16, ffn=17, n=25)


class Queue:

    def __init__(self, sem):
        self.sem, self.count, self.ops = sem, 0, []

    def __call__(self, make, *after, signal=True):
        self.ops.append((_tokens(after), make, (self.sem, 1) if signal else None))
        if not signal:
            return None
        self.count += 1
        return (self.sem, self.count)

    def dma(self, out, src, slot, *after):
        slot.count += 16
        self.ops.append((_tokens(after), lambda e: e.dma_start(out, src), (slot.sem, 16)))
        return (slot.sem, slot.count)

    def last(self):
        return (self.sem, self.count)

    def play(self, e):
        self.regs = {}
        self.run(e, self.ops, {})

    def run(self, e, ops, seen):
        for op in ops:
            if op[0] == "register":
                _, name, ap, after, top = op
                e.wait_ge(*after)
                self.regs[name] = e.value_load(ap, min_val=0, max_val=top)
                continue
            if op[0] == "guard":
                _, test, body, raised = op
                with e.If(test(self.regs)):
                    self.run(e, body, dict(seen))
                with e.Else():
                    for sem, before, by in raised:
                        e.wait_ge(sem, before)
                        e.sem_inc(sem, by)
                continue
            after, make, signal = op
            for sem, value in after:
                if seen.get(sem.num, 0) < value:
                    e.wait_ge(sem, value)
                    seen[sem.num] = value
            ins = make(e)
            if signal:
                ins.then_inc(*signal)


class Slot:

    def __init__(self, sem):
        self.sem, self.count = sem, 0

    def token(self):
        self.count += 16
        return (self.sem, self.count)


class Buf:

    def __init__(self, ap, slot=None):
        self.ap, self.free, self.slot, self.was = ap, [], slot, None


class Ring:
    def __init__(self, bufs):
        self.bufs = list(bufs)

    def take(self):
        b = self.bufs.pop(0)
        assert b.free is not None, "taken before its last readers are known"
        b.was, b.free = b.free, None
        self.bufs.append(b)
        return b

    def hold(self):
        b = self.take()
        self.bufs.remove(b)
        return b

    def release(self, b):
        self.bufs.append(b)


def _tokens(after):
    out = []
    for a in after:
        if a is None:
            continue
        if isinstance(a, tuple) and len(a) == 2 and isinstance(a[1], int):
            out.append(a)
        else:
            out += _tokens(a)
    return out


def plan(items, base, end):
    rng = np.random.default_rng(0)
    order = sorted(items, key=lambda x: (-(x[3] - x[2]), -x[1]))
    weight = {x[0]: float(i) for i, x in enumerate(order)}
    for _ in range(20000):
        placed = []
        for name, size, a, b in sorted(items, key=lambda x: weight[x[0]]):
            size = (size + 31) // 32 * 32
            spans = sorted((o, o + s) for _, o, s, p, q in placed if not (q < a or b < p))
            at = base
            for lo, hi in spans:
                if at + size <= lo:
                    break
                at = max(at, hi)
            if at + size > end:
                weight[name] -= 8 + 8 * rng.random()
                break
            placed.append((name, at, size, a, b))
        else:
            return {name: at for name, at, _, _, _ in placed}
    assert False, "no room"


class Ctx:
    pass


def setup(nc, ctx, dram):
    K = Ctx()
    K.nc, K.d = nc, dram
    sem = lambda name: ctx.enter_context(nc.semaphore(name))
    K.pe, K.act, K.dve, K.pool, K.sp = (Queue(sem(n)) for n in ("s_pe", "s_act", "s_dve", "s_pool", "s_sp"))
    K.slot = lambda name: Slot(sem(name))

    kb = 1024
    row = NT * 4
    items = [
        ("ident", 512, 0, 199), ("ones", 512, 0, 199), ("ctab", 512, 0, 75), ("stab", 512, 0, 75),
        ("small", 4 * SMALL["n"], 0, 99), ("c2T", 1024, 0, 20), ("nhalf", 64, 0, 199),
        ("mod", 2 * 4 * 8 * 2 * 4, 0, 99), ("rope_w", 4 * 128, 0, 75), ("rope_t", 4 * 512, 0, 75),
        ("stat", 4 * 256, 0, 199),
        ("raw", 2 * 4 * kb, 0, 130), ("whi", 2 * 4 * kb, 0, 113), ("wlo", 2 * 4 * kb, 0, 113),
        ("xc", 8 * row, 0, 0), ("wmod0", 16 * kb, 0, 0), ("wx", 16 * kb, 0, 10), ("wgate", 16 * kb, 0, 10), ("wgate2", 32 * kb, 0, 10), ("modrow", 2 * kb, 0, 10),
        ("tmpa", 5 * 3264, 0, 24), ("tmpc", 5 * 3264, 40, 74), ("tmpe", 5 * 3264, 90, 100),
        ("x1", 8 * 512 * 4, 40, 100), ("xc1", 8 * 256 * 4, 42, 60), ("xr", 3 * 2 * kb, 40, 42), ("acc", 2 * kb, 40, 44), ("accc", 1024, 42, 60), ("acc2", 2 * kb, 90, 100),
        ("wv", 16 * kb, 92, 100), ("wv2", 32 * kb, 100, 100),
    ]
    for l, a in ((0, 0), (1, 50)):
        nt = 6 if l == 0 else 4
        r = row if l == 0 else 512 * 4
        kv = a + 20 if l == 0 else a + 10
        items += [
            (f"hxh{l}", 16 * kb, a if l == 0 else 42, a + 24), (f"hxl{l}", 16 * kb, a if l == 0 else 42, a + 24),
            (f"hch{l}", 8 * kb, a if l == 0 else 44, a + (24 if l == 0 else 10)), (f"hcl{l}", 8 * kb, a if l == 0 else 44, a + (24 if l == 0 else 10)),
            (f"cqw{l}", 3 * row, a + 10, a + 20), (f"krT{l}", row, a + 10, a + 10), (f"krN{l}", 6 * 32 * 4, a + 10, a + 20),
            (f"wkr{l}", 1024, a + 10, a + 10), (f"wkrh{l}", 1024, a + 10, a + 10), (f"wkrl{l}", 1024, a + 10, a + 10),
            (f"wuq{l}", 6 * kb, a + 10, a + 20), (f"wukv{l}", 4 * kb, a + 10, a + 20), (f"pw{l}", 2 * kb, a + 10, a + 24),
            (f"glu{l}", 2 * 828 * 4, a + 10, a + 24), (f"z{l}", 2 * 798 * 4, a + 10, a + 24),
            (f"scp{l}", 2 * 772 * 4, a + 20, a + 20), (f"scz{l}", 772 * 4, a + 20, a + 20),
            (f"qN{l}", nt * 768 * 4, kv, a + 30), (f"kN{l}", 6 * 768 * 4, kv, a + 30), (f"vN{l}", 6 * 512 * 4, kv, a + 30),
            (f"ga{l}", 4 * r, a + 24, a + 30), (f"gc{l}", 2 * r, a + 24, a + 24),
            (f"qT{l}", 4 * r, a + 30, a + 30), (f"kT{l}", 4 * row, a + 30, a + 30),
            (f"P{l}", 4 * row, a + 30, a + 30), (f"PTa{l}", 12 * kb, a + 30, a + 30), (f"PTb{l}", 6 * kb, a + 30, a + 30),
            (f"PTc{l}", 4 * kb if l == 0 else 32, a + 30, a + 30), (f"og{l}", 3 * kb, a + 30, a + 30),
            (f"wo{l}", 48 * kb, a + 40, a + 42),
            (f"yax{l}", 16 * kb, a + 30, a + 40 + 2 * l), (f"ysx{l}", 8 * kb, a + 20, a + 40 + 2 * l), (f"ypx{l}", 8 * kb, a + 24, a + 40 + 2 * l),
        ]
        if l == 0:
            items += [("zero", 4 * kb, 30, 30), ("yac0", 8 * kb, 30, 42), ("ysc0", 4 * kb, 20, 42), ("ypc0", 4 * kb, 24, 42)]
    items += [
        ("small2", 4 * SMALL2["n"], 0, 199), ("xN", 16 * kb, 100, 199), ("hh2", 16 * kb, 92, 113), ("hl2", 16 * kb, 92, 113),
        ("wf", 256, 92, 110), ("wfh", 256, 92, 110), ("wfl", 256, 92, 110),
        ("tmpf", 4 * 2 * kb, 110, 130), ("fC", 2 * kb, 110, 120), ("self", 4 * kb, 110, 110), ("sel", 4 * kb, 110, 120),
        ("vdil", 8 * kb, 100, 113), ("vfox", 8 * kb, 100, 120), ("q2", 8 * kb, 110, 120), ("k2", 8 * kb, 110, 120),
        ("tab", 3 * 2 * kb, 110, 113), ("lnn", 2 * kb, 110, 113), ("tri", 2 * kb, 110, 120),
        ("P2", 6 * 2 * kb, 110, 120), ("PT2", 16 * kb, 110, 120),
        ("y2hd", 8 * kb, 110, 120), ("y2ld", 8 * kb, 110, 120), ("y2hf", 8 * kb, 110, 130), ("y2lf", 8 * kb, 110, 130),
        ("wo2d", 32 * kb, 114, 120), ("wo2f", 32 * kb, 114, 130),
        ("row1", 4 * kb, 130, 139), ("kept", 4 * (3 * (GROUPS + MORE) + 28), 130, 199), ("ctl", 64, 130, 199), ("iota", 512, 130, 199),
        ("h2N", 12 * kb, 130, 139), ("xT", 8 * kb, 130, 139), ("wr", 8 * 36 * 4, 130, 139), ("rt", 16 * kb, 130, 139), ("rc", 4 * RC["all"], 130, 139),
        ("xg", 2 * 4 * kb, 131, 149), ("xg2_", 4 * kb, 140, 149), ("XT", 4 * kb, 140, 149),
        ("he", 3 * kb, 140, 149), ("Y", 2 * 4 * kb, 140, 199),
    ] + [(f"gu{i}", 16 * kb, 114 if i < 1 else 130 if i < 3 else 131 if i < 5 else 140, 199) for i in range(N_GU)] \
      + [(f"dn{i}", 8 * kb, 130 if i < 3 else 131 if i < 5 else 140, 199) for i in range(N_DN)]
    base = 16512
    K.at = plan(items, base, 229344)

    def sb(name, shape, dt=F32, where=None, skip=0):
        return nc.alloc_sbuf_tensor_at(name, shape, dt, offset=K.at[where or name] + skip)
    K.sb = sb
    return K


class Weights:

    def __init__(self, K, srcs):
        self.K, self.srcs, self.done = K, srcs, []
        self.raw = [Buf(K.sb(f"raw{i}", [128, 1024], F32, "raw", 4096 * i), K.slot(f"s_raw{i}")) for i in range(2)]
        self.hi = [Buf(K.sb(f"whi{i}", [128, 1024], F32R, "whi", 4096 * i)) for i in range(2)]
        self.lo = [Buf(K.sb(f"wlo{i}", [128, 1024], F32R, "wlo", 4096 * i)) for i in range(2)]
        self.loaded, self.limit, self.place, self.on_dve = [], len(srcs), {}, ()
        self.load()
        self.load()

    def load(self):
        i = len(self.loaded)
        if i < len(self.srcs):
            b = self.raw[i % 2]
            self.loaded.append(self.K.sp.dma(b.ap[:, :], self.srcs[i], b.slot, b.free))

    def split(self):
        K, i = self.K, len(self.done)
        if i >= len(self.srcs):
            return
        raw, hi, lo = self.raw[i % 2], *self.place.get(i, (self.hi[i % 2], self.lo[i % 2]))
        assert hi.free is not None and lo.free is not None
        t_hi = K.act(lambda e: e.activation(hi.ap[:, :], raw.ap[:, :], ACT.Copy), self.loaded[i], hi.free)
        t_lo = (K.dve if i in self.on_dve else K.pool)(lambda e: e.tensor_tensor(lo.ap[:, :], raw.ap[:, :], hi.ap[:, :].bitcast(F32), ALU.subtract),
                                                       self.loaded[i], t_hi, lo.free)
        raw.free = [t_hi, t_lo]
        hi.free = lo.free = None
        self.done.append((hi, lo, t_hi, t_lo))
        self.load()

    def get(self, i):
        while len(self.done) < min(i + 2, self.limit):
            self.split()
        return self.done[i]

    def release(self, i, tok):
        hi, lo, _, _ = self.done[i]
        hi.free = lo.free = [tok]


class Beside:

    def __init__(self):
        self.jobs = []

    def add(self, steps, rate, wait=0):
        self.jobs.append([steps, rate, -wait])

    def gap(self):
        for j in list(self.jobs):
            j[2] += j[1]
            while j[2] >= 1:
                j[2] -= 1
                if next(j[0], self) is self:
                    self.jobs.remove(j)
                    break

    def drain(self, steps=None):
        for j in list(self.jobs):
            if steps is None or j[0] is steps:
                for _ in j[0]:
                    pass
                self.jobs.remove(j)


class Pair:

    def __init__(self, hi, lo, t_hi, t_lo):
        self.hi, self.lo, self.t_hi, self.t_lo = hi, lo, t_hi, t_lo


def mm3(K, dst, ws, xs, gap=None, order=None):
    tok = None
    order = order or list(range(len(ws)))
    for k in order:
        w = ws[k]
        for a, part, p in ((w.hi, 0, 0), (w.hi, 1, 1), (w.lo, 0, 2)):
            for j, (o, seg, c, cols) in enumerate(dst):
                x = xs[seg][k]
                b = (x.hi, x.lo)[part][:, c:c + cols]
                start, stop = k == order[0] and p == 0, k == order[-1] and p == 2
                tok = K.pe(lambda e, o=o, a=a, b=b, start=start, stop=stop: e.matmul(o, a, b, start=start, stop=stop),
                           (w.t_hi, x.t_hi, w.t_lo)[p], (x.t_hi, x.t_lo, x.t_hi)[p], signal=stop and j == len(dst) - 1)
        if gap and order.index(k) % 2:
            gap()
    return tok


def tile_pairs(w, m=128):
    hi, lo, t_hi, t_lo = w
    return [Pair(hi.ap[:, 128 * k:128 * k + m], lo.ap[:, 128 * k:128 * k + m], t_hi, t_lo) for k in range(KT)]


def begin(K):
    nc, d = K.nc, K.d
    pe, act, dve, pool, sp = K.pe, K.act, K.dve, K.pool, K.sp
    sb = K.sb
    K.ident = sb("ident", [128, 128])
    K.ones = sb("ones", [128, 128])
    K.ctab = sb("ctab", [128, 4, 32])
    K.stab = sb("stab", [128, 4, 32])
    K.small = sb("small", [128, SMALL["n"]])
    K.c2T = sb("c2T", [128, KT, 32])
    K.nhalf = sb("nhalf", [128, 16])
    K.mod = sb("mod", [128, 2, 4, KT, 2])
    K.rope_w = sb("rope_w", [128, 4, 32])
    K.rope_t = sb("rope_t", [128, 4, 4, 32])
    K.stat = sb("stat", [128, 256])
    K.modrow = sb("modrow", [128, 512])
    K.t_small = sp.dma(K.small[:, :], d["small"], K.slot("s_small"))
    K.t_ident = act.dma(K.ident[:, :], d["ident"], K.slot("s_ident"))
    K.t_ones = dve(lambda e: e.memset(K.ones[:, :], 1.0))
    K.t_nhalf = dve(lambda e: e.memset(K.nhalf[:, :], -0.5))
    t = dve(lambda e: e.memset(K.c2T[:, :, :], 0.0))
    K.t_c2 = act(lambda e: e.activation(K.c2T[:, :, 0:2],
                                        K.small[:, SMALL["c"]:SMALL["c"] + 16].rearrange("p (k v) -> p k v", v=2),
                                        ACT.Silu), K.t_small, t)
    K.psum = K.ctx.enter_context(nc.psum_tensor("ps", [128, 4096], F32))
    ps = [Buf(K.psum[:, 1024 * i:1024 * i + 1024]) for i in range(4)]
    K.ps, K.px = Ring(ps[:2]), Ring(ps[2:])
    K.s_rope = K.slot("s_rope")
    K.t_mod_read = []
    K.beside = Beside()


def fence(K):
    return [q.last() for q in (K.pe, K.act, K.dve, K.pool)]


def small(K, name, l, n, i=0, cols=1):
    at = SMALL[name] + n * l + i
    return K.small[:, at:at + cols]


def mod_columns(K, l, part, view, pairs, tok, *after):
    dve, mod = K.dve, K.mod
    for c, js in enumerate(pairs):
        b = small(K, "b_mod", l, 24, 8 * part + 4 * c, 4).unsqueeze(2).to_broadcast([128, 4, 2])
        dst = mod[:, l, part, 4 * c:4 * c + 4, :]
        for j in js:
            t = dve(lambda e, dst=dst, j=j, b=b: e.tensor_tensor(dst, view[:, :, j, 0:2], b, ALU.add), tok, K.t_small, *after)
            b, tok = dst, t
    t_read = t
    if part == 1:
        nw = small(K, "norm_w", l, 8, 0, 8).unsqueeze(2).to_broadcast([128, KT, 2])
        t = dve(lambda e: e.scalar_tensor_tensor(mod[:, l, 1, :, :], mod[:, l, 1, :, :], 1.0, nw, ALU.add, ALU.mult), t)
    return t_read, t



def quarter_mod(K, w, t_w, t_read):
    s = K.px.take()
    for k in range(KT):
        for j in range(4):
            tok = K.pe(lambda e, k=k, j=j: e.matmul(s.ap[32 * j:32 * j + 32, 0:128], K.c2T[:, k, :], w[:, k, 128 * j:128 * j + 128],
                                                    start=k == 0, stop=k == KT - 1, skip_group_check=True),
                       K.t_c2, t_w, s.was if k == 0 else None, signal=k == KT - 1 and j == 3)
    t_row = K.act(lambda e: e.activation(K.modrow[:, 0:128], s.ap[:, 0:128], ACT.Copy), tok, t_read)
    return s, tok, t_row


def quarter_columns(K, q, s, t_row):
    mod = K.mod
    tok = K.pe(lambda e: e.transpose(s.ap[:, 512:640], K.modrow[:, 0:128], K.ident[:, :]), t_row, K.t_ident)
    view = s.ap[:, 512:640].rearrange("p (j r) -> p j r", j=4)
    k = slice(2 * q, 2 * q + 2)
    b = [small(K, "b_mod", 0, 24, 8 * part + 2 * q, 2).unsqueeze(2).to_broadcast([128, 2, 2]) for part in range(2)]
    nw = small(K, "norm_w", 0, 8, 2 * q, 2).unsqueeze(2).to_broadcast([128, 2, 2])
    t = K.dve(lambda e: e.tensor_tensor(mod[:, 0, 1, k, :], view[:, 2:4, 0:2], b[1], ALU.add), tok, K.t_small)
    t_shift = K.dve(lambda e: e.tensor_tensor(mod[:, 0, 0, k, :], view[:, 0:2, 0:2], b[0], ALU.add), tok, K.t_small)
    t_scale = K.dve(lambda e: e.scalar_tensor_tensor(mod[:, 0, 1, k, :], mod[:, 0, 1, k, :], 1.0, nw, ALU.add, ALU.mult), t)
    s.free = [t, t_shift]
    return [tok], [t_scale, t_shift]


def quarter_h(K, q, x, t_x, r, t_r, t_mod, tmps, hx, hT):
    rest = []
    for k in (2 * q, 2 * q + 1):
        b = tmps.take()
        b.free = []
        for v, (c, n) in enumerate(((0, NX), (NX, NC))):
            scale, shift = K.mod[:, 0, 1, k, v:v + 1], K.mod[:, 0, 0, k, v:v + 1]
            xk, o, rk = x[:, k, c:c + n], b.ap[:, c:c + n], r[:, c:c + n]
            hi, lo = (h_[:, k, :] for h_ in hx[v])
            t = K.dve(lambda e, o=o, xk=xk, rk=rk, scale=scale: e.scalar_tensor_tensor(o, xk, scale, rk, ALU.mult, ALU.mult), t_mod, t_x[k], t_r, b.was)
            t_hi = K.act(lambda e, hi=hi, o=o, shift=shift: e.activation(hi, o, ACT.Identity, bias=shift), t, t_mod)
            rest.append((v, b, o, hi, lo, shift, t_hi))
    for v, b, o, hi, lo, shift, t_hi in rest:
        t_lo = K.dve(lambda e, o=o, hi=hi, lo=lo, shift=shift: e.scalar_tensor_tensor(lo, o, shift, hi.bitcast(F32), ALU.add, ALU.subtract), t_hi)
        hT[v].append(Pair(hi, lo, t_hi, t_lo))
        b.free = b.free + [t_lo]
    return t


def quarter_product(K, q, s, w, hT):
    for k in (2 * q, 2 * q + 1):
        for a, part, p in ((w[k].hi, 0, 0), (w[k].lo, 0, 1), (w[k].hi, 1, 2)):
            for v, (c, n) in enumerate(((0, NX), (NX, NC))):
                x = hT[v][k]
                b = (x.hi, x.lo)[part]
                start, stop = k == 0 and p == 0, k == KT - 1 and p == 2
                tok = K.pe(lambda e, a=a, b=b, c=c, n=n, start=start, stop=stop: e.matmul(s.ap[:, c:c + n], a, b, start=start, stop=stop),
                           (w[k].t_hi, w[k].t_lo, w[k].t_hi)[p], (x.t_hi, x.t_hi, x.t_lo)[p], s.was if start else None, signal=stop and v == 1)
    return tok


HEAD = 3


def mod_loads(K):
    d = K.d
    wg = [Buf(K.sb(f"wgate_{i}", [128, 2, 1024], F32, "wgate" if i < 2 else "wgate2", 8192 * (i % 2 if i < 2 else i - 2)), K.slot(f"s_gate{i}")) for i in range(6)]
    jobs = [(l, part, q) for l, part in ((0, 2), (1, 0), (1, 1), (1, 2)) for q in range(4)]

    def load(j):
        if j < len(jobs):
            l, part, q = jobs[j]
            g = wg[j % 6]
            g.tok = K.sp.dma(g.ap[:, :, :], d["w_mod"][l, 2 * q:2 * q + 2, :, 1024 * part:1024 * part + 1024].rearrange("k p c -> p k c"), g.slot, g.free)
    load(0)
    load(1)
    K.mod_jobs = wg, jobs, load


def mod_rest(K):
    pe, act = K.pe, K.act
    wg, jobs, load = K.mod_jobs
    t_done = {}

    def steps():
        for at, (l, part, q) in enumerate(jobs):
            if q == 0:
                s = K.px.hold()
            g = wg[at % 6]
            for k in range(2):
                for c in range(2):
                    j = 2 * k + c
                    tok = pe(lambda e, g=g, k=k, c=c, j=j, q=q, s=s: e.matmul(
                        s.ap[32 * j:32 * j + 32, 0:512], K.c2T[:, 2 * q + k, :], g.ap[:, k, 512 * c:512 * c + 512],
                        start=q == 0, stop=q == 3, skip_group_check=True),
                        g.tok, s.was if q == 0 else None, signal=k == 1 and c == 1)
            g.free = [tok]
            load(at + 6)
            if q < 3:
                yield
                continue
            t = act(lambda e, s=s: e.activation(K.modrow[:, :], s.ap[:, 0:512], ACT.Copy), tok, K.t_mod_read)
            yield
            for r in range(4):
                tok = pe(lambda e, r=r, s=s: e.transpose(s.ap[:, 512 + 128 * r:640 + 128 * r], K.modrow[:, 128 * r:128 * r + 128], K.ident[:, :]), t, signal=r == 3)
            K.t_mod_read = [tok]
            yield
            view = s.ap[:, 512:1024].rearrange("p (t j r) -> p t j r", t=4, j=4)
            t_read, t_done[l, part] = mod_columns(K, l, part, view, ((0, 2), (1, 3)), tok)
            s.free = [t_read]
            K.px.release(s)
            yield
        K.t_mod[1] = [t_done[1, 0], t_done[1, 1]]
        K.t_gate = [t_done[0, 2], t_done[1, 2]]
    return steps()


class Norm:

    def __init__(self, K, nt, d=D, eps=EPS, nk=KT, ring=None, c=0):
        self.K, self.nt, self.d, self.eps, self.nk, self.k, self.c = K, nt, d, eps, nk, 0, c
        self.ring = ring or K.px
        self.s = self.ring.hold()

    def add(self, sq, tok):
        K, k = self.K, self.k
        for i in range(self.nt):
            self.tok = K.pe(lambda e, i=i: e.matmul(self.s.ap[:, i:i + 1], sq[:, 128 * i:128 * i + 128], K.ones[:, 0:1],
                                                    start=k == 0 and i == 0, stop=k == self.nk - 1, skip_group_check=True),
                            tok, K.t_ones, self.s.was if k == 0 and i == 0 else None, signal=i == self.nt - 1)
        self.k += 1
        return self.tok

    def finish(self, ms, rstd, *after):
        K, n = self.K, self.nt
        t = K.dve(lambda e: e.tensor_scalar(ms, self.s.ap[:, 0:n], 1.0 / self.d, self.eps, ALU.mult, ALU.add), self.tok, *after)
        self.s.free = [t]
        self.ring.release(self.s)
        return K.pool(lambda e: e.tensor_tensor(rstd, ms, K.nhalf[:, 0:n], ALU.pow), t, K.t_nhalf)


def across(K, rstd, t_rstd, nt, diag, t_diag_free, c=0):
    s = K.px.take()
    for i in range(nt):
        g = diag[i % len(diag)]
        t = K.dve(lambda e, g=g, i=i: e.tensor_scalar(g.ap, K.ident[:, :], rstd[:, i:i + 1], None, ALU.mult), t_rstd, K.t_ident, g.free, t_diag_free)
        tok = K.pe(lambda e, g=g, i=i: e.matmul(s.ap[:, 128 * i:128 * i + 128], K.ones[:, :], g.ap, start=True, stop=True),
                   t, s.was if i == 0 else None)
        g.free = [tok]
    return s, tok


def spread(K, nt, rstd, t_r, tmps):
    db = tmps.take()
    rb, t = across(K, rstd, t_r, nt, [Buf(db.ap[:, 128 * q:128 * q + 128]) for q in range(6)], db.was)
    db.free = [t]
    return rb, t


def next_h(K, acc, t_acc, nt, c, n, x, t_x, v, out, l, tmps, at, after, res):
    N = Norm(K, nt, nk=1)
    N.add(acc, t_acc)
    ms, rs = K.stat[:, at:at + nt], K.stat[:, at + 8:at + 8 + nt]
    t_r = N.finish(ms, rs, after)
    yield
    rb, t_rb = spread(K, nt, rs, t_r, tmps)
    yield
    hh, hl = out
    pend = None
    for k in range(KT):
        b = tmps.hold()
        o = b.ap[:, 0:n]
        w = K.mod[:, l, 1, k, v:v + 1] if l < 2 else K.small2[:, k:k + 1]
        t = K.dve(lambda e, k=k, o=o, w=w: e.scalar_tensor_tensor(o, x(k), w, rb.ap[:, 0:n], ALU.mult, ALU.mult),
                  t_rb, K.t_mod[l] if l < 2 else K.t_small2, t_x[k], b.was)
        if k == KT - 1:
            rb.free = [t]
        hi, lo = hh[:, k, c:c + n], hl[:, k, c:c + n]
        if l < 2:
            shift = K.mod[:, l, 0, k, v:v + 1]
            t_hi = K.act(lambda e, hi=hi, o=o, shift=shift: e.activation(hi, o, ACT.Identity, bias=shift), t, after)
            make = lambda o=o, hi=hi, lo=lo, shift=shift, t_hi=t_hi: K.dve(
                lambda e: e.scalar_tensor_tensor(lo, o, shift, hi.bitcast(F32), ALU.add, ALU.subtract), t_hi, after)
        else:
            t_hi = K.act(lambda e, hi=hi, o=o: e.activation(hi, o, ACT.Copy), t, after)
            make = lambda o=o, hi=hi, lo=lo, t=t, t_hi=t_hi: K.pool(
                lambda e: e.tensor_tensor(lo, o, hi.bitcast(F32), ALU.subtract), t, t_hi, after)

        def finish(k=k, b=b, make=make, t_hi=t_hi):
            t_lo = make()
            b.free = [t_hi, t_lo]
            tmps.release(b)
            res.append(Pair(hh[:, k, :], hl[:, k, :], t_hi, t_lo))
        if pend:
            pend()
        pend = finish
        if k == KT - 1:
            pend()
        yield


def tmp_ring(K, name, n, width=816):
    return Ring([Buf(K.sb(f"{name}_{i}", [128, width], F32, name, 4 * width * i)) for i in range(n)])


def first_layer_block(K, l, hT, wt, w0, tmps, head=(), after=None):
    pe, act, dve, pool, sp, d, px = K.pe, K.act, K.dve, K.pool, K.sp, K.d, K.px
    both = l == 0
    n_own = NT if both else NX
    segs = [(0, NX), (NX, NC)] if both else [(0, NX)]
    all_segs = [(0, NX), (NX, NC)]
    nt_q = 6 if both else 4
    sb = lambda name, shape, dt=F32: K.sb(name + str(l), shape, dt)
    beside = K.beside

    st = Ctx()
    wuq, wukv, pw = sb("wuq", [128, 2, 768]), sb("wukv", [128, 1024]), sb("pw", [128, 2, 256])
    wkr = sb("wkr", [128, KT, 32])
    wkrh, wkrl = sb("wkrh", [128, KT, 32], F32R), sb("wkrl", [128, KT, 32], F32R)
    after = after or fence(K)
    wt.get(w0 + len(head))
    t_wkr = sp.dma(wkr[:, :, :], d["w_kr"][l], K.s_wkr, after)
    t_wuq = sp.dma(wuq[:, :, :], d["w_uq"][l], K.s_wuq, after)
    t_wukv = sp.dma(wukv[:, :], d["w_ukv"][l], K.s_wukv, after)
    t_pw = sp.dma(pw[:, :, :], d["pw"][l], K.s_pw, after)
    t_rw = sp.dma(K.rope_w[:, :, :], d["rope_w"][l], K.s_rope, K.free_rope)
    if both:
        K.t_tab = [sp.dma(K.ctab[:, :, :], d["ctab"], K.slot("s_ctab")), sp.dma(K.stab[:, :, :], d["stab"], K.slot("s_stab"))]
        st.mod = mod_rest(K)
        beside.add(st.mod, 1, 0)

    cqw = sb("cqw", [128, 3, NT])
    krT, krN = sb("krT", [32, NT]), sb("krN", [128, 6, 32])
    glu, z = sb("glu", [128, 2, 828]), sb("z", [128, 2, 798])
    t_pad = pool(lambda e: e.memset(glu[:, :, :], 0.0), after)
    yp = [[None] * KT, [None] * KT]
    stat = K.stat
    rq, rkv = stat[:, 0:6], stat[:, 8:14]

    def product(i, m=128, cols=None, pairs=None):
        if pairs is None and i - w0 < len(head):
            return head[i - w0]
        s = K.ps.take()
        dst = [(s.ap[0:m, c:c + n], c // NX, 0, n) for c, n in (cols or segs)]
        ws = pairs or tile_pairs(wt.get(i), m)
        ws2 = [Pair(p.hi, p.lo, [p.t_hi, s.was], p.t_lo) for p in ws[:1]] + ws[1:]
        tok = mm3(K, dst, ws2, hT, beside.gap)
        if pairs is None:
            wt.release(i, tok)
        return s, tok

    def ev_c(s, tok, name, i):
        f = i if name == "cq" else 2
        nn = NT if (both or name == "ckv") else NX
        w = small(K, "qn_w", l, 2, i) if name == "cq" else small(K, "kvn_w", l, 1)
        t = act(lambda e: e.activation(cqw[:, f, 0:nn], s.ap[:, 0:nn], ACT.Copy, scale=w), tok, K.t_small, after)
        b = tmps.hold()
        t2 = act(lambda e: e.activation(b.ap[:, 0:nn], s.ap[:, 0:nn], ACT.Square), tok, b.was)
        s.free = [t2]
        st.cqw[f] = t
        if name == "cq" and i == 0:
            st.sq0 = (b, t2)
            return
        if name == "cq":
            b0, t0 = st.sq0
            t2 = pool(lambda e: e.tensor_tensor(b.ap[:, 0:nn], b.ap[:, 0:nn], b0.ap[:, 0:nn], ALU.add), t0, t2)
            b0.free = [t2]
            tmps.release(b0)

        def go():
            N = Norm(K, nn // 128, 256 if name == "cq" else 128, EPS, 1)
            b.free = [N.add(b.ap, t2)]
            tmps.release(b)
            if name == "cq":
                st.t_rq = N.finish(stat[:, 16:16 + nt_q], rq[:, 0:nt_q], K.free_stat)
            else:
                st.t_rkv = N.finish(stat[:, 24:30], rkv, K.free_stat)
        st.later.append(go)

    st.cqw, st.later = [None] * 3, []

    def ev_glu(s, tok, i):
        if i >= 2:
            b = st.sig[i - 2] = tmps.hold()
            st.t_sig[i - 2] = act(lambda e: e.activation(b.ap[:, 0:n_own], s.ap[:, 0:n_own], ACT.Sigmoid), tok, b.was)
            s.free = [st.t_sig[i - 2]]
            return
        b = st.sig[i]
        for c, n in segs:
            o = 15 + (c if c == 0 else c + 30)
            t = dve(lambda e, c=c, n=n, o=o: e.tensor_tensor(glu[:, i, o:o + n], s.ap[:, c:c + n], b.ap[:, c:c + n], ALU.mult),
                    tok, st.t_sig[i], t_pad)
        s.free = b.free = [t]
        tmps.release(b)
        st.t_glu[i] = t

    st.sig, st.t_sig, st.t_glu = [None, None], [None, None], [None, None]
    width = 798 if both else 512
    wide = 770 if both else 512

    st.t_z = [None, None]

    def conv(i):
        o = z[:, i, 0:width]
        for j in range(31):
            w, x = small(K, "cf_w", l, 62, 31 * i + j), glu[:, i, j:j + width]
            if j == 0:
                t = dve(lambda e, x=x, w=w: e.tensor_scalar(o, x, w, small(K, "cf_b", l, 2, i), ALU.mult, ALU.add), st.t_glu[i], K.t_small, after)
            else:
                t = dve(lambda e, x=x, w=w: e.scalar_tensor_tensor(o, x, w, o, ALU.mult, ALU.add), t)
            yield
        st.t_z[i] = t

    def split_y(k, name, src, t_src, buf, after):
        for g, (c, n) in enumerate(segs):
            hi, lo = (K.sb(f"{name}{g}{k}{l}{p}", [128, n], F32R, f"{name}{'xc'[g]}{l}", 4 * n * (2 * (k % 2) + p)) for p in range(2))
            t_hi = act(lambda e, hi=hi, c=c, n=n: e.activation(hi[:, :], src[:, c:c + n], ACT.Copy), t_src, after)
            t_lo = pool(lambda e, hi=hi, lo=lo, c=c, n=n: e.tensor_tensor(lo[:, :], src[:, c:c + n], hi[:, :].bitcast(F32), ALU.subtract), t_src, t_hi, after)
            yp[g][k] = Pair(hi, lo, t_hi, t_lo)
        buf.free = [t_hi, t_lo]

    def ev_sc(s, tok, name, i):
        if name == "sc_in":
            b = st.sin = tmps.hold()
            st.t_sin = act(lambda e: e.activation(b.ap[:, 0:n_own], s.ap[:, 0:n_own], ACT.Copy), tok, b.was)
            s.free = [st.t_sin]
        elif name == "sc_c":
            b = st.sin
            for c, n in segs:
                o = 1 + (c if c == 0 else c + 2)
                t = dve(lambda e, c=c, n=n, o=o: e.tensor_tensor(scp[:, i, o:o + n], s.ap[:, c:c + n], b.ap[:, c:c + n], ALU.mult),
                        tok, st.t_sin, st.t_padp)
            s.free = b.free = [t]
            tmps.release(b)
            zz = scz[:, 0:wide]
            t = dve(lambda e: e.tensor_scalar(zz, scp[:, i, 0:wide], small(K, "sc_w", l, 6, 3 * i), None, ALU.mult), t, st.t_u, after20)
            for j in (1, 2):
                t = dve(lambda e, j=j: e.scalar_tensor_tensor(zz, scp[:, i, j:j + wide], small(K, "sc_w", l, 6, 3 * i + j), zz, ALU.mult, ALU.add), t)
            st.t_scz = t
        elif name == "sc_b":
            b = st.u = tmps.hold()
            for c, n in segs:
                o = c if c == 0 else c + 2
                t = dve(lambda e, c=c, n=n, o=o: e.tensor_tensor(b.ap[:, c:c + n], s.ap[:, c:c + n], scz[:, o:o + n], ALU.mult), tok, st.t_scz, b.was)
            s.free = [t]
            st.t_u = t
        else:
            b, u = tmps.take(), st.u
            t = act(lambda e: e.activation(b.ap[:, 0:n_own], s.ap[:, 0:n_own], ACT.Silu), tok, b.was)
            s.free = [t]
            t = pool(lambda e: e.tensor_tensor(u.ap[:, 0:n_own], u.ap[:, 0:n_own], b.ap[:, 0:n_own], ALU.mult), t, st.t_u)
            b.free = [t]
            split_y(4 + i, "ys", u.ap, t, u, after20)
            tmps.release(u)

    st.t_u = None
    t_g = [None] * 6

    def ev_g(s, tok, name, i):
        dst = ga[:, i, :] if name == "ga" else gc[:, i, :]
        j = i if name == "ga" else 4 + i
        t_g[j] = act(lambda e: e.activation(dst, s.ap[:, 0:n_own], ACT.Silu), tok, after24)
        s.free = [t_g[j]]

    t_q, t_k, t_v = [None] * 6, [None] * 6, [None] * 6

    def rope(x, i, q):
        h = x.shape[1]
        r = 0 if q else 2
        if i >= 4:
            w = K.rope_w[:, r, :].unsqueeze(1).to_broadcast([128, h, 32])
            return lambda t: pool(lambda e: e.tensor_tensor(x, x, w, ALU.mult), t, t_rw)
        cs = K.rope_t[:, r, i, :].unsqueeze(1).to_broadcast([128, h, 32])
        sn = K.rope_t[:, r + 1, i, :]

        def go(t):
            b = tmps.take()
            o = b.ap[:, 0:32 * h].rearrange("p (h c) -> p h c", c=32)
            for a in range(2):
                t1 = pool(lambda e, a=a: e.tensor_tensor(o[:, :, 16 * a:16 * a + 16], x[:, :, 16 - 16 * a:32 - 16 * a],
                                                         sn[:, 16 * a:16 * a + 16].unsqueeze(1).to_broadcast([128, h, 16]), ALU.mult), t, st.t_rope, b.was)
            t2 = pool(lambda e: e.tensor_tensor(x, x, cs, ALU.mult), t1)
            t3 = pool(lambda e: e.tensor_tensor(x, x, o, ALU.add), t2)
            b.free = [t3]
            return t3
        return go

    def qkv():
        qN, kN, vN = st.qN, st.kN, st.vN
        krS = stat[:, 32:38]
        for i, tab in ((0, K.ctab), (1, K.stab), (2, K.ctab), (3, K.stab)):
            st.t_rope = pool(lambda e, i=i, tab=tab: e.tensor_tensor(
                K.rope_t[:, i, :, :], tab[:, :, :], K.rope_w[:, i, :].unsqueeze(1).to_broadcast([128, 4, 32]), ALU.mult), t_rw, K.t_tab, K.free_rope)
        t_kr2 = []
        for i in range(6):
            b = tmps.take()
            t_kr2.append(act(lambda e, i=i, b=b: e.activation(b.ap[:, 0:32], krN[:, i, :], ACT.Square, accum_out=krS[:, i:i + 1]), st.t_krN, b.was, K.free_stat))
            b.free = [t_kr2[-1]]
        yield
        for i in range(6):
            b16 = 64 + 64 * (i % 2)
            ss, rs, ff = stat[:, b16:b16 + 16], stat[:, b16 + 16:b16 + 32], stat[:, b16 + 32:b16 + 48]
            has_q = i < nt_q
            cols = slice(128 * i, 128 * i + 128)
            if has_q:
                sq_ = px.take()
                for c in range(2):
                    for k in range(2):
                        tok_q = pe(lambda e, sq_=sq_, cols=cols, c=c, k=k: e.matmul(sq_.ap[:, 512 * c:512 * c + 384], cqw[:, k, cols], wuq[:, k, 384 * c:384 * c + 384],
                                                                start=k == 0, stop=k == 1),
                                   st.cqw[0], st.cqw[1], t_wuq, sq_.was, signal=c == 1 and k == 1)
                q4 = sq_.ap[:, :].rearrange("p (c n) -> p c n", c=2)[:, :, 0:384]
            sk_ = px.take()
            for c in range(2):
                tok_k = pe(lambda e, sk_=sk_, cols=cols, c=c: e.matmul(sk_.ap[:, 512 * c:512 * c + 512], cqw[:, 2, cols], wukv[:, 512 * c:512 * c + 512], start=True, stop=True),
                           st.cqw[2], t_wukv, sk_.was, signal=c == 1)
            b1 = tmps.hold()
            if has_q:
                t_q2 = act(lambda e, b1=b1, q4=q4, i=i: e.activation(b1.ap[:, 0:768].rearrange("p (c n) -> p c n", c=2), q4, ACT.Square, scale=rq[:, i:i + 1]),
                           tok_q, st.t_rq, b1.was)
                t_qc = act(lambda e, i=i, q4=q4: e.activation(qN[:, i, :, :].rearrange("p (c h) w -> p c (h w)", c=2), q4, ACT.Copy), tok_q, st.after_q)
                sq_.free = [t_q2, t_qc]
            b2 = tmps.hold()
            t_k2 = act(lambda e, b2=b2, i=i, sk_=sk_: e.activation(b2.ap[:, 0:512], sk_.ap[:, 0:512], ACT.Square, scale=rkv[:, i:i + 1]), tok_k, st.t_rkv, b2.was)
            t_v[i] = act(lambda e, i=i, sk_=sk_: e.activation(vN[:, i, :], sk_.ap[:, 512:1024], ACT.Copy, scale=rkv[:, i:i + 1]), tok_k, st.after_q)
            t_kc = act(lambda e, i=i, sk_=sk_: e.activation(kN[:, i, :, 0:64], sk_.ap[:, 0:512].rearrange("p (h c) -> p h c", c=64), ACT.Copy), tok_k, st.after_q)
            sk_.free = [t_k2, t_v[i], t_kc]
            yield
            t = []
            if has_q:
                t.append(dve(lambda e, b1=b1, ss=ss: e.tensor_reduce(ss[:, 0:8], b1.ap[:, 0:768].rearrange("p (h c) -> p h c", c=QK), AX.X, ALU.add), t_q2, K.st_free[i % 2]))
            b1.free = t or b1.was
            tmps.release(b1)
            t.append(dve(lambda e, b2=b2, ss=ss: e.tensor_reduce(ss[:, 8:16], b2.ap[:, 0:512].rearrange("p (h c) -> p h c", c=64), AX.X, ALU.add), t_k2, K.st_free[i % 2]))
            b2.free = [t[-1]]
            tmps.release(b2)
            t.append(dve(lambda e, ss=ss, i=i: e.tensor_scalar(ss[:, 8:16], ss[:, 8:16], krS[:, i:i + 1], None, ALU.add), t[-1], t_kr2[i]))
            lo = 0 if has_q else 8
            t = dve(lambda e, ss=ss, lo=lo: e.tensor_scalar(ss[:, lo:16], ss[:, lo:16], 1.0 / QK, EPS, ALU.mult, ALU.add), t)
            t_r = pool(lambda e, ss=ss, rs=rs, lo=lo: e.tensor_tensor(rs[:, lo:16], ss[:, lo:16], K.nhalf[:, lo:16], ALU.pow), t, K.t_nhalf, K.st_free[i % 2])
            yield
            yield
            yield
            t = dve(lambda e, ff=ff, rs=rs, i=i: e.tensor_scalar(ff[:, 8:16], rs[:, 8:16], rkv[:, i:i + 1], None, ALU.mult), t_r, st.t_rkv)
            if has_q:
                t1 = dve(lambda e, ff=ff, rs=rs, i=i: e.tensor_scalar(ff[:, 0:8], rs[:, 0:8], rq[:, i:i + 1], None, ALU.mult), t_r, st.t_rq)
            t2 = dve(lambda e, i=i, ff=ff: e.tensor_tensor(kN[:, i, :, 0:64], kN[:, i, :, 0:64], ff[:, 8:16].unsqueeze(2).to_broadcast([128, 8, 64]), ALU.mult), t, t_kc)
            if has_q:
                t = dve(lambda e, i=i, ff=ff: e.tensor_tensor(qN[:, i, :, :], qN[:, i, :, :], ff[:, 0:8].unsqueeze(2).to_broadcast([128, 8, QK]), ALU.mult), t1, t_qc)
            t3 = rope(krN[:, i:i + 1, :], i, False)(t_kr2[i])
            t4 = pool(lambda e, i=i, rs=rs: e.tensor_tensor(kN[:, i, :, 64:96], krN[:, i:i + 1, :].to_broadcast([128, 8, 32]),
                                                            rs[:, 8:16].unsqueeze(2).to_broadcast([128, 8, 32]), ALU.mult), t3, t_r, st.after_q)
            t_k[i] = [t2, t4]
            K.st_free[i % 2] = [t2, t4]
            if has_q:
                t_q[i] = rope(qN[:, i, :, 64:96], i, True)(t)
                K.st_free[i % 2] = [t2, t4, t]
            yield
        K.free_rope = [pool.last()]

    def layer_norm():
        nn = n_own
        zc = [(c, n, c if c == 0 else c + 30) for c, n in segs]
        s = px.take()
        for c, n, o in zc:
            for k in range(2):
                tok = pe(lambda e, s=s, c=c, n=n, o=o, k=k: e.matmul(s.ap[:, c:c + n], K.ones[:, :], z[:, k, o:o + n], start=k == 0, stop=k == 1),
                         st.t_z, s.was, signal=k == 1)
        yield
        sq = []
        for k in range(2):
            b = tmps.hold()
            for c, n, o in zc:
                t = dve(lambda e, s=s, k=k, c=c, n=n, o=o: e.scalar_tensor_tensor(
                    z[:, k, o:o + n], s.ap[:, c:c + n], -1.0 / 256, z[:, k, o:o + n], ALU.mult, ALU.add), tok)
                t2 = act(lambda e, b=b, k=k, c=c, n=n, o=o: e.activation(b.ap[:, c:c + n], z[:, k, o:o + n], ACT.Square), t, b.was)
            sq.append((b, t2))
        s.free = [t]
        (b0, ta), (b1, tb) = sq
        t2 = pool(lambda e: e.tensor_tensor(b1.ap[:, 0:nn], b1.ap[:, 0:nn], b0.ap[:, 0:nn], ALU.add), ta, tb)
        b0.free = [t2]
        tmps.release(b0)
        yield
        yield
        nz = Norm(K, nn // 128, 256, LN_EPS, 1)
        b1.free = [nz.add(b1.ap, t2)]
        tmps.release(b1)
        t_r = nz.finish(stat[:, 40:40 + nn // 128], stat[:, 48:48 + nn // 128], K.free_stat)
        yield
        rb, t_rb = spread(K, nn // 128, stat[:, 48:54], t_r, tmps)
        yield
        t_zs = [None, None]
        for k in range(2):
            for c, n, o in zc:
                t = dve(lambda e, k=k, c=c, n=n, o=o: e.tensor_tensor(z[:, k, o:o + n], z[:, k, o:o + n], rb.ap[:, c:c + n], ALU.mult), t_rb)
                t_zs[k] = act(lambda e, k=k, n=n, o=o: e.activation(z[:, k, o:o + n], z[:, k, o:o + n], ACT.Silu,
                                                                   scale=small(K, "ln_w", l, 2, k), bias=small(K, "ln_b", l, 2, k)), t)
        rb.free = [t]
        yield
        for f in range(2):
            s = px.take()
            for c, n, o in zc:
                for k in range(2):
                    tok = pe(lambda e, s=s, c=c, n=n, o=o, k=k, f=f: e.matmul(s.ap[:, c:c + n], pw[:, k, 128 * f:128 * f + 128], z[:, k, o:o + n],
                                                                             start=k == 0, stop=k == 1), t_zs, t_pw, s.was, signal=k == 1)
            b = tmps.take()
            t = dve(lambda e, b=b, f=f, s=s: e.scalar_tensor_tensor(b.ap[:, 0:nn], s.ap[:, 0:nn], small(K, "pw_b", l, 2, f), gc[:, f, :], ALU.add, ALU.mult),
                    tok, t_g[4 + f], b.was)
            s.free = [t]
            split_y(6 + f, "yp", b.ap, t, b, after24)
            yield

    def begin_qkv():
        st.after_q = fence(K)
        st.qN, st.kN, st.vN = sb("qN", [128, nt_q, HEADS, QK]), sb("kN", [128, 6, HEADS, QK]), sb("vN", [128, 6, 512])
        beside.add(qkv(), 1 if both else 1, 8 if both else 7)

    for at, (name, i) in enumerate(TILES):
        if at == TILES.index(("sc_in", 0)):
            beside.drain(st.mod) if both else None
            after20 = fence(K)
            scp, scz = sb("scp", [128, 2, 772]), sb("scz", [128, 772])
            st.t_padp = pool(lambda e: e.memset(scp[:, :, :], 0.0), after20)
            begin_qkv()
        if at == TILES.index(("gc", 0)):
            after24 = fence(K)
            ga, gc = sb("ga", [128, 4, n_own]), sb("gc", [128, 2, n_own])
        if (name, i) == ("ga", 1):
            beside.drain()
            beside.add(layer_norm(), 1)
        s, tok = product(w0 + at, cols=all_segs if name == "ckv" else segs)
        if at >= len(head):
            for go in st.later:
                go()
            st.later = []
        if name in ("cq", "ckv"):
            ev_c(s, tok, name, i)
        elif name == "glu":
            ev_glu(s, tok, i)
            if i < 2:
                beside.add(conv(i), 0.9 if both else 0.9, 1)
        elif name in ("ga", "gc"):
            ev_g(s, tok, name, i)
        else:
            ev_sc(s, tok, name, i)
        if at < len(head) and s not in K.ps.bufs:
            px.release(s)
        if name == "ckv":
            s, tok = product(None, m=32, cols=all_segs, pairs=[Pair(wkrh[:, k, :], wkrl[:, k, :], st.t_kh, st.t_kl) for k in range(KT)])
            t = act(lambda e, s=s: e.activation(krT[:, :], s.ap[0:32, 0:NT], ACT.Copy), tok, after)
            s.free = [t]
            st.t_krT = t
        if at == 3:
            st.t_kh = act(lambda e: e.activation(wkrh[:, :, :], wkr[:, :, :], ACT.Copy), t_wkr, after)
            st.t_kl = pool(lambda e: e.tensor_tensor(wkrl[:, :, :], wkr[:, :, :], wkrh[:, :, :].bitcast(F32), ALU.subtract), st.t_kh, t_wkr, after)
        if at and TILES[at - 1][0] == "ckv":
            s = px.take()
            for j in range(6):
                tok = pe(lambda e, s=s, j=j: e.transpose(s.ap[:, 32 * j:32 * j + 32], krT[:, 128 * j:128 * j + 128], K.ident[0:32, 0:32]),
                         st.t_krT, K.t_ident, s.was if j == 0 else None, signal=j == 5)
            t = act(lambda e, s=s: e.activation(krN[:, :, :], s.ap[:, 0:192].rearrange("p (t c) -> p t c", c=32), ACT.Copy), tok, after)
            s.free = [t]
            st.t_krN = t
    beside.drain()
    K.free_stat = fence(K)
    attention(K, l, st.qN, st.kN, st.vN, t_q, t_k, t_v, ga, t_g, yp)
    return yp


def attention(K, l, qN, kN, vN, t_q, t_k, t_v, ga, t_g, yp):
    pe, act, dve, pool = K.pe, K.act, K.dve, K.pool
    both = l == 0
    n_own = NT if both else NX
    sm = float(np.float32(QK) ** np.float32(-0.5))
    after = [pe.last(), act.last(), dve.last(), pool.last()]
    ring = lambda name, n, shape: Ring([Buf(K.sb(f"{name}{l}_{i}", [128, *shape], F32, f"{name}{l}", 4 * int(np.prod(shape)) * i)) for i in range(n)])
    qT = K.sb(f"qT{l}", [128, 2, 2, n_own], F32R)
    kT = K.sb(f"kT{l}", [128, 2, 2, NT], F32R)
    P, PT0, PT1, gate = ring("P", 4, (NT,)), ring("PTa", 4, (6, 128)), ring("PTb", 2, (6, 128)), ring("og", 3, (256,))
    PTc = ring("PTc", 2, (2, 256)) if both else None
    for r in (P, PT0, PT1, gate) + ((PTc,) if both else ()):
        for b in r.bufs:
            b.free = after
    ps = K.psum
    S2 = [Buf(ps[:, o:o + NT]) for o in (0, 1024)]
    G = Ring([Buf(ps[:, 512 * i:512 * i + 512]) for i in range(4, 8)])
    for b in S2 + G.bufs:
        b.free = after
    ya = [[K.sb(f"ya{c}{l}{i}", [128, 4, n], F32R, f"ya{c}{l}", 16 * n * i) for i in range(2)] for c, n in ((("x", NX), ("c", NC)) if both else (("x", NX),))]
    stat = K.stat
    if both:
        zero = K.sb("zero", [128, D])
        t = pool(lambda e: e.memset(zero[:, :], 0.0), after)
        K.t_zero = K.sp.dma(K.moe.ybuf.rearrange("(p c) n -> p c n", c=8), zero[:, :].unsqueeze(1).to_broadcast([128, 8, D]), K.slot("s_zero"), t)
    qs = stat[:, 60:61]
    t_qs = dve(lambda e: e.tensor_scalar(qs, small(K, "qh_w", l, 1), sm, None, ALU.mult), after, K.t_small)
    per = 5 if both else 4
    units = [(h, i) for h in range(HEADS) for i in range(per)]
    heads, Pn, PTs = {}, {}, {}
    rests = []

    def finish_turns():
        while rests:
            rests.pop(0)()

    def turn(h):
        b = h % 2
        need = heads[h - 2][2] if h >= 2 else after
        heads[h] = [[None, None], [None, None], None]
        pieces = [(1, 0), (1, 4), (0, 0)] + ([(0, 4)] if both else [])
        for which, t0 in pieces:
            src, toks, dst = ((qN, t_q, qT), (kN, t_k, kT))[which]
            w = (qs if which == 0 else small(K, "kh_w", l, 1))[0:QK, :]
            nt = 4 if t0 == 0 else 2
            s = G.take()
            for j in range(nt):
                tok = pe(lambda e, j=j, s=s, src=src, t0=t0: e.transpose(s.ap[0:QK, 128 * j:128 * j + 128], src[:, t0 + j, h, :], K.ident[:, :]),
                         toks[t0 + j], s.was if j == 0 else None, signal=j == nt - 1)
            c, n = 128 * t0, 128 * nt
            hi, lo = dst[0:QK, b, 0, c:c + n], dst[0:QK, b, 1, c:c + n]
            t_hi = act(lambda e, s=s, hi=hi, w=w, n=n: e.activation(hi, s.ap[0:QK, 0:n], ACT.Copy, scale=w), tok, need, t_qs)

            def rest(s=s, hi=hi, lo=lo, w=w, n=n, t_hi=t_hi, which=which, t0=t0):
                t_lo = dve(lambda e: e.scalar_tensor_tensor(lo, s.ap[0:QK, 0:n], w, hi.bitcast(F32), ALU.mult, ALU.subtract), t_hi, need)
                s.free = [t_lo]
                heads[h][which][t0 // 4] = (t_hi, t_lo)
            rests.append(rest)
            yield

    def scores(u):
        h, i = units[u]
        b = h % 2
        tq, tk = heads[h][0][i // 4], heads[h][1]
        s = S2[u % 2]
        if i < 4:
            jobs = [(i, [(0, 0, NX), (512, NX, NC)])]
        else:
            jobs = [(4, [(0, NX, NC)]), (5, [(256, NX, NC)])]
        for n, (t, outs) in enumerate(jobs):
            qh, ql = qT[0:QK, b, 0, 128 * t:128 * t + 128], qT[0:QK, b, 1, 128 * t:128 * t + 128]
            tkh = [x[0] for x in (tk if i < 4 else tk[1:])]
            tkl = [x[1] for x in (tk if i < 4 else tk[1:])]
            for p, (a, x, need) in enumerate(((qh, 0, (tq[0], tkh, s.free)), (qh, 1, (tkl,)), (ql, 0, (tq[1],)))):
                for o, c, w in outs:
                    tok = pe(lambda e, o=o, c=c, w=w, a=a, x=x, p=p: e.matmul(s.ap[:, o:o + w], a, kT[0:QK, b, x, c:c + w], start=p == 0, stop=p == 2),
                             need, signal=p == 2 and n == len(jobs) - 1 and o == outs[-1][0])
        heads[h][2] = [tok]
        c0 = 192 + 8 * (u % 4)
        P_ = P.take()
        n, w = (1, NT) if i < 4 else (2, NC)
        t = dve(lambda e: e.tensor_reduce(stat[:, c0:c0 + n], s.ap[:, 0:n * w].rearrange("p (n w) -> p n w", w=w), AX.X, ALU.max, negate=True),
                tok, K.stat_free[u % 4])
        for j in range(n):
            t1 = act(lambda e, j=j: e.activation(P_.ap[:, w * j:w * j + w], s.ap[:, w * j:w * j + w], ACT.Exp, bias=stat[:, c0 + j:c0 + j + 1],
                                                 accum_out=stat[:, c0 + 2 + j:c0 + 3 + j]), t, P_.was)
        s.free = [t1]
        Pn[u] = [P_, t1, c0, n, w]

    def normalise(u):
        P_, t, c0, n, w = Pn[u]
        t = dve(lambda e: e.reciprocal(stat[:, c0 + 4:c0 + 4 + n], stat[:, c0 + 2:c0 + 2 + n]), t)
        for j in range(n):
            t1 = pool(lambda e, j=j: e.tensor_scalar(P_.ap[:, w * j:w * j + w], P_.ap[:, w * j:w * j + w], stat[:, c0 + 4 + j:c0 + 5 + j], 0.0, ALU.mult, ALU.add), t)
        Pn[u][1] = t1
        K.stat_free[u % 4] = [t1]

    def turn_p(u):
        h, i = units[u]
        P_, t, _, _, _ = Pn.pop(u)
        if i < 4:
            d = (PT0, PT1)[h % 2].take()
            jobs = [([128 * j for j in range(4)], d.ap[:, 0:4, :]), ([512, 640], d.ap[:, 4:6, :])]
        else:
            d = PTc.take()
            jobs = [([256 * j + 128 * kt for kt in range(2) for j in range(2)], d.ap[:, :, :])]
        done = []
        for n, (cols, dst) in enumerate(jobs):
            s = G.take()
            for j, c in enumerate(cols):
                tok = pe(lambda e, s=s, j=j, c=c: e.transpose(s.ap[:, 128 * j:128 * j + 128], P_.ap[:, c:c + 128], K.ident[:, :]),
                         t, s.was if j == 0 else None, signal=j == len(cols) - 1)
            src = s.ap[:, 0:128 * len(cols)].rearrange("p (t q) -> p t q", q=dst.shape[2])
            if (u + n) % 2:
                t1 = act(lambda e, dst=dst, src=src: e.activation(dst, src, ACT.Copy), tok, d.was)
            else:
                t1 = dve(lambda e, dst=dst, src=src: e.tensor_copy(dst, src), tok, d.was)
            s.free = [t1]
            done.append(t1)
        P_.free = [tok]
        PTs[u] = (d, done)

    def values(u):
        h, i = units[u]
        p = h // 2
        pt = [PTs.pop(u - per), PTs.pop(u)]
        s = G.take()
        c, n = 128 * i, 128 if i < 4 else NC
        kts = range(6) if i < 4 else (4, 5)
        for kt in kts:
            for e_ in range(2):
                d, t = pt[e_]
                o = 64 * (h - 1 + e_)
                tok = pe(lambda e, kt=kt, e_=e_, d=d, o=o: e.matmul(
                    s.ap[64 * e_:64 * e_ + 64, 0:n], vN[:, kt, o:o + 64], d.ap[:, kt - kts[0], :],
                    start=kt == kts[0], stop=kt == 5, skip_group_check=True), t, t_v, s.was, signal=kt == 5 and e_ == 1)
        pt[0][0].free = pt[1][0].free = [tok]
        b = gate.take()
        t = dve(lambda e: e.tensor_tensor(b.ap[:, 0:n], s.ap[:, 0:n], ga[:, p, c:c + n], ALU.mult), tok, t_g[p], b.was)
        s.free = [t]
        yh, yl = ya[i // 4]
        hi, lo = (y[:, p, c % NX:c % NX + n] for y in (yh, yl))
        t_hi = act(lambda e: e.activation(hi, b.ap[:, 0:n], ACT.Copy), t, after)
        t_lo = pool(lambda e: e.tensor_tensor(lo, b.ap[:, 0:n], hi.bitcast(F32), ALU.subtract), t, t_hi, after)
        b.free = [t_hi, t_lo]
        yp[i // 4][p] = Pair(yh[:, p, :], yl[:, p, :], t_hi, t_lo)

    for _ in turn(0):
        finish_turns()
    n = len(units)
    due = {2 * per * p + d: 2 * per * p + per + i for p in range(HEADS // 2) for i, d in enumerate((6, 8, 10, 12, 14) if both else (5, 7, 9, 10))}
    nxt = turn(1)
    for u in range(3):
        scores(u)
        normalise(u) if u < 2 else None
    for u in range(n):
        h, i = units[u]
        if u in due:
            values(due.pop(u))
        turn_p(u)
        if i < 2:
            next(nxt, None)
            if i or h == 0:
                for _ in nxt:
                    pass
        elif i >= per - 2 and h + 2 < HEADS:
            if i == per - 2:
                nxt = turn(h + 2)
            next(nxt)
        if u + 2 < n:
            normalise(u + 2)
        if u + 3 < n:
            scores(u + 3)
        finish_turns()
    for u in sorted(due):
        values(due[u])
    for b in K.ps.bufs + K.px.bufs:
        b.free = fence(K)


def out_pass(K, l, seg, c, n, wt, w0, yp, src, dst, acc, tmps, after, last, side=None):
    pe, act, dve, pool = K.pe, K.act, K.dve, K.pool
    out = []
    for f in range(KT):
        s = K.ps.take()
        ws = tile_pairs(wt.get(w0 + f))
        ws[4] = Pair(ws[4].hi, ws[4].lo, [ws[4].t_hi, s.was], ws[4].t_lo)
        tok = mm3(K, [(s.ap[:, 0:n], seg, c, n)], ws, yp, None, [4, 5, 6, 7, 0, 1, 2, 3])
        if last:
            wt.release(w0 + f, tok)
        if side:
            side(f)
        x, t_x, done = src(f)
        o = dst(f)
        t = dve(lambda e, s=s, x=x, o=o, f=f: e.scalar_tensor_tensor(o, s.ap[:, 0:n], K.mod[:, l, 2, f, seg:seg + 1], x, ALU.mult, ALU.add),
                tok, t_x, K.t_gate[l], after)
        s.free = [t]
        done([t])
        out.append(t)
        if f == 0:
            t_acc = act(lambda e, o=o: e.activation(acc, o, ACT.Square), t, after)
        else:
            b = tmps.take()
            t = act(lambda e, o=o, b=b: e.activation(b.ap[:, 0:n], o, ACT.Square), t, b.was)
            t_acc = pool(lambda e, b=b: e.tensor_tensor(acc, acc, b.ap[:, 0:n], ALU.add), t, t_acc)
            b.free = [t_acc]
    return out, t_acc


def place_out(K, l, w0, after):
    for f in range(2, KT):
        K.wt.place[w0 + f] = tuple(Buf(K.sb(f"wo{l}{f}{p}", [128, 1024], F32R, f"wo{l}", 4096 * (2 * (f - 2) + p))) for p in range(2))
        for b in K.wt.place[w0 + f]:
            b.free = after
    K.wt.limit = w0 + KT


def first_block(K):
    pe, act, dve, pool, sp, d, sb = K.pe, K.act, K.dve, K.pool, K.sp, K.d, K.sb
    begin(K)
    K.s_wkr, K.s_wuq, K.s_wukv, K.s_pw = (K.slot("s_" + n) for n in ("wkr", "wuq", "wukv", "pw"))
    xc = sb("xc", [128, KT, NT])
    t_xc = []
    for i in range(4):
        t_xc += 2 * [sp.dma(xc[:, 2 * i:2 * i + 2, :], d["xc"][:, 2 * i:2 * i + 2, :], K.slot(f"s_xc{i}"))]
    wq = [sb(f"wmod0_{i}", [128, KT, 512], F32, *(("wgate2", 16384 * i - 16384) if i else ("wmod0", 0))) for i in range(3)]
    load = lambda q, *after: sp.dma(wq[q % 3][:, :, :], d["w_mod0"][q], K.slot(f"s_mod{q}"), *after)
    t_wq = [load(0)]
    w_in, w_out = [], []
    srcs = []
    for l in range(2):
        w_in.append(len(srcs))
        srcs += [d["w_in"][l, i] for i in range(len(TILES))]
        w_out.append(len(srcs))
        srcs += [d["w_out"][l, i] for i in range(KT)]
    K.w_out = w_out
    M = K.moe = Ctx()
    M.h2d = K.nc.dram_tensor("h2d", [NX, D], F32).ap()
    M.ybuf = K.nc.dram_tensor("ybuf", [2 * NX, D], F32).ap()
    K.w2 = len(srcs)
    srcs += [d["w_in2"][i] for i in range(24)]
    srcs += [d["w_out2"][k] for k in range(KT)]
    wt = K.wt = Weights(K, srcs)
    wt.on_dve = (*range(58, 69), 83, 85, 87)
    for b in wt.hi + wt.lo:
        b.free = []
    for i in (2, 3):
        wt.place[i] = tuple(Buf(sb(f"wx{i}{p}", [128, 1024], F32R, "wx", 4096 * (2 * i - 4 + j))) for j, p in enumerate("hl"))
        for b in wt.place[i]:
            b.free = []
    wt.limit = w_out[0] + 2
    K.free_rope, K.free_stat, K.st_free, K.stat_free = [], [], [[], []], [[], [], [], []]
    stat = K.stat
    tmps = tmp_ring(K, "tmpa", 5)

    sums = tmps.hold()
    for k in range(KT):
        if k == 0:
            t_s = act(lambda e: e.activation(sums.ap[:, 0:NT], xc[:, 0, :], ACT.Square), t_xc[0])
            continue
        b = tmps.take()
        t = act(lambda e, k=k, b=b: e.activation(b.ap[:, 0:NT], xc[:, k, :], ACT.Square), t_xc[k], b.was)
        t_s = dve(lambda e, b=b: e.tensor_tensor(sums.ap[:, 0:NT], sums.ap[:, 0:NT], b.ap[:, 0:NT], ALU.add), t, t_s)
        b.free = [t_s]
    hx = [[sb(f"h{c}{p}0", [128, KT, n], F32R) for p in "hl"] for c, n in (("x", NX), ("c", NC))]
    hT = [[], []]
    N = Norm(K, 6, nk=1)
    sums.free = [N.add(sums.ap, t_s)]
    tmps.release(sums)
    t_r = N.finish(stat[:, 0:6], stat[:, 8:14])
    wt.split()
    t_wq += [load(1), load(2)]
    wt.split()
    rows = quarter_mod(K, wq[0], t_wq[0], [])
    s, t = spread(K, 6, stat[:, 8:14], t_r, tmps)
    rb = tmps.hold()
    t_rb = act(lambda e: e.activation(rb.ap[:, 0:NT], s.ap[:, 0:NT], ACT.Copy), t, rb.was)
    s.free = [t_rb]
    K.t_mod_read, t_mod = quarter_columns(K, 0, rows[0], rows[2])
    t_wq.append(load(3, rows[1]))
    places = [K.ps.take(), K.ps.take(), K.px.hold()]
    wt.split()
    mod_loads(K)
    t_h = quarter_h(K, 0, xc, t_xc, rb.ap, t_rb, t_mod, tmps, hx, hT)
    for q in range(4):
        if q == 3:
            wt.split()
            after = fence(K)
        toks = [quarter_product(K, q, places[0], tile_pairs(wt.done[0]), hT)]
        if q < 3:
            rows = quarter_mod(K, wq[(q + 1) % 3], t_wq[q + 1], K.t_mod_read)
            if q < 2:
                for j in (2 * q + 2, 2 * q + 3):
                    K.mod_jobs[0][j].free = [rows[1]]
                    K.mod_jobs[2](j)
        toks.append(quarter_product(K, q, places[1], tile_pairs(wt.done[1]), hT))
        if q < 3:
            K.t_mod_read, t_mod = quarter_columns(K, q + 1, rows[0], rows[2])
            t_h = quarter_h(K, q + 1, xc, t_xc, rb.ap, t_rb, t_mod, tmps, hx, hT)
        toks.append(quarter_product(K, q, places[2], tile_pairs(wt.done[2]), hT))
    K.t_mod = [None, None]
    for i in range(HEAD):
        wt.release(i, toks[i])
    rb.free = [t_h]
    tmps.release(rb)
    yp = first_layer_block(K, 0, hT, wt, w_in[0], tmps, list(zip(places, toks)), after)

    after = fence(K) + [K.t_zero]
    place_out(K, 0, w_out[0], after)
    x1, xc1 = sb("x1", [128, KT, NX]), sb("xc1", [128, KT, NC])
    xr = Ring([Buf(sb(f"xr_{i}", [128, NX], F32, "xr", 4 * NX * i), K.slot(f"s_xr{i}")) for i in range(3)])
    tmps = K.tmps = tmp_ring(K, "tmpc", 5)
    for b in xr.bufs + tmps.bufs:
        b.free = after

    def source(c, n):
        ahead = []

        def load(f):
            if f < KT:
                b = xr.take()
                ahead.append((b, act.dma(b.ap[:, 0:n], d["xc"][:, f, c:c + n], b.slot, b.was)))

        def src(f):
            if f == 0:
                load(0)
                load(1)
            load(f + 2)
            b, t = ahead[f]

            def done(t):
                b.free = t
            return b.ap[:, 0:n], t, done
        return src
    acc = sb("acc", [128, NX])
    t_x1, t_acc = out_pass(K, 0, 0, 0, NX, wt, w_out[0], yp, source(0, NX), lambda f: x1[:, f, :], acc[:, :], tmps, after, False)
    after = fence(K)
    hT = [[], []]
    hx = [[sb(f"h{c}{p}1", [128, KT, n], F32R) for p in "hl"] for c, n in (("x", NX), ("c", NC))]
    steps = next_h(K, acc, t_acc, 4, 0, NX, lambda k: x1[:, k, :], t_x1, 0, hx[0], 1, tmps, 0, after, hT[0])
    acc_c = sb("accc", [128, NC])
    t_xc1, t_acc = out_pass(K, 0, 1, 0, NC, wt, w_out[0], yp, source(NX, NC), lambda f: xc1[:, f, :], acc_c[:, :], tmps, after, True,
                            lambda f: [next(steps, None) for _ in range((0, 1, 1, 1, 2, 2, 2, 2)[f])])
    for _ in steps:
        pass
    wt.limit = w_out[1] + 2
    K.beside.add(next_h(K, acc_c, t_acc, 2, 0, NC, lambda k: xc1[:, k, :], t_xc1, 1, hx[1], 1, tmps, 32, fence(K), hT[1]), 1)
    yp = first_layer_block(K, 1, hT, wt, w_in[1], tmps)
    return x1, t_x1, yp


NE, DE = 32, 256
PAIRS, GROUPS = 16, 32
N_GU, N_DN = 7, 6
MORE = 7
BIG = 1.0e30
T2 = 4
RC = dict(desc4=0, desc32=4, thr=36, base=40, over=72, ids=104, pow2=120, past64=136, bias=168, tri=204, nth=332, past128=371, all=403)
NONE = 4096.0


def second_block(K, x1, t_x1, yp, out):
    pe, act, dve, pool, sp, d, sb, nc = K.pe, K.act, K.dve, K.pool, K.sp, K.d, K.sb, K.nc
    stat, wt, w0 = K.stat, K.wt, K.w2
    after = fence(K)
    place_out(K, 1, K.w_out[1], after)
    tmps = tmp_ring(K, "tmpe", 5)
    for b in tmps.bufs:
        b.free = after
    small2 = K.small2 = sb("small2", [128, SMALL2["n"]])
    t_small2 = K.t_small2 = sp.dma(small2[:, :], d["small2"], K.slot("s_small2"))
    acc = [sb(f"acc_{i}", [128, 256], F32, "acc2", 1024 * i) for i in range(2)]
    hh, hl = sb("hh2", [128, KT, NX], F32R), sb("hl2", [128, KT, NX], F32R)
    halves, t_x, steps = [[], []], [None, None], [None, None]
    for i in range(2):
        c = 256 * i
        x = lambda k, c=c: x1[:, k, c:c + 256]
        side = None if i == 0 else lambda f: [next(steps[0], None) for _ in range((0, 1, 1, 1, 2, 2, 2, 2)[f])]
        t_x[i], t_acc = out_pass(K, 1, 0, c, 256, wt, K.w_out[1], [yp[0]], lambda f, x=x: (x(f), t_x1[f], lambda t: None), x, acc[i][:, :], tmps, after, i == 1, side)
        if i == 0:
            after2 = fence(K)
            wf, wfh, wfl = sb("wf", [128, KT, 8]), sb("wfh", [128, KT, 8], F32R), sb("wfl", [128, KT, 8], F32R)
            t_wf = sp.dma(wf[:, :, :], d["w_f"], K.slot("s_wf"), after2)
            t_wfh = act(lambda e: e.activation(wfh[:, :, :], wf[:, :, :], ACT.Copy), t_wf)
            t_wfl = pool(lambda e: e.tensor_tensor(wfl[:, :, :], wf[:, :, :], wfh[:, :, :].bitcast(F32), ALU.subtract), t_wfh, t_wf)
        steps[i] = next_h(K, acc[i], t_acc, 2, c, 256, x, t_x[i], 0, (hh, hl), 2, tmps, 40 * i, after2, halves[i])
    for _ in steps[0]:
        pass
    start = fence(K)
    xN = sb("xN", [128, T2, D])
    vT = [sb(n, [128, T2, 512]) for n in ("vdil", "vfox")]
    t_vT = [[None] * T2, [None] * T2]
    for kk in range(2, 8):
        where, at = ("wv", kk - 2) if kk < 4 else ("wv2", kk - 4)
        wt.place[w0 + kk] = tuple(Buf(sb(f"wv{kk}{p}", [128, 1024], F32R, where, 4096 * (2 * at + p))) for p in range(2))
        for b in wt.place[w0 + kk]:
            b.free = after2 if kk < 4 else start
    wt.limit = w0 + 8
    t_xN = [None] * T2
    for i in range(2):
        places = [(K.ps, K.px)[i].take() for _ in range(2)]
        hT = halves[i]
        for kk in range(8):
            hi, lo, t_hi, t_lo = wt.get(w0 + kk)
            which, k2_ = kk // 4, kk % 4
            for t_ in range(2):
                c = slice(256 * i + 128 * t_, 256 * i + 128 * t_ + 128)
                o = places[t_].ap[:, 512 * which:512 * which + 512]
                for j in range(2):
                    x = hT[2 * k2_ + j]
                    for p, (a, b, need) in enumerate(((x.hi, hi, (x.t_hi, t_hi, places[t_].was)), (x.lo, hi, (x.t_lo,)), (x.hi, lo, (t_lo,)))):
                        last = k2_ == 3 and j == 1 and p == 2
                        tok = pe(lambda e, o=o, a=a, b=b, c=c, j=j, k2_=k2_, p=p, last=last: e.matmul(
                            o, a[:, c], b.ap[:, 512 * j:512 * j + 512], start=k2_ == 0 and j == 0 and p == 0, stop=last),
                            need, signal=last or (t_ == 1 and j == 1 and p == 2))
                if k2_ == 3:
                    t = t_vT[which][2 * i + t_] = act(lambda e, o=o, t_=t_, i=i, which=which: e.activation(vT[which][:, 2 * i + t_, :], o, ACT.Copy), tok, start)
                    if which:
                        places[t_].free = [t]
            if i == 0:
                for _ in range((1, 1, 2, 2, 2, 2, 2, 2)[kk]):
                    next(steps[1], None)
            else:
                wt.release(w0 + kk, tok)
                wt.limit = w0 + 24
        if i == 0:
            for _ in steps[1]:
                pass
    hT = [Pair(hh[:, k, :], hl[:, k, :], [h[k].t_hi for h in halves], [h[k].t_lo for h in halves]) for k in range(KT)]
    for t_ in range(T2):
        s = (K.ps, K.px)[t_ // 2].take()
        for k in range(KT):
            tok = pe(lambda e, s=s, t_=t_, k=k: e.transpose(s.ap[:, 128 * k:128 * k + 128], x1[:, k, 128 * t_:128 * t_ + 128], K.ident[:, :]),
                     t_x[t_ // 2], s.was, signal=k == KT - 1)
        t_xN[t_] = act(lambda e, s=s, t_=t_: e.activation(xN[:, t_, :], s.ap[:, :], ACT.Copy), tok, start)
        s.free = [t_xN[t_]]
    K.bk = Ring([Buf(b.ap[:, 512 * i:512 * i + 512]) for r in (K.ps, K.px) for b in r.bufs for i in range(2)])
    for i, b in enumerate(K.bk.bufs):
        b.free = (K.ps.bufs + K.px.bufs)[i // 2].free
    bk = K.bk
    after = fence(K)

    tmps = tmp_ring(K, "tmpf", 4, 512)
    for b in tmps.bufs:
        b.free = after
    self_, sel = sb("self", [128, 1024]), sb("sel", [128, HEADS, 128], F32R)
    tri, lnn = sb("tri", [128, 512]), sb("lnn", [128, 512])
    t_lnn = sp.dma(lnn[:, :], d["lnn"], K.slot("s_lnn"), after)
    tabs = Ring([Buf(sb(f"tab{i}", [128, 512], F32, "tab", 2048 * i), K.slot(f"s_tab{i}")) for i in range(3)])
    for b in tabs.bufs:
        b.free = after
    q2 = [[sb(f"q2_{i}{p}", [128, NX], F32R, "q2", 2048 * (2 * i + p)) for p in range(2)] for i in range(2)]
    k2 = [[sb(f"k2_{i}{p}", [128, NX], F32R, "k2", 2048 * (2 * i + p)) for p in range(2)] for i in range(2)]
    P = Ring([Buf(sb(f"P2_{i}", [128, 512], F32, "P2", 2048 * i)) for i in range(6)])
    for b in P.bufs:
        b.free = after
    PT = sb("PT2", [128, 2, T2, 512])
    yh = [sb(f"y2h{g}", [128, 4, NX], F32R) for g in "df"]
    yl = [sb(f"y2l{g}", [128, 4, NX], F32R) for g in "df"]
    yp = [None] * KT
    heads, Pn, t_pt = {}, {}, []
    pv = Ctx()
    pv.t, pv.norm, pv.rstd = after, [None, None], [None, None]
    qk_read = {}
    st_free = [[] for _ in range(8)]
    fx = Ctx()

    def table(h):
        b = tabs.take()
        t = sp.dma(b.ap[:, :], d["bias"][h], b.slot, b.was)
        tab_of[h] = b
        yield
        b.tok = pool(lambda e: e.tensor_tensor(b.ap[:, :], b.ap[:, :], lnn[:, :], ALU.add), t, t_lnn)
        yield

    tab_of = {}

    def tile_product(p, which, at):
        s = bk.hold()
        w = tile_pairs(wt.get(at))
        w[0] = Pair(w[0].hi, w[0].lo, [w[0].t_hi, s.was], w[0].t_lo)
        for c in range(4):
            for k in (2 * c, 2 * c + 1):
                for a, b, need, q in ((w[k].hi, hT[k].hi, (w[k].t_hi, hT[k].t_hi), 0), (w[k].hi, hT[k].lo, (hT[k].t_lo,), 1), (w[k].lo, hT[k].hi, (w[k].t_lo,), 2)):
                    tok = pe(lambda e, a=a, b=b, k=k, q=q: e.matmul(s.ap[:, :], a, b, start=k == 0 and q == 0, stop=k == KT - 1 and q == 2),
                             need, signal=k == KT - 1 and q == 2)
            if c < 3:
                yield
        wt.release(at, tok)
        i = p % 2
        need = qk_read.get(p - 2, after)
        h_, l_ = (q2, k2)[which][i]
        sc = (0.125, 1.0)[which]
        th = act(lambda e: e.activation(h_[:, :], s.ap[:, :], ACT.Copy, scale=sc), tok, need)

        def rest():
            if which == 0:
                tl = dve(lambda e: e.scalar_tensor_tensor(l_[:, :], s.ap[:, :], 0.125, h_[:, :].bitcast(F32), ALU.mult, ALU.subtract), th, need)
            else:
                tl = dve(lambda e: e.tensor_tensor(l_[:, :], s.ap[:, :], h_[:, :].bitcast(F32), ALU.subtract), th, need)
            s.free = [tl]
            bk.release(s)
            heads.setdefault(p, [None, None])[which] = Pair(h_, l_, th, tl)
        rests.append(rest)
        yield

    rests = []

    def finish_turns():
        while rests:
            rests.pop(0)()

    def products():
        at = w0 + 8
        for p in range(HEADS):
            for which in range(2):
                yield from tile_product(p, which, at)
                at += 1

    def forget_product():
        fx.s = bk.hold()
        fx.tok = mm3(K, [(fx.s.ap[0:8, 0:NX], 0, 0, NX)], [Pair(wfh[:, k, :], wfl[:, k, :], [t_wfh, fx.s.was], t_wfl) for k in range(KT)], [hT])

    def forget():
        fa, fb, fc = tmps.hold(), tmps.hold(), tmps.hold()
        A, B_, C_ = fa.ap[0:8, :], fb.ap[0:8, :], fc.ap[0:8, :]
        t = dve(lambda e: e.tensor_scalar(A, fx.s.ap[0:8, 0:NX], small2[0:8, 16:17], None, ALU.add), fx.tok, t_small2, fa.was)
        fx.s.free = [t]
        bk.release(fx.s)
        t = dve(lambda e: e.scalar_tensor_tensor(B_, A, -1.0, A, ALU.mult, ALU.max), t, fb.was)
        yield
        t = act(lambda e: e.activation(B_, B_, ACT.Exp, scale=-1.0), t)
        t2 = dve(lambda e: e.tensor_scalar(C_, A, -1.0, 0.0, ALU.mult, ALU.max), fc.was)
        yield
        t = act(lambda e: e.activation(B_, B_, ACT.Ln, bias=1.0), t)
        yield
        t = dve(lambda e: e.tensor_tensor(B_, B_, C_, ALU.add), t2, t)
        t_o8 = dve(lambda e: e.memset(A, 1.0), t)
        yield
        t = dve(lambda e: e.tensor_tensor_scan(C_, A, B_, 0.0, ALU.mult, ALU.add), t, t_o8)
        fC = fx.fC = sb("fC", [128, NX], F32R)
        t0 = pool(lambda e: e.memset(fC[:, :].bitcast(F32), 0.0), after)
        yield
        t_c = act(lambda e: e.activation(fC[0:8, :], C_, ACT.Copy), t, t0)
        yield
        t1 = dve(lambda e: e.tensor_tensor(B_, C_, fC[0:8, :].bitcast(F32), ALU.subtract), t_c)
        yield
        t2 = act(lambda e: e.activation(fC[32:40, :], B_, ACT.Copy), t1, t0)
        fx.t_fC = [t_c, t2]
        fa.free = fb.free = fc.free = [t2, t]
        for b in (fa, fb, fc):
            tmps.release(b)
        yield
        t = sp.dma(self_[:, :], d["sel"], K.slot("s_sel"), after)
        fx.t_tri = sp.dma(tri[:, :], d["causal"], K.slot("s_tri"), after)
        yield
        yield
        fx.t_sel = act(lambda e: e.activation(sel[:, :, :].rearrange("p h c -> p (h c)"), self_[:, :], ACT.Copy), t, after)
        yield

    units = [(p, e_, i) for p in range(HEADS) for e_ in range(2) for i in range(T2)]

    def scores(u):
        p, e_, i = units[u]
        q, k = heads[p]
        fox = p >= 4
        s = bk.take()
        n, w = 128 * (i + 1), max(256, 128 * (i + 1))
        c = slice(128 * i, 128 * i + 128)
        r = slice(64 * e_, 64 * e_ + 64)
        jobs = [(q.hi[r, c], k.hi[r, 0:w], (q.t_hi, k.t_hi, s.was)), (q.hi[r, c], k.lo[r, 0:w], (k.t_lo,)), (q.lo[r, c], k.hi[r, 0:w], (q.t_lo,))]
        if fox:
            jobs.append((sel[:, 2 * (p - 4) + e_, :], fx.fC[:, 0:w], (fx.t_sel, fx.t_fC)))
        for j, (a, b, need) in enumerate(jobs):
            tok = pe(lambda e, j=j, a=a, b=b: e.matmul(s.ap[:, 0:w], a, b, start=j == 0, stop=j == len(jobs) - 1), need, signal=j == len(jobs) - 1)
        qk_read[p] = [tok]
        c0 = 192 + 8 * (u % 8)
        P_ = P.take()
        if fox:
            tab, t_tab = tri[:, 512 - n:512], fx.t_tri
        else:
            b = tab_of[2 * p + e_]
            tab, t_tab = b.ap[:, 512 - n:512], b.tok
        t = dve(lambda e: e.tensor_tensor_reduce(P_.ap[:, 0:n], s.ap[:, 0:n], tab, 1.0, -3.0e38, ALU.add, ALU.max, stat[:, c0:c0 + 1]),
                tok, t_tab, P_.was, st_free[u % 8])
        s.free = [t]
        if not fox and i == 3:
            b.free = [t]
        t = dve(lambda e: e.tensor_scalar(stat[:, c0 + 1:c0 + 2], stat[:, c0:c0 + 1], -1.0, None, ALU.mult), t)
        t = act(lambda e: e.activation(P_.ap[:, 0:n], P_.ap[:, 0:n], ACT.Exp, bias=stat[:, c0 + 1:c0 + 2], accum_out=stat[:, c0 + 2:c0 + 3]), t)
        Pn[u] = [P_, t, c0, n, None]

    def normalise(u):
        P_, t, c0, n, _ = Pn[u]
        t = dve(lambda e: e.reciprocal(stat[:, c0 + 3:c0 + 4], stat[:, c0 + 2:c0 + 3]), t)
        t = pool(lambda e: e.tensor_scalar(P_.ap[:, 0:n], P_.ap[:, 0:n], stat[:, c0 + 3:c0 + 4], 0.0, ALU.mult, ALU.add), t)
        Pn[u][4] = t
        st_free[u % 8] = [t]

    def turn_p(u):
        p, e_, i = units[u]
        P_, _, _, n, t = Pn[u]
        s = bk.take()
        for kt in range(i + 1):
            tok = pe(lambda e, kt=kt: e.transpose(s.ap[:, 128 * kt:128 * kt + 128], P_.ap[:, 128 * kt:128 * kt + 128], K.ident[:, :]), t, s.was, signal=kt == i)
        P_.free = [tok]
        dst = PT[:, e_, 0:i + 1, 128 * i:128 * i + 128]
        src = s.ap[:, 0:n].rearrange("p (t q) -> p t q", q=128)
        if u % 2:
            t1 = act(lambda e: e.activation(dst, src, ACT.Copy), tok, pv.t)
        else:
            t1 = dve(lambda e: e.tensor_copy(dst, src), tok, pv.t)
        s.free = [t1]
        t_pt.append(t1)

    def weigh(p):
        s = bk.take()
        fox = p // 4
        for kt in range(T2):
            for e_ in range(2):
                h = 2 * (p % 4) + e_
                tok = pe(lambda e, kt=kt, e_=e_, h=h: e.matmul(s.ap[64 * e_:64 * e_ + 64, 128 * kt:512], vT[fox][:, kt, 64 * h:64 * h + 64], PT[:, e_, kt, 128 * kt:512],
                                                               start=kt == 0, stop=kt == 3, skip_group_check=True),
                         t_pt, t_vT[fox], s.was, signal=kt == 3 and e_ == 1)
        pv.t = [tok]
        t_pt.clear()
        b = tmps.take()
        w = small2[:, 8 + p:9 + p]
        yh_, yl_ = yh[fox][:, p % 4, :], yl[fox][:, p % 4, :]
        t_hi = act(lambda e: e.activation(yh_, s.ap[:, :], ACT.Copy, scale=w), tok, after)
        t_sq = act(lambda e: e.activation(b.ap[:, :], s.ap[:, :], ACT.Square), tok, b.was)

        def rest():
            t_lo = dve(lambda e: e.scalar_tensor_tensor(yl_, s.ap[:, :], w, yh_.bitcast(F32), ALU.mult, ALU.subtract), t_hi, t_sq, after)
            s.free = [t_lo]
            yp[p] = Pair(yh_, yl_, t_hi, t_lo)
        rests.append(rest)

        def add():
            if p % 4 == 0:
                pv.norm[fox] = Norm(K, T2, 512, EPS, 4, bk)
            b.free = [pv.norm[fox].add(b.ap, t_sq)]
            if p % 4 == 3:
                pv.rstd[fox] = pv.norm[fox].finish(stat[:, 16 + 8 * fox:20 + 8 * fox], stat[:, 32 + 8 * fox:36 + 8 * fox], K.free_stat)
        return add

    t_x = list(t_xN)
    wo = []

    def out_product(half, t_, c):
        s = bk.take()
        cols = slice(128 * t_, 128 * t_ + 128)
        for k in range(4 * half, 4 * half + 4):
            y, w = yp[k], wo[k][c]
            for q, (a, b, need) in enumerate(((y.hi[:, cols], w.hi, (y.t_hi, w.t_hi, s.was)), (y.lo[:, cols], w.hi, (y.t_lo,)), (y.hi[:, cols], w.lo, (w.t_lo,)))):
                last = k == 4 * half + 3 and q == 2
                tok = pe(lambda e, s=s, a=a, b=b, k=k, q=q, last=last: e.matmul(s.ap[:, :], a, b, start=k == 4 * half and q == 0, stop=last), need, signal=last)
        x = xN[:, t_, 512 * c:512 * c + 512]
        r = stat[:, 32 + 8 * half + t_:33 + 8 * half + t_]
        t = dve(lambda e: e.scalar_tensor_tensor(x, s.ap[:, :], r, x, ALU.mult, ALU.add), tok, pv.rstd[half], t_x[t_])
        s.free = [t]
        t_x[t_] = t

    def split_out(done):
        for half, name in enumerate(("wo2d", "wo2f")):
            for k in range(4):
                hb, lb = (Buf(K.sb(f"{name}{p}{k}", [128, 1024], F32R, name, 4096 * (2 * k + j))) for j, p in enumerate("hl"))
                hb.free = lb.free = done
                wt.place[K.w2 + 24 + 4 * half + k] = (hb, lb)
        wt.limit = len(wt.srcs)
        for _ in range(8):
            wt.split()
            hb, lb, t_hi, t_lo = wt.done[-1]
            wo.append([Pair(hb.ap[:, 512 * c:512 * c + 512], lb.ap[:, 512 * c:512 * c + 512], t_hi, t_lo) for c in range(2)])
            yield

    def dilated_out():
        for t_ in range(T2):
            for c in range(2):
                out_product(0, t_, c)
                yield

    bg = products()
    more = lambda n: [next(bg, None) for _ in range(n)]
    for h in range(2):
        for _ in table(h):
            pass
    for _ in range(8):
        more(1)
        finish_turns()
    forget_product()
    more(3)
    fg = forget()
    LA = 3
    side = {}
    for u in range(LA):
        scores(u)
        normalise(u) if u < LA - 1 else None
    pend = None
    nu = len(units)
    splits = outs = iter(())
    for u in range(nu):
        p, e_, i = units[u]
        r = u % 8
        more(1)
        if i == 1 and u // 4 + 2 < 8:
            tg = table(u // 4 + 2)
            next(tg)
        if i == 3 and u // 4 + 2 < 8:
            next(tg)
        if r == 0 and p:
            pend2 = weigh(p - 1)
        turn_p(u)
        if u + LA - 1 < nu:
            normalise(u + LA - 1)
        if u + LA < nu:
            scores(u + LA)
        finish_turns()
        if r == 0 and p:
            pend = pend2
        elif pend:
            pend()
            pend = None
        if u >= 2:
            next(fg, None)
        if u == 53:
            fence_out = fence(K)
            splits, outs = split_out(fence_out), dilated_out()
        if u >= 53:
            next(splits, None)
        if u >= 56:
            next(outs, None)
    E = K.moe.experts = Experts(K)
    E.gu[0].free = fence_out
    for _ in splits:
        pass
    E.load(1)
    weigh(HEADS - 1)()
    finish_turns()
    for _ in outs:
        pass
    last_part(K, xN, t_x, lambda t_, c: out_product(1, t_, c), small2, t_small2)
    experts(K, xN, t_x, out)


def last_part(K, xN, t_x, product, small2, t_small2):
    pe, act, dve, pool, sp, d, sb, stat, bk = K.pe, K.act, K.dve, K.pool, K.sp, K.d, K.sb, K.stat, K.bk
    M = K.moe
    after = fence(K)
    row1, wr, rc = sb("row1", [128, D]), sb("wr", [128, KT, 36]), sb("rc", [128, RC["all"]])
    t_rows = sp.dma(row1[:, :], d["rows"][:, 0, :], K.slot("s_row1"), after)
    t_wr = sp.dma(wr[:, :, :], d["w_r"], K.slot("s_wr"), after)
    M.rc, M.t_rc = rc, sp.dma(rc[:, :], d["rc"], K.slot("s_rc"), after)
    E = M.experts
    for b in E.gu[1:3] + E.dn[:3]:
        b.free = after
    E.load(5)
    M.iota = sb("iota", [128, 128])
    M.t_iota = sp.dma(M.iota[:, :], d["iota"], K.slot("s_iota"), after)
    R = room_for_choice(K, after)
    xT = Ring([Buf(sb(f"xT{i}", [128, KT, 128], F32, "xT", 4096 * i)) for i in range(2)])
    h2 = Ring([Buf(sb(f"h2{i}", [128, D], F32, "h2N", 4096 * i)) for i in range(3)])
    for b in xT.bufs + h2.bufs:
        b.free = after
    ms, rs = stat[:, 48:52], stat[:, 56:60]
    t_rs, turned, M.t_h2d = [None] * T2, {}, []

    def turn(t_, c):
        if c == 0:
            turned[t_] = (xT.take(), [])
        x, done = turned[t_]
        s = bk.take()
        for k in range(4):
            tok = pe(lambda e, k=k: e.transpose(s.ap[:, 128 * k:128 * k + 128], xN[:, t_, 512 * c + 128 * k:512 * c + 128 * k + 128], K.ident[:, :]),
                     t_h[t_][c], s.was, signal=k == 3)
        dst, src = x.ap[:, 4 * c:4 * c + 4, :], s.ap[:, :].rearrange("p (k q) -> p k q", q=128)
        if c:
            done.append(dve(lambda e: e.tensor_copy(dst, src), tok, x.was))
        else:
            done.append(act(lambda e: e.activation(dst, src, ACT.Copy), tok, x.was))
        s.free = [done[-1]]

    def squares(t_):
        b = h2.take()
        t = act(lambda e: e.activation(b.ap[:, :], xN[:, t_, :], ACT.Square, accum_out=ms[:, t_:t_ + 1]), t_x[t_], b.was)
        t = dve(lambda e: e.tensor_scalar(ms[:, t_:t_ + 1], ms[:, t_:t_ + 1], 1.0 / D, EPS, ALU.mult, ALU.add), t)
        t_rs[t_] = pool(lambda e: e.tensor_tensor(rs[:, t_:t_ + 1], ms[:, t_:t_ + 1], K.nhalf[:, 0:1], ALU.pow), t)
        return b

    def logits(t_, c):
        x, t_xT = turned[t_]
        if c == 0:
            places[t_] = bk.hold()
        s = places[t_]
        for k in range(4 * c, 4 * c + 4):
            tok = pe(lambda e, k=k: e.matmul(s.ap[:, 0:36], x.ap[:, k, :], wr[:, k, :], start=k == 0, stop=k == KT - 1), t_xT[c], t_wrs, s.was if k == 0 else None, signal=k == KT - 1)
        if c == 0:
            return
        x.free = [tok]
        t = dve(lambda e: e.scalar_tensor_tensor(R.L[:, t_, :], s.ap[:, 0:36], rs[:, t_:t_ + 1], rc[:, RC["bias"]:RC["bias"] + 36], ALU.mult, ALU.add),
                tok, t_rs[t_], M.t_rc)
        s.free = [t]
        bk.release(s)
        chosen[t_] = choose(K, R, t_, t)

    places, chosen = {}, {}

    def steps(t_, n=None):
        for _ in chosen[t_]:
            n = n and n - 1
            if n == 0:
                break

    def rows(t_, b):
        t = act(lambda e: e.activation(b.ap[:, :], xN[:, t_, :], ACT.Copy, scale=rs[:, t_:t_ + 1]), t_rs[t_])
        t = pool(lambda e: e.tensor_tensor(b.ap[:, :], b.ap[:, :], row1[:, :], ALU.mult), t, t_rows)
        M.t_h2d.append(pool.dma(M.h2d[128 * t_:128 * t_ + 128, :], b.ap[:, :], K.slot(f"s_h2{t_}"), t))
        b.free = [M.t_h2d[-1]]

    t_h = [[None, None] for _ in range(T2)]

    def both(t_, c):
        product(t_, c)
        t_h[t_][c] = t_x[t_]
    both(0, 0)
    t_wrs = dve(lambda e: e.tensor_tensor(wr[:, :, :], wr[:, :, :], small2[:, 17:25].unsqueeze(2).to_broadcast([128, KT, 36]), ALU.mult), t_wr, t_small2)
    both(0, 1)
    for t_ in range(T2 - 2):
        b = squares(t_)
        both(t_ + 1, 0)
        for c in range(2):
            turn(t_, c)
        if t_:
            steps(t_ - 1)
        both(t_ + 1, 1)
        logits(t_, 0)
        logits(t_, 1)
        rows(t_, b)
        steps(t_, 12)
    b2 = squares(2)
    both(3, 0)
    turn(2, 0)
    turn(2, 1)
    steps(1)
    both(3, 1)
    turn(3, 0)
    b3 = squares(3)
    logits(2, 0)
    turn(3, 1)
    logits(2, 1)
    done = after + [t_h[3][1]]
    for b_ in E.gu[3:5] + E.dn[3:5]:
        b_.free = done
    E.load(4)
    rows(2, b2)
    steps(2, 4)
    logits(3, 0)
    logits(3, 1)
    steps(3, 2)
    rows(3, b3)
    inputs_of_experts(K, done)
    place(K, R, chosen)


class Experts:

    def __init__(self, K):
        self.K, self.n, self.queued = K, 0, []
        self.gu = [Buf(K.sb(f"gu{i}", [128, KT, 2 * DE]), K.slot(f"s_gu{i}")) for i in range(N_GU)]
        self.dn = [Buf(K.sb(f"dn{i}", [128, 2, D]), K.slot(f"s_dn{i}")) for i in range(N_DN)]
        for b in self.gu + self.dn:
            b.free = None
        first = ["gu0", "gu1", "dn0", "dn1", "gu2", "dn2", "gu3", "dn3", "gu4", "dn4", "gu5", "dn5", "gu6"]
        self.order = [(w[:2], int(w[2:])) for w in first] + [(w, 2 * p + n + j) for p in range(PAIRS) for w, n in (("gu", N_GU), ("dn", N_DN)) for j in range(2) if 2 * p + n + j < NE]
        self.at = {}

    def place(self, w, e):
        bufs = self.gu if w == "gu" else self.dn
        return bufs[e % len(bufs)]

    def load(self, n):
        for w, e in self.order[self.n:self.n + n]:
            b = self.place(w, e)
            assert b.free is not None
            t = self.K.sp.dma(b.ap[:, :, :], self.K.d["w_" + w][e], b.slot, b.free, self.queued[-2:-1])
            b.free = None
            self.queued.append(t)
            self.at[w, e] = (b.ap, t)
            self.n += 1

    def pair(self, p):
        return [(*self.at["gu", e], *self.at["dn", e]) for e in (2 * p, 2 * p + 1)]

    def release(self, w, p, tok):
        for e in (2 * p, 2 * p + 1):
            self.place(w, e).free = [tok]
        return max(0, min(2, NE - 2 * p - dict(gu=N_GU, dn=N_DN)[w]))


def room_for_choice(K, after):
    R = Ctx()
    R.after, R.t_a, R.t_w = after, [], []
    rt, at = K.sb("rt", [128, 4096]), Ctx()
    at.n = 0

    def new(*shape, dt=None):
        n = int(np.prod(shape))
        v = rt[:, at.n:at.n + n]
        at.n += n
        assert at.n <= 4096
        if dt:
            v = v.bitcast(dt)
        if len(shape) == 2:
            v = v.rearrange("p (a b) -> p a b", b=shape[1])
        if len(shape) == 3:
            v = v.rearrange("p (a b c) -> p a b c", b=shape[1], c=shape[2])
        return v
    R.new = new
    R.L = new(T2, 36)
    R.nm, R.s4, R.m4, R.k1, R.k2, R.k3, R.v1, R.v2, R.r, R.g1, R.ed = (new(T2) for _ in range(11))
    R.E4, R.key4, R.far = new(T2, 4), new(T2, 4), new(T2, NE)
    R.inc = new(NE + 1)
    R.before, R.at = new(T2, NE), new(T2, NE)
    R.t_zero = K.dve(lambda e: e.memset(R.inc[:, 0:1], 0.0), after)
    R.t_before = [K.dve(lambda e: e.memset(R.before[:, 0, :], 0.0), after),
                  K.dve(lambda e: e.tensor_copy(R.at[:, 0, :], K.moe.rc[:, RC["base"]:RC["base"] + NE]), after, K.moe.t_rc)]
    R.M, R.A, R.w12 = new(2, T2, NE), new(T2, NE), new(2, T2)
    return R


def choose(K, R, t_, t):
    act, dve, M = K.act, K.dve, K.moe
    const = lambda name, m: M.rc[:, RC[name]:RC[name] + m]
    nm, s4, m4, k1, k2, k3, v1, v2, r, g1, ed = (v[:, t_:t_ + 1] for v in (R.nm, R.s4, R.m4, R.k1, R.k2, R.k3, R.v1, R.v2, R.r, R.g1, R.ed))
    E4, key4, far, M1, M2, A = R.E4[:, t_, :], R.key4[:, t_, :], R.far[:, t_, :], R.M[:, 0, t_, :], R.M[:, 1, t_, :], R.A[:, t_, :]
    Lg, Le = R.L[:, t_, 0:4], R.L[:, t_, 4:36]
    groups = lambda v: v.rearrange("p (g j) -> p g j", j=8)
    tt = lambda out, x, y, op, *after: dve(lambda e: e.tensor_tensor(out, x, y, op), after)
    ts = lambda out, x, s1, s2, op0, op1, *after: dve(lambda e: e.tensor_scalar(out, x, s1, s2, op0, op1) if op1 else e.tensor_scalar(out, x, s1, None, op0), after)
    red = lambda out, x, *after: dve(lambda e: e.tensor_reduce(out, x, AX.X, ALU.max), after)
    keys = lambda out, v, best, desc, *after: dve(lambda e: e.scalar_tensor_tensor(out, v, best, desc, ALU.is_ge, ALU.mult), after)
    plus_max = lambda out, x, y, best, *after: dve(lambda e: e.tensor_tensor_reduce(out, x, y, 1.0, -3.0e38, ALU.add, ALU.max, best), after)

    t = dve(lambda e: e.tensor_reduce(nm, Lg, AX.X, ALU.max, negate=True), t, R.after)
    yield t
    t_e = act(lambda e: e.activation(E4, Lg, ACT.Exp, bias=nm, accum_out=s4), t)
    t_m = t = red(m4, E4, t_e)
    yield t
    t = keys(key4, E4, m4, const("desc4", 4), t)
    yield t
    t = red(k1, key4, t)
    yield t
    t = ts(key4, key4, k1, -BIG, ALU.is_lt, ALU.mult, t)
    yield t
    t = plus_max(groups(Le), groups(Le), key4.unsqueeze(2).to_broadcast([128, 4, 8]), v1, t)
    yield t
    t = keys(M1, Le, v1, const("desc32", NE), t)
    yield t
    t = red(k2, M1, t)
    yield t
    t_f = ts(far, M1, k2, -10 * BIG, ALU.is_equal, ALU.mult, t)
    t_M1 = ts(M1, M1, k2, None, ALU.is_equal, None, t)
    yield t
    t = plus_max(Le, Le, far, v2, t_f)
    yield t
    t = keys(M2, Le, v2, const("desc32", NE), t)
    yield t
    t = red(k3, M2, t)
    yield t
    t = ts(M2, M2, k3, None, ALU.is_equal, None, t)
    yield t
    t_a = tt(A, M1, M2, ALU.add, t, t_M1)
    R.t_a.append(t_a)
    yield t_a
    if t_ + 1 < T2:
        R.t_before = [tt(after_, so_far, A, ALU.add, t_a, R.t_before) for after_, so_far in ((R.before[:, t_ + 1, :], R.before[:, t_, :]), (R.at[:, t_ + 1, :], R.at[:, t_, :]))]
        yield R.t_before[-1]
    t = tt(ed, v2, v1, ALU.subtract)
    t2 = dve(lambda e: e.reciprocal(s4, s4), t_e)
    t = act(lambda e: e.activation(ed, ed, ACT.Exp), t)
    t2 = tt(g1, m4, s4, ALU.mult, t2, t_m)
    yield t2
    t = ts(r, ed, 1.0, None, ALU.add, None, t)
    yield t
    t = dve(lambda e: e.reciprocal(r, r), t)
    yield t
    t = tt(R.w12[:, 0, t_:t_ + 1], g1, r, ALU.mult, t, t2)
    yield t
    R.t_w.append(tt(R.w12[:, 1, t_:t_ + 1], R.w12[:, 0, t_:t_ + 1], ed, ALU.mult, t))


def place(K, R, chosen):
    pe, dve, pool, M, bk, new = K.pe, K.dve, K.pool, K.moe, K.bk, R.new
    const = lambda name, n: M.rc[:, RC[name]:RC[name] + n]
    over = lambda v, m: v.unsqueeze(2).to_broadcast([128, v.shape[1], m])
    along = lambda v, m: v.unsqueeze(1).to_broadcast([128, m, v.shape[1]])
    fl = lambda v: v.rearrange("p a b -> p (a b)")
    w12 = R.w12
    tt = lambda out, x, y, op, *after: dve(lambda e: e.tensor_tensor(out, x, y, op), after)
    red = lambda out, x, op, *after: dve(lambda e: e.tensor_reduce(out, x, AX.X, op), after)
    ts = lambda out, x, s1, s2, op0, op1, *after: dve(lambda e: e.tensor_scalar(out, x, s1, s2, op0, op1) if op1 else e.tensor_scalar(out, x, s1, None, op0), after)
    copy = lambda out, x, *after: dve(lambda e: e.tensor_copy(out, x), after)
    warm = bk.hold()

    def keep_warm(t):
        pe(lambda e: e.matmul(warm.ap[:, 0:128], K.ones[:, :], K.ones[:, :], start=True, stop=True), t, warm.was, signal=False)
        return t

    last = chosen[3]
    for i, _ in enumerate(chosen[2]):
        t = next(last)
        if True:
            keep_warm(t)
    s = bk.take()
    tri, ones = M.rc[:, RC["tri"]:RC["tri"] + 128], K.ones[:, :]
    place_at, cnt = s.ap[:, 0:NE * T2], s.ap[:, NE * T2:NE * T2 + NE]
    pe(lambda e: e.matmul(place_at, ones, fl(R.at), start=True, stop=False, skip_group_check=True), R.t_before, s.was, signal=False)
    pe(lambda e: e.matmul(cnt, ones, R.before[:, T2 - 1, :], start=False, stop=False, skip_group_check=True), signal=False)
    while len(R.t_a) < T2:
        t = next(last)
        if len(R.t_a) < T2:
            keep_warm(t)
    pe(lambda e: e.matmul(cnt, ones, R.A[:, T2 - 1, :], start=False, stop=True, skip_group_check=True), R.t_a, signal=False)
    tok = pe(lambda e: e.matmul(place_at, tri, fl(R.A), start=False, stop=True, skip_group_check=True))
    at3 = place_at.rearrange("p (t e) -> p t e", e=NE)
    cmp, nb, far = new(NE, 4), new(NE), new(NE)
    inc = R.inc
    many, p16 = new(NE), new(PAIRS)
    ctl, eq = new(2 + MORE), new(MORE, NE)
    G, H = new(T2, NE), new(T2, NE)
    slot, (whole, low, hi) = new(2 * T2), (new(2 * T2, dt=U32) for _ in range(3))
    M.ctl = K.sb("ctl", [128, 2 + MORE], I32)
    more = lambda: next(last, None)
    t1 = keep_warm(tt(cmp, over(cnt, 4), along(const("thr", 4), NE), ALU.is_gt, tok))
    t2 = tt(G, at3, along(const("past64", NE), T2), ALU.is_gt, tok)
    more()
    t1 = keep_warm(red(nb, cmp, ALU.add, t1))
    t2 = dve(lambda e: e.scalar_tensor_tensor(fl(G), fl(G), 64.0, place_at, ALU.mult, ALU.add), t2)
    t_inc = t1 = dve(lambda e: e.tensor_tensor_scan(inc[:, 1:NE + 1], K.ones[:, 0:NE], nb, 0.0, ALU.mult, ALU.add), t1)
    t3 = tt(H, at3, along(const("past128", NE), T2), ALU.is_gt, tok)
    more()
    t1 = keep_warm(dve(lambda e: e.scalar_tensor_tensor(far, inc[:, 0:NE], 128.0, const("over", NE), ALU.mult, ALU.add), t1, R.t_zero))
    t4 = t_cnt = ts(many, cnt, 64.5, None, ALU.is_gt, None, tok)
    s.free = [t3, t_cnt]
    t1 = keep_warm(tt(H, H, along(far, T2), ALU.mult, t1, t3))
    more()
    t4 = red(p16, many.rearrange("p (a b) -> p a b", b=2), ALU.max, t4)
    t1 = keep_warm(tt(fl(G), fl(G), fl(H), ALU.add, t1, t2))
    t4 = tt(p16, p16, const("pow2", PAIRS), ALU.mult, t4)
    MM = R.M.rearrange("p w t e -> p w (t e)")
    t1 = keep_warm(tt(MM, MM, along(fl(G), 2), ALU.mult, t1))
    more()
    more()
    t4 = red(ctl[:, 0:1], p16, ALU.add, t4)
    t1 = keep_warm(red(slot, R.M.rearrange("p w t e -> p (w t) e"), ALU.add, t1))
    t4 = [t4, copy(ctl[:, 1:2], inc[:, NE:NE + 1], t_inc)]
    t1 = copy(whole, slot, t1)
    t_low = ts(low, whole, 127, None, ALU.bitwise_and, None, t1)
    t_hi = keep_warm(ts(hi, whole, 7, None, ALU.logical_shift_right, None, t1))
    g = GROUPS + MORE
    s3 = bk.take()
    n = 2 * T2
    ones_at, here, what = new(n, 128), new(n, g), new(n, 3, g)
    ids = const("ids", 2 * n).rearrange("p (c w) -> p c w", w=2)
    that = lambda q, w, v: q(lambda e: e.tensor_tensor(what[:, :, w, :], here, over(v, g), ALU.mult), t2, R.t_w)
    t2 = keep_warm(tt(here, along(const("nth", g), n), over(hi, g), ALU.is_equal, t_hi))
    t3 = [that(pool, 2, fl(w12)), that(pool, 1, ids[:, :, 1])]
    t1 = keep_warm(tt(ones_at, along(M.iota[:, :], n), over(low, 128), ALU.is_equal, t_low, M.t_iota))
    t3.append(keep_warm(that(dve, 0, ids[:, :, 0])))
    for j in range(n):
        tok = pe(lambda e, j=j: e.matmul(s3.ap[:, 0:3 * g], ones_at[:, j, :], what[:, j, :, :].rearrange("p w g -> p (w g)"), start=j == 0, stop=j == n - 1),
                 t1, t3, s3.was if j == 0 else None, signal=j == n - 1)
    t5 = tt(eq, along(inc[:, 1:NE + 1], MORE), over(const("nth", MORE), NE), ALU.is_le, t_inc)
    t5 = red(ctl[:, 2:2 + MORE], eq, ALU.add, t5)
    t5 = ts(ctl[:, 2:2 + MORE], ctl[:, 2:2 + MORE], float(NE - 1), None, ALU.min, None, t5)
    M.t_ctl = copy(M.ctl[:, :], ctl, t4, t5)
    kept = K.sb("kept", [128, 3 * g + 28])
    M.tok, M.row, M.w = kept[:, 0:g].bitcast(U32), kept[:, g:2 * g].bitcast(U32), kept[:, 2 * g:3 * g]
    M.tick, M.own = kept[:, 3 * g:3 * g + 24], kept[:, 3 * g + 24:3 * g + 28]
    M.t_tok = ts(M.tok, s3.ap[:, 0:g], NONE, None, ALU.add, None, tok, R.after)
    ts(M.row, s3.ap[:, g:2 * g], NONE, None, ALU.add, None, tok)
    copy(M.own, s3.ap[:, GROUPS - 4:GROUPS], tok)
    M.t_list = copy(M.w, s3.ap[:, 2 * g:3 * g], tok)
    s3.free = [M.t_list]
    for i in range(WARM):
        keep_warm(tok)
    warm.free = [pe.last()]
    bk.release(warm)


WARM = 20


def buffers(K, after, name, n, shape=(D,), slots=True):
    out = []
    for i in range(n):
        b = Buf(K.sb(f"{name}{i}", [128, *shape], F32, name, 4096 * i), K.slot(f"s_{name}{i}") if slots else None)
        b.free, b.at = after, i
        out.append(b)
    return Ring(out)


def inputs_of_experts(K, after):
    M = K.moe
    M.xg = buffers(K, after, "xg", 2)
    empty(K, M.xg, after)


def empty(K, ring, after):
    for b in ring.bufs:
        b.free = [K.pool(lambda e, b=b: e.memset(b.ap[:, :], 0.0), after)]


class Guarded:

    def __init__(self, queues):
        self.at = [(q, len(q.ops)) for q in queues]

    def close(self, test):
        for q, start in self.at:
            body = q.ops[start:]
            del q.ops[start:]
            if not body:
                continue
            n = raises(body, q.sem)
            q.ops.append(("guard", test, body, [(q.sem, q.count - n, n)] if n else []))


def raises(ops, sem):
    n = 0
    for op in ops:
        if op[0] == "guard":
            n += sum(by for _, _, by in op[3])
        elif op[0] != "register" and op[2] and op[2][0].num == sem.num:
            n += 1
    return n


def experts(K, xN, t_x, out):
    pe, act, dve, pool, sp, d, M, sb = K.pe, K.act, K.dve, K.pool, K.sp, K.d, K.moe, K.sb
    E, bk = M.experts, K.bk
    start = fence(K) + [M.t_list, M.t_h2d]
    for q in (pe, act, dve, pool, sp):
        q.ops.append(("register", "pairs", M.ctl[0:1, 0:1], M.t_ctl, 2 ** PAIRS - 1))
        q.ops.append(("register", "more", M.ctl[0:1, 1:2], M.t_ctl, MORE))

    bufs = lambda *a: buffers(K, start, *a)
    xg, xg2, XT, Y = M.xg, bufs("xg2_", 1, (D,), False), bufs("XT", 1, (KT, 128), False), bufs("Y", 2)
    he, heT = [sb(f"he{j}", [128, 256], F32, "he", 1024 * j) for j in range(2)], sb("heT", [128, 2, 128], F32, "he", 2048)
    t_he, t_heT = [start, start], [start]

    def gather(b, g, slot):
        t = slot.token()
        pool.ops.append((_tokens([b.was, M.t_list, M.t_h2d]), lambda e: e.indirect_dma_start(
            out=b.ap[:, :], out_offset=None, in_=M.h2d, in_offset=bass.IndirectOffsetOnAxis(ap=M.tok[:, g:g + 1], axis=0),
            bounds_check=NX - 1, oob_is_err=False), (slot.sem, 16)))
        return b, t

    def turn_x(b, t, x=None):
        x = x or XT.take()
        for c in range(2):
            s = bk.take()
            for k in range(4):
                tok = pe(lambda e, s=s, c=c, k=k: e.transpose(s.ap[:, 128 * k:128 * k + 128], b.ap[:, 512 * c + 128 * k:512 * c + 128 * k + 128], K.ident[:, :]),
                         t, s.was, signal=k == 3)
            src = s.ap[:, :].rearrange("p (k q) -> p k q", q=128)
            if c:
                t1 = act(lambda e, src=src: e.activation(x.ap[:, 4:8, :], src, ACT.Copy), tok, x.was)
            else:
                t0 = t1 = dve(lambda e, src=src: e.tensor_copy(x.ap[:, 0:4, :], src), tok, x.was)
            s.free = [t1]
        b.free = [tok]
        return x, [t0, t1]

    def store(y, g):
        def emit(c, s, tok):
            w = M.w[:, g:g + 1]
            if c:
                return dve(lambda e: e.tensor_scalar(y.ap[:, 512:1024], s.ap[:, :], w, None, ALU.mult), tok, y.was, M.t_list)
            return act(lambda e: e.activation(y.ap[:, 0:512], s.ap[:, :], ACT.Copy, scale=w), tok, y.was, M.t_list)
        return emit

    def up(x, t_x_, ws, j=0, s=None):
        n = 128 // len(ws)
        s = s or bk.take()
        for k in range(KT):
            for i, (gu, t_gu, dn, t_dn) in enumerate(ws):
                o = slice(n * i, n * i + n)
                tok = pe(lambda e, k=k, o=o, gu=gu: e.matmul(s.ap[o, :], x.ap[:, k, o], gu[:, k, :], start=k == 0, stop=k == KT - 1, skip_group_check=True),
                         t_x_, t_gu, s.was, signal=k == KT - 1 and i == len(ws) - 1)
        x.free = [tok]
        t = act(lambda e: e.activation(he[j][:, :], s.ap[:, 0:256], ACT.Silu), tok, t_he[j])
        t = dve(lambda e: e.tensor_tensor(he[j][:, :], s.ap[:, 256:512], he[j][:, :], ALU.mult), t)
        s.free = [t]
        return t

    def turn_up(t, j=0):
        s2 = bk.take()
        for k in range(2):
            tok = pe(lambda e, k=k: e.transpose(s2.ap[:, 128 * k:128 * k + 128], he[j][:, 128 * k:128 * k + 128], K.ident[:, :]), t, s2.was, signal=k == 1)
        t_he[j] = tok
        t = dve(lambda e: e.tensor_copy(heT[:, :, :], s2.ap[:, 0:256].rearrange("p (k q) -> p k q", q=128)), tok, t_heT[0])
        s2.free = [t]
        return t

    def down(t, ws, emit):
        n = 128 // len(ws)
        ts = []
        for c in range(2):
            s = bk.take()
            for k in range(2):
                for i, (gu, t_gu, dn, t_dn) in enumerate(ws):
                    o = slice(n * i, n * i + n)
                    tok = pe(lambda e, s=s, k=k, o=o, dn=dn, c=c: e.matmul(s.ap[o, :], heT[:, k, o], dn[:, k, 512 * c:512 * c + 512], start=k == 0, stop=k == 1, skip_group_check=True),
                             t, t_dn, s.was, signal=k == 1 and i == len(ws) - 1)
            ts.append(emit(c, s, tok))
            s.free = [ts[-1]]
        t_heT[0] = tok
        return ts

    def scatter(y, g, slot, *after):
        t = slot.token()
        pool.ops.append((_tokens(after + (K.t_zero,)), lambda e: e.indirect_dma_start(
            out=M.ybuf, out_offset=bass.IndirectOffsetOnAxis(ap=M.row[:, g:g + 1], axis=0), in_=y.ap[:, :], in_offset=None,
            bounds_check=2 * NX - 1, oob_is_err=False), (slot.sem, 16)))
        return t

    def guarded(queues, test, body):
        before = {id(b): b.free for b in bk.bufs}
        he_before, heT_before = list(t_he), list(t_heT)
        g = Guarded(queues)
        got = body()
        g.close(test)
        for b in bk.bufs:
            if b.free is not before[id(b)]:
                b.free = [before[id(b)], b.free]
        for now, was in ((t_he, he_before), (t_heT, heT_before)):
            now[:] = [[x, y] for x, y in zip(was, now)]
        return got

    crowded = lambda i: lambda r: ((r["pairs"] >> i) & 1) > 0
    second = {}

    def gather2(i):
        st = second[i] = Ctx()
        st.slots = [K.slot(f"s_second{i}_{c}") for c in range(2)]
        b = xg2.take()
        g = Guarded((pool,))
        st.x = gather(b, 2 * i + 1, st.slots[0])
        g.close(crowded(i))

    def more_up(i, ws):
        st = second[i]
        st.t = guarded((pe, act, dve), crowded(i), lambda: up(*turn_x(*st.x), ws, 1))

    def more_down(i, ws):
        st = second[i]
        y = st.y = Y.take()
        ts = guarded((pe, act, dve), crowded(i), lambda: down(turn_up(st.t, 1), ws, store(y, 2 * i + 1)))
        g = Guarded((pool,))
        st.stored = scatter(y, 2 * i + 1, st.slots[1], ts)
        g.close(crowded(i))

    def stored2(i):
        g = Guarded((pool,))
        y = second[i].y
        y.free = [y.was, pool(lambda e: e.memset(M.tick[:, i:i + 1], 0.0), second[i].stored)]
        g.close(crowded(i))

    firsts = []

    def gather1():
        if len(firsts) < PAIRS:
            b = xg.take()
            firsts.append(gather(b, 2 * len(firsts), b.slot))
    gather1()
    gather1()
    for b in E.gu[5:] + E.dn[5:]:
        b.free = start + [x[1] for x in firsts]
    E.load(3)
    empty(K, xg2, start)
    gather2(0)
    read, stored = [], []
    for i in range(PAIRS - 2):
        ws = E.pair(i)
        y = Y.take()
        x = turn_x(*firsts[i])
        gather1()
        if i:
            stored2(i - 1)
        t = up(*x, ws)
        more_up(i, ws)
        E.load(E.release("gu", i, pe.last()))
        ts = down(turn_up(t), ws, store(y, 2 * i))
        y.free = [scatter(y, 2 * i, y.slot, ts)]
        stored.append(y.free)
        more_down(i, ws)
        if i + 3 < PAIRS:
            gather2(i + 1)
        read.append(pe.last())
        n = E.release("dn", i, pe.last())
        if i < PAIRS - N_DN // 2 - 1:
            E.load(n)
    stored2(i)
    w_gu, w_dn = E.place("gu", 2 * PAIRS).ap, E.place("dn", 2 * i).ap

    def far(n):
        after = [read[-1], pe.last()]

        def load(e, dst, src):
            v = e.value_load(M.ctl[0:1, 2 + n:3 + n], min_val=0, max_val=NE - 1)
            return e.dma_start(dst, src[bass.ds(v, 1)].rearrange("o p k c -> (o p) k c"))
        s_far = [K.slot(f"s_far_{n}{c}") for c in range(4)]
        t = [s_.token() for s_ in s_far[0:2]]
        sp.ops.append((_tokens(after), lambda e: load(e, w_gu[:, :, :], d["w_gu"]), (s_far[0].sem, 16)))
        sp.ops.append(([], lambda e: load(e, w_dn[:, :, :], d["w_dn"]), (s_far[1].sem, 16)))
        y, b = Y.take(), xg2.take()
        ws = [(w_gu, t[0], w_dn, t[1])]
        ts = down(turn_up(up(*turn_x(*gather(b, GROUPS + n, s_far[2])), ws)), ws, store(y, GROUPS + n))
        y.free = [y.was, pool(lambda e: e.memset(M.tick[:, PAIRS + n:PAIRS + n + 1], 0.0), scatter(y, GROUPS + n, s_far[3], y.was, ts))]

    def all_far():
        far(0)
        for n in range(1, MORE):
            g = Guarded((pe, act, dve, pool, sp))
            far(n)
            g.close(lambda r, n=n: r["more"] > n)
    guarded((pe, act, dve, pool, sp), lambda r: r["more"] > 0, all_far)

    free = [read[-1], pe.last()]
    gather2(i + 1)
    row2 = sb("row2", [128, D], F32, f"dn{(2 * i + 1) % N_DN}")
    stored.append(pool.last())
    yin = []
    for t_ in range(T2):
        if t_ == 2:
            E.load(2)
        b = Buf(sb(f"yin{t_}", [128, 2, D], F32, f"gu{(2 * i + t_ // 2) % N_GU}", 8192 * (t_ % 2)))
        b.tok = sp.dma(b.ap[:, :, :], M.ybuf[256 * t_:256 * t_ + 256, :].rearrange("(p c) n -> p c n", c=2), K.slot(f"s_yin{t_}"), free, stored)
        yin.append(b)
    t_row2 = sp.dma(row2[:, :], d["rows"][:, 1, :], K.slot("s_row2"), free)
    t_x = list(t_x)

    def rows_sum(t_):
        y = yin[t_].ap
        return pool(lambda e: e.tensor_tensor(y[:, 0, :], y[:, 0, :], y[:, 1, :], ALU.add), yin[t_].tok)

    def take_in(t_, t):
        x, y = xN[:, t_, :], yin[t_].ap[:, 0, :]
        t_x[t_] = dve(lambda e: e.tensor_tensor(x, x, y, ALU.add), t, t_x[t_])

    place = f"gu{2 * PAIRS % N_GU}"
    Yb = [Y.take(), Y.take()]
    parts = [[sb(f"y{j}{p}", [128, D], F32R, *((place, 4096 * c) if j else ("Y", 4096 * Yb[c].at))) for c, p in enumerate("hl")] for j in range(2)]
    read_parts = [[Yb[0].was, Yb[1].was], free]

    def owner(j, q):
        at = sb(f"own{j}", [128, T2, 128], F32R, place, 8192 + 2048 * j)
        for t_ in range(T2):
            t = q(lambda e, t_=t_: e.tensor_scalar(at[:, t_, :], M.iota[:, :], 128.0 * t_ - NONE, M.own[:, j:j + 1], ALU.add, ALU.is_equal), free, M.t_list)
        return at, t

    def split(j, q, t_y):
        hi, lo = parts[q]
        g = GROUPS - 4 + j

        def emit(c, s, tok):
            o, w = slice(512 * c, 512 * c + 512), M.w[:, g:g + 1]
            t_hi = act(lambda e: e.activation(hi[:, o], s.ap[:, :], ACT.Copy, scale=w), tok, read_parts[q], M.t_list)
            t_lo = dve(lambda e: e.scalar_tensor_tensor(lo[:, o], s.ap[:, :], w, hi[:, o].bitcast(F32), ALU.mult, ALU.subtract), tok, t_hi, read_parts[q])
            t_y.append((t_hi, t_lo))
            return t_lo
        return emit

    def add(s, t_, c, own, q, t_y, start=True, stop=True):
        at, t_at = own
        hi, lo = parts[q]
        o = slice(512 * c, 512 * c + 512)
        pe(lambda e: e.matmul(s.ap[:, :], at[:, t_, :], hi[:, o], start=start, stop=False), t_y[c][0], t_at, s.was if start else None, signal=False)
        return pe(lambda e: e.matmul(s.ap[:, :], at[:, t_, :], lo[:, o], start=False, stop=stop), t_y[c][1])

    def to_x(s, t_, c, tok):
        x = xN[:, t_, 512 * c:512 * c + 512]
        t_x[t_] = dve(lambda e: e.tensor_tensor(x, s.ap[:, :], x, ALU.add), tok, t_x[t_])
        s.free = [t_x[t_]]

    def own_second(p, j, q, ws):
        def body():
            own, t_y = owner(j, dve), []
            down(turn_up(up(*turn_x(*second[p].x), ws)), ws, split(j, q, t_y))
            for t_ in range(T2):
                for c in range(2):
                    s = bk.take()
                    tok = add(s, t_, c, own, q, t_y)
                    to_x(s, t_, c, tok)
            return tok
        read_parts[q] = [read_parts[q], guarded((pe, act, dve), crowded(p), body)]

    ms, rs = K.stat[:, 64:68], K.stat[:, 72:76]
    t_out = []

    def squares(t_):
        y = yin[t_].ap
        m, r = ms[:, t_:t_ + 1], rs[:, t_:t_ + 1]
        t = act(lambda e: e.activation(y[:, 0, :], xN[:, t_, :], ACT.Square, accum_out=m), t_x[t_])
        t = pool(lambda e: e.tensor_scalar(m, m, 1.0 / D, EPS, ALU.mult, ALU.add), t)
        return pool(lambda e: e.tensor_tensor(r, m, K.nhalf[:, 0:1], ALU.pow), t)

    def finish_apart(t_, t):
        x, y = xN[:, t_, :], yin[t_].ap[:, 1, :]
        t_y = pool(lambda e: e.tensor_tensor(y, x, row2[:, :], ALU.mult), t_x[t_], t_row2)
        t = act(lambda e: e.activation(y, y, ACT.Copy, scale=rs[:, t_:t_ + 1]), t, t_y)
        t_out.append(sp.dma(out[128 * t_:128 * t_ + 128, :], y, K.slot(f"s_out{t_}"), t))

    def finish(t_, t):
        x, y = xN[:, t_, :], yin[t_].ap[:, 1, :]
        t = dve(lambda e: e.scalar_tensor_tensor(y, x, rs[:, t_:t_ + 1], row2[:, :], ALU.mult, ALU.mult), t, t_row2)
        t_out.append(sp.dma(out[128 * t_:128 * t_ + 128, :], y, K.slot(f"s_out{t_}"), t))

    own = [owner(0, pool), owner(2, pool)]
    p, q = PAIRS - 2, PAIRS - 1
    ws, ws_last = E.pair(p), E.pair(q)
    t_y, t_y_last = [], []
    down(turn_up(up(*turn_x(*firsts[p]), ws)), ws, split(0, 0, t_y))
    x2 = Buf(sb("XT2", [128, KT, 128], F32, f"dn{(2 * p - 1) % N_DN}", 4096))
    x2.was = free
    x = turn_x(*firsts[q], x2)
    s_up = bk.hold()
    own_second(p, 1, 1, ws)
    gather2(q)
    own_second(q, 3, 1, ws_last)
    take_in(0, rows_sum(0))
    t = up(*x, ws_last, 0, s_up)
    bk.release(s_up)
    places = {}

    def begin_sum(t_):
        for c in range(2):
            places[t_, c] = bk.hold()
            add(places[t_, c], t_, c, own[0], 0, t_y, stop=False)

    def end_sum(t_):
        for c in range(2):
            s = places[t_, c]
            to_x(s, t_, c, add(s, t_, c, own[1], 1, t_y_last, start=False))
            bk.release(s)
    begin_sum(0)
    begin_sum(1)
    t = turn_up(t)
    take_in(1, rows_sum(1))
    down(t, ws_last, split(2, 1, t_y_last))
    rows = [rows_sum(2), rows_sum(3)]
    begin_sum(2)
    end_sum(0)
    finish_apart(0, squares(0))
    end_sum(1)
    t1 = squares(1)
    take_in(2, rows[0])
    begin_sum(3)
    end_sum(2)
    t2 = squares(2)
    take_in(3, rows[1])
    end_sum(3)
    finish(1, t1)
    t3 = squares(3)
    finish(2, t2)
    finish(3, t3)
    sp.ops.append((_tokens(t_out), lambda e: None, None))


def buckets(dist):
    d32 = np.maximum(dist, 1).astype(np.float32)
    large = 16 + (np.log(d32 / np.float32(16)) / np.float32(np.log(128.0)) * np.float32(16)).astype(np.int32)
    return np.where(dist < 16, dist, np.minimum(large, 31))


def host(inputs):
    f = lambda n: np.asarray(inputs[n])
    out = {}
    x, ctx = f("x")[0], f("ctx")[0]
    cols = lambda a, n: a.reshape(n, 128).T
    out["xc"] = np.concatenate([x.T.reshape(KT, 128, NX), ctx.T.reshape(KT, 128, NC)], 2).transpose(1, 0, 2)
    sm = np.zeros((128, SMALL["n"]), np.float32)

    def put(name, a):
        a = a.reshape(128, -1)
        sm[:, SMALL[name]:SMALL[name] + a.shape[1]] = a
    put("norm_w", np.concatenate([cols(a, 8) for a in f("norm_w")], 1))
    put("b_mod", np.concatenate([cols(a, 24) for a in f("b_mod")], 1))
    put("qn_w", np.concatenate([cols(a, 2) for a in f("q_norm_w")], 1))
    put("kvn_w", f("kv_norm_w").T)
    put("sc_w", f("sc_conv_w").reshape(2, 3, 2, 128).transpose(3, 0, 2, 1))
    put("cf_w", f("cf_conv_w").reshape(2, 31, 2, 128).transpose(3, 0, 2, 1))
    for n, s in (("cf_b", "cf_conv_b"), ("ln_w", "cf_ln_w"), ("ln_b", "cf_ln_b"), ("pw_b", "cf_pw_b")):
        put(n, np.concatenate([cols(a, 2) for a in f(s)], 1))
    for n, s in (("qh_w", "q_head_norm_w"), ("kh_w", "k_head_norm_w")):
        a = np.ones((128, 2), np.float32)
        a[0:64] = f(s)[:, 0:64].T
        put(n, a)
    put("c", np.stack([cols(f("c")[0], 8), cols(f("c_ctx"), 8)], 2))
    out["small"] = sm
    out["ident"] = np.eye(128, dtype=np.float32)
    pos = np.arange(NX)
    inv = (10000.0 ** (-np.arange(8, dtype=np.float64) / 8)).astype(np.float32)
    ang = np.concatenate([(pos // 64)[:, None].astype(np.float32) * inv, (pos % 64)[:, None].astype(np.float32) * inv], 1)
    cos, sin = np.cos(ang), np.sin(ang)
    lay = lambda a: a.reshape(4, 128, 32).transpose(1, 0, 2).astype(np.float32)
    out["ctab"] = lay(np.concatenate([cos, cos], 1))
    out["stab"] = lay(np.concatenate([-sin, sin], 1))
    rw = []
    for l in range(2):
        q, k = f("q_head_norm_w")[l, 64:], f("k_head_norm_w")[l, 64:]
        rw.append(np.stack([q, np.concatenate([q[16:], q[:16]]), k, np.concatenate([k[16:], k[:16]])]))
    out["rope_w"] = np.broadcast_to(np.stack(rw)[:, None], (2, 128, 4, 32))
    out["w_mod"] = f("w_mod").reshape(2, KT, 128, 3072)
    out["w_mod0"] = f("w_mod")[0][:, 0:2048].reshape(KT, 128, 2, 4, 256).transpose(3, 1, 0, 2, 4).reshape(4, 128, KT, 512)
    w = f("w_in")
    tile = lambda l, c: w[l][:, c:c + 128].reshape(KT, 128, 128).transpose(1, 0, 2).reshape(128, 1024)
    out["w_in"] = np.stack([np.stack([tile(l, COLS[n] + 128 * i) for n, i in TILES]) for l in range(2)])
    out["w_kr"] = np.stack([w[l][:, 384:416].reshape(KT, 128, 32).transpose(1, 0, 2) for l in range(2)])
    out["w_uq"] = f("w_uq").reshape(2, 2, 128, 768).transpose(0, 2, 1, 3)
    kv = f("w_ukv").reshape(2, 128, HEADS, 128)
    out["w_ukv"] = np.concatenate([kv[..., :64].reshape(2, 128, 512), kv[..., 64:].reshape(2, 128, 512)], 2)
    out["pw"] = f("cf_pw_w").reshape(2, 2, 128, 256).transpose(0, 2, 1, 3)
    out["w_out"] = f("w_out").reshape(2, KT, 128, KT, 128).transpose(0, 3, 2, 1, 4).reshape(2, KT, 128, 1024)
    s2 = np.zeros((128, SMALL2["n"]), np.float32)
    s2[:, 0:8] = cols(f("attn_norm_2")[0], 8)
    s2[:, 8:12] = cols(f("out_norm_dil_2")[0], 4)
    s2[:, 12:16] = cols(f("out_norm_fox_2")[0], 4)
    s2[0:8, 16] = f("b_forget_2")[0]
    s2[:, 17:25] = cols(f("ffn_norm_2")[0], 8)
    out["small2"] = s2
    w = f("w_in_2")[0]
    t2 = lambda c: w[:, c:c + 128].reshape(KT, 128, 128).transpose(1, 0, 2).reshape(128, 1024)
    v2 = lambda c: [w[256 * k:256 * k + 256, c:c + 512].reshape(2, 128, 512).transpose(1, 0, 2).reshape(128, 1024) for k in range(4)]
    tiles = v2(1024) + v2(2560)
    for p in range(8):
        o = 128 * p if p < 4 else 1536 + 128 * (p - 4)
        tiles += [t2(o), t2(o + 512)]
    out["w_in2"] = np.stack(tiles)
    out["w_out2"] = f("w_out_2").reshape(KT, 128, 1024)
    out["rows"] = np.broadcast_to(np.stack([f("ffn_norm_2")[0], f("final_norm_2")]), (128, 2, 1024))
    w_r = np.concatenate([f("w_router_group_2")[0], f("w_router_expert_2")[0]], 1)
    out["w_r"] = w_r.reshape(KT, 128, 36).transpose(1, 0, 2)
    gu = np.concatenate([f("w_expert_gate_2")[0], f("w_expert_up_2")[0]], 2)
    out["w_gu"] = gu.reshape(NE, KT, 128, 2 * DE).transpose(0, 2, 1, 3)
    out["w_dn"] = f("w_expert_down_2")[0].reshape(NE, 2, 128, D).transpose(0, 2, 1, 3)
    rc = np.zeros((128, RC["all"]), np.float32)
    e = np.arange(NE)
    rc[:, 0:4] = 4 - np.arange(4)
    rc[:, 4:36] = 32 - e
    rc[:, 36:40] = 128 * np.arange(1, 5) + 0.5
    base = 256 * (e // 2) + 64 * (e % 2)
    rc[:, RC["base"]:RC["base"] + NE] = base / 128
    rc[:, RC["past64"]:RC["past64"] + NE] = base + 63.5
    rc[:, RC["past128"]:RC["past128"] + NE] = base + 127.5
    rc[:, RC["over"]:RC["over"] + NE] = 128 * GROUPS - 128 - 64 - base - 0
    tok = 128 * np.arange(T2)[None, :] + np.arange(128)[:, None]
    ids = np.zeros((128, 2, T2, 2), np.float32)
    ids[..., 0] = tok[:, None, :]
    ids[..., 1] = 2 * tok[:, None, :] + np.arange(2)[:, None]
    rc[:, RC["ids"]:RC["ids"] + 16] = ids.reshape(128, 16) - NONE
    rc[:, RC["pow2"]:RC["pow2"] + PAIRS] = 2.0 ** np.arange(PAIRS)
    rc[:, RC["nth"]:RC["nth"] + GROUPS + MORE] = np.arange(GROUPS + MORE)
    rc[:, RC["tri"]:RC["tri"] + 128] = np.arange(128)[:, None] < np.arange(128)[None, :]
    out["iota"] = np.broadcast_to(np.arange(128, dtype=np.float32), (128, 128))
    rc[:, RC["bias"]:RC["bias"] + 36] = np.concatenate([f("b_router_group_2")[0], f("b_router_expert_2")[0]])
    out["rc"] = rc
    out["w_f"] = w[:, 3072:3080].reshape(KT, 128, 8).transpose(1, 0, 2)
    sel = np.zeros((128, 8, 128), np.float32)
    for h in range(8):
        sel[h, h] = sel[32 + h, h] = 1
    out["sel"] = sel.reshape(128, 1024)
    dist = np.arange(128)[:, None] + 384 - np.arange(512)[None, :]
    n = (dist <= 128) * 1 + (dist % 4 == 0) + (dist % 16 == 0)
    ok = (dist >= 0) & (n > 0)
    out["lnn"] = np.where(ok, np.log(np.maximum(n, 1)), -BIG).astype(np.float32)
    out["causal"] = np.where(dist >= 0, 0, -BIG).astype(np.float32)
    out["bias"] = f("rel_bias_2")[buckets(np.maximum(dist, 0))].transpose(2, 0, 1)
    return {k: np.ascontiguousarray(v) for k, v in out.items()}


def play(K):
    with K.nc.Block() as block:
        block.sync(K.sp.play)
        block.tensor(K.pe.play)
        block.vector(K.dve.play)
        block.scalar(K.act.play)
        block.gpsimd(K.pool.play)


def program(nc, dram, out):
    with ExitStack() as ctx:
        K = setup(nc, ctx, dram)
        K.ctx = ctx
        second_block(K, *first_block(K), out)
        play(K)


def kernel(**inputs):
    import concourse.bacc as _bacc
    from concourse.bass_utils import run_bass_kernel_spmd as _run

    nc = _bacc.Bacc("TRN2", target_bir_lowering=False, num_devices=1)
    arrays, dram = {}, {}
    for name, a in host(inputs).items():
        arrays[f"in_{name}_dram"] = a
        dram[name] = nc.dram_tensor(f"in_{name}_dram", a.shape, mybir.dt.from_np(a.dtype), kind="ExternalInput").ap()
    out = nc.dram_tensor("out_0_dram", (NX, D), F32, kind="ExternalOutput").ap()
    program(nc, dram, out)
    r = _run(nc, [arrays], core_ids=[0])
    return r.results[0]["out_0_dram"].reshape(1, NX, D)
```
